# Optimizing a Trainium2 kernel written in Bass

```python
import math
import jax, jax.numpy as jnp
from jax import lax
import numpy as np
import jax
import jax.numpy as jnp

D_MODEL = 1024
BATCH = 1
SEQ = 256
DEPTH = 1

GDN_HEADS = 4
GDN_HEAD_DIM = 128
MLSTM_HEADS = 4
MLSTM_HEAD_DIM = 128
GDN_W = GDN_HEADS * GDN_HEAD_DIM
MLSTM_W = MLSTM_HEADS * MLSTM_HEAD_DIM
CONV_WIDTH = 4
GDN_CHUNK = 64
MLSTM_CHUNK = 64
PROJ_SIZES = (3 * GDN_W, GDN_W, GDN_HEADS, GDN_HEADS,
              2 * MLSTM_W, MLSTM_W, MLSTM_W, MLSTM_HEADS, MLSTM_HEADS)
PROJ_DIM = sum(PROJ_SIZES)
MEM_TOKENS = 256
XA_HEADS = 4
XA_HEAD_DIM = D_MODEL // XA_HEADS
PEER_HEADS = 8
PEER_N_KEYS = 128
PEER_N_EXPERTS = PEER_N_KEYS * PEER_N_KEYS
PEER_TOPK = 16
PEER_HALF = 128
PEER_QUERY_DIM = 2 * PEER_HALF
PEER_BLOCK = 128
NORM_EPS = 1e-6


def rmsnorm(x, w):
    xf = x.astype(jnp.float32)
    y = xf * lax.rsqrt(jnp.mean(xf * xf, axis=-1, keepdims=True) + NORM_EPS)
    return (y * w.astype(jnp.float32)).astype(x.dtype)

def l2norm(x):
    return x * lax.rsqrt(jnp.sum(x * x, axis=-1, keepdims=True) + NORM_EPS)

def causal_dwconv(x, w):
    kw = w.shape[0]
    return lax.conv_general_dilated(x, w[:, None, :].astype(x.dtype), window_strides=(1,),
                                    padding=[(kw - 1, 0)],
                                    dimension_numbers=('NWC', 'WIO', 'NWC'),
                                    feature_group_count=x.shape[-1])

def to_chunks(t, nc, lc):
    b, h = t.shape[0], t.shape[1]
    return jnp.moveaxis(t.reshape(b, h, nc, lc, *t.shape[3:]), 2, 0)

def gated_delta_rule(q, k, v, log_alpha, beta):
    b, nh, s, dk = q.shape
    dv = v.shape[-1]
    lc = GDN_CHUNK
    nc = s // lc
    q = q * dk ** -0.5
    q, k, v, log_alpha, beta = (to_chunks(t, nc, lc) for t in (q, k, v, log_alpha, beta))
    gc = jnp.cumsum(log_alpha, axis=-1)
    idx = jnp.arange(lc)
    causal = idx[:, None] >= idx[None, :]
    strict = idx[:, None] > idx[None, :]
    decay = jnp.exp(jnp.where(causal, gc[..., :, None] - gc[..., None, :], -jnp.inf))
    kb = k * beta[..., None]
    a = jnp.where(strict, jnp.einsum('nbhid,nbhjd->nbhij', kb, k) * decay, 0.0)
    eye = jnp.eye(lc, dtype=q.dtype)
    t_inv = lax.linalg.triangular_solve(a + eye, jnp.broadcast_to(eye, a.shape), left_side=True,
                                        lower=True, unit_diagonal=True)
    u = t_inv @ (v * beta[..., None])
    w = t_inv @ (kb * jnp.exp(gc)[..., None])
    qk = jnp.einsum('nbhid,nbhjd->nbhij', q, k) * decay
    q_dec = q * jnp.exp(gc)[..., None]
    k_dec = k * jnp.exp(gc[..., -1:] - gc)[..., None]
    g_last = jnp.exp(gc[..., -1])

    def step(state, xs):
        u_c, w_c, qk_c, qd_c, kd_c, gl_c = xs
        v_new = u_c - w_c @ state
        o = qd_c @ state + qk_c @ v_new
        state = state * gl_c[..., None, None] + jnp.einsum('bhld,bhle->bhde', kd_c, v_new)
        return state, o

    s0 = jnp.zeros((b, nh, dk, dv), q.dtype)
    _, o = lax.scan(step, s0, (u, w, qk, q_dec, k_dec, g_last))
    return jnp.moveaxis(o, 0, 2).reshape(b, nh, s, dv)

def mlstm_chunkwise(q, k, v, log_i, log_f):
    b, nh, s, dk = q.shape
    dv = v.shape[-1]
    lc = MLSTM_CHUNK
    nc = s // lc
    k = k * dk ** -0.5
    q, k, v, log_i, log_f = (to_chunks(t, nc, lc) for t in (q, k, v, log_i, log_f))
    bcum = jnp.cumsum(log_f, axis=-1)
    idx = jnp.arange(lc)
    causal = idx[:, None] >= idx[None, :]
    d_intra = jnp.where(causal, bcum[..., :, None] - bcum[..., None, :] + log_i[..., None, :], -jnp.inf)
    d_last = bcum[..., -1:] - bcum + log_i
    qk = jnp.einsum('nbhid,nbhjd->nbhij', q, k)

    def step(carry, xs):
        c, n, m = carry
        q_c, k_c, v_c, b_c, d_c, qk_c, dl_c = xs
        inter = b_c + m[..., None]
        m_t = jnp.maximum(inter, jnp.max(d_c, axis=-1))
        p = qk_c * jnp.exp(d_c - m_t[..., None])
        sc = jnp.exp(inter - m_t)
        num = sc[..., None] * (q_c @ c) + p @ v_c
        den = sc * jnp.einsum('bhld,bhd->bhl', q_c, n) + jnp.sum(p, axis=-1)
        h = num / jnp.maximum(jnp.abs(den), jnp.exp(-m_t))[..., None]
        b_last = b_c[..., -1]
        m_new = jnp.maximum(b_last + m, jnp.max(dl_c, axis=-1))
        wgt = jnp.exp(dl_c - m_new[..., None])
        dec = jnp.exp(b_last + m - m_new)
        c = dec[..., None, None] * c + jnp.einsum('bhld,bhle->bhde', k_c * wgt[..., None], v_c)
        n = dec[..., None] * n + jnp.einsum('bhld,bhl->bhd', k_c, wgt)
        return (c, n, m_new), h

    init = (jnp.zeros((b, nh, dk, dv), q.dtype), jnp.zeros((b, nh, dk), q.dtype),
            jnp.zeros((b, nh), q.dtype))
    _, hs = lax.scan(step, init, (q, k, v, bcum, d_intra, qk, d_last))
    return jnp.moveaxis(hs, 0, 2).reshape(b, nh, s, dv)

def hybrid_mixer(h, w_in, gdn_conv_w, gdn_a_log, gdn_dt_bias, gdn_norm_w,
                 mlstm_conv_w, mlstm_i_bias, mlstm_f_bias, mlstm_norm_w, w_out):
    b, s, _ = h.shape
    f32 = jnp.float32
    proj = (h @ w_in).astype(f32)
    cuts = np.cumsum(PROJ_SIZES)[:-1].tolist()
    g_qkv, g_z, g_a, g_b, m_qk, m_v, m_o, m_i, m_f = jnp.split(proj, cuts, axis=-1)

    def heads(t, nh):
        return t.reshape(b, s, nh, -1).transpose(0, 2, 1, 3)

    g_qkv = jax.nn.silu(causal_dwconv(g_qkv, gdn_conv_w.astype(f32)))
    gq, gk, gv = (heads(t, GDN_HEADS) for t in jnp.split(g_qkv, 3, axis=-1))
    gq, gk = l2norm(gq), l2norm(gk)
    log_alpha = -jnp.exp(gdn_a_log.astype(f32)) * jax.nn.softplus(g_a + gdn_dt_bias.astype(f32))
    beta = jax.nn.sigmoid(g_b)
    go = gated_delta_rule(gq, gk, gv, log_alpha.transpose(0, 2, 1), beta.transpose(0, 2, 1))
    go = rmsnorm(go.transpose(0, 2, 1, 3), gdn_norm_w) * jax.nn.silu(
        g_z.reshape(b, s, GDN_HEADS, GDN_HEAD_DIM))

    m_qk = jax.nn.silu(causal_dwconv(m_qk, mlstm_conv_w.astype(f32)))
    mq, mk = (heads(t, MLSTM_HEADS) for t in jnp.split(m_qk, 2, axis=-1))
    mv = heads(m_v, MLSTM_HEADS)
    log_i = (m_i + mlstm_i_bias.astype(f32)).transpose(0, 2, 1)
    log_f = jax.nn.log_sigmoid(m_f + mlstm_f_bias.astype(f32)).transpose(0, 2, 1)
    mh = mlstm_chunkwise(mq, mk, mv, log_i, log_f)
    mh = rmsnorm(mh.transpose(0, 2, 1, 3), mlstm_norm_w.reshape(MLSTM_HEADS, MLSTM_HEAD_DIM)) * \
        jax.nn.sigmoid(m_o.reshape(b, s, MLSTM_HEADS, MLSTM_HEAD_DIM))

    mixed = jnp.concatenate([go.reshape(b, s, GDN_W), mh.reshape(b, s, MLSTM_W)], axis=-1)
    return mixed.astype(h.dtype) @ w_out

def memory_cross_attention(h, m, wq, wkv, wo):
    b, s, _ = h.shape
    q = (h @ wq).reshape(b, s, XA_HEADS, XA_HEAD_DIM)
    k, v = jnp.split(m @ wkv, 2, axis=-1)
    k = k.reshape(b, -1, XA_HEADS, XA_HEAD_DIM)
    v = v.reshape(b, -1, XA_HEADS, XA_HEAD_DIM)
    scores = jnp.einsum('bshd,bmhd->bhsm', q, k).astype(jnp.float32) * XA_HEAD_DIM ** -0.5
    p = jax.nn.softmax(scores, axis=-1).astype(v.dtype)
    o = jnp.einsum('bhsm,bmhd->bshd', p, v).reshape(b, s, D_MODEL)
    return o @ wo

def peer_ffn(h, wq, sub_keys, u_table, v_table):
    b, s, d = h.shape
    t = b * s
    hf = h.reshape(t, d)
    q = (hf @ wq).reshape(t, PEER_HEADS, 2, PEER_HALF)
    sc = jnp.einsum('thpd,hpnd->thpn', q, sub_keys).astype(jnp.float32)
    top_v, top_i = lax.top_k(sc, PEER_TOPK)
    kk = PEER_TOPK * PEER_TOPK
    cand = (top_v[:, :, 0, :, None] + top_v[:, :, 1, None, :]).reshape(t, PEER_HEADS, kk)
    cand_id = (top_i[:, :, 0, :, None] * PEER_N_KEYS + top_i[:, :, 1, None, :]).reshape(t, PEER_HEADS, kk)
    best_v, best_pos = lax.top_k(cand, PEER_TOPK)
    expert_id = jnp.take_along_axis(cand_id, best_pos, axis=-1)
    gate = jax.nn.softmax(best_v, axis=-1)
    nb = t // PEER_BLOCK

    def block(args):
        xb, eb, gb = args
        u = jnp.take(u_table, eb, axis=0)
        act = jax.nn.gelu(jnp.einsum('phkd,pd->phk', u, xb).astype(jnp.float32), approximate=False)
        wgt = (gb * act).astype(v_table.dtype)
        return jnp.einsum('phk,phkd->pd', wgt, jnp.take(v_table, eb, axis=0))

    out = lax.map(block, (hf.reshape(nb, PEER_BLOCK, d),
                          expert_id.reshape(nb, PEER_BLOCK, PEER_HEADS, PEER_TOPK),
                          gate.reshape(nb, PEER_BLOCK, PEER_HEADS, PEER_TOPK)))
    return out.reshape(b, s, d).astype(h.dtype)

def first_inputs(seed: int = 0) -> dict:
    key = jax.random.key(seed)
    ks = jax.random.split(key, 24)
    f32 = jnp.float32
    L, D = DEPTH, D_MODEL

    def nrm(k, shape, scale):
        return jax.random.normal(k, shape, f32) * scale

    def gain(k, shape):
        return 1.0 + 0.01 * jax.random.normal(k, shape, f32)

    dt = jnp.exp(jax.random.uniform(ks[6], (L, GDN_HEADS), f32, math.log(1e-3), math.log(1e-1)))
    return {
        'x': nrm(ks[0], (BATCH, SEQ, D), 1.0),
        'mem': nrm(ks[1], (BATCH, MEM_TOKENS, D), 1.0),
        'norm_mix_w': gain(ks[2], (L, D)),
        'w_in': nrm(ks[3], (L, D, PROJ_DIM), D ** -0.5),
        'gdn_conv_w': nrm(ks[4], (L, CONV_WIDTH, 3 * GDN_W), CONV_WIDTH ** -0.5),
        'gdn_a_log': jnp.log(jax.random.uniform(ks[5], (L, GDN_HEADS), f32, 1.0, 16.0)),
        'gdn_dt_bias': dt + jnp.log(-jnp.expm1(-dt)),
        'gdn_norm_w': gain(ks[7], (L, GDN_HEAD_DIM)),
        'mlstm_conv_w': nrm(ks[8], (L, CONV_WIDTH, 2 * MLSTM_W), CONV_WIDTH ** -0.5),
        'mlstm_i_bias': nrm(ks[9], (L, MLSTM_HEADS), 0.5),
        'mlstm_f_bias': jax.random.uniform(ks[10], (L, MLSTM_HEADS), f32, 3.0, 6.0),
        'mlstm_norm_w': gain(ks[11], (L, MLSTM_W)),
        'w_out': nrm(ks[12], (L, GDN_W + MLSTM_W, D), (GDN_W + MLSTM_W) ** -0.5),
        'norm_xa_w': gain(ks[13], (L, D)),
        'norm_mem_w': gain(ks[14], (L, D)),
        'xa_wq': nrm(ks[15], (L, D, D), D ** -0.5),
        'xa_wkv': nrm(ks[16], (L, D, 2 * D), D ** -0.5),
        'xa_wo': nrm(ks[17], (L, D, D), D ** -0.5),
        'norm_ffn_w': gain(ks[18], (L, D)),
        'peer_wq': nrm(ks[19], (L, D, PEER_HEADS * PEER_QUERY_DIM), D ** -0.5),
        'peer_sub_keys': nrm(ks[20], (L, PEER_HEADS, 2, PEER_N_KEYS, PEER_HALF), PEER_HALF ** -0.5),
        'peer_u': nrm(ks[21], (L, PEER_N_EXPERTS, D), D ** -0.5),
        'peer_v': nrm(ks[22], (L, PEER_N_EXPERTS, D), (PEER_HEADS * PEER_TOPK) ** -0.5),
        'norm_final_w': gain(ks[23], (D,)),
    }

def first_block(x, mem, norm_mix_w, w_in, gdn_conv_w, gdn_a_log, gdn_dt_bias, gdn_norm_w,
              mlstm_conv_w, mlstm_i_bias, mlstm_f_bias, mlstm_norm_w, w_out,
              norm_xa_w, norm_mem_w, xa_wq, xa_wkv, xa_wo,
              norm_ffn_w, peer_wq, peer_sub_keys, peer_u, peer_v, norm_final_w):
    for l in range(DEPTH):
        x = x + hybrid_mixer(rmsnorm(x, norm_mix_w[l]), w_in[l], gdn_conv_w[l], gdn_a_log[l],
                             gdn_dt_bias[l], gdn_norm_w[l], mlstm_conv_w[l], mlstm_i_bias[l],
                             mlstm_f_bias[l], mlstm_norm_w[l], w_out[l])
        x = x + memory_cross_attention(rmsnorm(x, norm_xa_w[l]), rmsnorm(mem, norm_mem_w[l]),
                                       xa_wq[l], xa_wkv[l], xa_wo[l])
        x = x + peer_ffn(rmsnorm(x, norm_ffn_w[l]), peer_wq[l], peer_sub_keys[l], peer_u[l], peer_v[l])
    return rmsnorm(x, norm_final_w)


DEPTH_2 = 2

N_A_LAYERS = DEPTH_2 // 2
N_B_LAYERS = DEPTH_2 - N_A_LAYERS
DN_ALPHA = (2.0 * DEPTH_2) ** 0.25
DN_BETA = (8.0 * DEPTH_2) ** -0.25
LN_EPS = 1e-5
FFN_DIM = int(math.ceil(8 * D_MODEL / 3 / 256)) * 256
SGU_HIDDEN = 4 * D_MODEL
SGU_HALF = SGU_HIDDEN // 2
SGU_GROUPS = 8
SGU_GROUP_DIM = SGU_HALF // SGU_GROUPS
SGU_CHUNK = 128
N_HEADS = 16
N_KV_GROUPS = 4
HEADS_PER_GROUP = N_HEADS // N_KV_GROUPS
HEAD_DIM = D_MODEL // N_HEADS
CMP_LEN = 32
CMP_STRIDE = 16
PHI_HIDDEN = 256
SEL_LEN = 64
SEL_TOP_N = 8
N_LOCAL_BLOCKS = 2
WINDOW = 512
NSA_Q_BLOCK = 32
N_KV_SLOTS = 6
REL_BUCKETS = 32
REL_MAX_DIST = 128
NEG = -1e30


def layer_norm(x, g, b):
    xf = x.astype(jnp.float32)
    mu = jnp.mean(xf, axis=-1, keepdims=True)
    var = jnp.mean(jnp.square(xf - mu), axis=-1, keepdims=True)
    y = (xf - mu) * lax.rsqrt(var + LN_EPS)
    return (y * g.astype(jnp.float32) + b.astype(jnp.float32)).astype(x.dtype)

def post_norm(x, sub, g, b):
    return layer_norm(DN_ALPHA * x + sub, g, b)

def swiglu(x, w1, w3, w2):
    return (jax.nn.silu(x @ w1) * (x @ w3)) @ w2

def rel_bucket(dist):
    n = jnp.maximum(dist, 0)
    max_exact = REL_BUCKETS // 2
    nf = jnp.maximum(n, 1).astype(jnp.float32)
    large = max_exact + (jnp.log(nf / max_exact) / math.log(REL_MAX_DIST / max_exact)
                         * (REL_BUCKETS - max_exact)).astype(jnp.int32)
    return jnp.where(n < max_exact, n, jnp.minimum(large, REL_BUCKETS - 1))

def chunked_sgu_mixer(x, w_in, ln_g, ln_b, w_s, b_s, w_out):
    B, S, _ = x.shape
    z = jax.nn.gelu(x @ w_in, approximate=False)
    u, v = jnp.split(z, 2, axis=-1)
    v = layer_norm(v, ln_g, ln_b)
    n_chunks = S // SGU_CHUNK
    v = v.reshape(B, n_chunks, SGU_CHUNK, SGU_GROUPS, SGU_GROUP_DIM)
    causal = jnp.tril(jnp.ones((SGU_CHUNK, SGU_CHUNK), dtype=bool))
    w = jnp.where(causal[None], w_s, jnp.zeros_like(w_s))
    mixed = jnp.einsum('gts,bnsgc->bntgc', w, v) + b_s.T[None, None, :, :, None]
    return (u * mixed.reshape(B, S, SGU_HALF)) @ w_out

def compress(kv, pe, w1, b1, w2):
    B, S, G, Dh = kv.shape
    n_sub = CMP_LEN // CMP_STRIDE
    n_chunks = S // CMP_STRIDE
    n_cmp = n_chunks - n_sub + 1
    chunks = kv.reshape(B, n_chunks, CMP_STRIDE, G, Dh)
    blocks = jnp.concatenate([chunks[:, i:i + n_cmp] for i in range(n_sub)], axis=2)
    blocks = blocks + pe[None, None, :, None, :]
    flat = blocks.transpose(0, 1, 3, 2, 4).reshape(B, n_cmp, G, CMP_LEN * Dh)
    return jax.nn.gelu(flat @ w1 + b1, approximate=False) @ w2

def nsa_shared_kv(h, kv_w, cmp_pe, cmp_w1, cmp_b1, cmp_w2):
    B, S, _ = h.shape
    kv = (h @ kv_w).reshape(B, S, N_KV_SLOTS, N_KV_GROUPS, HEAD_DIM)
    k_cmp = compress(kv[:, :, 0], cmp_pe[0], cmp_w1[0], cmp_b1[0], cmp_w2[0])
    v_cmp = compress(kv[:, :, 1], cmp_pe[1], cmp_w1[1], cmp_b1[1], cmp_w2[1])
    n_sel = S // SEL_LEN
    k_sel = kv[:, :, 2].reshape(B, n_sel, SEL_LEN, N_KV_GROUPS, HEAD_DIM).transpose(0, 3, 1, 2, 4)
    v_sel = kv[:, :, 3].reshape(B, n_sel, SEL_LEN, N_KV_GROUPS, HEAD_DIM).transpose(0, 3, 1, 2, 4)
    pad = ((0, 0), (WINDOW, 0), (0, 0), (0, 0))
    k_win = jnp.pad(kv[:, :, 4], pad)
    v_win = jnp.pad(kv[:, :, 5], pad)
    return (k_cmp, v_cmp, k_sel, v_sel, k_win, v_win)

def masked_softmax(s, mask):
    p = jax.nn.softmax(jnp.where(mask, s, NEG), axis=-1)
    return jnp.where(mask, p, 0.0)

def cmp_to_sel_overlap(n_cmp, n_sel):
    i = np.arange(n_cmp)[:, None]
    j = np.arange(n_sel)[None, :]
    ov = (i * CMP_STRIDE < (j + 1) * SEL_LEN) & (i * CMP_STRIDE + CMP_LEN > j * SEL_LEN)
    return ov.astype(np.float32)

def nsa_mixer(h, shared, w_qg, w_o, rel_table):
    k_cmp, v_cmp, k_sel, v_sel, k_win, v_win = shared
    B, S, _ = h.shape
    G, HG, Dh, QB = N_KV_GROUPS, HEADS_PER_GROUP, HEAD_DIM, NSA_Q_BLOCK
    qg = h @ w_qg
    q = qg[..., :N_HEADS * Dh].reshape(B, S, G, HG, Dh) * (Dh ** -0.5)
    gates = jax.nn.sigmoid(qg[..., N_HEADS * Dh:]).reshape(B, S, G, HG, 3)
    n_qb = S // QB
    n_cmp = k_cmp.shape[1]
    n_sel = k_sel.shape[2]
    n_top = min(SEL_TOP_N, n_sel)
    overlap = jnp.asarray(cmp_to_sel_overlap(n_cmp, n_sel))
    cmp_end = jnp.arange(n_cmp, dtype=jnp.int32) * CMP_STRIDE + (CMP_LEN - 1)
    sel_ids = jnp.arange(n_sel, dtype=jnp.int32)
    b_idx = jnp.arange(B)[:, None, None]
    g_idx = jnp.arange(G)[None, :, None]
    g_idx4 = jnp.arange(G)[None, :, None, None]
    tbl_g = rel_table.reshape(REL_BUCKETS, G, HG)

    def head_bias(dist):
        return rel_table[rel_bucket(dist)].reshape(dist.shape + (G, HG)).transpose(2, 3, 0, 1).astype(jnp.float32)

    def block(args):
        q_b, g_b, q0 = args
        t = q0 + jnp.arange(QB, dtype=jnp.int32)
        dist_c = t[:, None] - cmp_end[None, :]
        mask_c = dist_c >= 0
        s_c = jnp.einsum('bqghd,bngd->bghqn', q_b, k_cmp).astype(jnp.float32) + head_bias(dist_c)
        p_c = masked_softmax(s_c, mask_c)
        o_c = jnp.einsum('bghqn,bngd->bqghd', p_c.astype(v_cmp.dtype), v_cmp)
        imp = jnp.einsum('bghqn,nj->bgqj', p_c, overlap)
        cur = t // SEL_LEN
        valid = sel_ids[None, :] <= cur[:, None]
        forced = valid & ((sel_ids[None, :] == 0) | (sel_ids[None, :] > cur[:, None] - N_LOCAL_BLOCKS))
        imp = jnp.where(forced, -NEG, jnp.where(valid, imp, NEG))
        _, idx = lax.top_k(imp, n_top)
        flat = idx.reshape(B, G, QB * n_top)
        k_g = k_sel[b_idx, g_idx, flat].reshape(B, G, QB, n_top * SEL_LEN, Dh)
        v_g = v_sel[b_idx, g_idx, flat].reshape(B, G, QB, n_top * SEL_LEN, Dh)
        pos = (idx[..., None] * SEL_LEN + jnp.arange(SEL_LEN, dtype=jnp.int32)).reshape(B, G, QB, n_top * SEL_LEN)
        dist_s = t[None, None, :, None] - pos
        mask_s = (dist_s >= 0)[:, :, None]
        bias_s = tbl_g[rel_bucket(dist_s), g_idx4].transpose(0, 1, 4, 2, 3).astype(jnp.float32)
        s_s = jnp.einsum('bqghd,bgqkd->bghqk', q_b, k_g).astype(jnp.float32) + bias_s
        p_s = masked_softmax(s_s, mask_s)
        o_s = jnp.einsum('bghqk,bgqkd->bqghd', p_s.astype(v_g.dtype), v_g)
        k_w = lax.dynamic_slice_in_dim(k_win, q0, WINDOW + QB, axis=1)
        v_w = lax.dynamic_slice_in_dim(v_win, q0, WINDOW + QB, axis=1)
        pos_w = q0 - WINDOW + jnp.arange(WINDOW + QB, dtype=jnp.int32)
        dist_w = t[:, None] - pos_w[None, :]
        mask_w = (dist_w >= 0) & (dist_w < WINDOW) & (pos_w[None, :] >= 0)
        s_w = jnp.einsum('bqghd,bkgd->bghqk', q_b, k_w).astype(jnp.float32) + head_bias(dist_w)
        p_w = masked_softmax(s_w, mask_w)
        o_w = jnp.einsum('bghqk,bkgd->bqghd', p_w.astype(v_w.dtype), v_w)
        return g_b[..., 0:1] * o_c + g_b[..., 1:2] * o_s + g_b[..., 2:3] * o_w

    q_blocks = q.reshape(B, n_qb, QB, G, HG, Dh).swapaxes(0, 1)
    g_blocks = gates.reshape(B, n_qb, QB, G, HG, 3).swapaxes(0, 1)
    starts = jnp.arange(n_qb, dtype=jnp.int32) * QB
    out = lax.map(block, (q_blocks, g_blocks, starts))
    out = out.swapaxes(0, 1).reshape(B, S, N_HEADS * Dh)
    return out @ w_o

def second_inputs(seed: int = 0) -> dict:
    key = jax.random.key(seed)
    ks = jax.random.split(key, 24)
    f32 = jnp.float32

    def nrm(k, shape, scale):
        return jax.random.normal(k, shape, f32) * scale

    kv_scale = jnp.array([1.0, DN_BETA, 1.0, DN_BETA, 1.0, DN_BETA], f32)[None, :, None]
    kv_w = (nrm(ks[13], (D_MODEL, N_KV_SLOTS, N_KV_GROUPS * HEAD_DIM), D_MODEL ** -0.5) * kv_scale)
    return {
        'x': nrm(ks[0], (BATCH, SEQ, D_MODEL), 1.0),
        'rel_table': nrm(ks[1], (REL_BUCKETS, N_HEADS), 0.5),
        'ln_g': 1.0 + nrm(ks[2], (DEPTH_2, 3, D_MODEL), 0.05),
        'ln_b': nrm(ks[3], (DEPTH_2, 3, D_MODEL), 0.02),
        'ffn_w1': nrm(ks[4], (DEPTH_2, 2, D_MODEL, FFN_DIM), D_MODEL ** -0.5),
        'ffn_w3': nrm(ks[5], (DEPTH_2, 2, D_MODEL, FFN_DIM), D_MODEL ** -0.5),
        'ffn_w2': nrm(ks[6], (DEPTH_2, 2, FFN_DIM, D_MODEL), DN_BETA * FFN_DIM ** -0.5),
        'sgu_w_in': nrm(ks[7], (N_A_LAYERS, D_MODEL, SGU_HIDDEN), D_MODEL ** -0.5),
        'sgu_ln_g': 1.0 + nrm(ks[8], (N_A_LAYERS, SGU_HALF), 0.05),
        'sgu_ln_b': nrm(ks[9], (N_A_LAYERS, SGU_HALF), 0.02),
        'sgu_w_s': nrm(ks[10], (N_A_LAYERS, SGU_GROUPS, SGU_CHUNK, SGU_CHUNK), 0.05),
        'sgu_b_s': 1.0 + nrm(ks[11], (N_A_LAYERS, SGU_GROUPS, SGU_CHUNK), 0.05),
        'sgu_w_out': nrm(ks[12], (N_A_LAYERS, SGU_HALF, D_MODEL), DN_BETA * SGU_HALF ** -0.5),
        'kv_w': kv_w.reshape(D_MODEL, N_KV_SLOTS * N_KV_GROUPS * HEAD_DIM),
        'cmp_pe': nrm(ks[14], (2, CMP_LEN, HEAD_DIM), 0.5),
        'cmp_w1': nrm(ks[15], (2, CMP_LEN * HEAD_DIM, PHI_HIDDEN), (CMP_LEN * HEAD_DIM) ** -0.5),
        'cmp_b1': nrm(ks[16], (2, PHI_HIDDEN), 0.02),
        'cmp_w2': nrm(ks[17], (2, PHI_HIDDEN, HEAD_DIM), PHI_HIDDEN ** -0.5),
        'nsa_w_qg': nrm(ks[18], (N_B_LAYERS, D_MODEL, N_HEADS * HEAD_DIM + 3 * N_HEADS), D_MODEL ** -0.5),
        'nsa_w_o': nrm(ks[19], (N_B_LAYERS, N_HEADS * HEAD_DIM, D_MODEL), DN_BETA * (N_HEADS * HEAD_DIM) ** -0.5),
    }

def second_block(x, rel_table, ln_g, ln_b, ffn_w1, ffn_w3, ffn_w2, sgu_w_in, sgu_ln_g, sgu_ln_b, sgu_w_s,
              sgu_b_s, sgu_w_out, kv_w, cmp_pe, cmp_w1, cmp_b1, cmp_w2, nsa_w_qg, nsa_w_o):
    h = x
    shared = None
    for layer in range(DEPTH_2):
        if layer == N_A_LAYERS:
            shared = nsa_shared_kv(h, kv_w, cmp_pe, cmp_w1, cmp_b1, cmp_w2)
        h = post_norm(h, 0.5 * swiglu(h, ffn_w1[layer, 0], ffn_w3[layer, 0], ffn_w2[layer, 0]),
                      ln_g[layer, 0], ln_b[layer, 0])
        if layer < N_A_LAYERS:
            a = layer
            mix = chunked_sgu_mixer(h, sgu_w_in[a], sgu_ln_g[a], sgu_ln_b[a], sgu_w_s[a], sgu_b_s[a], sgu_w_out[a])
        else:
            bl = layer - N_A_LAYERS
            mix = nsa_mixer(h, shared, nsa_w_qg[bl], nsa_w_o[bl], rel_table)
        h = post_norm(h, mix, ln_g[layer, 1], ln_b[layer, 1])
        h = post_norm(h, 0.5 * swiglu(h, ffn_w1[layer, 1], ffn_w3[layer, 1], ffn_w2[layer, 1]),
                      ln_g[layer, 2], ln_b[layer, 2])
    return h


def setup_inputs(seed=0):
    out = dict(first_inputs(seed))
    for name, value in second_inputs(seed + 1).items():
        if name != "x":
            out[name + "_2"] = value
    return out


def reference(
    x, mem, norm_mix_w, w_in, gdn_conv_w, gdn_a_log, gdn_dt_bias, gdn_norm_w, mlstm_conv_w,
    mlstm_i_bias, mlstm_f_bias, mlstm_norm_w, w_out, norm_xa_w, norm_mem_w, xa_wq, xa_wkv,
    xa_wo, norm_ffn_w, peer_wq, peer_sub_keys, peer_u, peer_v, norm_final_w, rel_table_2,
    ln_g_2, ln_b_2, ffn_w1_2, ffn_w3_2, ffn_w2_2, sgu_w_in_2, sgu_ln_g_2, sgu_ln_b_2, sgu_w_s_2,
    sgu_b_s_2, sgu_w_out_2, kv_w_2, cmp_pe_2, cmp_w1_2, cmp_b1_2, cmp_w2_2, nsa_w_qg_2,
    nsa_w_o_2,
):
    x = first_block(
        x, mem, norm_mix_w, w_in, gdn_conv_w, gdn_a_log, gdn_dt_bias, gdn_norm_w, mlstm_conv_w,
        mlstm_i_bias, mlstm_f_bias, mlstm_norm_w, w_out, norm_xa_w, norm_mem_w, xa_wq, xa_wkv,
        xa_wo, norm_ffn_w, peer_wq, peer_sub_keys, peer_u, peer_v, norm_final_w,
    )
    return second_block(
        x, rel_table_2, ln_g_2, ln_b_2, ffn_w1_2, ffn_w3_2, ffn_w2_2, sgu_w_in_2, sgu_ln_g_2,
        sgu_ln_b_2, sgu_w_s_2, sgu_b_s_2, sgu_w_out_2, kv_w_2, cmp_pe_2, cmp_w1_2, cmp_b1_2,
        cmp_w2_2, nsa_w_qg_2, nsa_w_o_2,
    )


_drawn_inputs = setup_inputs


def setup_inputs(seed=0):
    import zlib

    import numpy as np

    out = dict(_drawn_inputs(seed))
    spreads = {}
    factors = {'norm_mix_w': 5.847,
     'gdn_norm_w': 8.0,
     'mlstm_i_bias': 23.307,
     'mlstm_norm_w': 54.413,
     'norm_xa_w': 8.0,
     'norm_mem_w': 8.0,
     'norm_ffn_w': 64.0,
     'norm_final_w': 24.575,
     'rel_table_2': 3.962,
     'sgu_ln_g_2': 8.0,
     'sgu_ln_b_2': 51.489,
     'sgu_b_s_2': 4.709,
     'cmp_b1_2': 24.497}
    for name, (base, spread) in spreads.items():
        noise = np.random.default_rng([zlib.crc32(name.encode()), seed]).standard_normal(out[name].shape)
        drawn = base * np.exp(spread * noise) if base else spread * noise
        out[name] = jnp.asarray(drawn.astype(out[name].dtype))
    for name, factor in factors.items():
        out[name] = (out[name] * factor).astype(out[name].dtype)
    return out
```

```python
from contextlib import ExitStack, contextmanager

import numpy as np
import concourse.bass as bass
from concourse import mybir

F32 = mybir.dt.float32
U32 = mybir.dt.uint32
ALU = mybir.AluOpType
ACT = mybir.ActivationFunctionType
AX_X = mybir.AxisListType.X

P = 128
D = 1024
SEQ = 256
TILES = SEQ // P
DC = D // P
COLS = 256
SLOT = DC * COLS
RING = 6
NEG = -1e30
EPS = 1e-6
LN_EPS = 1e-5

HEADS = 4
HD = 128
CHUNK = 64
NCHUNK = SEQ // CHUNK
GW = HEADS * HD
PAIRS = HEADS * TILES

PEER_HEADS = 8
TOPK = 16
KEYS = 128

DN_ALPHA = 4.0 ** 0.25
FFN_DIM = 2816
SGU_HALF = 2048
SGU_GROUPS = 8
NH = 16
KVG = 4
HDIM = 64
CMP_LEN = 32
CMP_STRIDE = 16
NCMP = SEQ // CMP_STRIDE - CMP_LEN // CMP_STRIDE + 1
SLOTS_KV = 6

(C_IDENT, C_ONES, C_NEG_LOW, C_NEG_UP, C_STRICT, C_TRI, C_SAME, C_IOTA, C_CAUSAL_T, C_MISC) = range(10)
C_LEVEL = 10
LEVELS = 6
NCONST = C_LEVEL + LEVELS
DISTS = 2 * SEQ
BIAS_W = 384


def constants():
    c = np.zeros((P, NCONST, P), np.float32)
    i, j = np.arange(P)[:, None], np.arange(P)[None, :]
    same = i // CHUNK == j // CHUNK
    c[:, C_IDENT] = i == j
    c[:, C_ONES] = 1
    c[:, C_NEG_LOW] = np.where(same & (i >= j), 0, NEG)
    c[:, C_NEG_UP] = np.where(same & (i <= j), 0, NEG)
    c[:, C_STRICT] = same & (i > j)
    c[:, C_TRI] = same & (i <= j)
    c[:, C_SAME] = same
    c[:, C_IOTA] = j + 0 * i
    c[:, C_CAUSAL_T] = i <= j
    c[:, C_MISC, 0:2] = (i // CHUNK) == np.arange(2)[None, :]
    for tile in range(TILES):
        ends = np.arange(NCMP)[None, :] * CMP_STRIDE + CMP_LEN - 1
        c[:, C_MISC, 16 + 16 * tile:16 + 16 * tile + NCMP] = (tile * P + i) >= ends
    for k in range(LEVELS):
        b = 1 << k
        c[:, C_LEVEL + k] = (i // (2 * b) == j // (2 * b)) & ((i // b) % 2 == 1) & ((j // b) % 2 == 0)
    onehot = np.zeros((33, DISTS), np.float32)
    for x in range(DISTS):
        dist = SEQ - 1 - x
        if dist < 0:
            onehot[32, x] = 1
        elif dist < 16:
            onehot[dist, x] = 1
        else:
            large = 16 + int(np.float32(np.log(np.float32(dist) / np.float32(16)) / np.float32(np.log(8.0)) * 16))
            onehot[min(large, 31), x] = 1
    return c.reshape(P, NCONST * P), onehot


class Signals:

    def __init__(self, nc, ctx, size):
        self.pools = [[ctx.enter_context(nc.semaphore(f"stage_{'even' if n == 0 else 'odd'}_{m}"))
                       for m in range(size)] for n in range(2)]
        self.stage = 0
        self.taken = 0

    def new(self):
        self.taken += 1
        return self.pools[self.stage % 2][self.taken - 1]

    def next_stage(self):
        self.stage += 1
        self.taken = 0

    def clear_other(self, pool):
        if self.stage > 1:
            other = self.pools[(self.stage + 1) % 2]
            pool.sem_clear(range(other[0].num, other[-1].num + 1))


class Weights:

    def __init__(self, ring, loaded, used):
        self.ring, self.loaded, self.used = ring, loaded, used
        self.segments = []
        self.count = 0
        self.issued = 0
        self.taken = 0

    def take(self, n):
        self.taken += n
        return self.taken - n

    def add(self, units, *sources):
        seg = (self.count, units, sources)
        self.segments.append(seg)
        self.count += units * len(sources)
        return seg[0]

    def slot(self, g):
        return self.ring[:, g % RING, :]

    def panel(self, g):
        return self.ring[:, g % RING, :].rearrange("p (c n) -> p c n", c=DC)

    def rows(self, g):
        return self.ring[:, g % RING, :].rearrange("p (r n) -> p r n", r=2)

    def _one(self, sp, g, source, unit, turn):
        r = g % RING
        if g >= RING:
            sp.wait_ge(self.used[r], turn)
        src = source(unit)
        dst = self.ring[:, r, :]
        if len(src.shape) == 3:
            dst = dst.rearrange("p (a b) -> p a b", a=src.shape[1])
        sp.dma_start(dst, src).then_inc(self.loaded[r], 16)

    def issue(self, sp, end):
        end = min(end, self.count)
        while self.issued < end:
            g = self.issued
            start, units, sources = [s for s in self.segments if s[0] <= g][-1]
            per = len(sources)
            body = RING // per
            u, k = divmod(g - start, per)
            last = min(start + units * per, end)
            turns = (last - g) // RING
            if k == 0 and turns >= 3 and g >= RING and units > 16 // per + 3:
                with sp.Fori(0, turns) as i:
                    for b in range(body):
                        for kk in range(per):
                            at = g + b * per + kk
                            self._one(sp, at, sources[kk], u + b + body * i, at // RING + i)
                self.issued += turns * RING
            else:
                self._one(sp, g, sources[k], u, g // RING)
                self.issued += 1


class Program:

    def __init__(self, nc, ctx, a):
        self.nc, self.ctx, self.a = nc, ctx, a
        self.names = {}
        self.sig = Signals(nc, ctx, 36)
        ring = self.sb(ctx, "ring", [P, RING, SLOT])
        loaded = [ctx.enter_context(nc.semaphore(f"slot_loaded_{r}")) for r in range(RING)]
        used = [ctx.enter_context(nc.semaphore(f"slot_used_{r}")) for r in range(RING)]
        self.w = Weights(ring, loaded, used)
        self.x = self.sb(ctx, "x_natural", [P, TILES, D])
        self.xT = self.sb(ctx, "x_transposed", [P, DC, SEQ])
        self.ident = self.sb(ctx, "ident", [P, P])
        self.ones = self.sb(ctx, "ones", [P, P])
        self.cols = self.sb(ctx, "parameter_columns", [P, 120])
        self.eps = self.sb(ctx, "epsilons", [P, 2])
        self.stored = ctx.enter_context(nc.semaphore("output_stored"))
        self.boot = ctx.enter_context(nc.semaphore("booted"))
        self.psum = ctx.enter_context(nc.psum_tensor("banks", [P, 8, 512], F32))

    def sb(self, ctx, name, shape, dt=F32):
        self.names[name] = self.names.get(name, 0) + 1
        if self.names[name] > 1:
            name = f"{name}_{self.names[name]}"
        return ctx.enter_context(self.nc.sbuf_tensor(name, shape, dt))

    @contextmanager
    def stage(self):
        self.sig.next_stage()
        with self.nc.Block() as block:
            yield block

    def stream(self, sp):
        self.w.issue(sp, self.w.taken + RING)

    def idle_pool(self, block):
        @block.gpsimd
        def _(pool):
            self.sig.clear_other(pool)


def use_slot(pe, k, g, turn=None):
    pe.wait_ge(k.w.loaded[g % RING], 16 * ((g // RING if turn is None else turn) + 1))


def used_slot(engine, k, g, turn=None):
    engine.wait_ge(k.w.used[g % RING], (g // RING if turn is None else turn) + 1)


def linker(engine, step):
    count = [0]

    def link(ins):
        count[0] += 1
        ins.then_inc(step, 1)
        engine.wait_ge(step, count[0])
    return link


def over_last(ap, n):
    return ap.unsqueeze(2).broadcast_to([ap.shape[0], ap.shape[1], n])


def over_middle(ap, n):
    return ap.unsqueeze(1).broadcast_to([ap.shape[0], n, ap.shape[1]])



def load_parameters(k):
    a = k.a
    rows = [(a["norm_mix_w"][0], DC), (a["norm_xa_w"][0], DC), (a["norm_mem_w"][0], DC), (a["norm_ffn_w"][0], DC)]
    at = 0
    with ExitStack() as ctx, k.stage() as block:
        raw = k.sb(ctx, "parameter_rows", [P, P])
        landed, rows_landed, turned = (k.sig.new() for _ in range(3))

        @block.sync
        def _(sp):
            consts = a["constants"].rearrange("p (c n) -> p c n", n=P)
            sp.dma_start(k.ident[:, :], consts[:, C_IDENT, :]).then_inc(landed, 16)
            sp.dma_start(k.ones[:, :], consts[:, C_ONES, :]).then_inc(landed, 16)
            sp.dma_start(k.x[:, :, :], a["x"][0].rearrange("(i p) d -> p i d", p=P)).then_inc(landed, 16)
            k.w.issue(sp, RING)

        @block.scalar
        def _(act):
            n = 0
            for v, chunks in rows:
                act.dma_start(raw[n:n + chunks, :], v.rearrange("(c p) -> c p", p=P)).then_inc(rows_landed, 16)
                n += chunks
            g = a["gdn_conv_w"][0].rearrange("k (c p) -> k c p", p=P)
            m = a["mlstm_conv_w"][0].rearrange("k (c p) -> k c p", p=P)
            for tap in range(4):
                act.dma_start(raw[n:n + 12, :], g[tap]).then_inc(rows_landed, 16)
                act.dma_start(raw[n + 12:n + 20, :], m[tap]).then_inc(rows_landed, 16)
                n += 20
            act.dma_start(raw[n:n + 4, :], a["cmp_b1_2"].rearrange("s (c p) -> (s c) p", p=P)).then_inc(rows_landed, 16)

        @block.tensor
        def _(pe):
            pe.wait_ge(landed, 48)
            pe.wait_ge(rows_landed, 16 * (len(rows) + 9))
            pe.transpose(k.psum[:, 0, 0:116], raw[0:116, :], k.ident[0:116, 0:116]).then_inc(turned, 1)

        @block.vector
        def _(dve):
            dve.memset(k.eps[:, 0:1], EPS).then_inc(k.boot, 1)
            dve.memset(k.eps[:, 1:2], LN_EPS).then_inc(k.boot, 1)
            dve.wait_ge(turned, 1)
            dve.tensor_copy(k.cols[:, 0:116], k.psum[:, 0, 0:116]).then_inc(k.boot, 1)

        @block.gpsimd
        def _(pool):
            k.sig.clear_other(pool)


COL_MIX, COL_XA, COL_MEM, COL_FFN, COL_CONV, COL_B1 = 0, 8, 16, 24, 32, 112


def turn_chunks(pe, k, src, tile, ready):
    for c in range(DC):
        at = (c % 2) * SEQ + tile * P
        ins = pe.transpose(k.psum[:, c // 2, at:at + P], src[:, c * P:(c + 1) * P], k.ident[:, :])
        if tile == TILES - 1 and c % 2 == 1:
            ins.then_inc(ready, 1)


def norm_transpose(k, src, dst, col):
    with ExitStack() as ctx, k.stage() as block:
        xn = k.sb(ctx, "normed", [P, TILES, D])
        stat = k.sb(ctx, "row_stats", [P, 3, TILES])
        squares, rooted, recip, normed, banks, written = (k.sig.new() for _ in range(6))

        @block.sync
        def _(sp):
            k.stream(sp)

        @block.scalar
        def _(act):
            for i in range(TILES):
                act.activation(xn[:, i, :], src[:, i, :], ACT.Square, accum_out=stat[:, 0, i:i + 1]).then_inc(squares, 1)
            act.wait_ge(squares, TILES)
            act.activation(stat[:, 1, :], stat[:, 0, :], ACT.Sqrt, bias=k.eps[:, 0:1], scale=1.0 / D).then_inc(rooted, 1)
            for b in (1, 3):
                act.wait_ge(banks, b + 1)
                for c in (2 * b, 2 * b + 1):
                    act.activation(dst[:, c, :], k.psum[:, b, (c % 2) * SEQ:(c % 2 + 1) * SEQ], ACT.Copy,
                                   scale=k.cols[:, col + c:col + c + 1]).then_inc(written, 1)

        @block.vector
        def _(dve):
            dve.wait_ge(rooted, 1)
            dve.reciprocal(stat[:, 2, :], stat[:, 1, :]).then_inc(recip, 1)
            dve.wait_ge(recip, 1)
            for i in range(TILES):
                dve.tensor_scalar(xn[:, i, :], src[:, i, :], stat[:, 2, i:i + 1], None, ALU.mult).then_inc(normed, 1)
            for b in (0, 2):
                dve.wait_ge(banks, b + 1)
                for c in (2 * b, 2 * b + 1):
                    dve.tensor_scalar(dst[:, c, :], k.psum[:, b, (c % 2) * SEQ:(c % 2 + 1) * SEQ],
                                      k.cols[:, col + c:col + c + 1], None, ALU.mult).then_inc(written, 1)

        @block.tensor
        def _(pe):
            for i in range(TILES):
                pe.wait_ge(normed, i + 1)
                turn_chunks(pe, k, xn[:, i, :], i, banks)

        k.idle_pool(block)


def transpose_natural(k, src, dst):
    with k.stage() as block:
        banks, written = k.sig.new(), k.sig.new()

        @block.sync
        def _(sp):
            k.stream(sp)

        @block.tensor
        def _(pe):
            for i in range(TILES):
                turn_chunks(pe, k, src[:, i, :], i, banks)

        @block.scalar
        def _(act):
            for b in (1, 3):
                act.wait_ge(banks, b + 1)
                act.activation(dst[:, 2 * b:2 * b + 2, :], bank2(k, b), ACT.Copy).then_inc(written, 1)

        @block.vector
        def _(dve):
            for b in (0, 2):
                dve.wait_ge(banks, b + 1)
                dve.tensor_copy(dst[:, 2 * b:2 * b + 2, :], bank2(k, b)).then_inc(written, 1)

        k.idle_pool(block)


def bank2(k, b):
    return k.psum[:, b, :].rearrange("p (a n) -> p a n", a=2)


def panels(k, items, small=None):
    g0 = k.w.take(len(items))
    by_act = [m for m, it in enumerate(items) if it[3] is not None or m % 2 == 1]
    by_dve = [m for m in range(len(items)) if m not in by_act]
    with ExitStack() as ctx, k.stage() as block:
        act_read, dve_read, narrow_landed, narrow_done = (k.sig.new() for _ in range(4))
        if small:
            view, small_x, small_dest, small_func, width = small
            narrow = k.sb(ctx, "narrow_panel", [P, DC, width])

        @block.sync
        def _(sp):
            k.stream(sp)

        @block.tensor
        def _(pe):
            for m, (form, xT, dest, func, scale) in enumerate(items):
                if m >= 6:
                    if m - 6 in by_act:
                        pe.wait_ge(act_read, by_act.index(m - 6) + 1)
                    else:
                        pe.wait_ge(dve_read, by_dve.index(m - 6) + 1)
                g = g0 + m
                use_slot(pe, k, g)
                w = k.w.panel(g)
                for j in range(2):
                    for c in range(DC):
                        if form == "T":
                            left, right = w[:, c, j * P:(j + 1) * P], xT[:, c, :]
                        else:
                            left, right = xT[:, c, j * P:(j + 1) * P], w[:, c, :]
                        ins = pe.matmul(k.psum[:, m % 6, j * SEQ:(j + 1) * SEQ], left, right,
                                        start=(c == 0), stop=(c == DC - 1))
                ins.then_inc(k.w.used[g % RING], 1)
            if small:
                pe.wait_ge(narrow_landed, 16 * (len(view) if isinstance(view, list) else 1))
                for i in range(TILES):
                    for c in range(DC):
                        ins = pe.matmul(k.psum[:, 6, i * width:(i + 1) * width], small_x[:, c, i * P:(i + 1) * P],
                                        narrow[:, c, :], start=(c == 0), stop=(c == DC - 1))
                ins.then_inc(narrow_done, 1)

        @block.scalar
        def _(act):
            if small:
                parts = view if isinstance(view, list) else [view]
                at = 0
                for v in parts:
                    act.dma_start(narrow[:, :, at:at + v.shape[2]], v).then_inc(narrow_landed, 16)
                    at += v.shape[2]
            for m in by_act:
                func, scale = items[m][3], items[m][4]
                used_slot(act, k, g0 + m)
                act.activation(items[m][2], bank2(k, m % 6), func or ACT.Copy, scale=scale).then_inc(act_read, 1)
            if small:
                act.wait_ge(narrow_done, 1)
                act.activation(small_dest, k.psum[:, 6, 0:TILES * width].rearrange("p (i n) -> p i n", i=TILES),
                               small_func or ACT.Copy).then_inc(act_read, 1)

        @block.vector
        def _(dve):
            for m in by_dve:
                used_slot(dve, k, g0 + m)
                dve.tensor_scalar(items[m][2], bank2(k, m % 6), items[m][4], None, ALU.mult).then_inc(dve_read, 1)

        k.idle_pool(block)


def rows_product(k, aT, slots, finish):
    g0 = k.w.take(slots)
    with ExitStack() as ctx, k.stage() as block:
        @block.sync
        def _(sp):
            k.stream(sp)

        @block.tensor
        def _(pe):
            for m in range(slots):
                g = g0 + m
                use_slot(pe, k, g)
                w = k.w.rows(g)
                for r in range(2):
                    ins = down(pe, k, aT[:, 2 * m + r, :], w[:, r, :], m == 0 and r == 0, m == slots - 1 and r == 1)
                ins.then_inc(k.w.used[g % RING], 1)

        finish(ctx, block, g0 + slots - 1)
        k.idle_pool(block)


def down(pe, k, aT, w, start, stop):
    for i in range(TILES):
        for half in range(2):
            ins = pe.matmul(k.psum[:, 2 * i + half, :], aT[:, i * P:(i + 1) * P], w[:, half * 512:(half + 1) * 512],
                            start=start, stop=stop)
    return ins


def accumulated(k, i):
    return k.psum[:, 2 * i:2 * i + 2, :].rearrange("p b n -> p (b n)")


def add_to(k, dst):
    def finish(ctx, block, last):
        added = k.sig.new()

        @block.vector
        def _(dve):
            used_slot(dve, k, last)
            for i in range(TILES):
                dve.tensor_tensor(dst[:, i, :], accumulated(k, i), dst[:, i, :], ALU.add).then_inc(added, 1)
    return finish


def copy_to(k, dst):
    def finish(ctx, block, last):
        copied = k.sig.new()

        @block.vector
        def _(dve):
            used_slot(dve, k, last)
            dve.tensor_copy(dst[:, 0, :], accumulated(k, 0)).then_inc(copied, 1)

        @block.scalar
        def _(act):
            used_slot(act, k, last)
            act.activation(dst[:, 1, :], accumulated(k, 1), ACT.Copy).then_inc(copied, 1)
    return finish



def conv_silu(k, padded, out):
    with ExitStack() as ctx, k.stage() as block:
        summed, shaped = k.sig.new(), k.sig.new()
        tmp = k.sb(ctx, "convolved", [P, 20, SEQ])
        step = k.sig.new()

        @block.sync
        def _(sp):
            k.stream(sp)

        @block.vector
        def _(dve):
            for quad in range(4):
                for tap in range(4):
                    for n in range(5 * quad, 5 * quad + 5):
                        w = k.cols[:, COL_CONV + 20 * tap + n:COL_CONV + 20 * tap + n + 1]
                        src = padded[:, n, tap:tap + SEQ]
                        if tap == 0:
                            ins = dve.tensor_scalar(tmp[:, n, :], src, w, None, ALU.mult)
                        else:
                            ins = dve.scalar_tensor_tensor(tmp[:, n, :], src, w, tmp[:, n, :], ALU.mult, ALU.add)
                        ins.then_inc(step, 1)
                    dve.wait_ge(step, 20 * quad + 5 * (tap + 1))

        @block.scalar
        def _(act):
            for quad in range(4):
                act.wait_ge(step, 20 * (quad + 1))
                act.activation(out[:, 5 * quad:5 * quad + 5, :], tmp[:, 5 * quad:5 * quad + 5, :],
                               ACT.Silu).then_inc(shaped, 1)

        k.idle_pool(block)


def normalise_and_gate(k, s):
    with ExitStack() as ctx, k.stage() as block:
        sq = k.sb(ctx, "qk_squares", [P, 8, SEQ])
        root = k.sb(ctx, "qk_norms", [P, 8, SEQ])
        row = k.sb(ctx, "gate_parameters", [P, 4, HEADS])
        g = k.sb(ctx, "gate_work", [P, 6, TILES, 8])
        lh = k.sb(ctx, "log_by_half", [P, 2, 16])
        squared, sums, rooted, vstep, scaled, gates_landed, expd, logs, cums, turned, copied, gstep = \
            (k.sig.new() for _ in range(12))
        qk = s.conv[:, 0:8, :]

        @block.sync
        def _(sp):
            for n, name in enumerate(("gdn_dt_bias", "gdn_a_log", "mlstm_i_bias", "mlstm_f_bias")):
                sp.dma_start(row[:, n, :], k.a[name].partition_broadcast(P).rearrange("p a h -> p (a h)")
                             ).then_inc(gates_landed, 16)
            k.stream(sp)

        @block.gpsimd
        def _(pool):
            k.sig.clear_other(pool)
            pool.tensor_tensor(sq[:, 0:4, :], s.conv[:, 0:4, :], s.conv[:, 0:4, :], ALU.mult).then_inc(squared, 1)
            pool.tensor_scalar(s.conv[:, 16:20, :], s.conv[:, 16:20, :], HD ** -0.5, None, ALU.mult).then_inc(scaled, 1)

        @block.scalar
        def _(act):
            act.activation(sq[:, 4:8, :], s.conv[:, 4:8, :], ACT.Square).then_inc(squared, 1)
            for b in range(4):
                act.wait_ge(sums, b + 1)
                act.activation(root[:, 2 * b:2 * b + 2, :], bank2(k, b), ACT.Sqrt, bias=k.eps[:, 0:1]).then_inc(rooted, 1)
            act.wait_ge(gstep, 3)
            act.activation(g[:, 2, :, :], g[:, 1, :, :], ACT.Exp, scale=-1.0).then_inc(expd, 1)
            act.activation(row[:, 1, :], row[:, 1, :], ACT.Exp).then_inc(expd, 1)
            act.wait_ge(expd, 2)
            act.activation(g[:, 3, :, :], g[:, 2, :, :], ACT.Ln, bias=1.0).then_inc(logs, 1)
            act.activation(s.beta[:, :, :], s.gates[:, :, 4:8], ACT.Sigmoid).then_inc(logs, 1)
            for n in (1, 3, 5):
                act.wait_ge(turned, n + 1)
                b = [4, 5, 6, 7, 0, 1][n]
                act.activation(s.natural[:, 4 * n:4 * n + 4, :], k.psum[:, b, :].rearrange("p (a n) -> p a n", a=4),
                               ACT.Copy).then_inc(copied, 1)

        @block.tensor
        def _(pe):
            for b in range(4):
                pe.wait_ge(squared, 2)
                pe.matmul(k.psum[:, b, :], k.ones[:, :], sq[:, 2 * b:2 * b + 2, :], start=True, stop=True).then_inc(sums, 1)
            pe.wait_ge(vstep, 8)
            pe.wait_ge(scaled, 1)
            for n in range(6):
                b = [4, 5, 6, 7, 0, 1][n]
                for q in range(4):
                    e = 4 * n + q
                    kind, head, tile = e // 8, (e % 8) // 2, e % 2
                    src = s.conv[:, (4, 8, 16)[kind] + head, tile * P:(tile + 1) * P]
                    ins = pe.transpose(k.psum[:, b, q * P:(q + 1) * P], src, k.ident[:, :])
                ins.then_inc(turned, 1)
            pe.wait_ge(gstep, 9)
            pe.matmul(k.psum[:, 2, 0:16], s.mask(C_TRI), s.logs[:, :, :, :].rearrange("p i t h -> p (i t h)"), start=True, stop=True)
            pe.matmul(k.psum[:, 2, 16:32], s.mask(C_SAME), s.logs[:, :, :, :].rearrange("p i t h -> p (i t h)"), start=True, stop=True)
            pe.matmul(k.psum[:, 2, 32:64], k.ones[:, :], lh[:, :, :].rearrange("p f n -> p (f n)"), start=True, stop=True).then_inc(cums, 1)

        @block.vector
        def _(dve):
            dve.wait_ge(gates_landed, 64)
            dve.tensor_tensor(g[:, 0, :, 0:4], s.gates[:, :, 0:4], over_middle(row[:, 0, :], TILES), ALU.add).then_inc(gstep, 1)
            dve.scalar_tensor_tensor(g[:, 0, :, 4:8], s.gates[:, :, 12:16], -1.0, over_middle(row[:, 3, :], TILES),
                                     ALU.mult, ALU.subtract).then_inc(gstep, 1)
            dve.wait_ge(gstep, 2)
            dve.scalar_tensor_tensor(g[:, 1, :, :], g[:, 0, :, :], -1.0, g[:, 0, :, :], ALU.mult, ALU.max).then_inc(gstep, 1)
            dve.tensor_tensor(s.log_i[:, :, :], s.gates[:, :, 8:12], over_middle(row[:, 2, :], TILES), ALU.add).then_inc(gstep, 1)
            dve.tensor_scalar(g[:, 4, :, :], g[:, 0, :, :], 0.0, None, ALU.max).then_inc(gstep, 1)
            for b in range(4):
                dve.wait_ge(rooted, b + 1)
                dve.reciprocal(root[:, 2 * b:2 * b + 2, :], root[:, 2 * b:2 * b + 2, :]).then_inc(vstep, 1)
                dve.wait_ge(vstep, 2 * b + 1)
                part = s.conv[:, 2 * b:2 * b + 2, :]
                dve.scalar_tensor_tensor(part, part, HD ** -0.5 if b < 2 else 1.0, root[:, 2 * b:2 * b + 2, :],
                                         ALU.mult, ALU.mult).then_inc(vstep, 1)
            dve.wait_ge(logs, 1)
            dve.wait_ge(gstep, 5)
            dve.tensor_tensor(g[:, 5, :, :], g[:, 4, :, :], g[:, 3, :, :], ALU.add).then_inc(gstep, 1)
            dve.wait_ge(gstep, 6)
            dve.scalar_tensor_tensor(s.logs[:, :, 0, :], g[:, 5, :, 0:4], -1.0, over_middle(row[:, 1, :], TILES),
                                     ALU.mult, ALU.mult).then_inc(gstep, 1)
            dve.tensor_scalar(s.logs[:, :, 1, :], g[:, 5, :, 4:8], -1.0, None, ALU.mult).then_inc(gstep, 1)
            dve.wait_ge(gstep, 8)
            dve.tensor_tensor(lh[:, :, :], over_middle(s.logs[:, :, :, :].rearrange("p i t h -> p (i t h)"), 2),
                              over_last(s.consts[:, C_MISC, 0:2], 16), ALU.mult).then_inc(gstep, 1)
            for n in (0, 2, 4):
                dve.wait_ge(turned, n + 1)
                b = [4, 5, 6, 7, 0, 1][n]
                dve.tensor_copy(s.natural[:, 4 * n:4 * n + 4, :],
                                k.psum[:, b, :].rearrange("p (a n) -> p a n", a=4)).then_inc(copied, 1)
            dve.wait_ge(cums, 1)
            for kind in range(2):
                for what in range(2):
                    src = k.psum[:, 2, 16 * what:16 * what + 16].rearrange("p (i t h) -> p t h i", i=TILES, t=2)
                    dve.tensor_copy(s.run[:, kind, what, :].rearrange("p (h i) -> p h i", h=HEADS),
                                    src[:, kind, :, :]).then_inc(copied, 1)
                for half in range(2):
                    src = k.psum[:, 2, 32 + 16 * half:48 + 16 * half].rearrange("p (i t h) -> p t h i", i=TILES, t=2)
                    dst = s.total[:, kind, :].rearrange("p (h i f) -> p h i f", h=HEADS, f=2)
                    dve.tensor_copy(dst[:, :, :, half], src[:, kind, :, :]).then_inc(copied, 1)


def gdn_prepare(k, s):
    gc = s.run[:, 0, 0, :]
    with ExitStack() as ctx, k.stage() as block:
        def mats(name):
            return k.sb(ctx, name, [P, PAIRS, P])
        diag, low, up, rowexp, A, B, Y, W, X = (mats(n) for n in
            ("gc_diagonal", "decay_low", "decay_up", "row_exp", "A", "A_level", "AtW", "inv_T", "inv"))
        vb, kbg = mats("v_beta"), mats("k_beta_exp")
        col = k.sb(ctx, "gdn_columns", [P, 4, PAIRS])
        vs, ps, acts, pools, As = (k.sig.new() for _ in range(5))
        kn, vn = s.natural[:, 0:8, :], s.natural[:, 8:16, :]

        def both(n):
            return k.psum[:, 2 * n:2 * n + 2, :].rearrange("p b (a n) -> p (b a) n", n=P)

        def square(n, e):
            return k.psum[:, 2 * n + e // 4, (e % 4) * P:(e % 4 + 1) * P]

        @block.sync
        def _(sp):
            k.stream(sp)

        @block.vector
        def _(dve):
            link = linker(dve, vs)
            link(dve.tensor_tensor(diag[:, :, :], over_middle(k.ident[:, :], PAIRS), over_last(gc, P), ALU.mult))
            link(dve.tensor_copy(col[:, 0, :].rearrange("p (h i) -> p h i", h=HEADS),
                                 s.beta[:, :, :].rearrange("p i h -> p h i")))
            link(dve.tensor_tensor(col[:, 3, :], s.run[:, 0, 1, :], gc, ALU.subtract))
            dve.wait_ge(ps, 1)
            link(dve.tensor_tensor(up[:, :, :], both(0), over_last(gc, P), ALU.subtract))
            link(dve.scalar_tensor_tensor(low[:, :, :], up[:, :, :], -1.0, over_middle(s.mask(C_NEG_LOW), PAIRS),
                                          ALU.mult, ALU.add))
            link(dve.tensor_tensor(up[:, :, :], up[:, :, :], over_middle(s.mask(C_NEG_UP), PAIRS), ALU.add))
            dve.wait_ge(acts, 1)
            link(dve.tensor_tensor(col[:, 1, :], col[:, 1, :], col[:, 0, :], ALU.mult))
            dve.wait_ge(ps, 2)
            dve.wait_ge(acts, 3)
            link(dve.tensor_tensor(A[:, :, :], both(1), low[:, :, :], ALU.mult))
            link(dve.tensor_tensor(A[:, :, :], A[:, :, :], over_last(col[:, 0, :], P), ALU.mult))
            link(dve.tensor_tensor(A[:, :, :], A[:, :, :], over_middle(s.mask(C_STRICT), PAIRS), ALU.mult))
            link(dve.tensor_copy(W[:, :, :], over_middle(k.ident[:, :], PAIRS)))
            link(dve.tensor_copy(X[:, :, :], over_middle(k.ident[:, :], PAIRS)))
            for level in range(LEVELS):
                link(dve.tensor_tensor(B[:, :, :], A[:, :, :], over_middle(s.mask(C_LEVEL + level), PAIRS), ALU.mult))
                dve.wait_ge(ps, 4 + 2 * level)
                link(dve.tensor_tensor(W[:, :, :], W[:, :, :], both(2), ALU.subtract))
                link(dve.tensor_tensor(X[:, :, :], X[:, :, :], both(3), ALU.subtract))

        @block.scalar
        def _(act):
            act.activation(col[:, 1, :], gc, ACT.Exp).then_inc(acts, 1)
            act.wait_ge(vs, 3)
            act.activation(col[:, 2, :], col[:, 3, :], ACT.Exp).then_inc(acts, 1)
            act.wait_ge(vs, 5)
            act.activation(low[:, :, :], low[:, :, :], ACT.Exp).then_inc(acts, 1)
            act.wait_ge(vs, 6)
            act.activation(up[:, :, :], up[:, :, :], ACT.Exp).then_inc(acts, 1)
            act.activation(rowexp[:, :, :], both(0), ACT.Exp).then_inc(acts, 1)
            act.activation(s.glast[:, 0, :], s.total[:, 0, :], ACT.Exp).then_inc(acts, 1)
            for level in range(LEVELS):
                act.wait_ge(ps, 3 + 2 * level)
                act.activation(Y[:, :, :], both(1), ACT.Copy).then_inc(As, 1)
            act.wait_ge(ps, 15)
            act.activation(s.u[:, :, :], both(0), ACT.Copy).then_inc(acts, 1)
            act.activation(s.wT[:, :, :], both(1), ACT.Copy).then_inc(acts, 1)

        @block.gpsimd
        def _(pool):
            k.sig.clear_other(pool)
            pool.wait_ge(vs, 2)
            pool.tensor_tensor(vb[:, :, :], vn, over_last(col[:, 0, :], P), ALU.mult).then_inc(pools, 1)
            pool.wait_ge(vs, 7)
            pool.tensor_tensor(kbg[:, :, :], kn, over_last(col[:, 1, :], P), ALU.mult).then_inc(pools, 1)
            pool.wait_ge(acts, 5)
            pool.tensor_tensor(s.kd[:, :, :], kn, over_last(col[:, 2, :], P), ALU.mult).then_inc(pools, 1)
            pool.tensor_tensor(s.qdT[:, :, :], s.conv[:, 0:4, :].rearrange("p h (i n) -> p (h i) n", n=P),
                               rowexp[:, :, :], ALU.mult).then_inc(pools, 1)
            pool.tensor_tensor(s.qkT[:, :, :], s.qk_raw[:, :, :], up[:, :, :], ALU.mult).then_inc(pools, 1)

        @block.tensor
        def _(pe):
            pe.wait_ge(vs, 1)
            for n in range(2):
                ins = pe.matmul(k.psum[:, n, :], k.ones[:, :], diag[:, 4 * n:4 * n + 4, :], start=True, stop=True)
            ins.then_inc(ps, 1)
            for e in range(PAIRS):
                kt = s.conv[:, 4 + e // 2, (e % 2) * P:(e % 2 + 1) * P]
                ins = pe.matmul(square(1, e), kt, kt, start=True, stop=True)
            ins.then_inc(ps, 1)
            for level in range(LEVELS):
                pe.wait_ge(vs, 13 + 3 * level)
                for e in range(PAIRS):
                    ins = pe.matmul(square(1, e), B[:, e, :], W[:, e, :], start=True, stop=True)
                ins.then_inc(ps, 1)
                pe.wait_ge(As, level + 1)
                for e in range(PAIRS):
                    pe.matmul(square(2, e), X[:, e, :], Y[:, e, :], start=True, stop=True)
                    ins = pe.matmul(square(3, e), Y[:, e, :], X[:, e, :], start=True, stop=True)
                ins.then_inc(ps, 1)
            pe.wait_ge(vs, 12 + 3 * LEVELS)
            pe.wait_ge(pools, 2)
            pe.wait_ge(acts, 6)
            for e in range(PAIRS):
                pe.matmul(square(0, e), W[:, e, :], vb[:, e, :], start=True, stop=True)
                ins = pe.matmul(square(1, e), kbg[:, e, :], W[:, e, :], start=True, stop=True)
            ins.then_inc(ps, 1)


def key_query_products(k, s):
    with k.stage() as block:
        ps, copied = k.sig.new(), k.sig.new()

        @block.sync
        def _(sp):
            k.stream(sp)

        @block.tensor
        def _(pe):
            for kind, (q0, k0) in enumerate(((0, 4), (12, 16))):
                for e in range(PAIRS):
                    t = slice((e % 2) * P, (e % 2 + 1) * P)
                    ins = pe.matmul(k.psum[:, 2 * kind + e // 4, (e % 4) * P:(e % 4 + 1) * P],
                                    s.conv[:, k0 + e // 2, t], s.conv[:, q0 + e // 2, t], start=True, stop=True)
                ins.then_inc(ps, 1)

        @block.vector
        def _(dve):
            dve.wait_ge(ps, 1)
            dve.tensor_copy(s.qk_raw[:, :, :], k.psum[:, 0:2, :].rearrange("p b (a n) -> p (b a) n", n=P)).then_inc(copied, 1)

        @block.scalar
        def _(act):
            act.wait_ge(ps, 2)
            act.activation(s.mqk_raw[:, :, :], k.psum[:, 2:4, :].rearrange("p b (a n) -> p (b a) n", n=P),
                           ACT.Copy).then_inc(copied, 1)

        k.idle_pool(block)


def mlstm_prepare(k, s):
    b, bl_own = s.run[:, 1, 0, :], s.run[:, 1, 1, :]
    bl_all = s.total[:, 1, :]
    with ExitStack() as ctx, k.stage() as block:
        def mats(name):
            return k.sb(ctx, name, [P, PAIRS, P])
        diag, work = mats("row_diagonal"), mats("row_work")
        c = k.sb(ctx, "mlstm_columns", [P, 16, PAIRS])
        amax = k.sb(ctx, "chunk_maxima", [P, HEADS, NCHUNK])
        m = k.sb(ctx, "running_maxima", [P, HEADS, NCHUNK + 1])
        tmp = k.sb(ctx, "decay_argument", [P, HEADS, NCHUNK])
        vs, ps, acts, pools = (k.sig.new() for _ in range(4))
        A_, MAXD, MPREV, MNEXT, INTER, MT, SCARG, WARG, R, WGT = range(10)

        def both(n):
            return k.psum[:, 2 * n:2 * n + 2, :].rearrange("p b (a n) -> p (b a) n", n=P)

        @block.sync
        def _(sp):
            k.stream(sp)

        @block.vector
        def _(dve):
            link = linker(dve, vs)
            link(dve.tensor_tensor(c[:, A_, :].rearrange("p (h i) -> p h i", h=HEADS),
                                   s.log_i[:, :, :].rearrange("p i h -> p h i"),
                                   b.rearrange("p (h i) -> p h i", h=HEADS), ALU.subtract))
            link(dve.tensor_tensor(diag[:, :, :], over_middle(k.ident[:, :], PAIRS), over_last(c[:, A_, :], P), ALU.mult))
            link(dve.memset(m[:, :, :], 0.0))
            dve.wait_ge(ps, 1)
            link(dve.tensor_reduce(amax[:, :, :].rearrange("p h n -> p (h n)"),
                                   both(0).rearrange("p e (f n) -> p (e f) n", f=2), AX_X, ALU.max))
            link(dve.tensor_tensor(work[:, :, :], both(0), over_middle(s.mask(C_NEG_LOW), PAIRS), ALU.add))
            link(dve.tensor_reduce(c[:, MAXD, :], work[:, :, :], AX_X, ALU.max))
            link(dve.tensor_tensor(c[:, MAXD, :], c[:, MAXD, :], b, ALU.add))
            total = bl_all.rearrange("p (h n) -> p h n", h=HEADS)
            for n in range(NCHUNK):
                link(dve.tensor_tensor(m[:, :, n + 1], m[:, :, n], amax[:, :, n], ALU.max))
                link(dve.tensor_tensor(m[:, :, n + 1], m[:, :, n + 1], total[:, :, n], ALU.add))
            for half in range(2):
                p = slice(half * CHUNK, (half + 1) * CHUNK)
                for what, off in ((MPREV, 0), (MNEXT, 1)):
                    src = m[p, :, off + half:off + half + 3:2]
                    link(dve.tensor_copy(c[p, what, :].rearrange("p (h i) -> p h i", h=HEADS), src))
            link(dve.tensor_tensor(c[:, INTER, :], b, c[:, MPREV, :], ALU.add))
            link(dve.tensor_tensor(c[:, MT, :], c[:, INTER, :], c[:, MAXD, :], ALU.max))
            link(dve.tensor_tensor(c[:, SCARG, :], c[:, INTER, :], c[:, MT, :], ALU.subtract))
            link(dve.tensor_tensor(c[:, WARG, :], c[:, A_, :], bl_own, ALU.add))
            link(dve.tensor_tensor(c[:, WARG, :], c[:, WARG, :], c[:, MNEXT, :], ALU.subtract))
            link(dve.tensor_tensor(tmp[:, :, :], total, m[:, :, 0:NCHUNK], ALU.add))
            link(dve.tensor_tensor(tmp[:, :, :], tmp[:, :, :], m[:, :, 1:NCHUNK + 1], ALU.subtract))
            link(dve.tensor_tensor(c[:, R, :], b, c[:, MT, :], ALU.subtract))
            link(dve.tensor_tensor(diag[:, :, :], over_middle(k.ident[:, :], PAIRS), over_last(c[:, R, :], P), ALU.mult))
            dve.wait_ge(ps, 2)
            link(dve.tensor_tensor(work[:, :, :], both(1), over_middle(s.mask(C_NEG_UP), PAIRS), ALU.add))
            link(dve.tensor_tensor(work[:, :, :], work[:, :, :], over_last(c[:, A_, :], P), ALU.add))
            dve.wait_ge(acts, 4)
            link(dve.tensor_tensor(diag[:, :, :], over_middle(k.ident[:, :], PAIRS), over_last(c[:, SCARG, :], P), ALU.mult))
            dve.wait_ge(ps, 3)
            link(dve.tensor_tensor(s.mqdT[:, :, :], s.conv[:, 12:16, :].rearrange("p h (i n) -> p (h i) n", n=P),
                                   both(2), ALU.mult))
            dve.wait_ge(acts, 5)
            link(dve.tensor_tensor(s.mqkT[:, :, :], s.mqk_raw[:, :, :], work[:, :, :], ALU.mult))

        @block.scalar
        def _(act):
            act.wait_ge(vs, 26)
            act.activation(s.emt[:, :], c[:, MT, :], ACT.Exp, scale=-1.0).then_inc(acts, 1)
            act.activation(c[:, SCARG, :], c[:, SCARG, :], ACT.Exp).then_inc(acts, 1)
            act.activation(c[:, WGT, :], c[:, WARG, :], ACT.Exp).then_inc(acts, 1)
            act.activation(s.glast[:, 1, :].rearrange("p (h n) -> p h n", h=HEADS), tmp[:, :, :], ACT.Exp).then_inc(acts, 1)
            act.wait_ge(vs, 30)
            act.activation(work[:, :, :], work[:, :, :], ACT.Exp).then_inc(acts, 1)

        @block.gpsimd
        def _(pool):
            k.sig.clear_other(pool)
            pool.memset(s.v1[:, :, :, HD:HD + 1], 1.0).then_inc(pools, 1)
            pool.tensor_copy(s.v1[:, :, :, 0:HD], s.mv[:, :, :].rearrange("p i (h d) -> p i h d", h=HEADS)).then_inc(pools, 1)
            pool.wait_ge(acts, 3)
            pool.tensor_tensor(s.kw[:, :, :], s.natural[:, 16:24, :], over_last(c[:, WGT, :], P), ALU.mult).then_inc(pools, 1)

        @block.tensor
        def _(pe):
            for n, at in enumerate((2, 28, 31)):
                pe.wait_ge(vs, at)
                for q in range(2):
                    ins = pe.matmul(k.psum[:, 2 * n + q, :], k.ones[:, :], diag[:, 4 * q:4 * q + 4, :], start=True, stop=True)
                ins.then_inc(ps, 1)


def recurrences(k, s):
    V1 = HD + 1
    with ExitStack() as ctx, k.stage() as block:
        S = k.sb(ctx, "gdn_state", [P, HEADS, HD])
        C = k.sb(ctx, "mlstm_state", [P, HEADS, V1])
        vnew = k.sb(ctx, "v_new", [P, HEADS, HD])
        den = k.sb(ctx, "denominator", [P, 2, HEADS])
        ws, outs, dstate, mouts, mdstate, vns, gds, mds, rd, mrd = (k.sig.new() for _ in range(10))
        gl = s.glast[:, 0, :].rearrange("p (h n) -> p h n", h=HEADS)
        dec = s.glast[:, 1, :].rearrange("p (h n) -> p h n", h=HEADS)

        def quad(b, p=slice(0, P)):
            return k.psum[p, b, :].rearrange("p (h d) -> p h d", h=HEADS)

        def two(b, p=slice(0, P)):
            return k.psum[p, b:b + 2, 0:2 * V1].rearrange("p b (h d) -> p b h d", h=2)

        def by_bank(ap):
            return ap.rearrange("p (b h) d -> p b h d", b=2)

        @block.sync
        def _(sp):
            k.stream(sp)

        @block.tensor
        def _(pe):
            for n in range(NCHUNK):
                tile, half = n // 2, n % 2
                p = slice(half * CHUNK, (half + 1) * CHUNK)
                if n > 0:
                    pe.wait_ge(gds, 2 * n + 1)
                    for h in range(HEADS):
                        ins = pe.matmul(k.psum[p, 0, h * HD:(h + 1) * HD], s.wT[:, 2 * h + tile, p], S[:, h, :],
                                        start=True, stop=True)
                    ins.then_inc(ws, 1)
                    pe.wait_ge(mds, 2 * n + 1)
                    pe.wait_ge(mrd, n)
                for h in range(HEADS):
                    o = k.psum[p, 3 + h // 2, (h % 2) * V1:(h % 2 + 1) * V1]
                    if n > 0:
                        pe.matmul(o, s.mqdT[:, 2 * h + tile, p], C[:, h, :], start=True, stop=False)
                    ins = pe.matmul(o, s.mqkT[p, 2 * h + tile, p], s.v1[p, tile, h, :], start=(n == 0), stop=True)
                ins.then_inc(mouts, 1)
                for h in range(HEADS):
                    ins = pe.matmul(k.psum[:, 5 + h // 2, (h % 2) * V1:(h % 2 + 1) * V1], s.kw[p, 2 * h + tile, :],
                                    s.v1[p, tile, h, :], start=True, stop=True)
                ins.then_inc(mdstate, 1)
                pe.wait_ge(vns, n + 1)
                for h in range(HEADS):
                    ins = pe.matmul(k.psum[:, 2, h * HD:(h + 1) * HD], s.kd[p, 2 * h + tile, :], vnew[p, h, :],
                                    start=True, stop=True)
                ins.then_inc(dstate, 1)
                if n > 0:
                    pe.wait_ge(rd, n)
                for h in range(HEADS):
                    o = k.psum[p, 1, h * HD:(h + 1) * HD]
                    if n > 0:
                        pe.matmul(o, s.qdT[:, 2 * h + tile, p], S[:, h, :], start=True, stop=False)
                    ins = pe.matmul(o, s.qkT[p, 2 * h + tile, p], vnew[p, h, :], start=(n == 0), stop=True)
                ins.then_inc(outs, 1)

        @block.vector
        def _(dve):
            dve.memset(S[:, :, :], 0.0).then_inc(gds, 1)
            dve.memset(C[:, :, :], 0.0).then_inc(mds, 1)
            for n in range(NCHUNK):
                tile, half = n // 2, n % 2
                p = slice(half * CHUNK, (half + 1) * CHUNK)
                u = s.u[p, :, :].rearrange("p (h i) d -> p h i d", i=TILES)[:, :, tile, :]
                if n == 0:
                    dve.tensor_copy(vnew[p, :, :], u).then_inc(vns, 1)
                else:
                    dve.wait_ge(ws, n)
                    dve.tensor_tensor(vnew[p, :, :], u, quad(0, p), ALU.subtract).then_inc(vns, 1)
                if n == NCHUNK - 1:
                    continue
                dve.wait_ge(mds, 2 * n + 1)
                dve.wait_ge(mouts, n + 1)
                dve.tensor_tensor(C[:, :, :], C[:, :, :], over_last(dec[:, :, n], V1), ALU.mult).then_inc(mds, 1)
                dve.wait_ge(mds, 2 * n + 2)
                dve.wait_ge(mdstate, n + 1)
                dve.tensor_tensor(by_bank(C[:, :, :]), by_bank(C[:, :, :]), two(5), ALU.add).then_inc(mds, 1)
                dve.wait_ge(outs, n + 1)
                dve.wait_ge(gds, 2 * n + 1)
                dve.tensor_tensor(S[:, :, :], S[:, :, :], over_last(gl[:, :, n], HD), ALU.mult).then_inc(gds, 1)
                dve.wait_ge(gds, 2 * n + 2)
                dve.wait_ge(dstate, n + 1)
                dve.tensor_tensor(S[:, :, :], S[:, :, :], quad(2), ALU.add).then_inc(gds, 1)

        @block.scalar
        def _(act):
            for n in range(NCHUNK):
                tile, half = n // 2, n % 2
                p = slice(half * CHUNK, (half + 1) * CHUNK)
                act.wait_ge(mouts, n + 1)
                act.activation(by_bank(s.mh[p, tile, :, :]), two(3, p), ACT.Copy).then_inc(mrd, 1)
                act.wait_ge(outs, n + 1)
                act.activation(s.go[p, tile, :, :], quad(1, p), ACT.Copy).then_inc(rd, 1)

        k.idle_pool(block)


def mixer_output(k, s, mixed):
    with ExitStack() as ctx, k.stage() as block:
        gain = k.sb(ctx, "head_gains", [P, HD + GW])
        sq = k.sb(ctx, "output_squares", [P, 2 * PAIRS, HD])
        c = k.sb(ctx, "output_columns", [P, 4, 2 * PAIRS])
        landed, vs, acts, pools = (k.sig.new() for _ in range(4))
        def heads(ap):
            return ap.rearrange("p i (h d) -> p i h d", h=HEADS)

        def per_head(col):
            return over_last(col, HD).rearrange("p (i h) d -> p i h d", h=HEADS)
        go, mo = mixed[:, :, 0:GW], mixed[:, :, GW:2 * GW]
        src_m = s.mh[:, :, :, 0:HD]
        sq_g, sq_m = (sq[:, 8 * n:8 * n + 8, :].rearrange("p (i h) d -> p i h d", h=HEADS) for n in range(2))

        @block.sync
        def _(sp):
            sp.dma_start(gain[:, 0:HD], k.a["gdn_norm_w"].partition_broadcast(P).rearrange("p a d -> p (a d)")).then_inc(landed, 16)
            sp.dma_start(gain[:, HD:], k.a["mlstm_norm_w"].partition_broadcast(P).rearrange("p a d -> p (a d)")).then_inc(landed, 16)
            k.stream(sp)

        @block.scalar
        def _(act):
            act.activation(sq_g, s.go[:, :, :, :], ACT.Square).then_inc(acts, 1)
            act.activation(s.z[:, :, :], s.z[:, :, :], ACT.Silu).then_inc(acts, 1)
            act.activation(s.mo[:, :, :], s.mo[:, :, :], ACT.Sigmoid).then_inc(acts, 1)
            act.wait_ge(vs, 4)
            act.activation(sq_m, heads(mo), ACT.Square).then_inc(acts, 1)
            act.wait_ge(vs, 6)
            act.activation(c[:, 2, :], c[:, 1, :], ACT.Sqrt, bias=k.eps[:, 0:1], scale=1.0 / HD).then_inc(acts, 1)

        @block.vector
        def _(dve):
            link = linker(dve, vs)
            d = c[:, 0, 0:8].rearrange("p (i h) -> p i h", h=HEADS)
            link(dve.scalar_tensor_tensor(d, s.mh[:, :, :, HD], -1.0, s.mh[:, :, :, HD], ALU.mult, ALU.max))
            link(dve.tensor_tensor(d, d, s.emt[:, :].rearrange("p (h i) -> p i h", h=HEADS), ALU.max))
            link(dve.reciprocal(c[:, 0, 0:8], c[:, 0, 0:8]))
            link(dve.tensor_tensor(heads(mo), src_m, per_head(c[:, 0, 0:8]), ALU.mult))
            dve.wait_ge(acts, 1)
            link(dve.tensor_reduce(c[:, 1, 0:8], sq[:, 0:8, :], AX_X, ALU.add))
            dve.wait_ge(acts, 4)
            link(dve.tensor_reduce(c[:, 1, 8:16], sq[:, 8:16, :], AX_X, ALU.add))
            dve.wait_ge(acts, 5)
            link(dve.reciprocal(c[:, 3, :], c[:, 2, :]))
            link(dve.tensor_tensor(heads(go), s.go[:, :, :, :], per_head(c[:, 3, 0:8]), ALU.mult))
            link(dve.tensor_tensor(heads(mo), heads(mo), per_head(c[:, 3, 8:16]), ALU.mult))
            dve.wait_ge(landed, 32)
            link(dve.tensor_tensor(heads(go), heads(go), over_middle(gain[:, 0:HD], PAIRS).rearrange("p (i h) d -> p i h d", h=HEADS), ALU.mult))
            link(dve.tensor_tensor(mo, mo, over_middle(gain[:, HD:], TILES), ALU.mult))
            link(dve.tensor_tensor(go, go, s.z[:, :, :], ALU.mult))
            link(dve.tensor_tensor(mo, mo, s.mo[:, :, :], ALU.mult))

        k.idle_pool(block)


class MixerState:

    def __init__(self, k, ctx):
        def sb(name, shape):
            return k.sb(ctx, name, shape)
        self.consts = sb("constants_sb", [P, NCONST, P])
        self.conv = sb("convolved_T", [P, 20, SEQ])
        self.z = sb("gdn_z", [P, TILES, GW])
        self.mv = sb("mlstm_v", [P, TILES, GW])
        self.mo = sb("mlstm_o", [P, TILES, GW])
        self.gates = sb("gates", [P, TILES, 16])
        self.beta = sb("beta", [P, TILES, HEADS])
        self.log_i = sb("log_i", [P, TILES, HEADS])
        self.logs = sb("log_alpha_f", [P, TILES, 2, HEADS])
        self.run = sb("running_logs", [P, 2, 2, PAIRS])
        self.total = sb("chunk_totals", [P, 2, HEADS * NCHUNK])
        self.glast = sb("chunk_decays", [P, 2, HEADS * NCHUNK])
        self.emt = sb("exp_minus_m", [P, PAIRS])

    def more(self, k, ctx):
        def mats(name):
            return k.sb(ctx, name, [P, PAIRS, P])
        self.natural = k.sb(ctx, "natural_k_v_mk", [P, 3 * PAIRS, P])
        self.qk_raw, self.mqk_raw = mats("key_query"), mats("mlstm_key_query")
        self.u, self.wT, self.qdT, self.kd = mats("u"), mats("w_T"), mats("q_decayed_T"), mats("k_decayed")
        self.qkT = self.qk_raw
        self.mqkT = self.mqk_raw
        self.mqdT = self.conv[:, 12:16, :].rearrange("p h (i n) -> p (h i) n", n=P)
        self.kw = self.natural[:, 16:24, :]
        self.v1 = k.sb(ctx, "mlstm_v_and_one", [P, TILES, HEADS, HD + 1])
        self.go = k.sb(ctx, "gdn_out", [P, TILES, HEADS, HD])
        self.mh = k.sb(ctx, "mlstm_out", [P, TILES, HEADS, HD + 1])

    def mask(self, n):
        return self.consts[:, n, :]



def cross_attention(k):
    a = k.a
    with ExitStack() as ctx:
        qT = k.sb(ctx, "xa_q_T", [P, DC, SEQ])
        kT = k.sb(ctx, "xa_k_T", [P, DC, SEQ])
        v = k.sb(ctx, "xa_v", [P, TILES, D])
        with ExitStack() as inner:
            mem = k.sb(inner, "memory", [P, TILES, D])
            memT = k.sb(inner, "memory_T", [P, DC, SEQ])
            with k.stage() as block:
                landed = k.sig.new()

                @block.sync
                def _(sp):
                    sp.dma_start(mem[:, :, :], a["mem"][0].rearrange("(i p) d -> p i d", p=P)).then_inc(landed, 16)
                    k.stream(sp)
                    sp.wait_ge(landed, 16)

                k.idle_pool(block)
            norm_transpose(k, mem, memT, COL_MEM)
            norm_transpose(k, k.x, k.xT, COL_XA)
            panels(k, [("T", k.xT, qT[:, 2 * n:2 * n + 2, :], None, 1.0) for n in range(4)]
                   + [("T", memT, kT[:, 2 * n:2 * n + 2, :], None, 1.0) for n in range(4)])
            rows_product(k, memT, 4, copy_to(k, v))
        attend_memory(k, qT, kT, v)
        rows_product(k, k.xT, 4, add_to(k, k.x))


def attend_memory(k, qT, kT, v):
    DH = D // HEADS
    scale = DH ** -0.5
    with ExitStack() as ctx, k.stage() as block:
        prob = k.sb(ctx, "xa_probabilities", [P, PAIRS, SEQ])
        probT = k.sb(ctx, "xa_probabilities_T", [P, HEADS, 2, SEQ])
        c = k.sb(ctx, "xa_columns", [P, 4, PAIRS])
        scored, maxed, negated, expd, recip, scaled, turned, copied, mixed, written = (k.sig.new() for _ in range(10))

        @block.sync
        def _(sp):
            k.stream(sp)

        @block.tensor
        def _(pe):
            for e in range(PAIRS):
                h, i = e // 2, e % 2
                for half in range(2):
                    ins = pe.matmul(k.psum[:, h, i * SEQ:(i + 1) * SEQ], qT[:, 2 * h + half, i * P:(i + 1) * P],
                                    kT[:, 2 * h + half, :], start=(half == 0), stop=(half == 1))
                if i == 1:
                    ins.then_inc(scored, 1)
            for h in range(HEADS):
                pe.wait_ge(scaled, h + 1)
                for i in range(TILES):
                    for m in range(2):
                        at = m * SEQ + i * P
                        ins = pe.transpose(k.psum[:, 4 + h, at:at + P], prob[:, 2 * h + i, m * P:(m + 1) * P], k.ident[:, :])
                ins.then_inc(turned, 1)
            for h in range(HEADS):
                pe.wait_ge(copied, h + 1)
                for half in range(2):
                    for m in range(2):
                        lo = h * DH + half * P
                        ins = pe.matmul(k.psum[:, h, half * SEQ:(half + 1) * SEQ], v[:, m, lo:lo + P],
                                        probT[:, h, m, :], start=(m == 0), stop=(m == 1))
                ins.then_inc(mixed, 1)

        @block.vector
        def _(dve):
            for h in range(HEADS):
                dve.wait_ge(scored, h + 1)
                dve.tensor_reduce(c[:, 0, 2 * h:2 * h + 2], bank2(k, h), AX_X, ALU.max).then_inc(maxed, 1)
                dve.wait_ge(maxed, h + 1)
                dve.tensor_scalar(c[:, 1, 2 * h:2 * h + 2], c[:, 0, 2 * h:2 * h + 2], -scale, None, ALU.mult).then_inc(negated, 1)
            for h in range(HEADS):
                dve.wait_ge(expd, 2 * (h + 1))
                dve.reciprocal(c[:, 3, 2 * h:2 * h + 2], c[:, 2, 2 * h:2 * h + 2]).then_inc(recip, 1)
                dve.wait_ge(recip, h + 1)
                part = prob[:, 2 * h:2 * h + 2, :]
                dve.tensor_tensor(part, part, over_last(c[:, 3, 2 * h:2 * h + 2], SEQ), ALU.mult).then_inc(scaled, 1)
            for h in range(HEADS):
                dve.wait_ge(mixed, h + 1)
                dve.tensor_copy(k.xT[:, 2 * h:2 * h + 2, :], bank2(k, h)).then_inc(written, 1)

        @block.scalar
        def _(act):
            for e in range(PAIRS):
                h, i = e // 2, e % 2
                act.wait_ge(negated, h + 1)
                act.activation(prob[:, e, :], k.psum[:, h, i * SEQ:(i + 1) * SEQ], ACT.Exp, bias=c[:, 1, e:e + 1],
                               scale=scale, accum_out=c[:, 2, e:e + 1]).then_inc(expd, 1)
            for h in range(HEADS):
                act.wait_ge(turned, h + 1)
                act.activation(probT[:, h, :, :], bank2(k, 4 + h), ACT.Copy).then_inc(copied, 1)

        k.idle_pool(block)



HALVES = 2 * PEER_HEADS
PICKS = PEER_HEADS * TOPK
LOW = -3.0e38


def peer(k):
    a = k.a
    with ExitStack() as ctx:
        picksT = k.sb(ctx, "picks_T", [P, 3, SEQ])
        iota = k.sb(ctx, "key_numbers", [P, P])
        norm_transpose(k, k.x, k.xT, COL_FFN)
        with ExitStack() as inner:
            qT = k.sb(inner, "peer_q_T", [P, HALVES, SEQ])
            keysT = k.sb(inner, "sub_keys_T", [P, HALVES, KEYS])
            panels(k, [("T", k.xT, qT[:, 2 * n:2 * n + 2, :], None, 1.0) for n in range(8)])
            turn_keys(k, keysT, iota)
            for tile in range(TILES):
                pick_experts(k, qT, keysT, iota, picksT, tile)
        with ExitStack() as inner:
            gates = k.sb(inner, "gate_matrix", [P, SEQ, KEYS])
            scatter_gates(k, picksT, iota, gates)
            every_expert(k, gates)
    final_norm(k)


def turn_keys(k, keysT, iota):
    with ExitStack() as ctx, k.stage() as block:
        keys = k.sb(ctx, "sub_keys", [P, HALVES, KEYS])
        landed, turned, copied, iota_landed = (k.sig.new() for _ in range(4))

        @block.sync
        def _(sp):
            src = k.a["peer_sub_keys"][0].rearrange("h s n d -> (h s) n d")
            for n in range(HALVES):
                sp.dma_start(keys[:, n, :], src[n]).then_inc(landed, 16)
            sp.dma_start(iota[:, :], k.a["constants"][:, C_IOTA * P:(C_IOTA + 1) * P]).then_inc(iota_landed, 16)
            k.stream(sp)
            sp.wait_ge(iota_landed, 16)

        @block.tensor
        def _(pe):
            pe.wait_ge(landed, 16 * HALVES)
            for b in range(4):
                for q in range(4):
                    ins = pe.transpose(k.psum[:, b, q * P:(q + 1) * P], keys[:, 4 * b + q, :], k.ident[:, :])
                ins.then_inc(turned, 1)

        @block.scalar
        def _(act):
            for b in range(4):
                act.wait_ge(turned, b + 1)
                act.activation(keysT[:, 4 * b:4 * b + 4, :], k.psum[:, b, :].rearrange("p (a n) -> p a n", a=4),
                               ACT.Copy).then_inc(copied, 1)

        k.idle_pool(block)


def pick_experts(k, qT, keysT, iota, picksT, tile):
    with ExitStack() as ctx, k.stage() as block:
        score = k.sb(ctx, "key_scores", [P, HALVES, KEYS])
        rest = k.sb(ctx, "scores_without_top", [P, HALVES, KEYS])
        top = k.sb(ctx, "top_scores", [P, HALVES, TOPK])
        topi = k.sb(ctx, "top_keys_int", [P, HALVES, TOPK], U32)
        topf = k.sb(ctx, "top_keys", [P, HALVES, TOPK])
        cand = k.sb(ctx, "candidates", [P, PEER_HEADS, TOPK, TOPK])
        crest = k.sb(ctx, "candidates_without_top", [P, PEER_HEADS, TOPK * TOPK])
        best = k.sb(ctx, "best", [P, PEER_HEADS, TOPK])
        pos = k.sb(ctx, "best_position", [P, PICKS], U32)
        ab = k.sb(ctx, "position_parts_int", [P, 2, PICKS], U32)
        abf = k.sb(ctx, "position_parts", [P, 2, PICKS])
        hit = k.sb(ctx, "position_hits", [P, 2, PICKS, TOPK])
        out3 = k.sb(ctx, "picks", [P, 3, PICKS])
        col = k.sb(ctx, "gate_sums", [P, 2, PEER_HEADS])
        scored, copied, found, vs, expd, turned, pools = (k.sig.new() for _ in range(7))

        @block.sync
        def _(sp):
            k.stream(sp)

        @block.tensor
        def _(pe):
            for b in range(4):
                for q in range(4):
                    n = 4 * b + q
                    ins = pe.matmul(k.psum[:, b, q * P:(q + 1) * P], qT[:, n, tile * P:(tile + 1) * P], keysT[:, n, :],
                                    start=True, stop=True)
                ins.then_inc(scored, 1)
            pe.wait_ge(vs, 10)
            for q in range(3):
                ins = pe.transpose(k.psum[:, 4, q * P:(q + 1) * P], out3[:, q, :], k.ident[:, :])
            ins.then_inc(turned, 1)

        @block.scalar
        def _(act):
            for b in range(4):
                act.wait_ge(scored, b + 1)
                act.activation(score[:, 4 * b:4 * b + 4, :], k.psum[:, b, :].rearrange("p (a n) -> p a n", a=4),
                               ACT.Copy).then_inc(copied, 1)
            act.wait_ge(vs, 2)
            act.activation(out3[:, 2, :], best[:, :, :].rearrange("p h n -> p (h n)"), ACT.Exp).then_inc(expd, 1)

        @block.vector
        def _(dve):
            steps = [0]

            def sweep(n, issue):
                for m in range(n):
                    issue(m).then_inc(found, 1)
                steps[0] += n
                dve.wait_ge(found, steps[0])

            def top16(n, values, without, v16, i16):
                sweep(n, lambda m: dve.max(v16(m, 0), values(m)))
                sweep(n, lambda m: dve.max_index(i16(m, 0), v16(m, 0), values(m)))
                sweep(n, lambda m: dve.match_replace(without(m), v16(m, 0), values(m), LOW))
                sweep(n, lambda m: dve.max(v16(m, 1), without(m)))
                sweep(n, lambda m: dve.max_index(i16(m, 1), v16(m, 1), without(m)))

            dve.wait_ge(copied, 4)
            top16(HALVES, lambda m: score[:, m, :], lambda m: rest[:, m, :],
                  lambda m, r: top[:, m, 8 * r:8 * r + 8], lambda m, r: topi[:, m, 8 * r:8 * r + 8])
            dve.tensor_copy(topf[:, :, :], topi[:, :, :]).then_inc(found, 1)
            pairs = top[:, :, :].rearrange("p (h s) n -> p h s n", s=2)
            for h in range(PEER_HEADS):
                dve.tensor_tensor(cand[:, h, :, :], over_last(pairs[:, h, 0, :], TOPK), over_middle(pairs[:, h, 1, :], TOPK),
                                  ALU.add).then_inc(found, 1)
            steps[0] += 9
            dve.wait_ge(found, steps[0])
            top16(PEER_HEADS, lambda m: cand[:, m, :, :].rearrange("p a b -> p (a b)"), lambda m: crest[:, m, :],
                  lambda m, r: best[:, m, 8 * r:8 * r + 8],
                  lambda m, r: pos[:, TOPK * m + 8 * r:TOPK * m + 8 * r + 8])
            link = linker(dve, vs)
            link(dve.tensor_copy(col[:, 0, :], best[:, :, 0]))
            link(dve.tensor_tensor(best[:, :, :], best[:, :, :], over_last(col[:, 0, :], TOPK), ALU.subtract))
            link(dve.tensor_scalar(ab[:, 0, :], pos[:, :], 4, None, ALU.logical_shift_right))
            link(dve.tensor_scalar(ab[:, 1, :], pos[:, :], 15, None, ALU.bitwise_and))
            link(dve.tensor_copy(abf[:, :, :], ab[:, :, :]))
            for s in range(2):
                link(dve.tensor_tensor(hit[:, s, :, :], over_last(abf[:, s, :], TOPK), over_middle(iota[:, 0:TOPK], PICKS),
                                       ALU.is_equal))
            keys = topf[:, :, :].rearrange("p (h s) n -> p s h n", s=2)
            for s in range(2):
                for h in range(PEER_HEADS):
                    part = hit[:, s, TOPK * h:TOPK * (h + 1), :]
                    dve.tensor_tensor(part, part, over_middle(keys[:, s, h, :], TOPK), ALU.mult).then_inc(found, 1)
            steps[0] += 2 * PEER_HEADS
            dve.wait_ge(found, steps[0])
            link(dve.tensor_reduce(out3[:, 0:2, :].rearrange("p s n -> p (s n)"),
                                   hit[:, :, :, :].rearrange("p s n a -> p (s n) a"), AX_X, ALU.add))
            dve.wait_ge(expd, 1)
            g = out3[:, 2, :].rearrange("p (h n) -> p h n", h=PEER_HEADS)
            dve.tensor_reduce(col[:, 0, :], g, AX_X, ALU.add).then_inc(found, 1)
            steps[0] += 1
            dve.wait_ge(found, steps[0])
            link(dve.reciprocal(col[:, 1, :], col[:, 0, :]))
            link(dve.tensor_tensor(g, g, over_last(col[:, 1, :], TOPK), ALU.mult))
            dve.wait_ge(turned, 1)
            link(dve.tensor_copy(picksT[:, :, tile * P:(tile + 1) * P],
                                 k.psum[:, 4, 0:3 * P].rearrange("p (a n) -> p a n", a=3)))

        k.idle_pool(block)


def scatter_gates(k, picksT, iota, gates):
    GROUP = 4
    TURN = 2 * GROUP
    with ExitStack() as ctx, k.stage() as block:
        rows = [k.sb(ctx, f"row_onehot_{b}", [P, GROUP, P]) for b in range(2)]
        cols = [k.sb(ctx, f"column_onehot_{b}", [P, GROUP, P]) for b in range(2)]
        rows_hit, rows_ready, cols_ready, made, emptied = (k.sig.new() for _ in range(5))
        turns = SEQ // TURN

        @block.sync
        def _(sp):
            k.stream(sp)

        def hits(dve, t, b):
            for which, dst, count in ((0, rows[b], rows_hit), (1, cols[b], cols_ready)):
                dve.tensor_tensor(dst[:, :, :], over_middle(iota[:, :], GROUP),
                                  over_last(picksT[:, which, bass.ds(t, GROUP)], P), ALU.is_equal).then_inc(count, 1)

        def weigh(pool, t, b):
            pool.tensor_tensor(rows[b][:, :, :], rows[b][:, :, :],
                               over_last(picksT[:, 2, bass.ds(t, GROUP)], P), ALU.mult).then_inc(rows_ready, 1)

        @block.vector
        def _(dve):
            for b in range(2):
                hits(dve, GROUP * b, b)
            with dve.Fori(1, turns) as i:
                for b in range(2):
                    dve.wait_ge(made, 2 * i - 1 + b)
                    hits(dve, TURN * i + GROUP * b, b)

        @block.gpsimd
        def _(pool):
            k.sig.clear_other(pool)
            with pool.Fori(0, turns) as i:
                for b in range(2):
                    pool.wait_ge(rows_hit, 2 * i + 1 + b)
                    weigh(pool, TURN * i + GROUP * b, b)

        def products(pe, b, ready, empty=None):
            pe.wait_ge(rows_ready, ready)
            pe.wait_ge(cols_ready, ready)
            if empty is not None:
                pe.wait_ge(emptied, empty)
            for q in range(GROUP):
                ins = pe.matmul(k.psum[:, b, q * P:(q + 1) * P], rows[b][:, q, :], cols[b][:, q, :], start=True, stop=True)
            ins.then_inc(made, 1)

        @block.tensor
        def _(pe):
            for b in range(2):
                products(pe, b, b + 1)
            with pe.Fori(1, turns) as i:
                for b in range(2):
                    products(pe, b, 2 * i + 1 + b, 2 * i - 1 + b)

        @block.scalar
        def _(act):
            with act.Fori(0, turns) as i:
                for b in range(2):
                    act.wait_ge(made, 2 * i + 1 + b)
                    act.activation(gates[:, bass.ds(TURN * i + GROUP * b, GROUP), :],
                                   k.psum[:, b, :].rearrange("p (a n) -> p a n", a=GROUP), ACT.Copy).then_inc(emptied, 1)


def every_expert(k, gates):
    TURN = 6
    turns = (KEYS - 2) // TURN
    assert KEYS == 2 + TURN * turns
    g0 = k.w.take(KEYS)
    with ExitStack() as ctx, k.stage() as block:
        uT = [k.sb(ctx, f"u_T_{b}", [P, DC, P]) for b in range(2)]
        wgt = [k.sb(ctx, f"weighted_{b}", [P, SEQ]) for b in range(2)]
        first_turned, second_turned, act_copied, dve_copied, products, gelus, weights, outs, added = \
            (k.sig.new() for _ in range(9))
        turned_half = (first_turned, second_turned)

        def slot(m, what):
            return g0 + 2 * (m // 2) + what

        @block.sync
        def _(sp):
            k.stream(sp)

        def turn_u(pe, m, i):
            g = slot(m, 0)
            if m % 2 == 0:
                use_slot(pe, k, g, g // RING + i)
            u = k.w.rows(g)[:, m % 2, :]
            for half in range(2):
                n = 2 * m + half
                if n >= 3:
                    last = n - 3
                    if last % 2 == 0:
                        pe.wait_ge(act_copied, last // 2 + 1 + TURN * i)
                    else:
                        pe.wait_ge(dve_copied, last // 2 + 1 + TURN * i)
                for q in range(4):
                    c = 4 * half + q
                    ins = pe.transpose(k.psum[:, 4 + n % 3, q * P:(q + 1) * P], u[:, c * P:(c + 1) * P], k.ident[:, :])
                if half == 1 and m % 2 == 1:
                    ins.then_inc(k.w.used[g % RING], 1)
                else:
                    ins.then_inc(turned_half[half], 1)

        def u_products(pe, m, i):
            pe.wait_ge(act_copied, m + 1 + TURN * i)
            pe.wait_ge(dve_copied, m + 1 + TURN * i)
            if m >= 1:
                pe.wait_ge(gelus, m + TURN * i)
            for c in range(DC):
                ins = pe.matmul(k.psum[:, 7, 0:SEQ], uT[m % 2][:, c, :], k.xT[:, c, :], start=(c == 0), stop=(c == DC - 1))
            ins.then_inc(products, 1)

        def v_products(pe, m, i, stop=False):
            g = slot(m, 1)
            if m % 2 == 0:
                use_slot(pe, k, g, g // RING + i)
            pe.wait_ge(weights, m + 1 + TURN * i)
            v = k.w.rows(g)[:, m % 2, :]
            ins = down(pe, k, wgt[m % 2][:, :], v, m == 0, stop)
            if m % 2 == 1:
                ins.then_inc(k.w.used[g % RING], 1)
            else:
                ins.then_inc(outs, 1)

        def v_done(engine, m, i):
            if m % 2 == 1:
                g = slot(m, 1)
                engine.wait_ge(k.w.used[g % RING], g // RING + 1 + i)
            else:
                engine.wait_ge(outs, m // 2 + 1 + TURN // 2 * i)

        @block.tensor
        def _(pe):
            turn_u(pe, 0, 0)
            turn_u(pe, 1, 0)
            u_products(pe, 0, 0)

            def step(m, i):
                turn_u(pe, m + 1, i)
                u_products(pe, m, i)
                v_products(pe, m - 1, i)
            for m in range(1, 1 + TURN):
                step(m, 0)
            with pe.Fori(0, turns - 1) as i:
                for m in range(1 + TURN, 1 + 2 * TURN):
                    step(m, i)
            u_products(pe, KEYS - 1, 0)
            v_products(pe, KEYS - 2, 0)
            v_products(pe, KEYS - 1, 0, True)

        def copy_u(engine, m, i, half):
            n = 2 * m + half
            if half == 0:
                engine.wait_ge(turned_half[0], m + 1 + TURN * i)
            elif m % 2 == 0:
                engine.wait_ge(turned_half[1], m // 2 + 1 + TURN // 2 * i)
            else:
                used_slot(engine, k, slot(m, 0), slot(m, 0) // RING + i)
            if m >= 2:
                engine.wait_ge(products, m - 1 + TURN * i)
            src = k.psum[:, 4 + n % 3, :].rearrange("p (a n) -> p a n", a=4)
            return uT[m % 2][:, 4 * half:4 * half + 4, :], src

        @block.scalar
        def _(act):
            def copy(m, i):
                dst, src = copy_u(act, m, i, 0)
                act.activation(dst, src, ACT.Copy).then_inc(act_copied, 1)

            def gelu_of(m, i):
                act.wait_ge(products, m + 1 + TURN * i)
                if m >= 2:
                    v_done(act, m - 2, i)
                act.activation(wgt[m % 2][:, :], k.psum[:, 7, 0:SEQ], ACT.Gelu).then_inc(gelus, 1)

            def step(m, i):
                copy(m + 1, i)
                gelu_of(m, i)
            copy(0, 0)
            copy(1, 0)
            gelu_of(0, 0)
            for m in range(1, 1 + TURN):
                step(m, 0)
            with act.Fori(0, turns - 1) as i:
                for m in range(1 + TURN, 1 + 2 * TURN):
                    step(m, i)
            gelu_of(KEYS - 1, 0)

        @block.vector
        def _(dve):
            def copy(m, i):
                dst, src = copy_u(dve, m, i, 1)
                dve.tensor_copy(dst, src).then_inc(dve_copied, 1)

            def weigh(m, i):
                dve.wait_ge(gelus, m + 1 + TURN * i)
                dve.tensor_tensor(wgt[m % 2][:, :], wgt[m % 2][:, :],
                                  gates[:, :, bass.ds(m + TURN * i, 1)].rearrange("p t o -> p (t o)"),
                                  ALU.mult).then_inc(weights, 1)

            def step(m, i):
                copy(m + 1, i)
                weigh(m, i)
            copy(0, 0)
            copy(1, 0)
            weigh(0, 0)
            for m in range(1, 1 + TURN):
                step(m, 0)
            with dve.Fori(0, turns - 1) as i:
                for m in range(1 + TURN, 1 + 2 * TURN):
                    step(m, i)
            weigh(KEYS - 1, 0)
            used_slot(dve, k, slot(KEYS - 1, 1))
            for t in range(TILES):
                dve.tensor_tensor(k.x[:, t, :], accumulated(k, t), k.x[:, t, :], ALU.add).then_inc(added, 1)

        k.idle_pool(block)


def final_norm(k):
    with ExitStack() as ctx, k.stage() as block:
        gain = k.sb(ctx, "final_gain", [P, D])
        sq = k.sb(ctx, "final_squares", [P, TILES, D])
        stat = k.sb(ctx, "final_stats", [P, 3, TILES])
        landed, squares, rooted, vs = (k.sig.new() for _ in range(4))

        @block.sync
        def _(sp):
            sp.dma_start(gain[:, :], k.a["norm_final_w"].partition_broadcast(P)).then_inc(landed, 16)
            k.stream(sp)

        @block.scalar
        def _(act):
            for i in range(TILES):
                act.activation(sq[:, i, :], k.x[:, i, :], ACT.Square, accum_out=stat[:, 0, i:i + 1]).then_inc(squares, 1)
            act.wait_ge(squares, TILES)
            act.activation(stat[:, 1, :], stat[:, 0, :], ACT.Sqrt, bias=k.eps[:, 0:1], scale=1.0 / D).then_inc(rooted, 1)

        @block.vector
        def _(dve):
            link = linker(dve, vs)
            dve.wait_ge(rooted, 1)
            link(dve.reciprocal(stat[:, 2, :], stat[:, 1, :]))
            dve.wait_ge(landed, 16)
            for i in range(TILES):
                link(dve.scalar_tensor_tensor(k.x[:, i, :], k.x[:, i, :], stat[:, 2, i:i + 1], gain[:, :], ALU.mult, ALU.mult))

        k.idle_pool(block)



def load_gains(k, sp, gains, landed, which):
    layer, n = divmod(which, 3)
    sp.dma_start(gains[:, 0, :], k.a["ln_g_2"][layer, n].partition_broadcast(P)).then_inc(landed, 16)
    sp.dma_start(gains[:, 1, :], k.a["ln_b_2"][layer, n].partition_broadcast(P)).then_inc(landed, 16)


def post_norm(k, gains):
    with ExitStack() as ctx, k.stage() as block:
        sq = k.sb(ctx, "centred_squares", [P, TILES, D])
        stat = k.sb(ctx, "norm_stats", [P, 5, TILES])
        summed, negated, squared, rooted, recip, scaled, gained, normed, banks, written = (k.sig.new() for _ in range(10))

        @block.sync
        def _(sp):
            k.stream(sp)

        @block.vector
        def _(dve):
            for i in range(TILES):
                dve.scalar_tensor_tensor(k.x[:, i, :], k.x[:, i, :], DN_ALPHA, accumulated(k, i), ALU.mult, ALU.add,
                                         accum_out=stat[:, 0, i:i + 1]).then_inc(summed, 1)
                dve.wait_ge(summed, i + 1)
                dve.tensor_scalar(stat[:, 1, i:i + 1], stat[:, 0, i:i + 1], -1.0 / D, None, ALU.mult).then_inc(negated, 1)
            for i in range(TILES):
                dve.wait_ge(rooted, i + 1)
                dve.reciprocal(stat[:, 4, i:i + 1], stat[:, 3, i:i + 1]).then_inc(recip, 1)
                dve.wait_ge(recip, i + 1)
                dve.tensor_scalar(k.x[:, i, :], k.x[:, i, :], stat[:, 1, i:i + 1], stat[:, 4, i:i + 1], ALU.add,
                                  ALU.mult).then_inc(scaled, 1)
                dve.wait_ge(scaled, i + 1)
                dve.tensor_tensor(k.x[:, i, :], k.x[:, i, :], gains[:, 0, :], ALU.mult).then_inc(gained, 1)
                dve.wait_ge(gained, i + 1)
                dve.tensor_tensor(k.x[:, i, :], k.x[:, i, :], gains[:, 1, :], ALU.add).then_inc(normed, 1)
            for b in (0, 2):
                dve.wait_ge(banks, b + 1)
                dve.tensor_copy(k.xT[:, 2 * b:2 * b + 2, :], bank2(k, 4 + b)).then_inc(written, 1)

        @block.scalar
        def _(act):
            for i in range(TILES):
                act.wait_ge(negated, i + 1)
                act.activation(sq[:, i, :], k.x[:, i, :], ACT.Square, bias=stat[:, 1, i:i + 1],
                               accum_out=stat[:, 2, i:i + 1]).then_inc(squared, 1)
                act.wait_ge(squared, i + 1)
                act.activation(stat[:, 3, i:i + 1], stat[:, 2, i:i + 1], ACT.Sqrt, bias=k.eps[:, 1:2],
                               scale=1.0 / D).then_inc(rooted, 1)
            for b in (1, 3):
                act.wait_ge(banks, b + 1)
                act.activation(k.xT[:, 2 * b:2 * b + 2, :], bank2(k, 4 + b), ACT.Copy).then_inc(written, 1)

        @block.tensor
        def _(pe):
            for i in range(TILES):
                pe.wait_ge(normed, i + 1)
                for c in range(DC):
                    at = (c % 2) * SEQ + i * P
                    ins = pe.transpose(k.psum[:, 4 + c // 2, at:at + P], k.x[:, i, c * P:(c + 1) * P], k.ident[:, :])
                    if i == TILES - 1 and c % 2 == 1:
                        ins.then_inc(banks, 1)

        k.idle_pool(block)


def swiglu(k, gains, which):
    UNITS = FFN_DIM // COLS
    TURN = 2
    turns = (UNITS - 1) // TURN
    assert UNITS == 1 + TURN * turns
    g0 = k.w.take(3 * UNITS)
    with ExitStack() as ctx, k.stage() as block:
        act_out = [k.sb(ctx, f"silu_{b}", [P, 2, SEQ]) for b in range(2)]
        hidden = [k.sb(ctx, f"hidden_{b}", [P, 2, SEQ]) for b in range(2)]
        gains_landed, silus, hiddens = (k.sig.new() for _ in range(3))

        def slot_used(engine, u, which_slot, i):
            g = g0 + 3 * u + which_slot
            used_slot(engine, k, g, g // RING + i)

        @block.sync
        def _(sp):
            load_gains(k, sp, gains, gains_landed, which)
            k.stream(sp)
            sp.wait_ge(gains_landed, 32)

        def up(pe, u, i):
            for n in range(2):
                g = g0 + 3 * u + n
                if u >= 2:
                    pe.wait_ge((silus, hiddens)[n], u - 1 + TURN * i)
                use_slot(pe, k, g, g // RING + i)
                w = k.w.panel(g)
                for j in range(2):
                    for c in range(DC):
                        ins = pe.matmul(k.psum[:, 4 + 2 * (u % 2) + n, j * SEQ:(j + 1) * SEQ], w[:, c, j * P:(j + 1) * P],
                                        k.xT[:, c, :], start=(c == 0), stop=(c == DC - 1))
                ins.then_inc(k.w.used[g % RING], 1)

        def down_unit(pe, u, i):
            g = g0 + 3 * u + 2
            use_slot(pe, k, g, g // RING + i)
            pe.wait_ge(hiddens, u + 1 + TURN * i)
            for r in range(2):
                ins = down(pe, k, hidden[u % 2][:, r, :], k.w.rows(g)[:, r, :], u == 0 and r == 0, u == UNITS - 1 and r == 1)
            ins.then_inc(k.w.used[g % RING], 1)

        @block.tensor
        def _(pe):
            up(pe, 0, 0)
            for u in range(1, 1 + TURN):
                up(pe, u, 0)
                down_unit(pe, u - 1, 0)
            with pe.Fori(0, turns - 1) as i:
                for u in range(1 + TURN, 1 + 2 * TURN):
                    up(pe, u, i)
                    down_unit(pe, u - 1, i)
            down_unit(pe, UNITS - 1, 0)

        def silu(act, u, i):
            slot_used(act, u, 0, i)
            if u >= 2:
                act.wait_ge(hiddens, u - 1 + TURN * i)
            act.activation(act_out[u % 2][:, :, :], bank2(k, 4 + 2 * (u % 2)), ACT.Silu).then_inc(silus, 1)

        def gate(dve, u, i):
            slot_used(dve, u, 1, i)
            dve.wait_ge(silus, u + 1 + TURN * i)
            if u >= 2:
                slot_used(dve, u - 2, 2, i)
            dve.scalar_tensor_tensor(hidden[u % 2][:, :, :], act_out[u % 2][:, :, :], 0.5, bank2(k, 5 + 2 * (u % 2)),
                                     ALU.mult, ALU.mult).then_inc(hiddens, 1)

        def loops(engine, work):
            for u in range(0, 1 + TURN):
                work(engine, u, 0)
            with engine.Fori(0, turns - 1) as i:
                for u in range(1 + TURN, 1 + 2 * TURN):
                    work(engine, u, i)

        @block.scalar
        def _(act):
            loops(act, silu)

        @block.vector
        def _(dve):
            loops(dve, gate)

        k.idle_pool(block)
    post_norm(k, gains)


def gains_only(k, gains, which):
    def finish(ctx, block, last):
        landed = k.sig.new()

        @block.scalar
        def _(act):
            load_gains(k, act, gains, landed, which)
            act.wait_ge(landed, 32)
    return finish


def spatial_gating(k, gains):
    with ExitStack() as ctx:
        gatedT = k.sb(ctx, "sgu_u_T", [P, 16, SEQ])
        with ExitStack() as inner:
            v = k.sb(inner, "sgu_v", [P, TILES, SGU_HALF])
            panels(k, [("T", k.xT, gatedT[:, 2 * n:2 * n + 2, :], ACT.Gelu, 1.0) for n in range(8)]
                   + [("N", k.xT, v[:, :, n * COLS:(n + 1) * COLS], ACT.Gelu, 1.0) for n in range(8)])
            mix_tokens(k, v, gatedT)
        rows_product(k, gatedT, 8, gains_only(k, gains, 1))
    post_norm(k, gains)


def mix_tokens(k, v, gatedT):
    with ExitStack() as ctx, k.stage() as block:
        gb = k.sb(ctx, "sgu_gain_bias", [P, 2, SGU_HALF])
        ws = k.sb(ctx, "sgu_ws", [P, SGU_GROUPS, P])
        wsT = k.sb(ctx, "sgu_ws_T", [P, SGU_GROUPS, P])
        bs = k.sb(ctx, "sgu_bias", [P, SGU_GROUPS, P])
        causal = k.sb(ctx, "sgu_causal", [P, P])
        sq = k.sb(ctx, "sgu_squares", [P, TILES, SGU_HALF])
        stat = k.sb(ctx, "sgu_stats", [P, 5, TILES])
        ws_landed, gb_landed, turned, masked, summed, negated, squared, rooted, recip, scaled, gained, normed, mixed, \
            biased, gated = (k.sig.new() for _ in range(15))
        a = k.a

        @block.sync
        def _(sp):
            sp.dma_start(ws[:, :, :], a["sgu_w_s_2"][0].rearrange("g t s -> t g s")).then_inc(ws_landed, 16)
            sp.dma_start(causal[:, :], a["constants"][:, C_CAUSAL_T * P:(C_CAUSAL_T + 1) * P]).then_inc(ws_landed, 16)
            sp.dma_start(bs[:, :, :].rearrange("p g t -> p (g t)"),
                         a["sgu_b_s_2"][0].rearrange("g t -> (g t)").partition_broadcast(P)).then_inc(ws_landed, 16)
            sp.dma_start(gb[:, 0, :], a["sgu_ln_g_2"][0].partition_broadcast(P)).then_inc(gb_landed, 16)
            sp.dma_start(gb[:, 1, :], a["sgu_ln_b_2"][0].partition_broadcast(P)).then_inc(gb_landed, 16)
            k.stream(sp)

        @block.tensor
        def _(pe):
            pe.wait_ge(ws_landed, 48)
            for b in range(2):
                for q in range(4):
                    ins = pe.transpose(k.psum[:, b, q * P:(q + 1) * P], ws[:, 4 * b + q, :], k.ident[:, :])
                ins.then_inc(turned, 1)
            pe.wait_ge(masked, 2)
            pe.wait_ge(normed, TILES)
            for g in range(SGU_GROUPS):
                for half in range(2):
                    for i in range(TILES):
                        lo = g * COLS + half * P
                        at = half * SEQ + i * P
                        ins = pe.matmul(k.psum[:, g, at:at + P], v[:, i, lo:lo + P], wsT[:, g, :], start=True, stop=True)
                ins.then_inc(mixed, 1)

        @block.scalar
        def _(act):
            for i in range(TILES):
                act.wait_ge(negated, i + 1)
                act.activation(sq[:, i, :], v[:, i, :], ACT.Square, bias=stat[:, 1, i:i + 1],
                               accum_out=stat[:, 2, i:i + 1]).then_inc(squared, 1)
                act.wait_ge(squared, i + 1)
                act.activation(stat[:, 3, i:i + 1], stat[:, 2, i:i + 1], ACT.Sqrt, bias=k.eps[:, 1:2],
                               scale=1.0 / SGU_HALF).then_inc(rooted, 1)

        @block.vector
        def _(dve):
            for i in range(TILES):
                dve.tensor_reduce(stat[:, 0, i:i + 1], v[:, i, :], AX_X, ALU.add).then_inc(summed, 1)
                dve.wait_ge(summed, i + 1)
                dve.tensor_scalar(stat[:, 1, i:i + 1], stat[:, 0, i:i + 1], -1.0 / SGU_HALF, None, ALU.mult).then_inc(negated, 1)
            dve.wait_ge(ws_landed, 48)
            for b in range(2):
                dve.wait_ge(turned, b + 1)
                dve.tensor_tensor(wsT[:, 4 * b:4 * b + 4, :], k.psum[:, b, :].rearrange("p (a n) -> p a n", a=4),
                                  over_middle(causal[:, :], 4), ALU.mult).then_inc(masked, 1)
            dve.wait_ge(gb_landed, 32)
            for i in range(TILES):
                dve.wait_ge(rooted, i + 1)
                dve.reciprocal(stat[:, 4, i:i + 1], stat[:, 3, i:i + 1]).then_inc(recip, 1)
                dve.wait_ge(recip, i + 1)
                dve.tensor_scalar(v[:, i, :], v[:, i, :], stat[:, 1, i:i + 1], stat[:, 4, i:i + 1], ALU.add,
                                  ALU.mult).then_inc(scaled, 1)
                dve.wait_ge(scaled, i + 1)
                dve.tensor_tensor(v[:, i, :], v[:, i, :], gb[:, 0, :], ALU.mult).then_inc(gained, 1)
                dve.wait_ge(gained, i + 1)
                dve.tensor_tensor(v[:, i, :], v[:, i, :], gb[:, 1, :], ALU.add).then_inc(normed, 1)
            work = sq[:, :, :].rearrange("p i (c n) -> p (i c) n", n=P)
            for g in range(SGU_GROUPS):
                dve.wait_ge(mixed, g + 1)
                part = work[:, 4 * g:4 * g + 4, :]
                dve.tensor_tensor(part, k.psum[:, g, :].rearrange("p (a n) -> p a n", a=4), over_middle(bs[:, g, :], 4),
                                  ALU.add).then_inc(biased, 1)
                dve.wait_ge(biased, g + 1)
                dst = gatedT[:, 2 * g:2 * g + 2, :]
                dve.tensor_tensor(dst, dst, part.rearrange("p (a b) n -> p a (b n)", a=2), ALU.mult).then_inc(gated, 1)

        k.idle_pool(block)


class SharedKV:

    def __init__(self, k, ctx):
        self.k_sel = k.sb(ctx, "k_sel_T", [P, KVG, SEQ])
        self.k_win = k.sb(ctx, "k_win_T", [P, KVG, SEQ])
        self.v_sel = k.sb(ctx, "v_sel", [P, TILES, KVG * HDIM])
        self.v_win = k.sb(ctx, "v_win", [P, TILES, KVG * HDIM])
        self.k_cmp = k.sb(ctx, "k_cmp_T", [P, KVG, 16])
        self.v_cmp = k.sb(ctx, "v_cmp", [16, KVG, HDIM])
        self.bias = k.sb(ctx, "position_bias", [P, NH, BIAS_W])


def shared_kv(k, s):
    with ExitStack() as ctx:
        raw = [k.sb(ctx, f"kv_T_{n}", [P, 2, SEQ]) for n in range(4)]
        panels(k, [("T", k.xT, raw[0][:, :, :], None, 1.0), ("T", k.xT, raw[1][:, :, :], None, 1.0),
                   ("T", k.xT, raw[2][:, :, :], None, 1.0), ("N", k.xT, s.v_sel[:, :, :], None, 1.0),
                   ("T", k.xT, raw[3][:, :, :], None, 1.0), ("N", k.xT, s.v_win[:, :, :], None, 1.0)])
        compress(k, s, raw)


def compress(k, s, raw):
    J = CMP_LEN // 2
    g0 = k.w.take(4)
    GN = KVG * NCMP
    with ExitStack() as ctx, k.stage() as block:
        two = [k.sb(ctx, f"token_pairs_{n}", [P, KVG, SEQ]) for n in range(2)]
        blocks = [k.sb(ctx, f"cmp_blocks_{n}", [P, J, KVG, NCMP]) for n in range(2)]
        hid = k.sb(ctx, "cmp_hidden", [P, 2, 2, GN])
        pe_rows = k.sb(ctx, "cmp_pe_rows", [2 * J, P])
        pe_cols = k.sb(ctx, "cmp_pe_columns", [P, 2 * J])
        w2 = k.sb(ctx, "cmp_w2", [P, 2, 2, HDIM])
        landed, vs, paired, pe_turned, blocked, gelud, outs, copied = (k.sig.new() for _ in range(8))
        half = [slice(0, HDIM), slice(HDIM, P)]

        @block.sync
        def _(sp):
            sp.dma_start(pe_rows[:, :], k.a["cmp_pe_2"].rearrange("s (j l) d -> (s j) (l d)", l=2)).then_inc(landed, 16)
            sp.dma_start(w2[:, :, :, :], k.a["cmp_w2_2"].rearrange("s (c p) d -> p s c d", p=P)).then_inc(landed, 16)
            k.stream(sp)

        @block.vector
        def _(dve):
            dve.wait_ge(pe_turned, 1)
            dve.tensor_copy(pe_cols[:, :], k.psum[:, 7, 0:2 * J]).then_inc(vs, 1)
            for n in range(2):
                for g in range(KVG):
                    src = raw[n][half[g % 2], g // 2, :]
                    dve.tensor_copy(two[n][half[0], g, :], src).then_inc(paired, 1)
                    dve.tensor_copy(two[n][half[1], g, 0:SEQ - 1], src[:, 1:SEQ]).then_inc(paired, 1)
            dve.wait_ge(paired, 4 * KVG)
            dve.wait_ge(vs, 1)
            for n in range(2):
                for j in range(J):
                    src = two[n][:, :, 2 * j:2 * j + CMP_STRIDE * (NCMP - 1) + 1:CMP_STRIDE]
                    ins = dve.tensor_scalar(blocks[n][:, j, :, :], src, pe_cols[:, J * n + j:J * n + j + 1], None, ALU.add)
                ins.then_inc(blocked, 1)
            for which, dst in ((2, s.k_sel), (3, s.k_win)):
                for g in range(KVG):
                    for h in range(2):
                        dve.tensor_copy(dst[half[h], g, :], raw[which][half[g % 2], g // 2, :]).then_inc(copied, 1)
            dve.wait_ge(outs, 1)
            for h in range(2):
                dve.tensor_copy(s.k_cmp[half[h], :, 0:NCMP], k.psum[half[h], 4, 0:GN].rearrange("p (g n) -> p g n", g=KVG)
                                ).then_inc(copied, 1)
            dve.wait_ge(outs, 2)
            dve.tensor_copy(s.v_cmp[0:NCMP, :, :], k.psum[0:NCMP, 5, 0:KVG * HDIM].rearrange("p (g d) -> p g d", g=KVG)
                            ).then_inc(copied, 1)

        @block.tensor
        def _(pe):
            pe.wait_ge(landed, 32)
            pe.transpose(k.psum[:, 7, 0:2 * J], pe_rows[:, :], k.ident[0:2 * J, 0:2 * J]).then_inc(pe_turned, 1)
            for n in range(2):
                pe.wait_ge(blocked, n + 1)
                for q in range(2):
                    use_slot(pe, k, g0 + 2 * n + q)
                for c in range(2):
                    for j in range(J):
                        w = k.w.panel(g0 + 2 * n + j // DC)
                        ins = pe.matmul(k.psum[:, 2 * n + c, 0:GN], w[:, j % DC, c * P:(c + 1) * P],
                                        blocks[n][:, j, :, :].rearrange("p g n -> p (g n)"), start=(j == 0), stop=(j == J - 1))
                        if c == 1 and j % DC == DC - 1:
                            ins.then_inc(k.w.used[(g0 + 2 * n + j // DC) % RING], 1)
            pe.wait_ge(gelud, 2)
            for h in range(2):
                for c in range(2):
                    ins = pe.matmul(k.psum[half[h], 4, 0:GN], w2[:, 0, c, :], hid[:, 0, c, :], start=(c == 0), stop=(c == 1))
            ins.then_inc(outs, 1)
            pe.wait_ge(gelud, 4)
            for g in range(KVG):
                for c in range(2):
                    ins = pe.matmul(k.psum[0:NCMP, 5, g * HDIM:(g + 1) * HDIM], hid[:, 1, c, g * NCMP:(g + 1) * NCMP],
                                    w2[:, 1, c, :], start=(c == 0), stop=(c == 1))
            ins.then_inc(outs, 1)

        @block.scalar
        def _(act):
            for n in range(2):
                used_slot(act, k, g0 + 2 * n + 1)
                for c in range(2):
                    act.activation(hid[:, n, c, :], k.psum[:, 2 * n + c, 0:GN], ACT.Gelu,
                                   bias=k.cols[:, COL_B1 + 2 * n + c:COL_B1 + 2 * n + c + 1]).then_inc(gelud, 1)

        k.idle_pool(block)


def position_bias(k, s):
    with ExitStack() as ctx, k.stage() as block:
        table = k.sb(ctx, "relative_table", [33, NH])
        onehot = k.sb(ctx, "bucket_onehot", [33, DISTS])
        rows = k.sb(ctx, "bias_by_distance", [NH, DISTS])
        landed, future, made, copied, stored, spread = (k.sig.new() for _ in range(6))

        @block.sync
        def _(sp):
            sp.dma_start(table[0:32, :], k.a["rel_table_2"]).then_inc(landed, 16)
            sp.dma_start(onehot[:, :], k.a["bucket_onehot"]).then_inc(landed, 16)
            k.stream(sp)
            sp.wait_ge(copied, 1)
            copies = k.a["bias_rows"]
            sp.dma_start(copies.rearrange("p h x -> h p x"), rows[:, :].unsqueeze(1).broadcast_to([NH, P, DISTS])
                         ).then_inc(stored, 16)
            sp.wait_ge(stored, 16)
            view = bass.AP(copies.tensor, SEQ // 2 - 1, [[NH * DISTS - 1, P], [DISTS, NH], [1, BIAS_W]])
            sp.dma_start(s.bias[:, :, :], view).then_inc(spread, 16)
            sp.wait_ge(spread, 16)

        @block.vector
        def _(dve):
            dve.memset(table[32:33, :], NEG).then_inc(future, 1)
            dve.wait_ge(made, 1)
            dve.tensor_copy(rows[:, :], k.psum[0:NH, 0, :]).then_inc(copied, 1)

        @block.tensor
        def _(pe):
            pe.wait_ge(landed, 32)
            pe.wait_ge(future, 1)
            pe.matmul(k.psum[0:NH, 0, :], table[:, :], onehot[:, :], start=True, stop=True).then_inc(made, 1)

        k.idle_pool(block)


def sparse_attention(k, s, gains):
    with ExitStack() as ctx:
        qT = k.sb(ctx, "nsa_q_T", [P, DC, SEQ])
        gates = k.sb(ctx, "nsa_gates", [P, TILES, 3 * NH])
        position_bias(k, s)
        view = k.a["nsa_w_qg_2"][0][:, NH * HDIM:NH * HDIM + 3 * NH].rearrange("(c p) n -> p c n", p=P)
        panels(k, [("T", k.xT, qT[:, 2 * n:2 * n + 2, :], None, HDIM ** -0.5) for n in range(4)],
               (view, k.xT, gates[:, :, :], ACT.Sigmoid, 3 * NH))
        attend(k, s, qT, gates)
    rows_product(k, k.xT, 4, gains_only(k, gains, 4))
    post_norm(k, gains)


def attend(k, s, qT, gates):
    E = NH * TILES
    with ExitStack() as ctx, k.stage() as block:
        masks = k.sb(ctx, "cmp_masks", [P, 2, 16])
        sc = [k.sb(ctx, f"scores_{b}", [P, 2, SEQ]) for b in range(2)]
        cs = [k.sb(ctx, f"cmp_scores_{b}", [P, 16]) for b in range(2)]
        pT = [k.sb(ctx, f"probabilities_T_{b}", [P, 4, P]) for b in range(2)]
        cT = [k.sb(ctx, f"cmp_probabilities_T_{b}", [16, P]) for b in range(2)]
        c = [k.sb(ctx, f"softmax_columns_{b}", [P, 3, 4]) for b in range(2)]
        landed, scored, biased, negmax, expd, vs, weighed, turned, copied, outs, written = (k.sig.new() for _ in range(11))

        def parts(e):
            h, i = e // 2, e % 2
            p = slice((h % 2) * HDIM, (h % 2 + 1) * HDIM)
            return h, i, h // 4, p

        @block.sync
        def _(sp):
            lo = C_MISC * P + 16
            sp.dma_start(masks[:, :, :], k.a["constants"][:, lo:lo + 32].rearrange("p (i n) -> p i n", i=2)).then_inc(landed, 16)
            k.stream(sp)

        def scores(pe, e):
            h, i, g, p = parts(e)
            if e >= 1:
                pe.wait_ge(biased, 2 * e)
            q = qT[p, h // 2, i * P:(i + 1) * P]
            pe.matmul(k.psum[:, e % 2, 0:SEQ], q, s.k_sel[p, g, :], start=True, stop=True)
            pe.matmul(k.psum[:, e % 2, SEQ:2 * SEQ], q, s.k_win[p, g, :], start=True, stop=True)
            pe.matmul(k.psum[:, 2, 0:NCMP], q, s.k_cmp[p, g, 0:NCMP], start=True, stop=True).then_inc(scored, 1)

        def turn(pe, e):
            pe.wait_ge(weighed, e + 1)
            if e >= 1:
                pe.wait_ge(copied, 2 * e)
            for n in range(4):
                pe.transpose(k.psum[:, 3 + 4 * (e % 2), n * P:(n + 1) * P], sc[e % 2][:, n // 2, (n % 2) * P:(n % 2 + 1) * P], k.ident[:, :])
            pe.transpose(k.psum[0:NCMP, 6, 0:P], cs[e % 2][:, 0:NCMP], k.ident[:, :]).then_inc(turned, 1)

        def mix(pe, e):
            h, i, g, p = parts(e)
            pe.wait_ge(copied, 2 * e + 2)
            j = h // 2
            if j >= 2 and e % 4 == 0:
                pe.wait_ge(written, j - 1)
            o = k.psum[p, 4 + j % 2, i * P:(i + 1) * P]
            d = slice(g * HDIM, (g + 1) * HDIM)
            for n in range(4):
                v = (s.v_sel, s.v_win)[n // 2]
                pe.matmul(o, v[:, n % 2, d], pT[e % 2][:, n, :], start=(n == 0), stop=False)
            pe.matmul(o, s.v_cmp[0:NCMP, g, :], cT[e % 2][0:NCMP, :], start=False, stop=True).then_inc(outs, 1)

        @block.tensor
        def _(pe):
            for e in range(E + 2):
                if e < E:
                    scores(pe, e)
                if 1 <= e <= E:
                    turn(pe, e - 1)
                if e >= 2:
                    mix(pe, e - 2)

        def bias_and_max(dve, e):
            h, i, g, p = parts(e)
            at = P * (TILES - 1 - i)
            dve.wait_ge(scored, e + 1)
            if e >= 2:
                dve.wait_ge(turned, e - 1)
            b = e % 2
            dve.tensor_tensor(sc[b][:, :, :], bank2(k, b), over_middle(s.bias[:, h, at:at + SEQ], 2), ALU.add).then_inc(biased, 1)
            last = at + CMP_LEN - 1 + CMP_STRIDE * (NCMP - 1)
            dve.tensor_tensor(cs[b][:, 0:NCMP], k.psum[:, 2, 0:NCMP], s.bias[:, h, at + CMP_LEN - 1:last + 1:CMP_STRIDE],
                              ALU.add).then_inc(biased, 1)
            dve.wait_ge(biased, 2 * e + 2)
            dve.tensor_reduce(c[b][:, 0, 0:2], sc[b][:, :, :], AX_X, ALU.max, negate=True).then_inc(negmax, 1)
            dve.tensor_reduce(c[b][:, 0, 2:3], cs[b][:, 0:NCMP], AX_X, ALU.max, negate=True).then_inc(negmax, 1)

        def weigh(dve, e):
            h, i, g, p = parts(e)
            b = e % 2
            dve.wait_ge(expd, 3 * e + 3)
            dve.tensor_tensor(cs[b][:, 0:NCMP], cs[b][:, 0:NCMP], masks[:, i, 0:NCMP], ALU.mult).then_inc(vs, 1)
            dve.wait_ge(vs, 5 * e + 1)
            dve.tensor_reduce(c[b][:, 1, 2:3], cs[b][:, 0:NCMP], AX_X, ALU.add).then_inc(vs, 1)
            dve.wait_ge(vs, 5 * e + 2)
            dve.tensor_scalar(c[b][:, 1, 0:3], c[b][:, 1, 0:3], 1e-30, None, ALU.max).then_inc(vs, 1)
            dve.wait_ge(vs, 5 * e + 3)
            dve.reciprocal(c[b][:, 2, 0:3], c[b][:, 1, 0:3]).then_inc(vs, 1)
            dve.wait_ge(vs, 5 * e + 4)
            for dst, src in ((slice(0, 2), slice(1, 3)), (slice(2, 3), slice(0, 1))):
                ins = dve.tensor_tensor(c[b][:, 2, dst], c[b][:, 2, dst], gates[:, i, 3 * h + src.start:3 * h + src.stop], ALU.mult)
            ins.then_inc(vs, 1)
            dve.wait_ge(vs, 5 * e + 5)
            dve.tensor_scalar(cs[b][:, 0:NCMP], cs[b][:, 0:NCMP], c[b][:, 2, 2:3], None, ALU.mult)
            dve.tensor_tensor(sc[b][:, :, :], sc[b][:, :, :], over_last(c[b][:, 2, 0:2], SEQ), ALU.mult).then_inc(weighed, 1)

        @block.vector
        def _(dve):
            dve.wait_ge(landed, 16)
            for e in range(E + 1):
                if e < E:
                    bias_and_max(dve, e)
                if e >= 1:
                    weigh(dve, e - 1)

        @block.scalar
        def _(act):
            def exps(e):
                b = e % 2
                act.wait_ge(negmax, 2 * e + 2)
                for n in range(2):
                    act.activation(sc[b][:, n, :], sc[b][:, n, :], ACT.Exp, bias=c[b][:, 0, n:n + 1],
                                   accum_out=c[b][:, 1, n:n + 1]).then_inc(expd, 1)
                act.activation(cs[b][:, 0:NCMP], cs[b][:, 0:NCMP], ACT.Exp, bias=c[b][:, 0, 2:3]).then_inc(expd, 1)

            def copy(e):
                b = e % 2
                act.wait_ge(turned, e + 1)
                if e >= 2:
                    act.wait_ge(outs, e - 1)
                act.activation(pT[b][:, :, :], k.psum[:, 3 + 4 * b, :].rearrange("p (a n) -> p a n", a=4), ACT.Copy).then_inc(copied, 1)
                act.activation(cT[b][0:NCMP, :], k.psum[0:NCMP, 6, 0:P], ACT.Copy).then_inc(copied, 1)

            def output(j):
                act.wait_ge(outs, 4 * (j + 1))
                act.activation(k.xT[:, j, :], k.psum[:, 4 + j % 2, 0:SEQ], ACT.Copy).then_inc(written, 1)

            for e in range(E + 1):
                if e < E:
                    exps(e)
                if e >= 1:
                    copy(e - 1)
                if e >= 5 and e % 4 == 1:
                    output((e - 5) // 4)
            output(NH // 2 - 1)

        k.idle_pool(block)


def second_block(k):
    with ExitStack() as ctx:
        gains = k.sb(ctx, "norm_gain_bias", [P, 2, D])
        transpose_natural(k, k.x, k.xT)
        swiglu(k, gains, 0)
        spatial_gating(k, gains)
        swiglu(k, gains, 2)
        s = SharedKV(k, ctx)
        shared_kv(k, s)
        swiglu(k, gains, 3)
        sparse_attention(k, s, gains)
        swiglu(k, gains, 5)


def column_panels(w, first=0):
    v = w.rearrange("(c p) n -> p c n", p=P)
    return lambda u: v[:, :, bass.ds(first + COLS * u, COLS)]


def row_slots(w, first=0):
    v = w.rearrange("(u r p) n -> u p r n", r=2, p=P)
    return lambda u: v[u, :, :, first:first + D]


def plan_weights(k):
    a, w = k.a, k.w
    w_in = a["w_in"][0]
    for first, n in ((0, 6), (1536, 2), (2056, 4), (3080, 2), (3592, 2)):
        w.add(n, column_panels(w_in, first))
    w.add(4, row_slots(a["w_out"][0]))
    w.add(4, column_panels(a["xa_wq"][0]))
    w.add(4, column_panels(a["xa_wkv"][0]))
    w.add(4, row_slots(a["xa_wkv"][0], D))
    w.add(4, row_slots(a["xa_wo"][0]))
    w.add(8, column_panels(a["peer_wq"][0]))
    u_pairs, v_pairs = (a[n][0].rearrange("(i j) d -> i j d", j=KEYS) for n in ("peer_u", "peer_v"))
    w.add(KEYS // 2, lambda u: u_pairs[:, bass.ds(2 * u, 2), :], lambda u: v_pairs[:, bass.ds(2 * u, 2), :])

    def ffn(layer, which):
        w2 = a["ffn_w2_2"][layer, which].rearrange("(u r p) n -> u p r n", r=2, p=P)
        w.add(FFN_DIM // COLS, column_panels(a["ffn_w1_2"][layer, which]), column_panels(a["ffn_w3_2"][layer, which]),
              lambda u: w2[u])
    ffn(0, 0)
    w.add(8, column_panels(a["sgu_w_in_2"][0]))
    w.add(8, column_panels(a["sgu_w_in_2"][0], SGU_HALF))
    w.add(8, row_slots(a["sgu_w_out_2"][0]))
    ffn(0, 1)
    w.add(SLOTS_KV, column_panels(a["kv_w_2"]))
    for n in range(2):
        v = a["cmp_w1_2"][n].rearrange("(u j p) n -> u p j n", j=DC, p=P)
        w.add(2, lambda u, v=v: v[u])
    ffn(1, 0)
    w.add(4, column_panels(a["nsa_w_qg_2"][0]))
    w.add(4, row_slots(a["nsa_w_o_2"][0]))
    ffn(1, 1)



def mixer(k):
    a = k.a
    with ExitStack() as ctx:
        s = MixerState(k, ctx)
        with ExitStack() as inner:
            padded = k.sb(inner, "conv_input_T", [P, 20, 3 + SEQ])
            mixer_load(k, s, padded)
            norm_transpose(k, k.x, k.xT, COL_MIX)
            gates = [a["w_in"][0][:, lo:lo + 8].rearrange("(c p) n -> p c n", p=P) for lo in (2048, 4104)]
            items = []
            for n in range(6):
                items.append(("T", k.xT, padded[:, 2 * n:2 * n + 2, 3:], None, 1.0))
            for n in range(2):
                items.append(("N", k.xT, s.z[:, :, n * COLS:(n + 1) * COLS], None, 1.0))
            for n in range(4):
                items.append(("T", k.xT, padded[:, 12 + 2 * n:14 + 2 * n, 3:], None, 1.0))
            for buf in (s.mv, s.mo):
                for n in range(2):
                    items.append(("N", k.xT, buf[:, :, n * COLS:(n + 1) * COLS], None, 1.0))
            panels(k, items, (gates, k.xT, s.gates[:, :, :], None, 16))
            conv_silu(k, padded, s.conv)
        s.more(k, ctx)
        normalise_and_gate(k, s)
        key_query_products(k, s)
        gdn_prepare(k, s)
        mlstm_prepare(k, s)
        recurrences(k, s)
        with ExitStack() as inner:
            mixed = k.sb(inner, "mixed", [P, TILES, D])
            mixer_output(k, s, mixed)
            transpose_natural(k, mixed, k.xT)
    rows_product(k, k.xT, 4, add_to(k, k.x))


def mixer_load(k, s, padded):
    with k.stage() as block:
        landed, zeroed = k.sig.new(), k.sig.new()

        @block.sync
        def _(sp):
            sp.dma_start(s.consts[:, :, :], k.a["constants"].rearrange("p (c n) -> p c n", n=P)).then_inc(landed, 16)
            k.stream(sp)
            sp.wait_ge(landed, 16)

        @block.vector
        def _(dve):
            dve.memset(padded[:, :, 0:3], 0.0).then_inc(zeroed, 1)

        k.idle_pool(block)


def store_output(k):
    with k.stage() as block:
        stored = k.stored

        @block.sync
        def _(sp):
            sp.dma_start(k.a["out"][0].rearrange("(i p) d -> p i d", p=P), k.x[:, :, :]).then_inc(stored, 16)
            sp.wait_ge(stored, 16)

        k.idle_pool(block)


def build(nc, a):
    with ExitStack() as ctx:
        k = Program(nc, ctx, a)
        plan_weights(k)
        load_parameters(k)
        mixer(k)
        cross_attention(k)
        peer(k)
        second_block(k)
        store_output(k)


_NAMES = ["x", "mem", "norm_mix_w", "w_in", "gdn_conv_w", "gdn_a_log", "gdn_dt_bias", "gdn_norm_w", "mlstm_conv_w",
          "mlstm_i_bias", "mlstm_f_bias", "mlstm_norm_w", "w_out", "norm_xa_w", "norm_mem_w", "xa_wq", "xa_wkv",
          "xa_wo", "norm_ffn_w", "peer_wq", "peer_sub_keys", "peer_u", "peer_v", "norm_final_w", "rel_table_2",
          "ln_g_2", "ln_b_2", "ffn_w1_2", "ffn_w3_2", "ffn_w2_2", "sgu_w_in_2", "sgu_ln_g_2", "sgu_ln_b_2",
          "sgu_w_s_2", "sgu_b_s_2", "sgu_w_out_2", "kv_w_2", "cmp_pe_2", "cmp_w1_2", "cmp_b1_2", "cmp_w2_2",
          "nsa_w_qg_2", "nsa_w_o_2"]


def kernel(**inputs):
    import concourse.bacc as bacc
    from concourse.bass_utils import run_bass_kernel_spmd

    nc = bacc.Bacc("TRN2", target_bir_lowering=False, num_devices=1)
    masks, buckets = constants()
    arrays = {f"in_{n}": np.ascontiguousarray(inputs[n]) for n in _NAMES}
    arrays["in_constants"] = masks
    arrays["in_bucket_onehot"] = buckets
    a = {n[3:]: nc.dram_tensor(n, v.shape, F32, kind="ExternalInput").ap() for n, v in arrays.items()}
    a["out"] = nc.dram_tensor("out_x", (1, SEQ, D), F32, kind="ExternalOutput").ap()
    a["bias_rows"] = nc.dram_tensor("bias_rows", (P, NH, DISTS), F32, kind="Internal").ap()
    build(nc, a)
    r = run_bass_kernel_spmd(nc, [arrays], core_ids=[0])
    return r.results[0]["out_x"]
```

```python
from contextlib import ExitStack, contextmanager

import numpy as np
import concourse.bass as bass
from concourse import mybir

F32 = mybir.dt.float32
U32 = mybir.dt.uint32
F32R = mybir.dt.float32r
ALU = mybir.AluOpType
ACT = mybir.ActivationFunctionType
AX_X = mybir.AxisListType.X

P = 128
D = 1024
SEQ = 256
TILES = SEQ // P
DC = D // P
COLS = 256
SLOT = DC * COLS
RING = 3
BUFFERS = 3
NEG = -1e30
EPS = 1e-6
LN_EPS = 1e-5

HEADS = 4
HD = 128
CHUNK = 64
NCHUNK = SEQ // CHUNK
GW = HEADS * HD
PAIRS = HEADS * TILES

PEER_HEADS = 8
TOPK = 16
KEYS = 128

DN_ALPHA = 4.0 ** 0.25
FFN_DIM = 2816
SGU_HALF = 2048
SGU_GROUPS = 8
NH = 16
KVG = 4
HDIM = 64
CMP_LEN = 32
CMP_STRIDE = 16
NCMP = SEQ // CMP_STRIDE - CMP_LEN // CMP_STRIDE + 1
SLOTS_KV = 6

(C_IDENT, C_ONES, C_NEG_LOW, C_NEG_UP, C_STRICT, C_TRI, C_SAME, C_IOTA, C_CAUSAL_T, C_MISC) = range(10)
C_LEVEL = 10
LEVELS = 6
NCONST = C_LEVEL + LEVELS
DISTS = 2 * SEQ
BIAS_W = 384


def constants():
    c = np.zeros((P, NCONST, P), np.float32)
    i, j = np.arange(P)[:, None], np.arange(P)[None, :]
    same = i // CHUNK == j // CHUNK
    c[:, C_IDENT] = i == j
    c[:, C_ONES] = 1
    c[:, C_NEG_LOW] = np.where(same & (i >= j), 0, NEG)
    c[:, C_NEG_UP] = np.where(same & (i <= j), 0, NEG)
    c[:, C_STRICT] = same & (i > j)
    c[:, C_TRI] = same & (i <= j)
    c[:, C_SAME] = same
    c[:, C_IOTA] = j + 0 * i
    c[:, C_CAUSAL_T] = i <= j
    c[:, C_MISC, 0:2] = (i // CHUNK) == np.arange(2)[None, :]
    for tile in range(TILES):
        ends = np.arange(NCMP)[None, :] * CMP_STRIDE + CMP_LEN - 1
        c[:, C_MISC, 16 + 16 * tile:16 + 16 * tile + NCMP] = (tile * P + i) >= ends
    for k in range(LEVELS):
        b = 1 << k
        c[:, C_LEVEL + k] = (i // (2 * b) == j // (2 * b)) & ((i // b) % 2 == 1) & ((j // b) % 2 == 0)
    onehot = np.zeros((33, DISTS), np.float32)
    for x in range(DISTS):
        dist = SEQ - 1 - x
        if dist < 0:
            onehot[32, x] = 1
        elif dist < 16:
            onehot[dist, x] = 1
        else:
            large = 16 + int(np.float32(np.log(np.float32(dist) / np.float32(16)) / np.float32(np.log(8.0)) * 16))
            onehot[min(large, 31), x] = 1
    return c.reshape(P, NCONST * P), onehot


class Signals:

    def __init__(self, nc, ctx, size):
        self.pools = [[ctx.enter_context(nc.semaphore(f"stage_{'even' if n == 0 else 'odd'}_{m}"))
                       for m in range(size)] for n in range(2)]
        self.stage = 0
        self.taken = 0

    def new(self):
        self.taken += 1
        return self.pools[self.stage % 2][self.taken - 1]

    def next_stage(self):
        self.stage += 1
        self.taken = 0

    def clear_other(self, pool):
        if self.stage > 1:
            other = self.pools[(self.stage + 1) % 2]
            pool.sem_clear(range(other[0].num, other[-1].num + 1))


class Weights:

    def __init__(self, ring, loaded, used):
        self.ring, self.loaded, self.used = ring, loaded, used
        self.segments = []
        self.count = 0
        self.issued = 0
        self.taken = 0
        self.hold = 1 << 30

    def take(self, n):
        self.taken += n
        return self.taken - n

    def add(self, units, *sources):
        seg = (self.count, units, sources)
        self.segments.append(seg)
        self.count += units * len(sources)
        return seg[0]

    def slot(self, g):
        return self.ring[:, g % RING, :]

    def panel(self, g):
        return self.ring[:, g % RING, :].rearrange("p (c n) -> p c n", c=DC)

    def rows(self, g):
        return self.ring[:, g % RING, :].rearrange("p (r n) -> p r n", r=2)

    def _one(self, sp, g, source, unit, turn):
        r = g % RING
        if g >= RING:
            sp.wait_ge(self.used[r], turn)
        src = source(unit)
        dst = self.ring[:, r, :]
        if len(src.shape) == 3:
            dst = dst.rearrange("p (a b) -> p a b", a=src.shape[1])
        sp.dma_start(dst, src).then_inc(self.loaded[r], 16)

    def issue(self, sp, end):
        end = min(end, self.count)
        while self.issued < end:
            g = self.issued
            start, units, sources = [s for s in self.segments if s[0] <= g][-1]
            per = len(sources)
            body = RING // per
            u, k = divmod(g - start, per)
            last = min(start + units * per, end)
            turns = (last - g) // RING
            if k == 0 and per == RING and turns >= 3 and g >= RING:
                with sp.Fori(0, turns) as i:
                    for b in range(body):
                        for kk in range(per):
                            at = g + b * per + kk
                            self._one(sp, at, sources[kk], u + b + body * i, at // RING + i)
                self.issued += turns * RING
            else:
                self._one(sp, g, sources[k], u, g // RING)
                self.issued += 1


class Split:

    def __init__(self, k, ctx, name, shape):
        self.hi = k.sb(ctx, name + "_hi", shape, F32R)
        self.lo = k.sb(ctx, name + "_lo", shape, F32R)

    def at(self, *index):
        return self.hi[index], self.lo[index]


class Splitter:

    def __init__(self, k, ctx, g0):
        self.k, self.g0 = k, g0
        self.parts = k.sb(ctx, "split_slots", [P, BUFFERS, 2, SLOT], F32R)
        self.high_done = k.sig.new()
        self.eaten = k.sig.new()

    def high(self, act, n, i=0, per=0):
        g, b = self.g0 + n, n % BUFFERS
        act.wait_ge(self.k.w.loaded[g % RING], 16 * (g // RING + per // RING * i + 1))
        if n >= BUFFERS:
            act.wait_ge(self.eaten, n - BUFFERS + 1 + per * i)
        for half in range(2):
            p = slice(half * SLOT // 2, (half + 1) * SLOT // 2)
            act.activation(self.parts[:, b, 0, p], self.k.w.slot(g)[:, p], ACT.Copy).then_inc(self.high_done, 1)

    def low(self, dve, n, i=0, per=0):
        g, b = self.g0 + n, n % BUFFERS
        for half in range(2):
            p = slice(half * SLOT // 2, (half + 1) * SLOT // 2)
            dve.wait_ge(self.high_done, 2 * n + half + 1 + 2 * per * i)
            ins = dve.tensor_tensor(self.parts[:, b, 1, p], self.k.w.slot(g)[:, p], self.parts[:, b, 0, p].bitcast(F32),
                                    ALU.subtract)
        ins.then_inc(self.k.w.used[g % RING], 1)

    def ready(self, pe, n, i=0, per=0):
        g = self.g0 + n
        pe.wait_ge(self.k.w.used[g % RING], g // RING + per // RING * i + 1)

    def panel(self, n):
        return [self.parts[:, n % BUFFERS, q, :].rearrange("p (c n) -> p c n", c=DC) for q in range(2)]

    def rows(self, n):
        return [self.parts[:, n % BUFFERS, q, :].rearrange("p (r n) -> p r n", r=2) for q in range(2)]

    def finished(self, engine, n, i=0, per=0):
        engine.wait_ge(self.eaten, n + 1 + per * i)


def passes(pe, out, left, right, start, stop):
    (lh, ll), (rh, rl) = left, right
    pe.matmul(out, lh, rh, start=start, stop=False)
    pe.matmul(out, lh, rl, start=False, stop=False)
    return pe.matmul(out, ll, rh, start=False, stop=stop)


def split_high(act, dst, src, scale=1.0):
    return act.activation(dst, src, ACT.Copy, scale=scale)


def split_low(dve, dst, src, hi, scale=1.0):
    return dve.scalar_tensor_tensor(dst, src, scale, hi.bitcast(F32), ALU.mult, ALU.subtract)


class Program:

    def __init__(self, nc, ctx, a):
        self.nc, self.ctx, self.a = nc, ctx, a
        self.names = {}
        self.sig = Signals(nc, ctx, 36)
        ring = self.sb(ctx, "ring", [P, RING, SLOT])
        loaded = [ctx.enter_context(nc.semaphore(f"slot_loaded_{r}")) for r in range(RING)]
        used = [ctx.enter_context(nc.semaphore(f"slot_used_{r}")) for r in range(RING)]
        self.w = Weights(ring, loaded, used)
        self.x = self.sb(ctx, "x_natural", [P, TILES, D])
        self.xT = Split(self, ctx, "x_transposed", [P, DC, SEQ])
        self.ident = self.sb(ctx, "ident", [P, P])
        self.ones = self.sb(ctx, "ones", [P, P])
        self.cols = self.sb(ctx, "parameter_columns", [P, 120])
        self.eps = self.sb(ctx, "epsilons", [P, 2])
        self.stored = ctx.enter_context(nc.semaphore("output_stored"))
        self.expert_landed = [ctx.enter_context(nc.semaphore(f"expert_rows_landed_{n}")) for n in range(6)]
        self.boot = ctx.enter_context(nc.semaphore("booted"))
        self.psum = ctx.enter_context(nc.psum_tensor("banks", [P, 8, 512], F32))

    def sb(self, ctx, name, shape, dt=F32):
        self.names[name] = self.names.get(name, 0) + 1
        if self.names[name] > 1:
            name = f"{name}_{self.names[name]}"
        return ctx.enter_context(self.nc.sbuf_tensor(name, shape, dt))

    @contextmanager
    def stage(self):
        self.sig.next_stage()
        with self.nc.Block() as block:
            yield block

    def stream(self, sp):
        self.w.issue(sp, min(self.w.taken + RING, self.w.hold))

    def idle_pool(self, block):
        @block.gpsimd
        def _(pool):
            self.sig.clear_other(pool)


def use_slot(pe, k, g, turn=None):
    pe.wait_ge(k.w.loaded[g % RING], 16 * ((g // RING if turn is None else turn) + 1))


def used_slot(engine, k, g, turn=None):
    engine.wait_ge(k.w.used[g % RING], (g // RING if turn is None else turn) + 1)


def linker(engine, step):
    count = [0]

    def link(ins):
        count[0] += 1
        ins.then_inc(step, 1)
        engine.wait_ge(step, count[0])
    return link


def over_last(ap, n):
    return ap.unsqueeze(2).broadcast_to([ap.shape[0], ap.shape[1], n])


def over_middle(ap, n):
    return ap.unsqueeze(1).broadcast_to([ap.shape[0], n, ap.shape[1]])



def load_parameters(k):
    a = k.a
    rows = [(a["norm_mix_w"][0], DC), (a["norm_xa_w"][0], DC), (a["norm_mem_w"][0], DC), (a["norm_ffn_w"][0], DC)]
    at = 0
    with ExitStack() as ctx, k.stage() as block:
        raw = k.sb(ctx, "parameter_rows", [P, P])
        landed, rows_landed, turned = (k.sig.new() for _ in range(3))

        @block.sync
        def _(sp):
            consts = a["constants"].rearrange("p (c n) -> p c n", n=P)
            sp.dma_start(k.ident[:, :], consts[:, C_IDENT, :]).then_inc(landed, 16)
            sp.dma_start(k.ones[:, :], consts[:, C_ONES, :]).then_inc(landed, 16)
            sp.dma_start(k.x[:, :, :], a["x"][0].rearrange("(i p) d -> p i d", p=P)).then_inc(landed, 16)
            k.w.issue(sp, RING)

        @block.scalar
        def _(act):
            n = 0
            for v, chunks in rows:
                act.dma_start(raw[n:n + chunks, :], v.rearrange("(c p) -> c p", p=P)).then_inc(rows_landed, 16)
                n += chunks
            g = a["gdn_conv_w"][0].rearrange("k (c p) -> k c p", p=P)
            m = a["mlstm_conv_w"][0].rearrange("k (c p) -> k c p", p=P)
            for tap in range(4):
                act.dma_start(raw[n:n + 12, :], g[tap]).then_inc(rows_landed, 16)
                act.dma_start(raw[n + 12:n + 20, :], m[tap]).then_inc(rows_landed, 16)
                n += 20
            act.dma_start(raw[n:n + 4, :], a["cmp_b1_2"].rearrange("s (c p) -> (s c) p", p=P)).then_inc(rows_landed, 16)

        @block.tensor
        def _(pe):
            pe.wait_ge(landed, 48)
            pe.wait_ge(rows_landed, 16 * (len(rows) + 9))
            pe.transpose(k.psum[:, 0, 0:116], raw[0:116, :], k.ident[0:116, 0:116]).then_inc(turned, 1)

        @block.vector
        def _(dve):
            dve.memset(k.eps[:, 0:1], EPS).then_inc(k.boot, 1)
            dve.memset(k.eps[:, 1:2], LN_EPS).then_inc(k.boot, 1)
            dve.wait_ge(turned, 1)
            dve.tensor_copy(k.cols[:, 0:116], k.psum[:, 0, 0:116]).then_inc(k.boot, 1)

        @block.gpsimd
        def _(pool):
            k.sig.clear_other(pool)


COL_MIX, COL_XA, COL_MEM, COL_FFN, COL_CONV, COL_B1 = 0, 8, 16, 24, 32, 112


def turn_chunks(pe, k, src, tile, ready):
    for c in range(DC):
        at = (c % 2) * SEQ + tile * P
        ins = pe.transpose(k.psum[:, c // 2, at:at + P], src[:, c * P:(c + 1) * P], k.ident[:, :])
        if tile == TILES - 1 and c % 2 == 1:
            ins.then_inc(ready, 1)


def norm_transpose(k, src, dst, col):
    with ExitStack() as ctx, k.stage() as block:
        xn = k.sb(ctx, "normed", [P, TILES, D])
        stat = k.sb(ctx, "row_stats", [P, 3, TILES])
        squares, rooted, recip, normed, banks, high, written = (k.sig.new() for _ in range(7))

        @block.sync
        def _(sp):
            k.stream(sp)

        @block.scalar
        def _(act):
            for i in range(TILES):
                act.activation(xn[:, i, :], src[:, i, :], ACT.Square, accum_out=stat[:, 0, i:i + 1]).then_inc(squares, 1)
            act.wait_ge(squares, TILES)
            act.activation(stat[:, 1, :], stat[:, 0, :], ACT.Sqrt, bias=k.eps[:, 0:1], scale=1.0 / D).then_inc(rooted, 1)
            for b in range(4):
                act.wait_ge(banks, b + 1)
                for c in (2 * b, 2 * b + 1):
                    ins = split_high(act, dst.hi[:, c, :], k.psum[:, b, (c % 2) * SEQ:(c % 2 + 1) * SEQ],
                                     k.cols[:, col + c:col + c + 1])
                ins.then_inc(high, 1)

        @block.vector
        def _(dve):
            dve.wait_ge(rooted, 1)
            dve.reciprocal(stat[:, 2, :], stat[:, 1, :]).then_inc(recip, 1)
            dve.wait_ge(recip, 1)
            for i in range(TILES):
                dve.tensor_scalar(xn[:, i, :], src[:, i, :], stat[:, 2, i:i + 1], None, ALU.mult).then_inc(normed, 1)
            for b in range(4):
                dve.wait_ge(high, b + 1)
                for c in (2 * b, 2 * b + 1):
                    split_low(dve, dst.lo[:, c, :], k.psum[:, b, (c % 2) * SEQ:(c % 2 + 1) * SEQ], dst.hi[:, c, :],
                              k.cols[:, col + c:col + c + 1]).then_inc(written, 1)

        @block.tensor
        def _(pe):
            for i in range(TILES):
                pe.wait_ge(normed, i + 1)
                turn_chunks(pe, k, xn[:, i, :], i, banks)

        k.idle_pool(block)


def split_banks(k, first, dst, banks, high, written):
    def highs(act):
        for b in range(4):
            act.wait_ge(banks, b + 1)
            split_high(act, dst.hi[:, 2 * b:2 * b + 2, :], bank2(k, first + b)).then_inc(high, 1)

    def lows(dve):
        for b in range(4):
            dve.wait_ge(high, b + 1)
            split_low(dve, dst.lo[:, 2 * b:2 * b + 2, :], bank2(k, first + b), dst.hi[:, 2 * b:2 * b + 2, :]
                      ).then_inc(written, 1)
    return highs, lows


def transpose_natural(k, src, dst):
    with k.stage() as block:
        banks, high, written = (k.sig.new() for _ in range(3))
        highs, lows = split_banks(k, 0, dst, banks, high, written)

        @block.sync
        def _(sp):
            k.stream(sp)

        @block.tensor
        def _(pe):
            for i in range(TILES):
                turn_chunks(pe, k, src[:, i, :], i, banks)

        @block.scalar
        def _(act):
            highs(act)

        @block.vector
        def _(dve):
            lows(dve)

        k.idle_pool(block)


def bank2(k, b):
    return k.psum[:, b, :].rearrange("p (a n) -> p a n", a=2)


def panels(k, items, small=None):
    g0 = k.w.take(len(items))
    by_act = [m for m, it in enumerate(items) if it[3] is not None or m % 2 == 1]
    by_dve = [m for m in range(len(items)) if m not in by_act]
    with ExitStack() as ctx, k.stage() as block:
        split = Splitter(k, ctx, g0)
        act_read, dve_read, narrow_landed, narrow_high, narrow_low, narrow_done = (k.sig.new() for _ in range(6))
        if small:
            view, small_x, small_dest, small_func, width = small
            narrow = k.sb(ctx, "narrow_panel", [P, DC, width])
            narrows = Split(k, ctx, "narrow_split", [P, DC, width])
            views = view if isinstance(view, list) else [view]

        @block.sync
        def _(sp):
            k.stream(sp)

        @block.tensor
        def _(pe):
            for m, (form, xT, dest, func, scale) in enumerate(items):
                if m >= 6:
                    if m - 6 in by_act:
                        pe.wait_ge(act_read, by_act.index(m - 6) + 1)
                    else:
                        pe.wait_ge(dve_read, by_dve.index(m - 6) + 1)
                split.ready(pe, m)
                wh, wl = split.panel(m)
                for j in range(2):
                    own = slice(j * P, (j + 1) * P)
                    for c in range(DC):
                        if form == "T":
                            left, right = (wh[:, c, own], wl[:, c, own]), xT.at(slice(0, P), c)
                        else:
                            left, right = xT.at(slice(0, P), c, own), (wh[:, c, :], wl[:, c, :])
                        ins = passes(pe, k.psum[:, m % 6, j * SEQ:(j + 1) * SEQ], left, right, c == 0, c == DC - 1)
                ins.then_inc(split.eaten, 1)
            if small:
                pe.wait_ge(narrow_low, 1)
                for i in range(TILES):
                    for c in range(DC):
                        ins = passes(pe, k.psum[:, 6, i * width:(i + 1) * width],
                                     small_x.at(slice(0, P), c, slice(i * P, (i + 1) * P)), narrows.at(slice(0, P), c),
                                     c == 0, c == DC - 1)
                ins.then_inc(narrow_done, 1)

        @block.scalar
        def _(act):
            if small:
                at = 0
                for v in views:
                    act.dma_start(narrow[:, :, at:at + v.shape[2]], v).then_inc(narrow_landed, 16)
                    at += v.shape[2]
            for m in range(min(BUFFERS, len(items))):
                split.high(act, m)
            if small:
                act.wait_ge(narrow_landed, 16 * len(views))
                split_high(act, narrows.hi[:, :, :], narrow[:, :, :]).then_inc(narrow_high, 1)
            for m in range(len(items)):
                if m + BUFFERS < len(items):
                    split.high(act, m + BUFFERS)
                if m in by_act:
                    func, scale = items[m][3], items[m][4]
                    split.finished(act, m)
                    act.activation(items[m][2], bank2(k, m % 6), func or ACT.Copy, scale=scale).then_inc(act_read, 1)
            if small:
                act.wait_ge(narrow_done, 1)
                act.activation(small_dest, k.psum[:, 6, 0:TILES * width].rearrange("p (i n) -> p i n", i=TILES),
                               small_func or ACT.Copy).then_inc(act_read, 1)

        @block.vector
        def _(dve):
            for m in range(min(BUFFERS, len(items))):
                split.low(dve, m)
            if small:
                dve.wait_ge(narrow_high, 1)
                split_low(dve, narrows.lo[:, :, :], narrow[:, :, :], narrows.hi[:, :, :]).then_inc(narrow_low, 1)
            for m in range(len(items)):
                if m + BUFFERS < len(items):
                    split.low(dve, m + BUFFERS)
                if m in by_dve:
                    split.finished(dve, m)
                    dve.tensor_scalar(items[m][2], bank2(k, m % 6), items[m][4], None, ALU.mult).then_inc(dve_read, 1)

        k.idle_pool(block)


def rows_product(k, aT, slots, finish):
    g0 = k.w.take(slots)
    with ExitStack() as ctx, k.stage() as block:
        split = Splitter(k, ctx, g0)

        @block.sync
        def _(sp):
            k.stream(sp)

        @block.tensor
        def _(pe):
            for m in range(slots):
                split.ready(pe, m)
                wh, wl = split.rows(m)
                for r in range(2):
                    ins = down(pe, k, aT.at(slice(0, P), 2 * m + r), (wh[:, r, :], wl[:, r, :]), m == 0 and r == 0,
                               m == slots - 1 and r == 1)
                ins.then_inc(split.eaten, 1)

        take_act, take_dve = finish(ctx, block, lambda engine: split.finished(engine, slots - 1))

        @block.scalar
        def _(act):
            for m in range(slots):
                split.high(act, m)
            take_act(act)

        @block.vector
        def _(dve):
            for m in range(slots):
                split.low(dve, m)
            take_dve(dve)

        k.idle_pool(block)


def down(pe, k, aT, w, start, stop):
    for i in range(TILES):
        own = slice(i * P, (i + 1) * P)
        for half in range(2):
            cols = slice(half * 512, (half + 1) * 512)
            ins = passes(pe, k.psum[:, 2 * i + half, :], (aT[0][:, own], aT[1][:, own]), (w[0][:, cols], w[1][:, cols]),
                         start, stop)
    return ins


def accumulated(k, i):
    return k.psum[:, 2 * i:2 * i + 2, :].rearrange("p b n -> p (b n)")


def add_to(k, dst):
    def finish(ctx, block, done):
        added = k.sig.new()

        def take(dve):
            done(dve)
            for i in range(TILES):
                dve.tensor_tensor(dst[:, i, :], accumulated(k, i), dst[:, i, :], ALU.add).then_inc(added, 1)
        return (lambda act: None), take
    return finish


def copy_to(k, dst):
    def finish(ctx, block, done):
        copied = k.sig.new()

        def take_dve(dve):
            done(dve)
            dve.tensor_copy(dst[:, 0, :], accumulated(k, 0)).then_inc(copied, 1)

        def take_act(act):
            done(act)
            act.activation(dst[:, 1, :], accumulated(k, 1), ACT.Copy).then_inc(copied, 1)
        return take_act, take_dve
    return finish



def conv_silu(k, padded, out):
    with ExitStack() as ctx, k.stage() as block:
        summed, shaped = k.sig.new(), k.sig.new()
        tmp = k.sb(ctx, "convolved", [P, 20, SEQ])
        step = k.sig.new()

        @block.sync
        def _(sp):
            k.stream(sp)

        @block.vector
        def _(dve):
            for quad in range(4):
                for tap in range(4):
                    for n in range(5 * quad, 5 * quad + 5):
                        w = k.cols[:, COL_CONV + 20 * tap + n:COL_CONV + 20 * tap + n + 1]
                        src = padded[:, n, tap:tap + SEQ]
                        if tap == 0:
                            ins = dve.tensor_scalar(tmp[:, n, :], src, w, None, ALU.mult)
                        else:
                            ins = dve.scalar_tensor_tensor(tmp[:, n, :], src, w, tmp[:, n, :], ALU.mult, ALU.add)
                        ins.then_inc(step, 1)
                    dve.wait_ge(step, 20 * quad + 5 * (tap + 1))

        @block.scalar
        def _(act):
            for quad in range(4):
                act.wait_ge(step, 20 * (quad + 1))
                act.activation(out[:, 5 * quad:5 * quad + 5, :], tmp[:, 5 * quad:5 * quad + 5, :],
                               ACT.Silu).then_inc(shaped, 1)

        k.idle_pool(block)


def normalise_and_gate(k, s):
    with ExitStack() as ctx, k.stage() as block:
        sq = k.sb(ctx, "qk_squares", [P, 8, SEQ])
        root = k.sb(ctx, "qk_norms", [P, 8, SEQ])
        row = k.sb(ctx, "gate_parameters", [P, 4, HEADS])
        g = k.sb(ctx, "gate_work", [P, 6, TILES, 8])
        lh = k.sb(ctx, "log_by_half", [P, 2, 16])
        squared, sums, rooted, vstep, scaled, gates_landed, expd, logs, cums, turned, copied, gstep = \
            (k.sig.new() for _ in range(12))
        qk = s.conv[:, 0:8, :]

        @block.sync
        def _(sp):
            for n, name in enumerate(("gdn_dt_bias", "gdn_a_log", "mlstm_i_bias", "mlstm_f_bias")):
                sp.dma_start(row[:, n, :], k.a[name].partition_broadcast(P).rearrange("p a h -> p (a h)")
                             ).then_inc(gates_landed, 16)
            k.stream(sp)

        @block.gpsimd
        def _(pool):
            k.sig.clear_other(pool)
            pool.tensor_tensor(sq[:, 0:4, :], s.conv[:, 0:4, :], s.conv[:, 0:4, :], ALU.mult).then_inc(squared, 1)
            pool.tensor_scalar(s.conv[:, 16:20, :], s.conv[:, 16:20, :], HD ** -0.5, None, ALU.mult).then_inc(scaled, 1)

        @block.scalar
        def _(act):
            act.activation(sq[:, 4:8, :], s.conv[:, 4:8, :], ACT.Square).then_inc(squared, 1)
            for b in range(4):
                act.wait_ge(sums, b + 1)
                act.activation(root[:, 2 * b:2 * b + 2, :], bank2(k, b), ACT.Sqrt, bias=k.eps[:, 0:1]).then_inc(rooted, 1)
            act.wait_ge(gstep, 3)
            act.activation(g[:, 2, :, :], g[:, 1, :, :], ACT.Exp, scale=-1.0).then_inc(expd, 1)
            act.activation(row[:, 1, :], row[:, 1, :], ACT.Exp).then_inc(expd, 1)
            act.wait_ge(expd, 2)
            act.activation(g[:, 3, :, :], g[:, 2, :, :], ACT.Ln, bias=1.0).then_inc(logs, 1)
            act.activation(s.beta[:, :, :], s.gates[:, :, 4:8], ACT.Sigmoid).then_inc(logs, 1)
            for n in (1, 3, 5):
                act.wait_ge(turned, n + 1)
                b = [4, 5, 6, 7, 0, 1][n]
                act.activation(s.natural[:, 4 * n:4 * n + 4, :], k.psum[:, b, :].rearrange("p (a n) -> p a n", a=4),
                               ACT.Copy).then_inc(copied, 1)

        @block.tensor
        def _(pe):
            for b in range(4):
                pe.wait_ge(squared, 2)
                pe.matmul(k.psum[:, b, :], k.ones[:, :], sq[:, 2 * b:2 * b + 2, :], start=True, stop=True).then_inc(sums, 1)
            pe.wait_ge(vstep, 8)
            pe.wait_ge(scaled, 1)
            for n in range(6):
                b = [4, 5, 6, 7, 0, 1][n]
                for q in range(4):
                    e = 4 * n + q
                    kind, head, tile = e // 8, (e % 8) // 2, e % 2
                    src = s.conv[:, (4, 8, 16)[kind] + head, tile * P:(tile + 1) * P]
                    ins = pe.transpose(k.psum[:, b, q * P:(q + 1) * P], src, k.ident[:, :])
                ins.then_inc(turned, 1)
            pe.wait_ge(gstep, 9)
            pe.matmul(k.psum[:, 2, 0:16], s.mask(C_TRI), s.logs[:, :, :, :].rearrange("p i t h -> p (i t h)"), start=True, stop=True)
            pe.matmul(k.psum[:, 2, 16:32], s.mask(C_SAME), s.logs[:, :, :, :].rearrange("p i t h -> p (i t h)"), start=True, stop=True)
            pe.matmul(k.psum[:, 2, 32:64], k.ones[:, :], lh[:, :, :].rearrange("p f n -> p (f n)"), start=True, stop=True).then_inc(cums, 1)

        @block.vector
        def _(dve):
            dve.wait_ge(gates_landed, 64)
            dve.tensor_tensor(g[:, 0, :, 0:4], s.gates[:, :, 0:4], over_middle(row[:, 0, :], TILES), ALU.add).then_inc(gstep, 1)
            dve.scalar_tensor_tensor(g[:, 0, :, 4:8], s.gates[:, :, 12:16], -1.0, over_middle(row[:, 3, :], TILES),
                                     ALU.mult, ALU.subtract).then_inc(gstep, 1)
            dve.wait_ge(gstep, 2)
            dve.scalar_tensor_tensor(g[:, 1, :, :], g[:, 0, :, :], -1.0, g[:, 0, :, :], ALU.mult, ALU.max).then_inc(gstep, 1)
            dve.tensor_tensor(s.log_i[:, :, :], s.gates[:, :, 8:12], over_middle(row[:, 2, :], TILES), ALU.add).then_inc(gstep, 1)
            dve.tensor_scalar(g[:, 4, :, :], g[:, 0, :, :], 0.0, None, ALU.max).then_inc(gstep, 1)
            for b in range(4):
                dve.wait_ge(rooted, b + 1)
                dve.reciprocal(root[:, 2 * b:2 * b + 2, :], root[:, 2 * b:2 * b + 2, :]).then_inc(vstep, 1)
                dve.wait_ge(vstep, 2 * b + 1)
                part = s.conv[:, 2 * b:2 * b + 2, :]
                dve.scalar_tensor_tensor(part, part, HD ** -0.5 if b < 2 else 1.0, root[:, 2 * b:2 * b + 2, :],
                                         ALU.mult, ALU.mult).then_inc(vstep, 1)
            dve.wait_ge(logs, 1)
            dve.wait_ge(gstep, 5)
            dve.tensor_tensor(g[:, 5, :, :], g[:, 4, :, :], g[:, 3, :, :], ALU.add).then_inc(gstep, 1)
            dve.wait_ge(gstep, 6)
            dve.scalar_tensor_tensor(s.logs[:, :, 0, :], g[:, 5, :, 0:4], -1.0, over_middle(row[:, 1, :], TILES),
                                     ALU.mult, ALU.mult).then_inc(gstep, 1)
            dve.tensor_scalar(s.logs[:, :, 1, :], g[:, 5, :, 4:8], -1.0, None, ALU.mult).then_inc(gstep, 1)
            dve.wait_ge(gstep, 8)
            dve.tensor_tensor(lh[:, :, :], over_middle(s.logs[:, :, :, :].rearrange("p i t h -> p (i t h)"), 2),
                              over_last(s.consts[:, C_MISC, 0:2], 16), ALU.mult).then_inc(gstep, 1)
            for n in (0, 2, 4):
                dve.wait_ge(turned, n + 1)
                b = [4, 5, 6, 7, 0, 1][n]
                dve.tensor_copy(s.natural[:, 4 * n:4 * n + 4, :],
                                k.psum[:, b, :].rearrange("p (a n) -> p a n", a=4)).then_inc(copied, 1)
            dve.wait_ge(cums, 1)
            for kind in range(2):
                for what in range(2):
                    src = k.psum[:, 2, 16 * what:16 * what + 16].rearrange("p (i t h) -> p t h i", i=TILES, t=2)
                    dve.tensor_copy(s.run[:, kind, what, :].rearrange("p (h i) -> p h i", h=HEADS),
                                    src[:, kind, :, :]).then_inc(copied, 1)
                for half in range(2):
                    src = k.psum[:, 2, 32 + 16 * half:48 + 16 * half].rearrange("p (i t h) -> p t h i", i=TILES, t=2)
                    dst = s.total[:, kind, :].rearrange("p (h i f) -> p h i f", h=HEADS, f=2)
                    dve.tensor_copy(dst[:, :, :, half], src[:, kind, :, :]).then_inc(copied, 1)


def gdn_prepare(k, s):
    gc = s.run[:, 0, 0, :]
    with ExitStack() as ctx, k.stage() as block:
        def mats(name):
            return k.sb(ctx, name, [P, PAIRS, P])
        diag, low, up, rowexp, A, B, Y, W, X = (mats(n) for n in
            ("gc_diagonal", "decay_low", "decay_up", "row_exp", "A", "A_level", "AtW", "inv_T", "inv"))
        vb, kbg = mats("v_beta"), mats("k_beta_exp")
        col = k.sb(ctx, "gdn_columns", [P, 4, PAIRS])
        vs, ps, acts, pools, As = (k.sig.new() for _ in range(5))
        kn, vn = s.natural[:, 0:8, :], s.natural[:, 8:16, :]

        def both(n):
            return k.psum[:, 2 * n:2 * n + 2, :].rearrange("p b (a n) -> p (b a) n", n=P)

        def square(n, e):
            return k.psum[:, 2 * n + e // 4, (e % 4) * P:(e % 4 + 1) * P]

        @block.sync
        def _(sp):
            k.stream(sp)

        @block.vector
        def _(dve):
            link = linker(dve, vs)
            link(dve.tensor_tensor(diag[:, :, :], over_middle(k.ident[:, :], PAIRS), over_last(gc, P), ALU.mult))
            link(dve.tensor_copy(col[:, 0, :].rearrange("p (h i) -> p h i", h=HEADS),
                                 s.beta[:, :, :].rearrange("p i h -> p h i")))
            link(dve.tensor_tensor(col[:, 3, :], s.run[:, 0, 1, :], gc, ALU.subtract))
            dve.wait_ge(ps, 1)
            link(dve.tensor_tensor(up[:, :, :], both(0), over_last(gc, P), ALU.subtract))
            link(dve.scalar_tensor_tensor(low[:, :, :], up[:, :, :], -1.0, over_middle(s.mask(C_NEG_LOW), PAIRS),
                                          ALU.mult, ALU.add))
            link(dve.tensor_tensor(up[:, :, :], up[:, :, :], over_middle(s.mask(C_NEG_UP), PAIRS), ALU.add))
            dve.wait_ge(acts, 1)
            link(dve.tensor_tensor(col[:, 1, :], col[:, 1, :], col[:, 0, :], ALU.mult))
            dve.wait_ge(ps, 2)
            dve.wait_ge(acts, 3)
            link(dve.tensor_tensor(A[:, :, :], both(1), low[:, :, :], ALU.mult))
            link(dve.tensor_tensor(A[:, :, :], A[:, :, :], over_last(col[:, 0, :], P), ALU.mult))
            link(dve.tensor_tensor(A[:, :, :], A[:, :, :], over_middle(s.mask(C_STRICT), PAIRS), ALU.mult))
            link(dve.tensor_copy(W[:, :, :], over_middle(k.ident[:, :], PAIRS)))
            link(dve.tensor_copy(X[:, :, :], over_middle(k.ident[:, :], PAIRS)))
            for level in range(LEVELS):
                link(dve.tensor_tensor(B[:, :, :], A[:, :, :], over_middle(s.mask(C_LEVEL + level), PAIRS), ALU.mult))
                dve.wait_ge(ps, 4 + 2 * level)
                link(dve.tensor_tensor(W[:, :, :], W[:, :, :], both(2), ALU.subtract))
                link(dve.tensor_tensor(X[:, :, :], X[:, :, :], both(3), ALU.subtract))

        @block.scalar
        def _(act):
            act.activation(col[:, 1, :], gc, ACT.Exp).then_inc(acts, 1)
            act.wait_ge(vs, 3)
            act.activation(col[:, 2, :], col[:, 3, :], ACT.Exp).then_inc(acts, 1)
            act.wait_ge(vs, 5)
            act.activation(low[:, :, :], low[:, :, :], ACT.Exp).then_inc(acts, 1)
            act.wait_ge(vs, 6)
            act.activation(up[:, :, :], up[:, :, :], ACT.Exp).then_inc(acts, 1)
            act.activation(rowexp[:, :, :], both(0), ACT.Exp).then_inc(acts, 1)
            act.activation(s.glast[:, 0, :], s.total[:, 0, :], ACT.Exp).then_inc(acts, 1)
            for level in range(LEVELS):
                act.wait_ge(ps, 3 + 2 * level)
                act.activation(Y[:, :, :], both(1), ACT.Copy).then_inc(As, 1)
            act.wait_ge(ps, 15)
            act.activation(s.u[:, :, :], both(0), ACT.Copy).then_inc(acts, 1)
            act.activation(s.wT[:, :, :], both(1), ACT.Copy).then_inc(acts, 1)

        @block.gpsimd
        def _(pool):
            k.sig.clear_other(pool)
            pool.wait_ge(vs, 2)
            pool.tensor_tensor(vb[:, :, :], vn, over_last(col[:, 0, :], P), ALU.mult).then_inc(pools, 1)
            pool.wait_ge(vs, 7)
            pool.tensor_tensor(kbg[:, :, :], kn, over_last(col[:, 1, :], P), ALU.mult).then_inc(pools, 1)
            pool.wait_ge(acts, 5)
            pool.tensor_tensor(s.kd[:, :, :], kn, over_last(col[:, 2, :], P), ALU.mult).then_inc(pools, 1)
            pool.tensor_tensor(s.qdT[:, :, :], s.conv[:, 0:4, :].rearrange("p h (i n) -> p (h i) n", n=P),
                               rowexp[:, :, :], ALU.mult).then_inc(pools, 1)
            pool.tensor_tensor(s.qkT[:, :, :], s.qk_raw[:, :, :], up[:, :, :], ALU.mult).then_inc(pools, 1)

        @block.tensor
        def _(pe):
            pe.wait_ge(vs, 1)
            for n in range(2):
                ins = pe.matmul(k.psum[:, n, :], k.ones[:, :], diag[:, 4 * n:4 * n + 4, :], start=True, stop=True)
            ins.then_inc(ps, 1)
            for e in range(PAIRS):
                kt = s.conv[:, 4 + e // 2, (e % 2) * P:(e % 2 + 1) * P]
                ins = pe.matmul(square(1, e), kt, kt, start=True, stop=True)
            ins.then_inc(ps, 1)
            for level in range(LEVELS):
                pe.wait_ge(vs, 13 + 3 * level)
                for e in range(PAIRS):
                    ins = pe.matmul(square(1, e), B[:, e, :], W[:, e, :], start=True, stop=True)
                ins.then_inc(ps, 1)
                pe.wait_ge(As, level + 1)
                for e in range(PAIRS):
                    pe.matmul(square(2, e), X[:, e, :], Y[:, e, :], start=True, stop=True)
                    ins = pe.matmul(square(3, e), Y[:, e, :], X[:, e, :], start=True, stop=True)
                ins.then_inc(ps, 1)
            pe.wait_ge(vs, 12 + 3 * LEVELS)
            pe.wait_ge(pools, 2)
            pe.wait_ge(acts, 6)
            for e in range(PAIRS):
                pe.matmul(square(0, e), W[:, e, :], vb[:, e, :], start=True, stop=True)
                ins = pe.matmul(square(1, e), kbg[:, e, :], W[:, e, :], start=True, stop=True)
            ins.then_inc(ps, 1)


def key_query_products(k, s):
    with k.stage() as block:
        ps, copied = k.sig.new(), k.sig.new()

        @block.sync
        def _(sp):
            k.stream(sp)

        @block.tensor
        def _(pe):
            for kind, (q0, k0) in enumerate(((0, 4), (12, 16))):
                for e in range(PAIRS):
                    t = slice((e % 2) * P, (e % 2 + 1) * P)
                    ins = pe.matmul(k.psum[:, 2 * kind + e // 4, (e % 4) * P:(e % 4 + 1) * P],
                                    s.conv[:, k0 + e // 2, t], s.conv[:, q0 + e // 2, t], start=True, stop=True)
                ins.then_inc(ps, 1)

        @block.vector
        def _(dve):
            dve.wait_ge(ps, 1)
            dve.tensor_copy(s.qk_raw[:, :, :], k.psum[:, 0:2, :].rearrange("p b (a n) -> p (b a) n", n=P)).then_inc(copied, 1)

        @block.scalar
        def _(act):
            act.wait_ge(ps, 2)
            act.activation(s.mqk_raw[:, :, :], k.psum[:, 2:4, :].rearrange("p b (a n) -> p (b a) n", n=P),
                           ACT.Copy).then_inc(copied, 1)

        k.idle_pool(block)


def mlstm_prepare(k, s):
    b, bl_own = s.run[:, 1, 0, :], s.run[:, 1, 1, :]
    bl_all = s.total[:, 1, :]
    with ExitStack() as ctx, k.stage() as block:
        def mats(name):
            return k.sb(ctx, name, [P, PAIRS, P])
        diag, work = mats("row_diagonal"), mats("row_work")
        c = k.sb(ctx, "mlstm_columns", [P, 16, PAIRS])
        amax = k.sb(ctx, "chunk_maxima", [P, HEADS, NCHUNK])
        m = k.sb(ctx, "running_maxima", [P, HEADS, NCHUNK + 1])
        tmp = k.sb(ctx, "decay_argument", [P, HEADS, NCHUNK])
        vs, ps, acts, pools = (k.sig.new() for _ in range(4))
        A_, MAXD, MPREV, MNEXT, INTER, MT, SCARG, WARG, R, WGT = range(10)

        def both(n):
            return k.psum[:, 2 * n:2 * n + 2, :].rearrange("p b (a n) -> p (b a) n", n=P)

        @block.sync
        def _(sp):
            k.stream(sp)

        @block.vector
        def _(dve):
            link = linker(dve, vs)
            link(dve.tensor_tensor(c[:, A_, :].rearrange("p (h i) -> p h i", h=HEADS),
                                   s.log_i[:, :, :].rearrange("p i h -> p h i"),
                                   b.rearrange("p (h i) -> p h i", h=HEADS), ALU.subtract))
            link(dve.tensor_tensor(diag[:, :, :], over_middle(k.ident[:, :], PAIRS), over_last(c[:, A_, :], P), ALU.mult))
            link(dve.memset(m[:, :, :], 0.0))
            dve.wait_ge(ps, 1)
            link(dve.tensor_reduce(amax[:, :, :].rearrange("p h n -> p (h n)"),
                                   both(0).rearrange("p e (f n) -> p (e f) n", f=2), AX_X, ALU.max))
            link(dve.tensor_tensor(work[:, :, :], both(0), over_middle(s.mask(C_NEG_LOW), PAIRS), ALU.add))
            link(dve.tensor_reduce(c[:, MAXD, :], work[:, :, :], AX_X, ALU.max))
            link(dve.tensor_tensor(c[:, MAXD, :], c[:, MAXD, :], b, ALU.add))
            total = bl_all.rearrange("p (h n) -> p h n", h=HEADS)
            for n in range(NCHUNK):
                link(dve.tensor_tensor(m[:, :, n + 1], m[:, :, n], amax[:, :, n], ALU.max))
                link(dve.tensor_tensor(m[:, :, n + 1], m[:, :, n + 1], total[:, :, n], ALU.add))
            for half in range(2):
                p = slice(half * CHUNK, (half + 1) * CHUNK)
                for what, off in ((MPREV, 0), (MNEXT, 1)):
                    src = m[p, :, off + half:off + half + 3:2]
                    link(dve.tensor_copy(c[p, what, :].rearrange("p (h i) -> p h i", h=HEADS), src))
            link(dve.tensor_tensor(c[:, INTER, :], b, c[:, MPREV, :], ALU.add))
            link(dve.tensor_tensor(c[:, MT, :], c[:, INTER, :], c[:, MAXD, :], ALU.max))
            link(dve.tensor_tensor(c[:, SCARG, :], c[:, INTER, :], c[:, MT, :], ALU.subtract))
            link(dve.tensor_tensor(c[:, WARG, :], c[:, A_, :], bl_own, ALU.add))
            link(dve.tensor_tensor(c[:, WARG, :], c[:, WARG, :], c[:, MNEXT, :], ALU.subtract))
            link(dve.tensor_tensor(tmp[:, :, :], total, m[:, :, 0:NCHUNK], ALU.add))
            link(dve.tensor_tensor(tmp[:, :, :], tmp[:, :, :], m[:, :, 1:NCHUNK + 1], ALU.subtract))
            link(dve.tensor_tensor(c[:, R, :], b, c[:, MT, :], ALU.subtract))
            link(dve.tensor_tensor(diag[:, :, :], over_middle(k.ident[:, :], PAIRS), over_last(c[:, R, :], P), ALU.mult))
            dve.wait_ge(ps, 2)
            link(dve.tensor_tensor(work[:, :, :], both(1), over_middle(s.mask(C_NEG_UP), PAIRS), ALU.add))
            link(dve.tensor_tensor(work[:, :, :], work[:, :, :], over_last(c[:, A_, :], P), ALU.add))
            dve.wait_ge(acts, 4)
            link(dve.tensor_tensor(diag[:, :, :], over_middle(k.ident[:, :], PAIRS), over_last(c[:, SCARG, :], P), ALU.mult))
            dve.wait_ge(ps, 3)
            link(dve.tensor_tensor(s.mqdT[:, :, :], s.conv[:, 12:16, :].rearrange("p h (i n) -> p (h i) n", n=P),
                                   both(2), ALU.mult))
            dve.wait_ge(acts, 5)
            link(dve.tensor_tensor(s.mqkT[:, :, :], s.mqk_raw[:, :, :], work[:, :, :], ALU.mult))

        @block.scalar
        def _(act):
            act.wait_ge(vs, 26)
            act.activation(s.emt[:, :], c[:, MT, :], ACT.Exp, scale=-1.0).then_inc(acts, 1)
            act.activation(c[:, SCARG, :], c[:, SCARG, :], ACT.Exp).then_inc(acts, 1)
            act.activation(c[:, WGT, :], c[:, WARG, :], ACT.Exp).then_inc(acts, 1)
            act.activation(s.glast[:, 1, :].rearrange("p (h n) -> p h n", h=HEADS), tmp[:, :, :], ACT.Exp).then_inc(acts, 1)
            act.wait_ge(vs, 30)
            act.activation(work[:, :, :], work[:, :, :], ACT.Exp).then_inc(acts, 1)

        @block.gpsimd
        def _(pool):
            k.sig.clear_other(pool)
            pool.memset(s.v1[:, :, :, HD:HD + 1], 1.0).then_inc(pools, 1)
            pool.tensor_copy(s.v1[:, :, :, 0:HD], s.mv[:, :, :].rearrange("p i (h d) -> p i h d", h=HEADS)).then_inc(pools, 1)
            pool.wait_ge(acts, 3)
            pool.tensor_tensor(s.kw[:, :, :], s.natural[:, 16:24, :], over_last(c[:, WGT, :], P), ALU.mult).then_inc(pools, 1)

        @block.tensor
        def _(pe):
            for n, at in enumerate((2, 28, 31)):
                pe.wait_ge(vs, at)
                for q in range(2):
                    ins = pe.matmul(k.psum[:, 2 * n + q, :], k.ones[:, :], diag[:, 4 * q:4 * q + 4, :], start=True, stop=True)
                ins.then_inc(ps, 1)


def recurrences(k, s):
    V1 = HD + 1
    with ExitStack() as ctx, k.stage() as block:
        S = k.sb(ctx, "gdn_state", [P, HEADS, HD])
        C = k.sb(ctx, "mlstm_state", [P, HEADS, V1])
        vnew = k.sb(ctx, "v_new", [P, HEADS, HD])
        den = k.sb(ctx, "denominator", [P, 2, HEADS])
        ws, outs, dstate, mouts, mdstate, vns, gds, mds, rd, mrd = (k.sig.new() for _ in range(10))
        gl = s.glast[:, 0, :].rearrange("p (h n) -> p h n", h=HEADS)
        dec = s.glast[:, 1, :].rearrange("p (h n) -> p h n", h=HEADS)

        def quad(b, p=slice(0, P)):
            return k.psum[p, b, :].rearrange("p (h d) -> p h d", h=HEADS)

        def two(b, p=slice(0, P)):
            return k.psum[p, b:b + 2, 0:2 * V1].rearrange("p b (h d) -> p b h d", h=2)

        def by_bank(ap):
            return ap.rearrange("p (b h) d -> p b h d", b=2)

        @block.sync
        def _(sp):
            k.stream(sp)

        @block.tensor
        def _(pe):
            for n in range(NCHUNK):
                tile, half = n // 2, n % 2
                p = slice(half * CHUNK, (half + 1) * CHUNK)
                if n > 0:
                    pe.wait_ge(gds, 2 * n + 1)
                    for h in range(HEADS):
                        ins = pe.matmul(k.psum[p, 0, h * HD:(h + 1) * HD], s.wT[:, 2 * h + tile, p], S[:, h, :],
                                        start=True, stop=True)
                    ins.then_inc(ws, 1)
                    pe.wait_ge(mds, 2 * n + 1)
                    pe.wait_ge(mrd, n)
                for h in range(HEADS):
                    o = k.psum[p, 3 + h // 2, (h % 2) * V1:(h % 2 + 1) * V1]
                    if n > 0:
                        pe.matmul(o, s.mqdT[:, 2 * h + tile, p], C[:, h, :], start=True, stop=False)
                    ins = pe.matmul(o, s.mqkT[p, 2 * h + tile, p], s.v1[p, tile, h, :], start=(n == 0), stop=True)
                ins.then_inc(mouts, 1)
                for h in range(HEADS):
                    ins = pe.matmul(k.psum[:, 5 + h // 2, (h % 2) * V1:(h % 2 + 1) * V1], s.kw[p, 2 * h + tile, :],
                                    s.v1[p, tile, h, :], start=True, stop=True)
                ins.then_inc(mdstate, 1)
                pe.wait_ge(vns, n + 1)
                for h in range(HEADS):
                    ins = pe.matmul(k.psum[:, 2, h * HD:(h + 1) * HD], s.kd[p, 2 * h + tile, :], vnew[p, h, :],
                                    start=True, stop=True)
                ins.then_inc(dstate, 1)
                if n > 0:
                    pe.wait_ge(rd, n)
                for h in range(HEADS):
                    o = k.psum[p, 1, h * HD:(h + 1) * HD]
                    if n > 0:
                        pe.matmul(o, s.qdT[:, 2 * h + tile, p], S[:, h, :], start=True, stop=False)
                    ins = pe.matmul(o, s.qkT[p, 2 * h + tile, p], vnew[p, h, :], start=(n == 0), stop=True)
                ins.then_inc(outs, 1)

        @block.vector
        def _(dve):
            dve.memset(S[:, :, :], 0.0).then_inc(gds, 1)
            dve.memset(C[:, :, :], 0.0).then_inc(mds, 1)
            for n in range(NCHUNK):
                tile, half = n // 2, n % 2
                p = slice(half * CHUNK, (half + 1) * CHUNK)
                u = s.u[p, :, :].rearrange("p (h i) d -> p h i d", i=TILES)[:, :, tile, :]
                if n == 0:
                    dve.tensor_copy(vnew[p, :, :], u).then_inc(vns, 1)
                else:
                    dve.wait_ge(ws, n)
                    dve.tensor_tensor(vnew[p, :, :], u, quad(0, p), ALU.subtract).then_inc(vns, 1)
                if n == NCHUNK - 1:
                    continue
                dve.wait_ge(mds, 2 * n + 1)
                dve.wait_ge(mouts, n + 1)
                dve.tensor_tensor(C[:, :, :], C[:, :, :], over_last(dec[:, :, n], V1), ALU.mult).then_inc(mds, 1)
                dve.wait_ge(mds, 2 * n + 2)
                dve.wait_ge(mdstate, n + 1)
                dve.tensor_tensor(by_bank(C[:, :, :]), by_bank(C[:, :, :]), two(5), ALU.add).then_inc(mds, 1)
                dve.wait_ge(outs, n + 1)
                dve.wait_ge(gds, 2 * n + 1)
                dve.tensor_tensor(S[:, :, :], S[:, :, :], over_last(gl[:, :, n], HD), ALU.mult).then_inc(gds, 1)
                dve.wait_ge(gds, 2 * n + 2)
                dve.wait_ge(dstate, n + 1)
                dve.tensor_tensor(S[:, :, :], S[:, :, :], quad(2), ALU.add).then_inc(gds, 1)

        @block.scalar
        def _(act):
            for n in range(NCHUNK):
                tile, half = n // 2, n % 2
                p = slice(half * CHUNK, (half + 1) * CHUNK)
                act.wait_ge(mouts, n + 1)
                act.activation(by_bank(s.mh[p, tile, :, :]), two(3, p), ACT.Copy).then_inc(mrd, 1)
                act.wait_ge(outs, n + 1)
                act.activation(s.go[p, tile, :, :], quad(1, p), ACT.Copy).then_inc(rd, 1)

        k.idle_pool(block)


def mixer_output(k, s, mixed):
    with ExitStack() as ctx, k.stage() as block:
        gain = k.sb(ctx, "head_gains", [P, HD + GW])
        sq = k.sb(ctx, "output_squares", [P, 2 * PAIRS, HD])
        c = k.sb(ctx, "output_columns", [P, 4, 2 * PAIRS])
        landed, vs, acts, pools = (k.sig.new() for _ in range(4))
        def heads(ap):
            return ap.rearrange("p i (h d) -> p i h d", h=HEADS)

        def per_head(col):
            return over_last(col, HD).rearrange("p (i h) d -> p i h d", h=HEADS)
        go, mo = mixed[:, :, 0:GW], mixed[:, :, GW:2 * GW]
        src_m = s.mh[:, :, :, 0:HD]
        sq_g, sq_m = (sq[:, 8 * n:8 * n + 8, :].rearrange("p (i h) d -> p i h d", h=HEADS) for n in range(2))

        @block.sync
        def _(sp):
            sp.dma_start(gain[:, 0:HD], k.a["gdn_norm_w"].partition_broadcast(P).rearrange("p a d -> p (a d)")).then_inc(landed, 16)
            sp.dma_start(gain[:, HD:], k.a["mlstm_norm_w"].partition_broadcast(P).rearrange("p a d -> p (a d)")).then_inc(landed, 16)
            k.stream(sp)

        @block.scalar
        def _(act):
            act.activation(sq_g, s.go[:, :, :, :], ACT.Square).then_inc(acts, 1)
            act.activation(s.z[:, :, :], s.z[:, :, :], ACT.Silu).then_inc(acts, 1)
            act.activation(s.mo[:, :, :], s.mo[:, :, :], ACT.Sigmoid).then_inc(acts, 1)
            act.wait_ge(vs, 4)
            act.activation(sq_m, heads(mo), ACT.Square).then_inc(acts, 1)
            act.wait_ge(vs, 6)
            act.activation(c[:, 2, :], c[:, 1, :], ACT.Sqrt, bias=k.eps[:, 0:1], scale=1.0 / HD).then_inc(acts, 1)

        @block.vector
        def _(dve):
            link = linker(dve, vs)
            d = c[:, 0, 0:8].rearrange("p (i h) -> p i h", h=HEADS)
            link(dve.scalar_tensor_tensor(d, s.mh[:, :, :, HD], -1.0, s.mh[:, :, :, HD], ALU.mult, ALU.max))
            link(dve.tensor_tensor(d, d, s.emt[:, :].rearrange("p (h i) -> p i h", h=HEADS), ALU.max))
            link(dve.reciprocal(c[:, 0, 0:8], c[:, 0, 0:8]))
            link(dve.tensor_tensor(heads(mo), src_m, per_head(c[:, 0, 0:8]), ALU.mult))
            dve.wait_ge(acts, 1)
            link(dve.tensor_reduce(c[:, 1, 0:8], sq[:, 0:8, :], AX_X, ALU.add))
            dve.wait_ge(acts, 4)
            link(dve.tensor_reduce(c[:, 1, 8:16], sq[:, 8:16, :], AX_X, ALU.add))
            dve.wait_ge(acts, 5)
            link(dve.reciprocal(c[:, 3, :], c[:, 2, :]))
            link(dve.tensor_tensor(heads(go), s.go[:, :, :, :], per_head(c[:, 3, 0:8]), ALU.mult))
            link(dve.tensor_tensor(heads(mo), heads(mo), per_head(c[:, 3, 8:16]), ALU.mult))
            dve.wait_ge(landed, 32)
            link(dve.tensor_tensor(heads(go), heads(go), over_middle(gain[:, 0:HD], PAIRS).rearrange("p (i h) d -> p i h d", h=HEADS), ALU.mult))
            link(dve.tensor_tensor(mo, mo, over_middle(gain[:, HD:], TILES), ALU.mult))
            link(dve.tensor_tensor(go, go, s.z[:, :, :], ALU.mult))
            link(dve.tensor_tensor(mo, mo, s.mo[:, :, :], ALU.mult))

        k.idle_pool(block)


class MixerState:

    def __init__(self, k, ctx):
        def sb(name, shape):
            return k.sb(ctx, name, shape)
        self.consts = sb("constants_sb", [P, NCONST, P])
        self.conv = sb("convolved_T", [P, 20, SEQ])
        self.z = sb("gdn_z", [P, TILES, GW])
        self.mv = sb("mlstm_v", [P, TILES, GW])
        self.mo = sb("mlstm_o", [P, TILES, GW])
        self.gates = sb("gates", [P, TILES, 16])
        self.beta = sb("beta", [P, TILES, HEADS])
        self.log_i = sb("log_i", [P, TILES, HEADS])
        self.logs = sb("log_alpha_f", [P, TILES, 2, HEADS])
        self.run = sb("running_logs", [P, 2, 2, PAIRS])
        self.total = sb("chunk_totals", [P, 2, HEADS * NCHUNK])
        self.glast = sb("chunk_decays", [P, 2, HEADS * NCHUNK])
        self.emt = sb("exp_minus_m", [P, PAIRS])

    def more(self, k, ctx):
        def mats(name):
            return k.sb(ctx, name, [P, PAIRS, P])
        self.natural = k.sb(ctx, "natural_k_v_mk", [P, 3 * PAIRS, P])
        self.qk_raw, self.mqk_raw = mats("key_query"), mats("mlstm_key_query")
        self.u, self.wT, self.qdT, self.kd = mats("u"), mats("w_T"), mats("q_decayed_T"), mats("k_decayed")
        self.qkT = self.qk_raw
        self.mqkT = self.mqk_raw
        self.mqdT = self.conv[:, 12:16, :].rearrange("p h (i n) -> p (h i) n", n=P)
        self.kw = self.natural[:, 16:24, :]
        self.v1 = k.sb(ctx, "mlstm_v_and_one", [P, TILES, HEADS, HD + 1])
        self.go = k.sb(ctx, "gdn_out", [P, TILES, HEADS, HD])
        self.mh = k.sb(ctx, "mlstm_out", [P, TILES, HEADS, HD + 1])

    def mask(self, n):
        return self.consts[:, n, :]



def cross_attention(k):
    a = k.a
    with ExitStack() as ctx:
        qT = k.sb(ctx, "xa_q_T", [P, DC, SEQ])
        kT = k.sb(ctx, "xa_k_T", [P, DC, SEQ])
        v = k.sb(ctx, "xa_v", [P, TILES, D])
        with ExitStack() as inner:
            mem = k.sb(inner, "memory", [P, TILES, D])
            memT = Split(k, inner, "memory_T", [P, DC, SEQ])
            with k.stage() as block:
                landed = k.sig.new()

                @block.sync
                def _(sp):
                    sp.dma_start(mem[:, :, :], a["mem"][0].rearrange("(i p) d -> p i d", p=P)).then_inc(landed, 16)
                    k.stream(sp)
                    sp.wait_ge(landed, 16)

                k.idle_pool(block)
            norm_transpose(k, mem, memT, COL_MEM)
            norm_transpose(k, k.x, k.xT, COL_XA)
            panels(k, [("T", k.xT, qT[:, 2 * n:2 * n + 2, :], None, 1.0) for n in range(4)]
                   + [("T", memT, kT[:, 2 * n:2 * n + 2, :], None, 1.0) for n in range(4)])
            rows_product(k, memT, 4, copy_to(k, v))
        attend_memory(k, qT, kT, v)
        rows_product(k, k.xT, 4, add_to(k, k.x))


def attend_memory(k, qT, kT, v):
    DH = D // HEADS
    scale = DH ** -0.5
    with ExitStack() as ctx, k.stage() as block:
        prob = k.sb(ctx, "xa_probabilities", [P, PAIRS, SEQ])
        probT = k.sb(ctx, "xa_probabilities_T", [P, HEADS, 2, SEQ])
        c = k.sb(ctx, "xa_columns", [P, 4, PAIRS])
        scored, maxed, negated, expd, recip, scaled, turned, copied, mixed, high, written = (k.sig.new() for _ in range(11))

        highs, lows = split_banks(k, 0, k.xT, mixed, high, written)

        @block.sync
        def _(sp):
            k.stream(sp)

        @block.tensor
        def _(pe):
            for e in range(PAIRS):
                h, i = e // 2, e % 2
                for half in range(2):
                    ins = pe.matmul(k.psum[:, h, i * SEQ:(i + 1) * SEQ], qT[:, 2 * h + half, i * P:(i + 1) * P],
                                    kT[:, 2 * h + half, :], start=(half == 0), stop=(half == 1))
                if i == 1:
                    ins.then_inc(scored, 1)
            for h in range(HEADS):
                pe.wait_ge(scaled, h + 1)
                for i in range(TILES):
                    for m in range(2):
                        at = m * SEQ + i * P
                        ins = pe.transpose(k.psum[:, 4 + h, at:at + P], prob[:, 2 * h + i, m * P:(m + 1) * P], k.ident[:, :])
                ins.then_inc(turned, 1)
            for h in range(HEADS):
                pe.wait_ge(copied, h + 1)
                for half in range(2):
                    for m in range(2):
                        lo = h * DH + half * P
                        ins = pe.matmul(k.psum[:, h, half * SEQ:(half + 1) * SEQ], v[:, m, lo:lo + P],
                                        probT[:, h, m, :], start=(m == 0), stop=(m == 1))
                ins.then_inc(mixed, 1)

        @block.vector
        def _(dve):
            for h in range(HEADS):
                dve.wait_ge(scored, h + 1)
                dve.tensor_reduce(c[:, 0, 2 * h:2 * h + 2], bank2(k, h), AX_X, ALU.max).then_inc(maxed, 1)
                dve.wait_ge(maxed, h + 1)
                dve.tensor_scalar(c[:, 1, 2 * h:2 * h + 2], c[:, 0, 2 * h:2 * h + 2], -scale, None, ALU.mult).then_inc(negated, 1)
            for h in range(HEADS):
                dve.wait_ge(expd, 2 * (h + 1))
                dve.reciprocal(c[:, 3, 2 * h:2 * h + 2], c[:, 2, 2 * h:2 * h + 2]).then_inc(recip, 1)
                dve.wait_ge(recip, h + 1)
                part = prob[:, 2 * h:2 * h + 2, :]
                dve.tensor_tensor(part, part, over_last(c[:, 3, 2 * h:2 * h + 2], SEQ), ALU.mult).then_inc(scaled, 1)
            lows(dve)

        @block.scalar
        def _(act):
            for e in range(PAIRS):
                h, i = e // 2, e % 2
                act.wait_ge(negated, h + 1)
                act.activation(prob[:, e, :], k.psum[:, h, i * SEQ:(i + 1) * SEQ], ACT.Exp, bias=c[:, 1, e:e + 1],
                               scale=scale, accum_out=c[:, 2, e:e + 1]).then_inc(expd, 1)
            for h in range(HEADS):
                act.wait_ge(turned, h + 1)
                act.activation(probT[:, h, :, :], bank2(k, 4 + h), ACT.Copy).then_inc(copied, 1)
            highs(act)

        k.idle_pool(block)



HALVES = 2 * PEER_HEADS
PICKS = PEER_HEADS * TOPK
LOW = -3.0e38


def peer(k):
    a = k.a
    picksT = k.w.ring[:, RING - 1, 0:3 * SEQ].rearrange("p (n t) -> p n t", n=3)
    iota = k.w.ring[:, RING - 1, 3 * SEQ:3 * SEQ + P]
    norm_transpose(k, k.x, k.xT, COL_FFN)
    with ExitStack() as ctx:
        qT = k.sb(ctx, "peer_q_T", [P, HALVES, SEQ])
        keysT = k.sb(ctx, "sub_keys_T", [P, HALVES, KEYS])
        k.w.hold = k.w.taken + 8
        panels(k, [("T", k.xT, qT[:, 2 * n:2 * n + 2, :], None, 1.0) for n in range(8)])
        turn_keys(k, keysT, iota)
        for tile in range(TILES):
            pick_experts(k, qT, keysT, iota, picksT, tile)
    with ExitStack() as ctx:
        loads = ExpertLoads(k)
        gates = k.sb(ctx, "gate_matrix", [P, SEQ, KEYS])
        scatter_gates(k, picksT, iota, gates, loads)
        every_expert(k, gates, loads)
    k.w.hold = 1 << 30
    final_norm(k)


def turn_keys(k, keysT, iota):
    with ExitStack() as ctx, k.stage() as block:
        keys = k.sb(ctx, "sub_keys", [P, HALVES, KEYS])
        landed, turned, copied, iota_landed = (k.sig.new() for _ in range(4))

        @block.sync
        def _(sp):
            src = k.a["peer_sub_keys"][0].rearrange("h s n d -> (h s) n d")
            for n in range(HALVES):
                sp.dma_start(keys[:, n, :], src[n]).then_inc(landed, 16)
            sp.dma_start(iota, k.a["constants"][:, C_IOTA * P:(C_IOTA + 1) * P]).then_inc(iota_landed, 16)
            k.stream(sp)
            sp.wait_ge(iota_landed, 16)

        @block.tensor
        def _(pe):
            pe.wait_ge(landed, 16 * HALVES)
            for b in range(4):
                for q in range(4):
                    ins = pe.transpose(k.psum[:, b, q * P:(q + 1) * P], keys[:, 4 * b + q, :], k.ident[:, :])
                ins.then_inc(turned, 1)

        @block.scalar
        def _(act):
            for b in range(4):
                act.wait_ge(turned, b + 1)
                act.activation(keysT[:, 4 * b:4 * b + 4, :], k.psum[:, b, :].rearrange("p (a n) -> p a n", a=4),
                               ACT.Copy).then_inc(copied, 1)

        k.idle_pool(block)


def pick_experts(k, qT, keysT, iota, picksT, tile):
    with ExitStack() as ctx, k.stage() as block:
        score = k.sb(ctx, "key_scores", [P, HALVES, KEYS])
        rest = k.sb(ctx, "scores_without_top", [P, HALVES, KEYS])
        top = k.sb(ctx, "top_scores", [P, HALVES, TOPK])
        topi = k.sb(ctx, "top_keys_int", [P, HALVES, TOPK], U32)
        topf = k.sb(ctx, "top_keys", [P, HALVES, TOPK])
        cand = k.sb(ctx, "candidates", [P, PEER_HEADS, TOPK, TOPK])
        crest = k.sb(ctx, "candidates_without_top", [P, PEER_HEADS, TOPK * TOPK])
        best = k.sb(ctx, "best", [P, PEER_HEADS, TOPK])
        pos = k.sb(ctx, "best_position", [P, PICKS], U32)
        ab = k.sb(ctx, "position_parts_int", [P, 2, PICKS], U32)
        abf = k.sb(ctx, "position_parts", [P, 2, PICKS])
        hit = k.sb(ctx, "position_hits", [P, 2, PICKS, TOPK])
        out3 = k.sb(ctx, "picks", [P, 3, PICKS])
        col = k.sb(ctx, "gate_sums", [P, 2, PEER_HEADS])
        scored, copied, found, vs, expd, turned, pools = (k.sig.new() for _ in range(7))

        @block.sync
        def _(sp):
            k.stream(sp)

        @block.tensor
        def _(pe):
            for b in range(4):
                for q in range(4):
                    n = 4 * b + q
                    ins = pe.matmul(k.psum[:, b, q * P:(q + 1) * P], qT[:, n, tile * P:(tile + 1) * P], keysT[:, n, :],
                                    start=True, stop=True)
                ins.then_inc(scored, 1)
            pe.wait_ge(vs, 10)
            for q in range(3):
                ins = pe.transpose(k.psum[:, 4, q * P:(q + 1) * P], out3[:, q, :], k.ident[:, :])
            ins.then_inc(turned, 1)

        @block.scalar
        def _(act):
            for b in range(4):
                act.wait_ge(scored, b + 1)
                act.activation(score[:, 4 * b:4 * b + 4, :], k.psum[:, b, :].rearrange("p (a n) -> p a n", a=4),
                               ACT.Copy).then_inc(copied, 1)
            act.wait_ge(vs, 2)
            act.activation(out3[:, 2, :], best[:, :, :].rearrange("p h n -> p (h n)"), ACT.Exp).then_inc(expd, 1)

        @block.vector
        def _(dve):
            steps = [0]

            def sweep(n, issue):
                for m in range(n):
                    issue(m).then_inc(found, 1)
                steps[0] += n
                dve.wait_ge(found, steps[0])

            def top16(n, values, without, v16, i16):
                sweep(n, lambda m: dve.max(v16(m, 0), values(m)))
                sweep(n, lambda m: dve.max_index(i16(m, 0), v16(m, 0), values(m)))
                sweep(n, lambda m: dve.match_replace(without(m), v16(m, 0), values(m), LOW))
                sweep(n, lambda m: dve.max(v16(m, 1), without(m)))
                sweep(n, lambda m: dve.max_index(i16(m, 1), v16(m, 1), without(m)))

            dve.wait_ge(copied, 4)
            top16(HALVES, lambda m: score[:, m, :], lambda m: rest[:, m, :],
                  lambda m, r: top[:, m, 8 * r:8 * r + 8], lambda m, r: topi[:, m, 8 * r:8 * r + 8])
            dve.tensor_copy(topf[:, :, :], topi[:, :, :]).then_inc(found, 1)
            pairs = top[:, :, :].rearrange("p (h s) n -> p h s n", s=2)
            for h in range(PEER_HEADS):
                dve.tensor_tensor(cand[:, h, :, :], over_last(pairs[:, h, 0, :], TOPK), over_middle(pairs[:, h, 1, :], TOPK),
                                  ALU.add).then_inc(found, 1)
            steps[0] += 9
            dve.wait_ge(found, steps[0])
            top16(PEER_HEADS, lambda m: cand[:, m, :, :].rearrange("p a b -> p (a b)"), lambda m: crest[:, m, :],
                  lambda m, r: best[:, m, 8 * r:8 * r + 8],
                  lambda m, r: pos[:, TOPK * m + 8 * r:TOPK * m + 8 * r + 8])
            link = linker(dve, vs)
            link(dve.tensor_copy(col[:, 0, :], best[:, :, 0]))
            link(dve.tensor_tensor(best[:, :, :], best[:, :, :], over_last(col[:, 0, :], TOPK), ALU.subtract))
            link(dve.tensor_scalar(ab[:, 0, :], pos[:, :], 4, None, ALU.logical_shift_right))
            link(dve.tensor_scalar(ab[:, 1, :], pos[:, :], 15, None, ALU.bitwise_and))
            link(dve.tensor_copy(abf[:, :, :], ab[:, :, :]))
            for s in range(2):
                link(dve.tensor_tensor(hit[:, s, :, :], over_last(abf[:, s, :], TOPK), over_middle(iota[:, 0:TOPK], PICKS),
                                       ALU.is_equal))
            keys = topf[:, :, :].rearrange("p (h s) n -> p s h n", s=2)
            for s in range(2):
                for h in range(PEER_HEADS):
                    part = hit[:, s, TOPK * h:TOPK * (h + 1), :]
                    dve.tensor_tensor(part, part, over_middle(keys[:, s, h, :], TOPK), ALU.mult).then_inc(found, 1)
            steps[0] += 2 * PEER_HEADS
            dve.wait_ge(found, steps[0])
            link(dve.tensor_reduce(out3[:, 0:2, :].rearrange("p s n -> p (s n)"),
                                   hit[:, :, :, :].rearrange("p s n a -> p (s n) a"), AX_X, ALU.add))
            dve.wait_ge(expd, 1)
            g = out3[:, 2, :].rearrange("p (h n) -> p h n", h=PEER_HEADS)
            dve.tensor_reduce(col[:, 0, :], g, AX_X, ALU.add).then_inc(found, 1)
            steps[0] += 1
            dve.wait_ge(found, steps[0])
            link(dve.reciprocal(col[:, 1, :], col[:, 0, :]))
            link(dve.tensor_tensor(g, g, over_last(col[:, 1, :], TOPK), ALU.mult))
            dve.wait_ge(turned, 1)
            link(dve.tensor_copy(picksT[:, :, tile * P:(tile + 1) * P],
                                 k.psum[:, 4, 0:3 * P].rearrange("p (a n) -> p a n", a=3)))

        k.idle_pool(block)


def scatter_gates(k, picksT, iota, gates, loads):
    GROUP = 4
    TURN = 2 * GROUP
    with ExitStack() as ctx, k.stage() as block:
        rows = [k.sb(ctx, f"row_onehot_{b}", [P, GROUP, P]) for b in range(2)]
        cols = [k.sb(ctx, f"column_onehot_{b}", [P, GROUP, P]) for b in range(2)]
        rows_hit, rows_ready, cols_ready, made, emptied = (k.sig.new() for _ in range(5))
        turns = SEQ // TURN

        @block.sync
        def _(sp):
            for m in range(2):
                loads.step(sp, m, 0)

        def hits(dve, t, b):
            for which, dst, count in ((0, rows[b], rows_hit), (1, cols[b], cols_ready)):
                dve.tensor_tensor(dst[:, :, :], over_middle(iota, GROUP),
                                  over_last(picksT[:, which, bass.ds(t, GROUP)], P), ALU.is_equal).then_inc(count, 1)

        def weigh(pool, t, b):
            pool.tensor_tensor(rows[b][:, :, :], rows[b][:, :, :],
                               over_last(picksT[:, 2, bass.ds(t, GROUP)], P), ALU.mult).then_inc(rows_ready, 1)

        @block.vector
        def _(dve):
            for b in range(2):
                hits(dve, GROUP * b, b)
            with dve.Fori(1, turns) as i:
                for b in range(2):
                    dve.wait_ge(made, 2 * i - 1 + b)
                    hits(dve, TURN * i + GROUP * b, b)

        @block.gpsimd
        def _(pool):
            k.sig.clear_other(pool)
            with pool.Fori(0, turns) as i:
                for b in range(2):
                    pool.wait_ge(rows_hit, 2 * i + 1 + b)
                    weigh(pool, TURN * i + GROUP * b, b)

        def products(pe, b, ready, empty=None):
            pe.wait_ge(rows_ready, ready)
            pe.wait_ge(cols_ready, ready)
            if empty is not None:
                pe.wait_ge(emptied, empty)
            for q in range(GROUP):
                ins = pe.matmul(k.psum[:, b, q * P:(q + 1) * P], rows[b][:, q, :], cols[b][:, q, :], start=True, stop=True)
            ins.then_inc(made, 1)

        @block.tensor
        def _(pe):
            for b in range(2):
                products(pe, b, b + 1)
            with pe.Fori(1, turns) as i:
                for b in range(2):
                    products(pe, b, 2 * i + 1 + b, 2 * i - 1 + b)

        @block.scalar
        def _(act):
            with act.Fori(0, turns) as i:
                for b in range(2):
                    act.wait_ge(made, 2 * i + 1 + b)
                    act.activation(gates[:, bass.ds(TURN * i + GROUP * b, GROUP), :],
                                   k.psum[:, b, :].rearrange("p (a n) -> p a n", a=GROUP), ACT.Copy).then_inc(emptied, 1)


class ExpertLoads:

    def __init__(self, k):
        self.k = k
        self.tables = [k.a[n][0].rearrange("(i j) d -> i j d", j=KEYS) for n in ("peer_u", "peer_v")]
        self.sixths = k.w.ring[:, :, :].rearrange("p r (f n) -> p (r f) n", f=2)
        self.u_turned = self.v_split = None

    def part(self, m, what):
        return self.sixths[:, 2 * (m % 3) + what, :]

    def step(self, sp, m, i):
        for what in range(2):
            if m >= 3:
                if what == 0:
                    sp.wait_ge(self.u_turned, 2 * (m - 2) + 12 * i)
                else:
                    sp.wait_ge(self.v_split, m - 2 + 6 * i)
            src = self.tables[what][:, bass.ds(m + 6 * i, 1), :].rearrange("p o d -> p (o d)")
            sp.dma_start(self.part(m, what), src).then_inc(self.k.expert_landed[2 * (m % 3) + what], 16)

    def landed(self, engine, m, what, i):
        engine.wait_ge(self.k.expert_landed[2 * (m % 3) + what], 16 * (m // 3 + 1 + 2 * i))


def every_expert(k, gates, loads):
    TURN = 6
    turns = (KEYS - 2) // TURN
    assert KEYS == 2 + TURN * turns
    with ExitStack() as ctx, k.stage() as block:
        uT = Split(k, ctx, "u_T", [P, DC, P])
        v_split = k.sb(ctx, "v_split", [P, 2, 2, D], F32R)
        w_split = k.sb(ctx, "weighted_split", [P, 2, 2, SEQ], F32R)
        gelu = k.sb(ctx, "gelu", [P, SEQ])
        turned, u_high, u_low, v_high, v_low, products, gelus, weights, w_high, w_low, outs, added = \
            (k.sig.new() for _ in range(12))
        loads.v_split = v_low
        loads.u_turned = turned

        @block.sync
        def _(sp):
            for m in range(2, 1 + TURN):
                loads.step(sp, m, 0)
            with sp.Fori(0, turns - 1) as i:
                for m in range(1 + TURN, 1 + 2 * TURN):
                    loads.step(sp, m, i)
            loads.step(sp, KEYS - 1, 0)

        def turn_u(pe, m, i):
            loads.landed(pe, m, 0, i)
            for half in range(2):
                n = 2 * m + half
                if n >= 3:
                    pe.wait_ge(u_low, n - 2 + 2 * TURN * i)
                for q in range(4):
                    c = 4 * half + q
                    ins = pe.transpose(k.psum[:, 4 + n % 3, q * P:(q + 1) * P], loads.part(m, 0)[:, c * P:(c + 1) * P],
                                       k.ident[:, :])
                ins.then_inc(turned, 1)

        def u_products(pe, m, i):
            if m >= 1:
                pe.wait_ge(gelus, m + TURN * i)
            for c in range(DC):
                if c % 4 == 0:
                    pe.wait_ge(u_low, 2 * m + c // 4 + 1 + 2 * TURN * i)
                ins = passes(pe, k.psum[:, 7, 0:SEQ], uT.at(slice(0, P), c), k.xT.at(slice(0, P), c), c == 0, c == DC - 1)
            ins.then_inc(products, 1)

        def v_products(pe, m, i, stop=False):
            pe.wait_ge(v_low, m + 1 + TURN * i)
            pe.wait_ge(w_low, m + 1 + TURN * i)
            b = m % 2
            down(pe, k, (w_split[:, b, 0, :], w_split[:, b, 1, :]), (v_split[:, b, 0, :], v_split[:, b, 1, :]),
                 m == 0, stop).then_inc(outs, 1)

        def run(engine, step):
            for m in range(1, 1 + TURN):
                step(m, 0)
            with engine.Fori(0, turns - 1) as i:
                for m in range(1 + TURN, 1 + 2 * TURN):
                    step(m, i)

        @block.tensor
        def _(pe):
            def step(m, i):
                turn_u(pe, m + 1, i)
                u_products(pe, m, i)
                v_products(pe, m - 1, i)
            turn_u(pe, 0, 0)
            turn_u(pe, 1, 0)
            u_products(pe, 0, 0)
            run(pe, step)
            u_products(pe, KEYS - 1, 0)
            v_products(pe, KEYS - 2, 0)
            v_products(pe, KEYS - 1, 0, True)

        def u_half(m, half):
            n = 2 * m + half
            return k.psum[:, 4 + n % 3, :].rearrange("p (a n) -> p a n", a=4), slice(4 * half, 4 * half + 4)

        @block.scalar
        def _(act):
            def u(m, i):
                if m >= 1:
                    act.wait_ge(products, m + TURN * i)
                for half in range(2):
                    src, c = u_half(m, half)
                    act.wait_ge(turned, 2 * m + half + 1 + 2 * TURN * i)
                    split_high(act, uT.hi[:, c, :], src).then_inc(u_high, 1)

            def v(m, i):
                loads.landed(act, m, 1, i)
                if m >= 2:
                    act.wait_ge(outs, m - 1 + TURN * i)
                split_high(act, v_split[:, m % 2, 0, :], loads.part(m, 1)).then_inc(v_high, 1)

            def activate(m, i):
                act.wait_ge(products, m + 1 + TURN * i)
                if m >= 1:
                    act.wait_ge(w_low, m + TURN * i)
                act.activation(gelu[:, :], k.psum[:, 7, 0:SEQ], ACT.Gelu).then_inc(gelus, 1)

            def weighted(m, i):
                act.wait_ge(weights, m + 1 + TURN * i)
                if m >= 2:
                    act.wait_ge(outs, m - 1 + TURN * i)
                split_high(act, w_split[:, m % 2, 0, :], gelu[:, :]).then_inc(w_high, 1)

            def step(m, i):
                v(m, i)
                activate(m, i)
                u(m + 1, i)
                weighted(m, i)
            u(0, 0)
            v(0, 0)
            activate(0, 0)
            u(1, 0)
            weighted(0, 0)
            run(act, step)
            v(KEYS - 1, 0)
            activate(KEYS - 1, 0)
            weighted(KEYS - 1, 0)

        @block.vector
        def _(dve):
            def u(m, i):
                for half in range(2):
                    src, c = u_half(m, half)
                    dve.wait_ge(u_high, 2 * m + half + 1 + 2 * TURN * i)
                    split_low(dve, uT.lo[:, c, :], src, uT.hi[:, c, :]).then_inc(u_low, 1)

            def v(m, i):
                dve.wait_ge(v_high, m + 1 + TURN * i)
                b = m % 2
                split_low(dve, v_split[:, b, 1, :], loads.part(m, 1), v_split[:, b, 0, :]).then_inc(v_low, 1)

            def weigh(m, i):
                dve.wait_ge(gelus, m + 1 + TURN * i)
                dve.tensor_tensor(gelu[:, :], gelu[:, :], gates[:, :, bass.ds(m + TURN * i, 1)].rearrange("p t o -> p (t o)"),
                                  ALU.mult).then_inc(weights, 1)

            def weighted(m, i):
                dve.wait_ge(w_high, m + 1 + TURN * i)
                split_low(dve, w_split[:, m % 2, 1, :], gelu[:, :], w_split[:, m % 2, 0, :]).then_inc(w_low, 1)

            def step(m, i):
                v(m, i)
                weigh(m, i)
                u(m + 1, i)
                weighted(m, i)
            u(0, 0)
            v(0, 0)
            weigh(0, 0)
            u(1, 0)
            weighted(0, 0)
            run(dve, step)
            v(KEYS - 1, 0)
            weigh(KEYS - 1, 0)
            weighted(KEYS - 1, 0)
            dve.wait_ge(outs, KEYS)
            for t in range(TILES):
                dve.tensor_tensor(k.x[:, t, :], accumulated(k, t), k.x[:, t, :], ALU.add).then_inc(added, 1)

        k.idle_pool(block)


def final_norm(k):
    with ExitStack() as ctx, k.stage() as block:
        gain = k.sb(ctx, "final_gain", [P, D])
        sq = k.sb(ctx, "final_squares", [P, TILES, D])
        stat = k.sb(ctx, "final_stats", [P, 3, TILES])
        landed, squares, rooted, vs = (k.sig.new() for _ in range(4))

        @block.sync
        def _(sp):
            sp.dma_start(gain[:, :], k.a["norm_final_w"].partition_broadcast(P)).then_inc(landed, 16)
            k.stream(sp)

        @block.scalar
        def _(act):
            for i in range(TILES):
                act.activation(sq[:, i, :], k.x[:, i, :], ACT.Square, accum_out=stat[:, 0, i:i + 1]).then_inc(squares, 1)
            act.wait_ge(squares, TILES)
            act.activation(stat[:, 1, :], stat[:, 0, :], ACT.Sqrt, bias=k.eps[:, 0:1], scale=1.0 / D).then_inc(rooted, 1)

        @block.vector
        def _(dve):
            link = linker(dve, vs)
            dve.wait_ge(rooted, 1)
            link(dve.reciprocal(stat[:, 2, :], stat[:, 1, :]))
            dve.wait_ge(landed, 16)
            for i in range(TILES):
                link(dve.scalar_tensor_tensor(k.x[:, i, :], k.x[:, i, :], stat[:, 2, i:i + 1], gain[:, :], ALU.mult, ALU.mult))

        k.idle_pool(block)



def load_gains(k, sp, gains, landed, which):
    layer, n = divmod(which, 3)
    sp.dma_start(gains[:, 0, :], k.a["ln_g_2"][layer, n].partition_broadcast(P)).then_inc(landed, 16)
    sp.dma_start(gains[:, 1, :], k.a["ln_b_2"][layer, n].partition_broadcast(P)).then_inc(landed, 16)


def post_norm(k, gains):
    with ExitStack() as ctx, k.stage() as block:
        sq = k.sb(ctx, "centred_squares", [P, TILES, D])
        stat = k.sb(ctx, "norm_stats", [P, 5, TILES])
        summed, negated, squared, rooted, recip, scaled, gained, normed, banks, high, written = (k.sig.new() for _ in range(11))
        highs, lows = split_banks(k, 4, k.xT, banks, high, written)

        @block.sync
        def _(sp):
            k.stream(sp)

        @block.vector
        def _(dve):
            for i in range(TILES):
                dve.scalar_tensor_tensor(k.x[:, i, :], k.x[:, i, :], DN_ALPHA, accumulated(k, i), ALU.mult, ALU.add,
                                         accum_out=stat[:, 0, i:i + 1]).then_inc(summed, 1)
                dve.wait_ge(summed, i + 1)
                dve.tensor_scalar(stat[:, 1, i:i + 1], stat[:, 0, i:i + 1], -1.0 / D, None, ALU.mult).then_inc(negated, 1)
            for i in range(TILES):
                dve.wait_ge(rooted, i + 1)
                dve.reciprocal(stat[:, 4, i:i + 1], stat[:, 3, i:i + 1]).then_inc(recip, 1)
                dve.wait_ge(recip, i + 1)
                dve.tensor_scalar(k.x[:, i, :], k.x[:, i, :], stat[:, 1, i:i + 1], stat[:, 4, i:i + 1], ALU.add,
                                  ALU.mult).then_inc(scaled, 1)
                dve.wait_ge(scaled, i + 1)
                dve.tensor_tensor(k.x[:, i, :], k.x[:, i, :], gains[:, 0, :], ALU.mult).then_inc(gained, 1)
                dve.wait_ge(gained, i + 1)
                dve.tensor_tensor(k.x[:, i, :], k.x[:, i, :], gains[:, 1, :], ALU.add).then_inc(normed, 1)
            lows(dve)

        @block.scalar
        def _(act):
            for i in range(TILES):
                act.wait_ge(negated, i + 1)
                act.activation(sq[:, i, :], k.x[:, i, :], ACT.Square, bias=stat[:, 1, i:i + 1],
                               accum_out=stat[:, 2, i:i + 1]).then_inc(squared, 1)
                act.wait_ge(squared, i + 1)
                act.activation(stat[:, 3, i:i + 1], stat[:, 2, i:i + 1], ACT.Sqrt, bias=k.eps[:, 1:2],
                               scale=1.0 / D).then_inc(rooted, 1)
            highs(act)

        @block.tensor
        def _(pe):
            for i in range(TILES):
                pe.wait_ge(normed, i + 1)
                for c in range(DC):
                    at = (c % 2) * SEQ + i * P
                    ins = pe.transpose(k.psum[:, 4 + c // 2, at:at + P], k.x[:, i, c * P:(c + 1) * P], k.ident[:, :])
                    if i == TILES - 1 and c % 2 == 1:
                        ins.then_inc(banks, 1)

        k.idle_pool(block)


def swiglu(k, gains, which):
    UNITS = FFN_DIM // COLS
    TURN = 2
    PER = 3 * TURN
    turns = (UNITS - 1) // TURN
    assert UNITS == 1 + TURN * turns and PER % RING == 0 and PER % BUFFERS == 0
    g0 = k.w.take(3 * UNITS)
    with ExitStack() as ctx, k.stage() as block:
        split = Splitter(k, ctx, g0)
        act_out = k.sb(ctx, "silu", [P, 2, 2, SEQ])
        hidden = Split(k, ctx, "hidden", [P, 2, 2, SEQ])
        gains_landed, silus, gated, highs, lows = (k.sig.new() for _ in range(5))

        def first(u, n):
            return n if u == 0 else 3 * u - 1 + n

        def last(u):
            return 3 * u + 4 if u < UNITS - 1 else 3 * UNITS - 1

        @block.sync
        def _(sp):
            load_gains(k, sp, gains, gains_landed, which)
            k.stream(sp)
            sp.wait_ge(gains_landed, 32)

        def up(pe, u, i):
            for n in range(2):
                if u >= 2:
                    pe.wait_ge((silus, gated)[n], u - 1 + TURN * i)
                split.ready(pe, first(u, n), i, PER)
                wh, wl = split.panel(first(u, n))
                for j in range(2):
                    own = slice(j * P, (j + 1) * P)
                    for c in range(DC):
                        ins = passes(pe, k.psum[:, 4 + 2 * (u % 2) + n, j * SEQ:(j + 1) * SEQ],
                                     (wh[:, c, own], wl[:, c, own]), k.xT.at(slice(0, P), c), c == 0, c == DC - 1)
                ins.then_inc(split.eaten, 1)

        def down_unit(pe, u, i):
            split.ready(pe, last(u), i, PER)
            wh, wl = split.rows(last(u))
            pe.wait_ge(lows, u + 1 + TURN * i)
            for r in range(2):
                ins = down(pe, k, hidden.at(slice(0, P), u % 2, r), (wh[:, r, :], wl[:, r, :]), u == 0 and r == 0,
                           u == UNITS - 1 and r == 1)
            ins.then_inc(split.eaten, 1)

        def run(engine, unit):
            for u in range(1, 1 + TURN):
                unit(u, 0)
            with engine.Fori(0, turns - 1) as i:
                for u in range(1 + TURN, 1 + 2 * TURN):
                    unit(u, i)

        @block.tensor
        def _(pe):
            def unit(u, i):
                up(pe, u, i)
                down_unit(pe, u - 1, i)
            up(pe, 0, 0)
            run(pe, unit)
            down_unit(pe, UNITS - 1, 0)

        @block.scalar
        def _(act):
            def silu(u, i):
                split.finished(act, first(u, 0), i, PER)
                if u >= 2:
                    act.wait_ge(gated, u - 1 + TURN * i)
                act.activation(act_out[:, u % 2, :, :], bank2(k, 4 + 2 * (u % 2)), ACT.Silu).then_inc(silus, 1)

            def high(u, i):
                act.wait_ge(gated, u + 1 + TURN * i)
                if u >= 2:
                    split.finished(act, last(u - 2), i, PER)
                split_high(act, hidden.hi[:, u % 2, :, :], act_out[:, u % 2, :, :]).then_inc(highs, 1)

            def unit(u, i):
                split.high(act, first(u, 0) + 1, i, PER)
                split.high(act, first(u, 0) + 2, i, PER)
                silu(u, i)
                split.high(act, first(u, 0) + 3, i, PER)
                high(u, i)
            split.high(act, 0)
            split.high(act, 1)
            split.high(act, 2)
            silu(0, 0)
            high(0, 0)
            run(act, unit)

        @block.vector
        def _(dve):
            def gate(u, i):
                split.finished(dve, first(u, 1), i, PER)
                dve.wait_ge(silus, u + 1 + TURN * i)
                if u >= 2:
                    dve.wait_ge(lows, u - 1 + TURN * i)
                out = act_out[:, u % 2, :, :]
                dve.scalar_tensor_tensor(out, out, 0.5, bank2(k, 5 + 2 * (u % 2)), ALU.mult, ALU.mult).then_inc(gated, 1)

            def low(u, i):
                dve.wait_ge(highs, u + 1 + TURN * i)
                split_low(dve, hidden.lo[:, u % 2, :, :], act_out[:, u % 2, :, :], hidden.hi[:, u % 2, :, :]).then_inc(lows, 1)

            def unit(u, i):
                split.low(dve, first(u, 0) + 1, i, PER)
                split.low(dve, first(u, 0) + 2, i, PER)
                split.low(dve, first(u, 0) + 3, i, PER)
                gate(u, i)
                low(u, i)
            split.low(dve, 0)
            split.low(dve, 1)
            split.low(dve, 2)
            gate(0, 0)
            low(0, 0)
            run(dve, unit)

        k.idle_pool(block)
    post_norm(k, gains)


def gains_only(k, gains, which):
    def finish(ctx, block, done):
        landed = k.sig.new()

        def take_act(act):
            load_gains(k, act, gains, landed, which)
            act.wait_ge(landed, 32)
        return take_act, (lambda dve: None)
    return finish


def spatial_gating(k, gains):
    with ExitStack() as ctx:
        mixedT = Split(k, ctx, "sgu_mixed_T", [P, 16, SEQ])
        with ExitStack() as inner:
            gatedT = k.sb(inner, "sgu_u_T", [P, 16, SEQ])
            v = k.sb(inner, "sgu_v", [P, TILES, SGU_HALF])
            panels(k, [("T", k.xT, gatedT[:, 2 * n:2 * n + 2, :], ACT.Gelu, 1.0) for n in range(8)]
                   + [("N", k.xT, v[:, :, n * COLS:(n + 1) * COLS], ACT.Gelu, 1.0) for n in range(8)])
            mix_tokens(k, v, gatedT, mixedT)
        rows_product(k, mixedT, 8, gains_only(k, gains, 1))
    post_norm(k, gains)


def mix_tokens(k, v, gatedT, mixedT):
    with ExitStack() as ctx, k.stage() as block:
        gb = k.sb(ctx, "sgu_gain_bias", [P, 2, SGU_HALF])
        ws = k.sb(ctx, "sgu_ws", [P, SGU_GROUPS, P])
        wsT = k.sb(ctx, "sgu_ws_T", [P, SGU_GROUPS, P])
        bs = k.sb(ctx, "sgu_bias", [P, SGU_GROUPS, P])
        causal = k.sb(ctx, "sgu_causal", [P, P])
        sq = k.sb(ctx, "sgu_squares", [P, TILES, SGU_HALF])
        stat = k.sb(ctx, "sgu_stats", [P, 5, TILES])
        ws_landed, gb_landed, turned, masked, summed, negated, squared, rooted, recip, scaled, gained, normed, mixed, \
            biased, gated, high, low = (k.sig.new() for _ in range(17))
        a = k.a

        @block.sync
        def _(sp):
            sp.dma_start(ws[:, :, :], a["sgu_w_s_2"][0].rearrange("g t s -> t g s")).then_inc(ws_landed, 16)
            sp.dma_start(causal[:, :], a["constants"][:, C_CAUSAL_T * P:(C_CAUSAL_T + 1) * P]).then_inc(ws_landed, 16)
            sp.dma_start(bs[:, :, :].rearrange("p g t -> p (g t)"),
                         a["sgu_b_s_2"][0].rearrange("g t -> (g t)").partition_broadcast(P)).then_inc(ws_landed, 16)
            sp.dma_start(gb[:, 0, :], a["sgu_ln_g_2"][0].partition_broadcast(P)).then_inc(gb_landed, 16)
            sp.dma_start(gb[:, 1, :], a["sgu_ln_b_2"][0].partition_broadcast(P)).then_inc(gb_landed, 16)
            k.stream(sp)

        @block.tensor
        def _(pe):
            pe.wait_ge(ws_landed, 48)
            for b in range(2):
                for q in range(4):
                    ins = pe.transpose(k.psum[:, b, q * P:(q + 1) * P], ws[:, 4 * b + q, :], k.ident[:, :])
                ins.then_inc(turned, 1)
            pe.wait_ge(masked, 2)
            pe.wait_ge(normed, TILES)
            for g in range(SGU_GROUPS):
                for half in range(2):
                    for i in range(TILES):
                        lo = g * COLS + half * P
                        at = half * SEQ + i * P
                        ins = pe.matmul(k.psum[:, g, at:at + P], v[:, i, lo:lo + P], wsT[:, g, :], start=True, stop=True)
                ins.then_inc(mixed, 1)

        @block.scalar
        def _(act):
            for i in range(TILES):
                act.wait_ge(negated, i + 1)
                act.activation(sq[:, i, :], v[:, i, :], ACT.Square, bias=stat[:, 1, i:i + 1],
                               accum_out=stat[:, 2, i:i + 1]).then_inc(squared, 1)
                act.wait_ge(squared, i + 1)
                act.activation(stat[:, 3, i:i + 1], stat[:, 2, i:i + 1], ACT.Sqrt, bias=k.eps[:, 1:2],
                               scale=1.0 / SGU_HALF).then_inc(rooted, 1)
            for g in range(SGU_GROUPS):
                act.wait_ge(gated, g + 1)
                split_high(act, mixedT.hi[:, 2 * g:2 * g + 2, :], gatedT[:, 2 * g:2 * g + 2, :]).then_inc(high, 1)

        @block.vector
        def _(dve):
            for i in range(TILES):
                dve.tensor_reduce(stat[:, 0, i:i + 1], v[:, i, :], AX_X, ALU.add).then_inc(summed, 1)
                dve.wait_ge(summed, i + 1)
                dve.tensor_scalar(stat[:, 1, i:i + 1], stat[:, 0, i:i + 1], -1.0 / SGU_HALF, None, ALU.mult).then_inc(negated, 1)
            dve.wait_ge(ws_landed, 48)
            for b in range(2):
                dve.wait_ge(turned, b + 1)
                dve.tensor_tensor(wsT[:, 4 * b:4 * b + 4, :], k.psum[:, b, :].rearrange("p (a n) -> p a n", a=4),
                                  over_middle(causal[:, :], 4), ALU.mult).then_inc(masked, 1)
            dve.wait_ge(gb_landed, 32)
            for i in range(TILES):
                dve.wait_ge(rooted, i + 1)
                dve.reciprocal(stat[:, 4, i:i + 1], stat[:, 3, i:i + 1]).then_inc(recip, 1)
                dve.wait_ge(recip, i + 1)
                dve.tensor_scalar(v[:, i, :], v[:, i, :], stat[:, 1, i:i + 1], stat[:, 4, i:i + 1], ALU.add,
                                  ALU.mult).then_inc(scaled, 1)
                dve.wait_ge(scaled, i + 1)
                dve.tensor_tensor(v[:, i, :], v[:, i, :], gb[:, 0, :], ALU.mult).then_inc(gained, 1)
                dve.wait_ge(gained, i + 1)
                dve.tensor_tensor(v[:, i, :], v[:, i, :], gb[:, 1, :], ALU.add).then_inc(normed, 1)
            def low_of(g):
                dve.wait_ge(high, g + 1)
                own = slice(2 * g, 2 * g + 2)
                split_low(dve, mixedT.lo[:, own, :], gatedT[:, own, :], mixedT.hi[:, own, :]).then_inc(low, 1)

            work = sq[:, :, :].rearrange("p i (c n) -> p (i c) n", n=P)
            for g in range(SGU_GROUPS):
                dve.wait_ge(mixed, g + 1)
                part = work[:, 4 * g:4 * g + 4, :]
                dve.tensor_tensor(part, k.psum[:, g, :].rearrange("p (a n) -> p a n", a=4), over_middle(bs[:, g, :], 4),
                                  ALU.add).then_inc(biased, 1)
                dve.wait_ge(biased, g + 1)
                dst = gatedT[:, 2 * g:2 * g + 2, :]
                dve.tensor_tensor(dst, dst, part.rearrange("p (a b) n -> p a (b n)", a=2), ALU.mult).then_inc(gated, 1)
                if g >= 1:
                    low_of(g - 1)
            low_of(SGU_GROUPS - 1)

        k.idle_pool(block)


class SharedKV:

    def __init__(self, k, ctx):
        self.k_sel = k.sb(ctx, "k_sel_T", [P, KVG, SEQ])
        self.k_win = k.sb(ctx, "k_win_T", [P, KVG, SEQ])
        self.v_sel = k.sb(ctx, "v_sel", [P, TILES, KVG * HDIM])
        self.v_win = k.sb(ctx, "v_win", [P, TILES, KVG * HDIM])
        self.k_cmp = k.sb(ctx, "k_cmp_T", [P, KVG, 16])
        self.v_cmp = k.sb(ctx, "v_cmp", [16, KVG, HDIM])
        self.bias = k.sb(ctx, "position_bias", [P, NH, BIAS_W])


def shared_kv(k, s):
    with ExitStack() as ctx:
        raw = [k.sb(ctx, f"kv_T_{n}", [P, 2, SEQ]) for n in range(4)]
        panels(k, [("T", k.xT, raw[0][:, :, :], None, 1.0), ("T", k.xT, raw[1][:, :, :], None, 1.0),
                   ("T", k.xT, raw[2][:, :, :], None, 1.0), ("N", k.xT, s.v_sel[:, :, :], None, 1.0),
                   ("T", k.xT, raw[3][:, :, :], None, 1.0), ("N", k.xT, s.v_win[:, :, :], None, 1.0)])
        compress(k, s, raw)


def compress(k, s, raw):
    J = CMP_LEN // 2
    g0 = k.w.take(4)
    GN = KVG * NCMP
    with ExitStack() as ctx, k.stage() as block:
        two = [k.sb(ctx, f"token_pairs_{n}", [P, KVG, SEQ]) for n in range(2)]
        blocks = [k.sb(ctx, f"cmp_blocks_{n}", [P, J, KVG, NCMP]) for n in range(2)]
        hid = k.sb(ctx, "cmp_hidden", [P, 2, 2, GN])
        pe_rows = k.sb(ctx, "cmp_pe_rows", [2 * J, P])
        pe_cols = k.sb(ctx, "cmp_pe_columns", [P, 2 * J])
        w2 = k.sb(ctx, "cmp_w2", [P, 2, 2, HDIM])
        landed, vs, paired, pe_turned, blocked, gelud, outs, copied = (k.sig.new() for _ in range(8))
        half = [slice(0, HDIM), slice(HDIM, P)]

        @block.sync
        def _(sp):
            sp.dma_start(pe_rows[:, :], k.a["cmp_pe_2"].rearrange("s (j l) d -> (s j) (l d)", l=2)).then_inc(landed, 16)
            sp.dma_start(w2[:, :, :, :], k.a["cmp_w2_2"].rearrange("s (c p) d -> p s c d", p=P)).then_inc(landed, 16)
            k.stream(sp)

        @block.vector
        def _(dve):
            dve.wait_ge(pe_turned, 1)
            dve.tensor_copy(pe_cols[:, :], k.psum[:, 7, 0:2 * J]).then_inc(vs, 1)
            for n in range(2):
                for g in range(KVG):
                    src = raw[n][half[g % 2], g // 2, :]
                    dve.tensor_copy(two[n][half[0], g, :], src).then_inc(paired, 1)
                    dve.tensor_copy(two[n][half[1], g, 0:SEQ - 1], src[:, 1:SEQ]).then_inc(paired, 1)
            dve.wait_ge(paired, 4 * KVG)
            dve.wait_ge(vs, 1)
            for n in range(2):
                for j in range(J):
                    src = two[n][:, :, 2 * j:2 * j + CMP_STRIDE * (NCMP - 1) + 1:CMP_STRIDE]
                    ins = dve.tensor_scalar(blocks[n][:, j, :, :], src, pe_cols[:, J * n + j:J * n + j + 1], None, ALU.add)
                ins.then_inc(blocked, 1)
            for which, dst in ((2, s.k_sel), (3, s.k_win)):
                for g in range(KVG):
                    for h in range(2):
                        dve.tensor_copy(dst[half[h], g, :], raw[which][half[g % 2], g // 2, :]).then_inc(copied, 1)
            dve.wait_ge(outs, 1)
            for h in range(2):
                dve.tensor_copy(s.k_cmp[half[h], :, 0:NCMP], k.psum[half[h], 4, 0:GN].rearrange("p (g n) -> p g n", g=KVG)
                                ).then_inc(copied, 1)
            dve.wait_ge(outs, 2)
            dve.tensor_copy(s.v_cmp[0:NCMP, :, :], k.psum[0:NCMP, 5, 0:KVG * HDIM].rearrange("p (g d) -> p g d", g=KVG)
                            ).then_inc(copied, 1)

        @block.tensor
        def _(pe):
            pe.wait_ge(landed, 32)
            pe.transpose(k.psum[:, 7, 0:2 * J], pe_rows[:, :], k.ident[0:2 * J, 0:2 * J]).then_inc(pe_turned, 1)
            for n in range(2):
                pe.wait_ge(blocked, n + 1)
                for q in range(2):
                    use_slot(pe, k, g0 + 2 * n + q)
                for c in range(2):
                    for j in range(J):
                        w = k.w.panel(g0 + 2 * n + j // DC)
                        ins = pe.matmul(k.psum[:, 2 * n + c, 0:GN], w[:, j % DC, c * P:(c + 1) * P],
                                        blocks[n][:, j, :, :].rearrange("p g n -> p (g n)"), start=(j == 0), stop=(j == J - 1))
                        if c == 1 and j % DC == DC - 1:
                            ins.then_inc(k.w.used[(g0 + 2 * n + j // DC) % RING], 1)
            pe.wait_ge(gelud, 2)
            for h in range(2):
                for c in range(2):
                    ins = pe.matmul(k.psum[half[h], 4, 0:GN], w2[:, 0, c, :], hid[:, 0, c, :], start=(c == 0), stop=(c == 1))
            ins.then_inc(outs, 1)
            pe.wait_ge(gelud, 4)
            for g in range(KVG):
                for c in range(2):
                    ins = pe.matmul(k.psum[0:NCMP, 5, g * HDIM:(g + 1) * HDIM], hid[:, 1, c, g * NCMP:(g + 1) * NCMP],
                                    w2[:, 1, c, :], start=(c == 0), stop=(c == 1))
            ins.then_inc(outs, 1)

        @block.scalar
        def _(act):
            for n in range(2):
                used_slot(act, k, g0 + 2 * n + 1)
                for c in range(2):
                    act.activation(hid[:, n, c, :], k.psum[:, 2 * n + c, 0:GN], ACT.Gelu,
                                   bias=k.cols[:, COL_B1 + 2 * n + c:COL_B1 + 2 * n + c + 1]).then_inc(gelud, 1)

        k.idle_pool(block)


def position_bias(k, s):
    with ExitStack() as ctx, k.stage() as block:
        table = k.sb(ctx, "relative_table", [33, NH])
        onehot = k.sb(ctx, "bucket_onehot", [33, DISTS])
        rows = k.sb(ctx, "bias_by_distance", [NH, DISTS])
        landed, future, made, copied, stored, spread = (k.sig.new() for _ in range(6))

        @block.sync
        def _(sp):
            sp.dma_start(table[0:32, :], k.a["rel_table_2"]).then_inc(landed, 16)
            sp.dma_start(onehot[:, :], k.a["bucket_onehot"]).then_inc(landed, 16)
            k.stream(sp)
            sp.wait_ge(copied, 1)
            copies = k.a["bias_rows"]
            sp.dma_start(copies.rearrange("p h x -> h p x"), rows[:, :].unsqueeze(1).broadcast_to([NH, P, DISTS])
                         ).then_inc(stored, 16)
            sp.wait_ge(stored, 16)
            view = bass.AP(copies.tensor, SEQ // 2 - 1, [[NH * DISTS - 1, P], [DISTS, NH], [1, BIAS_W]])
            sp.dma_start(s.bias[:, :, :], view).then_inc(spread, 16)
            sp.wait_ge(spread, 16)

        @block.vector
        def _(dve):
            dve.memset(table[32:33, :], NEG).then_inc(future, 1)
            dve.wait_ge(made, 1)
            dve.tensor_copy(rows[:, :], k.psum[0:NH, 0, :]).then_inc(copied, 1)

        @block.tensor
        def _(pe):
            pe.wait_ge(landed, 32)
            pe.wait_ge(future, 1)
            pe.matmul(k.psum[0:NH, 0, :], table[:, :], onehot[:, :], start=True, stop=True).then_inc(made, 1)

        k.idle_pool(block)


def sparse_attention(k, s, gains):
    with ExitStack() as ctx:
        qT = k.sb(ctx, "nsa_q_T", [P, DC, SEQ])
        gates = k.sb(ctx, "nsa_gates", [P, TILES, 3 * NH])
        position_bias(k, s)
        view = k.a["nsa_w_qg_2"][0][:, NH * HDIM:NH * HDIM + 3 * NH].rearrange("(c p) n -> p c n", p=P)
        panels(k, [("T", k.xT, qT[:, 2 * n:2 * n + 2, :], None, HDIM ** -0.5) for n in range(4)],
               (view, k.xT, gates[:, :, :], ACT.Sigmoid, 3 * NH))
        attend(k, s, qT, gates)
    rows_product(k, k.xT, 4, gains_only(k, gains, 4))
    post_norm(k, gains)


def attend(k, s, qT, gates):
    E = NH * TILES
    with ExitStack() as ctx, k.stage() as block:
        masks = k.sb(ctx, "cmp_masks", [P, 2, 16])
        sc = [k.sb(ctx, f"scores_{b}", [P, 2, SEQ]) for b in range(2)]
        cs = [k.sb(ctx, f"cmp_scores_{b}", [P, 16]) for b in range(2)]
        pT = [k.sb(ctx, f"probabilities_T_{b}", [P, 4, P]) for b in range(2)]
        cT = [k.sb(ctx, f"cmp_probabilities_T_{b}", [16, P]) for b in range(2)]
        c = [k.sb(ctx, f"softmax_columns_{b}", [P, 3, 4]) for b in range(2)]
        landed, scored, biased, negmax, expd, vs, weighed, turned, copied, outs, high, written = (k.sig.new() for _ in range(12))

        def parts(e):
            h, i = e // 2, e % 2
            p = slice((h % 2) * HDIM, (h % 2 + 1) * HDIM)
            return h, i, h // 4, p

        @block.sync
        def _(sp):
            lo = C_MISC * P + 16
            sp.dma_start(masks[:, :, :], k.a["constants"][:, lo:lo + 32].rearrange("p (i n) -> p i n", i=2)).then_inc(landed, 16)
            k.stream(sp)

        def scores(pe, e):
            h, i, g, p = parts(e)
            if e >= 1:
                pe.wait_ge(biased, 2 * e)
            q = qT[p, h // 2, i * P:(i + 1) * P]
            pe.matmul(k.psum[:, e % 2, 0:SEQ], q, s.k_sel[p, g, :], start=True, stop=True)
            pe.matmul(k.psum[:, e % 2, SEQ:2 * SEQ], q, s.k_win[p, g, :], start=True, stop=True)
            pe.matmul(k.psum[:, 2, 0:NCMP], q, s.k_cmp[p, g, 0:NCMP], start=True, stop=True).then_inc(scored, 1)

        def turn(pe, e):
            pe.wait_ge(weighed, e + 1)
            if e >= 1:
                pe.wait_ge(copied, 2 * e)
            for n in range(4):
                pe.transpose(k.psum[:, 3 + 4 * (e % 2), n * P:(n + 1) * P], sc[e % 2][:, n // 2, (n % 2) * P:(n % 2 + 1) * P], k.ident[:, :])
            pe.transpose(k.psum[0:NCMP, 6, 0:P], cs[e % 2][:, 0:NCMP], k.ident[:, :]).then_inc(turned, 1)

        def mix(pe, e):
            h, i, g, p = parts(e)
            pe.wait_ge(copied, 2 * e + 2)
            j = h // 2
            if j >= 2 and e % 4 == 0:
                pe.wait_ge(written, j - 1)
            o = k.psum[p, 4 + j % 2, i * P:(i + 1) * P]
            d = slice(g * HDIM, (g + 1) * HDIM)
            for n in range(4):
                v = (s.v_sel, s.v_win)[n // 2]
                pe.matmul(o, v[:, n % 2, d], pT[e % 2][:, n, :], start=(n == 0), stop=False)
            pe.matmul(o, s.v_cmp[0:NCMP, g, :], cT[e % 2][0:NCMP, :], start=False, stop=True).then_inc(outs, 1)

        @block.tensor
        def _(pe):
            for e in range(E + 2):
                if e < E:
                    scores(pe, e)
                if 1 <= e <= E:
                    turn(pe, e - 1)
                if e >= 2:
                    mix(pe, e - 2)

        def bias_and_max(dve, e):
            h, i, g, p = parts(e)
            at = P * (TILES - 1 - i)
            dve.wait_ge(scored, e + 1)
            if e >= 2:
                dve.wait_ge(turned, e - 1)
            b = e % 2
            dve.tensor_tensor(sc[b][:, :, :], bank2(k, b), over_middle(s.bias[:, h, at:at + SEQ], 2), ALU.add).then_inc(biased, 1)
            last = at + CMP_LEN - 1 + CMP_STRIDE * (NCMP - 1)
            dve.tensor_tensor(cs[b][:, 0:NCMP], k.psum[:, 2, 0:NCMP], s.bias[:, h, at + CMP_LEN - 1:last + 1:CMP_STRIDE],
                              ALU.add).then_inc(biased, 1)
            dve.wait_ge(biased, 2 * e + 2)
            dve.tensor_reduce(c[b][:, 0, 0:2], sc[b][:, :, :], AX_X, ALU.max, negate=True).then_inc(negmax, 1)
            dve.tensor_reduce(c[b][:, 0, 2:3], cs[b][:, 0:NCMP], AX_X, ALU.max, negate=True).then_inc(negmax, 1)

        def weigh(dve, e):
            h, i, g, p = parts(e)
            b = e % 2
            dve.wait_ge(expd, 3 * e + 3)
            dve.tensor_tensor(cs[b][:, 0:NCMP], cs[b][:, 0:NCMP], masks[:, i, 0:NCMP], ALU.mult).then_inc(vs, 1)
            dve.wait_ge(vs, 5 * e + 1)
            dve.tensor_reduce(c[b][:, 1, 2:3], cs[b][:, 0:NCMP], AX_X, ALU.add).then_inc(vs, 1)
            dve.wait_ge(vs, 5 * e + 2)
            dve.tensor_scalar(c[b][:, 1, 0:3], c[b][:, 1, 0:3], 1e-30, None, ALU.max).then_inc(vs, 1)
            dve.wait_ge(vs, 5 * e + 3)
            dve.reciprocal(c[b][:, 2, 0:3], c[b][:, 1, 0:3]).then_inc(vs, 1)
            dve.wait_ge(vs, 5 * e + 4)
            for dst, src in ((slice(0, 2), slice(1, 3)), (slice(2, 3), slice(0, 1))):
                ins = dve.tensor_tensor(c[b][:, 2, dst], c[b][:, 2, dst], gates[:, i, 3 * h + src.start:3 * h + src.stop], ALU.mult)
            ins.then_inc(vs, 1)
            dve.wait_ge(vs, 5 * e + 5)
            dve.tensor_scalar(cs[b][:, 0:NCMP], cs[b][:, 0:NCMP], c[b][:, 2, 2:3], None, ALU.mult)
            dve.tensor_tensor(sc[b][:, :, :], sc[b][:, :, :], over_last(c[b][:, 2, 0:2], SEQ), ALU.mult).then_inc(weighed, 1)

        @block.vector
        def _(dve):
            def output(j):
                dve.wait_ge(high, j + 1)
                split_low(dve, k.xT.lo[:, j, :], k.psum[:, 4 + j % 2, 0:SEQ], k.xT.hi[:, j, :]).then_inc(written, 1)

            dve.wait_ge(landed, 16)
            for e in range(E + 1):
                if e < E:
                    bias_and_max(dve, e)
                if e >= 1:
                    weigh(dve, e - 1)
                if e >= 6 and e % 4 == 2:
                    output((e - 6) // 4)
            output(NH // 2 - 1)

        @block.scalar
        def _(act):
            def exps(e):
                b = e % 2
                act.wait_ge(negmax, 2 * e + 2)
                for n in range(2):
                    act.activation(sc[b][:, n, :], sc[b][:, n, :], ACT.Exp, bias=c[b][:, 0, n:n + 1],
                                   accum_out=c[b][:, 1, n:n + 1]).then_inc(expd, 1)
                act.activation(cs[b][:, 0:NCMP], cs[b][:, 0:NCMP], ACT.Exp, bias=c[b][:, 0, 2:3]).then_inc(expd, 1)

            def copy(e):
                b = e % 2
                act.wait_ge(turned, e + 1)
                if e >= 2:
                    act.wait_ge(outs, e - 1)
                act.activation(pT[b][:, :, :], k.psum[:, 3 + 4 * b, :].rearrange("p (a n) -> p a n", a=4), ACT.Copy).then_inc(copied, 1)
                act.activation(cT[b][0:NCMP, :], k.psum[0:NCMP, 6, 0:P], ACT.Copy).then_inc(copied, 1)

            def output(j):
                act.wait_ge(outs, 4 * (j + 1))
                split_high(act, k.xT.hi[:, j, :], k.psum[:, 4 + j % 2, 0:SEQ]).then_inc(high, 1)

            for e in range(E + 1):
                if e < E:
                    exps(e)
                if e >= 1:
                    copy(e - 1)
                if e >= 5 and e % 4 == 1:
                    output((e - 5) // 4)
            output(NH // 2 - 1)

        k.idle_pool(block)


def second_block(k):
    with ExitStack() as ctx:
        gains = k.sb(ctx, "norm_gain_bias", [P, 2, D])
        transpose_natural(k, k.x, k.xT)
        swiglu(k, gains, 0)
        spatial_gating(k, gains)
        swiglu(k, gains, 2)
        s = SharedKV(k, ctx)
        shared_kv(k, s)
        swiglu(k, gains, 3)
        sparse_attention(k, s, gains)
        swiglu(k, gains, 5)


def column_panels(w, first=0):
    v = w.rearrange("(c p) n -> p c n", p=P)
    return lambda u: v[:, :, bass.ds(first + COLS * u, COLS)]


def row_slots(w, first=0):
    v = w.rearrange("(u r p) n -> u p r n", r=2, p=P)
    return lambda u: v[u, :, :, first:first + D]


def plan_weights(k):
    a, w = k.a, k.w
    w_in = a["w_in"][0]
    for first, n in ((0, 6), (1536, 2), (2056, 4), (3080, 2), (3592, 2)):
        w.add(n, column_panels(w_in, first))
    w.add(4, row_slots(a["w_out"][0]))
    w.add(4, column_panels(a["xa_wq"][0]))
    w.add(4, column_panels(a["xa_wkv"][0]))
    w.add(4, row_slots(a["xa_wkv"][0], D))
    w.add(4, row_slots(a["xa_wo"][0]))
    w.add(8, column_panels(a["peer_wq"][0]))
    def ffn(layer, which):
        w2 = a["ffn_w2_2"][layer, which].rearrange("(u r p) n -> u p r n", r=2, p=P)
        w1, w3 = (column_panels(a[n][layer, which]) for n in ("ffn_w1_2", "ffn_w3_2"))
        w.add(1, w1)
        w.add(1, w3)
        w.add(FFN_DIM // COLS - 1, lambda u: w1(u + 1), lambda u: w3(u + 1), lambda u: w2[u])
        w.add(1, lambda u: w2[u + FFN_DIM // COLS - 1])
    ffn(0, 0)
    w.add(8, column_panels(a["sgu_w_in_2"][0]))
    w.add(8, column_panels(a["sgu_w_in_2"][0], SGU_HALF))
    w.add(8, row_slots(a["sgu_w_out_2"][0]))
    ffn(0, 1)
    w.add(SLOTS_KV, column_panels(a["kv_w_2"]))
    for n in range(2):
        v = a["cmp_w1_2"][n].rearrange("(u j p) n -> u p j n", j=DC, p=P)
        w.add(2, lambda u, v=v: v[u])
    ffn(1, 0)
    w.add(4, column_panels(a["nsa_w_qg_2"][0]))
    w.add(4, row_slots(a["nsa_w_o_2"][0]))
    ffn(1, 1)



def mixer(k):
    a = k.a
    with ExitStack() as ctx:
        s = MixerState(k, ctx)
        with ExitStack() as inner:
            padded = k.sb(inner, "conv_input_T", [P, 20, 3 + SEQ])
            mixer_load(k, s, padded)
            norm_transpose(k, k.x, k.xT, COL_MIX)
            gates = [a["w_in"][0][:, lo:lo + 8].rearrange("(c p) n -> p c n", p=P) for lo in (2048, 4104)]
            items = []
            for n in range(6):
                items.append(("T", k.xT, padded[:, 2 * n:2 * n + 2, 3:], None, 1.0))
            for n in range(2):
                items.append(("N", k.xT, s.z[:, :, n * COLS:(n + 1) * COLS], None, 1.0))
            for n in range(4):
                items.append(("T", k.xT, padded[:, 12 + 2 * n:14 + 2 * n, 3:], None, 1.0))
            for buf in (s.mv, s.mo):
                for n in range(2):
                    items.append(("N", k.xT, buf[:, :, n * COLS:(n + 1) * COLS], None, 1.0))
            panels(k, items, (gates, k.xT, s.gates[:, :, :], None, 16))
            conv_silu(k, padded, s.conv)
        s.more(k, ctx)
        normalise_and_gate(k, s)
        key_query_products(k, s)
        gdn_prepare(k, s)
        mlstm_prepare(k, s)
        recurrences(k, s)
        with ExitStack() as inner:
            mixed = k.sb(inner, "mixed", [P, TILES, D])
            mixer_output(k, s, mixed)
            transpose_natural(k, mixed, k.xT)
    rows_product(k, k.xT, 4, add_to(k, k.x))


def mixer_load(k, s, padded):
    with k.stage() as block:
        landed, zeroed = k.sig.new(), k.sig.new()

        @block.sync
        def _(sp):
            sp.dma_start(s.consts[:, :, :], k.a["constants"].rearrange("p (c n) -> p c n", n=P)).then_inc(landed, 16)
            k.stream(sp)
            sp.wait_ge(landed, 16)

        @block.vector
        def _(dve):
            dve.memset(padded[:, :, 0:3], 0.0).then_inc(zeroed, 1)

        k.idle_pool(block)


def store_output(k):
    with k.stage() as block:
        stored = k.stored

        @block.sync
        def _(sp):
            sp.dma_start(k.a["out"][0].rearrange("(i p) d -> p i d", p=P), k.x[:, :, :]).then_inc(stored, 16)
            sp.wait_ge(stored, 16)

        k.idle_pool(block)


def build(nc, a):
    with ExitStack() as ctx:
        k = Program(nc, ctx, a)
        plan_weights(k)
        load_parameters(k)
        mixer(k)
        cross_attention(k)
        peer(k)
        second_block(k)
        store_output(k)


_NAMES = ["x", "mem", "norm_mix_w", "w_in", "gdn_conv_w", "gdn_a_log", "gdn_dt_bias", "gdn_norm_w", "mlstm_conv_w",
          "mlstm_i_bias", "mlstm_f_bias", "mlstm_norm_w", "w_out", "norm_xa_w", "norm_mem_w", "xa_wq", "xa_wkv",
          "xa_wo", "norm_ffn_w", "peer_wq", "peer_sub_keys", "peer_u", "peer_v", "norm_final_w", "rel_table_2",
          "ln_g_2", "ln_b_2", "ffn_w1_2", "ffn_w3_2", "ffn_w2_2", "sgu_w_in_2", "sgu_ln_g_2", "sgu_ln_b_2",
          "sgu_w_s_2", "sgu_b_s_2", "sgu_w_out_2", "kv_w_2", "cmp_pe_2", "cmp_w1_2", "cmp_b1_2", "cmp_w2_2",
          "nsa_w_qg_2", "nsa_w_o_2"]


def kernel(**inputs):
    import concourse.bacc as bacc
    from concourse.bass_utils import run_bass_kernel_spmd

    nc = bacc.Bacc("TRN2", target_bir_lowering=False, num_devices=1)
    masks, buckets = constants()
    arrays = {f"in_{n}": np.ascontiguousarray(inputs[n]) for n in _NAMES}
    arrays["in_constants"] = masks
    arrays["in_bucket_onehot"] = buckets
    a = {n[3:]: nc.dram_tensor(n, v.shape, F32, kind="ExternalInput").ap() for n, v in arrays.items()}
    a["out"] = nc.dram_tensor("out_x", (1, SEQ, D), F32, kind="ExternalOutput").ap()
    a["bias_rows"] = nc.dram_tensor("bias_rows", (P, NH, DISTS), F32, kind="Internal").ap()
    build(nc, a)
    r = run_bass_kernel_spmd(nc, [arrays], core_ids=[0])
    return r.results[0]["out_x"]
```

```python
from contextlib import ExitStack, contextmanager

import numpy as np
import concourse.bass as bass
from concourse import mybir

F32 = mybir.dt.float32
U32 = mybir.dt.uint32
F32R = mybir.dt.float32r
ALU = mybir.AluOpType
ACT = mybir.ActivationFunctionType
AX_X = mybir.AxisListType.X

P = 128
D = 1024
SEQ = 256
TILES = SEQ // P
DC = D // P
COLS = 256
SLOT = DC * COLS
RING = 3
BUFFERS = 3
NEG = -1e30
EPS = 1e-6
LN_EPS = 1e-5

HEADS = 4
HD = 128
CHUNK = 64
NCHUNK = SEQ // CHUNK
GW = HEADS * HD
PAIRS = HEADS * TILES

PEER_HEADS = 8
TOPK = 16
KEYS = 128

DN_ALPHA = 4.0 ** 0.25
FFN_DIM = 2816
SGU_HALF = 2048
SGU_GROUPS = 8
NH = 16
KVG = 4
HDIM = 64
CMP_LEN = 32
CMP_STRIDE = 16
NCMP = SEQ // CMP_STRIDE - CMP_LEN // CMP_STRIDE + 1
SLOTS_KV = 6

(C_IDENT, C_ONES, C_NEG_LOW, C_NEG_UP, C_STRICT, C_TRI, C_SAME, C_IOTA, C_CAUSAL_T, C_MISC) = range(10)
C_LEVEL = 10
LEVELS = 6
NCONST = C_LEVEL + LEVELS
DISTS = 2 * SEQ
BIAS_W = 384


def constants():
    c = np.zeros((P, NCONST, P), np.float32)
    i, j = np.arange(P)[:, None], np.arange(P)[None, :]
    same = i // CHUNK == j // CHUNK
    c[:, C_IDENT] = i == j
    c[:, C_ONES] = 1
    c[:, C_NEG_LOW] = np.where(same & (i >= j), 0, NEG)
    c[:, C_NEG_UP] = np.where(same & (i <= j), 0, NEG)
    c[:, C_STRICT] = same & (i > j)
    c[:, C_TRI] = same & (i <= j)
    c[:, C_SAME] = same
    c[:, C_IOTA] = j + 0 * i
    c[:, C_CAUSAL_T] = i <= j
    c[:, C_MISC, 0:2] = (i // CHUNK) == np.arange(2)[None, :]
    for tile in range(TILES):
        ends = np.arange(NCMP)[None, :] * CMP_STRIDE + CMP_LEN - 1
        c[:, C_MISC, 16 + 16 * tile:16 + 16 * tile + NCMP] = (tile * P + i) >= ends
    for k in range(LEVELS):
        b = 1 << k
        c[:, C_LEVEL + k] = (i // (2 * b) == j // (2 * b)) & ((i // b) % 2 == 1) & ((j // b) % 2 == 0)
    onehot = np.zeros((33, DISTS), np.float32)
    for x in range(DISTS):
        dist = SEQ - 1 - x
        if dist < 0:
            onehot[32, x] = 1
        elif dist < 16:
            onehot[dist, x] = 1
        else:
            large = 16 + int(np.float32(np.log(np.float32(dist) / np.float32(16)) / np.float32(np.log(8.0)) * 16))
            onehot[min(large, 31), x] = 1
    return c.reshape(P, NCONST * P), onehot


class Signals:

    def __init__(self, nc, ctx, size):
        self.pools = [[ctx.enter_context(nc.semaphore(f"stage_{'even' if n == 0 else 'odd'}_{m}"))
                       for m in range(size)] for n in range(2)]
        self.stage = 0
        self.taken = 0

    def new(self):
        self.taken += 1
        return self.pools[self.stage % 2][self.taken - 1]

    def next_stage(self):
        self.stage += 1
        self.taken = 0

    def clear_other(self, pool):
        if self.stage > 1:
            other = self.pools[(self.stage + 1) % 2]
            pool.sem_clear(range(other[0].num, other[-1].num + 1))


class Weights:

    def __init__(self, ring, loaded, used):
        self.ring, self.loaded, self.used = ring, loaded, used
        self.segments = []
        self.count = 0
        self.issued = 0
        self.taken = 0
        self.hold = 1 << 30

    def take(self, n):
        self.taken += n
        return self.taken - n

    def add(self, units, *sources):
        seg = (self.count, units, sources)
        self.segments.append(seg)
        self.count += units * len(sources)
        return seg[0]

    def slot(self, g):
        return self.ring[:, g % RING, :]

    def panel(self, g):
        return self.ring[:, g % RING, :].rearrange("p (c n) -> p c n", c=DC)

    def rows(self, g):
        return self.ring[:, g % RING, :].rearrange("p (r n) -> p r n", r=2)

    def _one(self, sp, g, source, unit, turn):
        r = g % RING
        if g >= RING:
            sp.wait_ge(self.used[r], turn)
        src = source(unit)
        dst = self.ring[:, r, :]
        if len(src.shape) == 3:
            dst = dst.rearrange("p (a b) -> p a b", a=src.shape[1])
        sp.dma_start(dst, src).then_inc(self.loaded[r], 16)

    def issue(self, sp, end):
        end = min(end, self.count)
        while self.issued < end:
            g = self.issued
            start, units, sources = [s for s in self.segments if s[0] <= g][-1]
            per = len(sources)
            body = RING // per
            u, k = divmod(g - start, per)
            last = min(start + units * per, end)
            turns = (last - g) // RING
            if k == 0 and per == RING and turns >= 3 and g >= RING:
                with sp.Fori(0, turns) as i:
                    for b in range(body):
                        for kk in range(per):
                            at = g + b * per + kk
                            self._one(sp, at, sources[kk], u + b + body * i, at // RING + i)
                self.issued += turns * RING
            else:
                self._one(sp, g, sources[k], u, g // RING)
                self.issued += 1


class Split:

    def __init__(self, k, ctx, name, shape):
        self.hi = k.sb(ctx, name + "_hi", shape, F32R)
        self.lo = k.sb(ctx, name + "_lo", shape, F32R)

    def at(self, *index):
        return self.hi[index], self.lo[index]


class Splitter:

    def __init__(self, k, ctx, g0):
        self.k, self.g0 = k, g0
        self.parts = k.split_parts
        if self.parts is None:
            self.parts = k.sb(ctx, "split_slots", [P, BUFFERS, 2, SLOT], F32R)
        self.begun = 1 if k.begun == g0 else 0
        self.high_done = k.sig.new()
        self.eaten = k.sig.new()

    def high(self, act, n, i=0, per=0):
        if n < self.begun:
            return
        g, b = self.g0 + n, n % BUFFERS
        act.wait_ge(self.k.w.loaded[g % RING], 16 * (g // RING + per // RING * i + 1))
        if n >= BUFFERS:
            act.wait_ge(self.eaten, n - BUFFERS + 1 + per * i)
        for half in range(2):
            p = slice(half * SLOT // 2, (half + 1) * SLOT // 2)
            act.activation(self.parts[:, b, 0, p], self.k.w.slot(g)[:, p], ACT.Copy).then_inc(self.high_done, 1)

    def low(self, dve, n, i=0, per=0):
        if n < self.begun:
            return
        g, b = self.g0 + n, n % BUFFERS
        for half in range(2):
            p = slice(half * SLOT // 2, (half + 1) * SLOT // 2)
            dve.wait_ge(self.high_done, 2 * (n - self.begun) + half + 1 + 2 * per * i)
            ins = dve.tensor_tensor(self.parts[:, b, 1, p], self.k.w.slot(g)[:, p], self.parts[:, b, 0, p].bitcast(F32),
                                    ALU.subtract)
        ins.then_inc(self.k.w.used[g % RING], 1)

    def ready(self, pe, n, i=0, per=0):
        g = self.g0 + n
        pe.wait_ge(self.k.w.used[g % RING], g // RING + per // RING * i + 1)

    def panel(self, n):
        return [self.parts[:, n % BUFFERS, q, :].rearrange("p (c n) -> p c n", c=DC) for q in range(2)]

    def rows(self, n):
        return [self.parts[:, n % BUFFERS, q, :].rearrange("p (r n) -> p r n", r=2) for q in range(2)]

    def finished(self, engine, n, i=0, per=0):
        engine.wait_ge(self.eaten, n + 1 + per * i)


class Beginning:

    def __init__(self, k):
        self.k, self.g = k, k.w.taken
        k.begun = self.g
        self.high_done = k.sig.new()

    def highs(self, act):
        for half in range(2):
            self.high(act, half)

    def lows(self, dve):
        for half in range(2):
            self.low(dve, half)

    def high(self, act, half):
        k, p = self.k, slice(half * SLOT // 2, (half + 1) * SLOT // 2)
        act.wait_ge(k.w.loaded[self.g % RING], 16 * (self.g // RING + 1))
        act.activation(k.split_parts[:, 0, 0, p], k.w.slot(self.g)[:, p], ACT.Copy).then_inc(self.high_done, 1)

    def low(self, dve, half):
        k, p = self.k, slice(half * SLOT // 2, (half + 1) * SLOT // 2)
        dve.wait_ge(self.high_done, half + 1)
        ins = dve.tensor_tensor(k.split_parts[:, 0, 1, p], k.w.slot(self.g)[:, p], k.split_parts[:, 0, 0, p].bitcast(F32),
                                ALU.subtract)
        if half == 1:
            ins.then_inc(k.w.used[self.g % RING], 1)


def passes(pe, out, left, right, start, stop):
    (lh, ll), (rh, rl) = left, right
    pe.matmul(out, lh, rh, start=start, stop=False)
    pe.matmul(out, lh, rl, start=False, stop=False)
    return pe.matmul(out, ll, rh, start=False, stop=stop)


def split_high(act, dst, src, scale=1.0):
    return act.activation(dst, src, ACT.Copy, scale=scale)


def split_low(dve, dst, src, hi, scale=1.0):
    return dve.scalar_tensor_tensor(dst, src, scale, hi.bitcast(F32), ALU.mult, ALU.subtract)


class Program:

    def __init__(self, nc, ctx, a):
        self.nc, self.ctx, self.a = nc, ctx, a
        self.names = {}
        self.split_parts = None
        self.begun = None
        self.sig = Signals(nc, ctx, 36)
        ring = self.sb(ctx, "ring", [P, RING, SLOT])
        loaded = [ctx.enter_context(nc.semaphore(f"slot_loaded_{r}")) for r in range(RING)]
        used = [ctx.enter_context(nc.semaphore(f"slot_used_{r}")) for r in range(RING)]
        self.w = Weights(ring, loaded, used)
        self.x = self.sb(ctx, "x_natural", [P, TILES, D])
        self.xT = Split(self, ctx, "x_transposed", [P, DC, SEQ])
        self.ident = self.sb(ctx, "ident", [P, P])
        self.ones = self.sb(ctx, "ones", [P, P])
        self.cols = self.sb(ctx, "parameter_columns", [P, 120])
        self.eps = self.sb(ctx, "epsilons", [P, 2])
        self.stored = ctx.enter_context(nc.semaphore("output_stored"))
        self.expert_landed = [ctx.enter_context(nc.semaphore(f"expert_rows_landed_{n}")) for n in range(6)]
        self.bias_stored = ctx.enter_context(nc.semaphore("bias_rows_stored"))
        self.bias_spread = ctx.enter_context(nc.semaphore("bias_spread"))
        self.masks_landed = ctx.enter_context(nc.semaphore("masks_landed"))
        self.boot = ctx.enter_context(nc.semaphore("booted"))
        self.psum = ctx.enter_context(nc.psum_tensor("banks", [P, 8, 512], F32))

    def sb(self, ctx, name, shape, dt=F32):
        self.names[name] = self.names.get(name, 0) + 1
        if self.names[name] > 1:
            name = f"{name}_{self.names[name]}"
        return ctx.enter_context(self.nc.sbuf_tensor(name, shape, dt))

    @contextmanager
    def lasting_splits(self):
        with ExitStack() as ctx:
            self.split_parts = self.sb(ctx, "split_slots", [P, BUFFERS, 2, SLOT], F32R)
            yield
            self.split_parts = None

    @contextmanager
    def stage(self):
        self.sig.next_stage()
        with self.nc.Block() as block:
            yield block

    def stream(self, sp):
        self.w.issue(sp, min(self.w.taken + RING, self.w.hold))

    def idle_pool(self, block):
        @block.gpsimd
        def _(pool):
            self.sig.clear_other(pool)


def use_slot(pe, k, g, turn=None):
    pe.wait_ge(k.w.loaded[g % RING], 16 * ((g // RING if turn is None else turn) + 1))


def used_slot(engine, k, g, turn=None):
    engine.wait_ge(k.w.used[g % RING], (g // RING if turn is None else turn) + 1)


def linker(engine, step):
    count = [0]

    def link(ins):
        count[0] += 1
        ins.then_inc(step, 1)
        engine.wait_ge(step, count[0])
    return link


def over_last(ap, n):
    return ap.unsqueeze(2).broadcast_to([ap.shape[0], ap.shape[1], n])


def over_middle(ap, n):
    return ap.unsqueeze(1).broadcast_to([ap.shape[0], n, ap.shape[1]])



def load_parameters(k):
    a = k.a
    rows = [(a["norm_mix_w"][0], DC), (a["norm_xa_w"][0], DC), (a["norm_mem_w"][0], DC), (a["norm_ffn_w"][0], DC)]
    at = 0
    with ExitStack() as ctx, k.stage() as block:
        raw = k.sb(ctx, "parameter_rows", [P, P])
        landed, rows_landed, turned = (k.sig.new() for _ in range(3))

        @block.sync
        def _(sp):
            consts = a["constants"].rearrange("p (c n) -> p c n", n=P)
            sp.dma_start(k.ident[:, :], consts[:, C_IDENT, :]).then_inc(landed, 16)
            sp.dma_start(k.ones[:, :], consts[:, C_ONES, :]).then_inc(landed, 16)
            sp.dma_start(k.x[:, :, :], a["x"][0].rearrange("(i p) d -> p i d", p=P)).then_inc(landed, 16)
            sp.wait_ge(rows_landed, 16 * (len(rows) + 9))
            k.w.issue(sp, RING)

        @block.scalar
        def _(act):
            n = 0
            for v, chunks in rows:
                act.dma_start(raw[n:n + chunks, :], v.rearrange("(c p) -> c p", p=P)).then_inc(rows_landed, 16)
                n += chunks
            g = a["gdn_conv_w"][0].rearrange("k (c p) -> k c p", p=P)
            m = a["mlstm_conv_w"][0].rearrange("k (c p) -> k c p", p=P)
            for tap in range(4):
                act.dma_start(raw[n:n + 12, :], g[tap]).then_inc(rows_landed, 16)
                act.dma_start(raw[n + 12:n + 20, :], m[tap]).then_inc(rows_landed, 16)
                n += 20
            act.dma_start(raw[n:n + 4, :], a["cmp_b1_2"].rearrange("s (c p) -> (s c) p", p=P)).then_inc(rows_landed, 16)

        @block.tensor
        def _(pe):
            pe.wait_ge(landed, 48)
            pe.wait_ge(rows_landed, 16 * (len(rows) + 9))
            pe.transpose(k.psum[:, 0, 0:116], raw[0:116, :], k.ident[0:116, 0:116]).then_inc(turned, 1)

        @block.vector
        def _(dve):
            dve.memset(k.eps[:, 0:1], EPS).then_inc(k.boot, 1)
            dve.memset(k.eps[:, 1:2], LN_EPS).then_inc(k.boot, 1)
            dve.wait_ge(turned, 1)
            dve.tensor_copy(k.cols[:, 0:116], k.psum[:, 0, 0:116]).then_inc(k.boot, 1)

        @block.gpsimd
        def _(pool):
            k.sig.clear_other(pool)


COL_MIX, COL_XA, COL_MEM, COL_FFN, COL_CONV, COL_B1 = 0, 8, 16, 24, 32, 112


def turn_chunks(pe, k, src, tile, ready, first=0, normed=None):
    for c in range(DC):
        if normed is not None and c % 4 == 0:
            pe.wait_ge(normed, 2 * tile + c // 4 + 1)
        ins = pe.transpose(k.psum[:, first + 2 * tile + c // 4, c % 4 * P:(c % 4 + 1) * P], src[:, c * P:(c + 1) * P],
                           k.ident[:, :])
        if c % 4 == 3:
            ins.then_inc(ready, 1)


def norm_transpose(k, jobs, loads=()):
    with ExitStack() as ctx, k.stage() as block:
        N = len(jobs)
        xn = [k.sb(ctx, f"normed_{n}", [P, TILES, D]) for n in range(N)]
        stat = k.sb(ctx, "row_stats", [P, 3, TILES * N])
        warm = k.sb(ctx, "unused_root", [P, 1])
        turned = [k.sb(ctx, f"normed_T_{n}", [P, 4, 4, P]) for n in range(N)]
        landed, squares, rooted, recip, normed, banks, weighted, high, written = (k.sig.new() for _ in range(9))
        begin = Beginning(k)

        @block.sync
        def _(sp):
            for dst, src in loads:
                sp.dma_start(dst, src).then_inc(landed, 16)
            k.stream(sp)

        @block.scalar
        def _(act):
            act.activation(warm[:, :], k.eps[:, 0:1], ACT.Sqrt)
            for e in range(TILES * N):
                n, i = divmod(e, TILES)
                if i == 0 and n >= N - len(loads):
                    act.wait_ge(landed, 16 * (n - N + len(loads) + 1))
                act.activation(xn[n][:, i, :], jobs[n][0][:, i, :], ACT.Square, accum_out=stat[:, 0, e:e + 1]).then_inc(squares, 1)
                act.wait_ge(squares, e + 1)
                act.activation(stat[:, 1, e:e + 1], stat[:, 0, e:e + 1], ACT.Sqrt, bias=k.eps[:, 0:1], scale=1.0 / D
                               ).then_inc(rooted, 1)
            begin.highs(act)
            for b in range(4 * N):
                act.wait_ge(weighted, b + 1)
                split_high(act, jobs[b // 4][1].hi[bank_part(b % 4)], turned[b // 4][:, b % 4, :, :]).then_inc(high, 1)

        @block.vector
        def _(dve):
            def low(b):
                dst = jobs[b // 4][1]
                dve.wait_ge(high, b + 1)
                split_low(dve, dst.lo[bank_part(b % 4)], turned[b // 4][:, b % 4, :, :], dst.hi[bank_part(b % 4)]
                          ).then_inc(written, 1)

            for e in range(TILES * N):
                n, i = divmod(e, TILES)
                dve.wait_ge(rooted, e + 1)
                dve.reciprocal(stat[:, 2, e:e + 1], stat[:, 1, e:e + 1]).then_inc(recip, 1)
                dve.wait_ge(recip, e + 1)
                dve.tensor_scalar(xn[n][:, i, :], jobs[n][0][:, i, :], stat[:, 2, e:e + 1], None, ALU.mult).then_inc(normed, 1)
            begin.lows(dve)
            for b in range(4 * N):
                col = jobs[b // 4][2] + 4 * (b % 2)
                dve.wait_ge(banks, b + 1)
                dve.tensor_tensor(turned[b // 4][:, b % 4, :, :], bank4(k, b), over_last(k.cols[:, col:col + 4], P), ALU.mult
                                  ).then_inc(weighted, 1)
                if b >= 1:
                    low(b - 1)
            low(4 * N - 1)

        @block.tensor
        def _(pe):
            for e in range(TILES * N):
                n, i = divmod(e, TILES)
                pe.wait_ge(normed, e + 1)
                turn_chunks(pe, k, xn[n][:, i, :], i, banks, 4 * n)

        k.idle_pool(block)


def bank4(k, b):
    return k.psum[:, b, :].rearrange("p (a n) -> p a n", a=4)


def bank_part(b):
    return slice(0, P), slice(4 * (b % 2), 4 * (b % 2) + 4), slice(b // 2 * P, (b // 2 + 1) * P)


def split_turned(k, first, dst, banks, high, written):
    def highs(act):
        for b in range(4):
            act.wait_ge(banks, b + 1)
            split_high(act, dst.hi[bank_part(b)], bank4(k, first + b)).then_inc(high, 1)

    def lows(dve):
        for b in range(4):
            dve.wait_ge(high, b + 1)
            split_low(dve, dst.lo[bank_part(b)], bank4(k, first + b), dst.hi[bank_part(b)]).then_inc(written, 1)
    return highs, lows


def split_banks(k, first, dst, banks, high, written):
    def highs(act):
        for b in range(4):
            act.wait_ge(banks, b + 1)
            split_high(act, dst.hi[:, 2 * b:2 * b + 2, :], bank2(k, first + b)).then_inc(high, 1)

    def lows(dve):
        for b in range(4):
            dve.wait_ge(high, b + 1)
            split_low(dve, dst.lo[:, 2 * b:2 * b + 2, :], bank2(k, first + b), dst.hi[:, 2 * b:2 * b + 2, :]
                      ).then_inc(written, 1)
    return highs, lows


def bank2(k, b):
    return k.psum[:, b, :].rearrange("p (a n) -> p a n", a=2)


def panels(k, items, small=None, along=None):
    g0 = k.w.take(len(items))
    by_act = [m for m, it in enumerate(items) if it[3] is not None or m % 2 == 1]
    by_dve = [m for m in range(len(items)) if m not in by_act]
    with ExitStack() as ctx, k.stage() as block:
        split = Splitter(k, ctx, g0)
        act_read, dve_read, narrow_landed, narrow_high, narrow_low, narrow_done = (k.sig.new() for _ in range(6))
        if along:
            along.begin()
        if small:
            view, small_x, small_dest, small_func, width = small
            narrow = k.sb(ctx, "narrow_panel", [P, DC, width])
            narrows = Split(k, ctx, "narrow_split", [P, DC, width])
            views = view if isinstance(view, list) else [view]

        @block.sync
        def _(sp):
            if along:
                along.load(sp)
            k.stream(sp)

        @block.tensor
        def _(pe):
            for m, (form, xT, dest, func, scale) in enumerate(items):
                if m >= 6:
                    if m - 6 in by_act:
                        pe.wait_ge(act_read, by_act.index(m - 6) + 1)
                    else:
                        pe.wait_ge(dve_read, by_dve.index(m - 6) + 1)
                split.ready(pe, m)
                wh, wl = split.panel(m)
                for j in range(2):
                    own = slice(j * P, (j + 1) * P)
                    for c in range(DC):
                        if form == "T":
                            left, right = (wh[:, c, own], wl[:, c, own]), xT.at(slice(0, P), c)
                        else:
                            left, right = xT.at(slice(0, P), c, own), (wh[:, c, :], wl[:, c, :])
                        ins = passes(pe, k.psum[:, m % 6, j * SEQ:(j + 1) * SEQ], left, right, c == 0, c == DC - 1)
                ins.then_inc(split.eaten, 1)
            if small:
                pe.wait_ge(narrow_low, 1)
                for i in range(TILES):
                    for c in range(DC):
                        ins = passes(pe, k.psum[:, 6, i * width:(i + 1) * width],
                                     small_x.at(slice(0, P), c, slice(i * P, (i + 1) * P)), narrows.at(slice(0, P), c),
                                     c == 0, c == DC - 1)
                ins.then_inc(narrow_done, 1)

        @block.scalar
        def _(act):
            if small:
                at = 0
                for v in views:
                    act.dma_start(narrow[:, :, at:at + v.shape[2]], v).then_inc(narrow_landed, 16)
                    at += v.shape[2]
            for m in range(min(BUFFERS, len(items))):
                split.high(act, m)
            if small:
                act.wait_ge(narrow_landed, 16 * len(views))
                split_high(act, narrows.hi[:, :, :], narrow[:, :, :]).then_inc(narrow_high, 1)
            for m in range(len(items)):
                if m + BUFFERS < len(items):
                    split.high(act, m + BUFFERS)
                if m in by_act:
                    func, scale = items[m][3], items[m][4]
                    split.finished(act, m)
                    act.activation(items[m][2], bank2(k, m % 6), func or ACT.Copy, scale=scale).then_inc(act_read, 1)
                if along:
                    along.act(act, m)
            if along:
                for m in range(len(items), len(items) + 4):
                    along.act(act, m)
            if small:
                act.wait_ge(narrow_done, 1)
                act.activation(small_dest, k.psum[:, 6, 0:TILES * width].rearrange("p (i n) -> p i n", i=TILES),
                               small_func or ACT.Copy).then_inc(act_read, 1)

        @block.vector
        def _(dve):
            def result(m):
                if m in by_act:
                    dve.wait_ge(act_read, by_act.index(m) + 1)
                else:
                    dve.wait_ge(dve_read, by_dve.index(m) + 1)

            for m in range(min(BUFFERS, len(items))):
                split.low(dve, m)
            if small:
                dve.wait_ge(narrow_high, 1)
                split_low(dve, narrows.lo[:, :, :], narrow[:, :, :], narrows.hi[:, :, :]).then_inc(narrow_low, 1)
            for m in range(len(items)):
                if m + BUFFERS < len(items):
                    split.low(dve, m + BUFFERS)
                if m in by_dve:
                    split.finished(dve, m)
                    dve.tensor_scalar(items[m][2], bank2(k, m % 6), items[m][4], None, ALU.mult).then_inc(dve_read, 1)
                if along:
                    along.dve(dve, m, result)
            if along:
                for m in range(len(items), len(items) + 4):
                    along.dve(dve, m, result)

        k.idle_pool(block)


def rows_product(k, aT, slots, finish, load=None):
    g0 = k.w.take(slots)
    with ExitStack() as ctx, k.stage() as block:
        split = Splitter(k, ctx, g0)
        loaded = k.sig.new()

        @block.sync
        def _(sp):
            if load:
                load_gains(k, sp, load[0], loaded, load[1])
            k.stream(sp)
            if load:
                sp.wait_ge(loaded, 32)

        @block.tensor
        def _(pe):
            for m in range(slots):
                split.ready(pe, m)
                wh, wl = split.rows(m)
                for r in range(2):
                    ins = down(pe, k, aT.at(slice(0, P), 2 * m + r), (wh[:, r, :], wl[:, r, :]), m == 0 and r == 0,
                               m == slots - 1 and r == 1)
                ins.then_inc(split.eaten, 1)

        take_act, take_dve = finish(ctx, block, lambda engine: split.finished(engine, slots - 1))

        @block.scalar
        def _(act):
            for m in range(slots):
                split.high(act, m)
            take_act(act)

        @block.vector
        def _(dve):
            for m in range(slots):
                split.low(dve, m)
            take_dve(dve)

        k.idle_pool(block)


def down(pe, k, aT, w, start, stop):
    for i in range(TILES):
        own = slice(i * P, (i + 1) * P)
        for half in range(2):
            cols = slice(half * 512, (half + 1) * 512)
            ins = passes(pe, k.psum[:, 2 * i + half, :], (aT[0][:, own], aT[1][:, own]), (w[0][:, cols], w[1][:, cols]),
                         start, stop)
    return ins


def accumulated(k, i):
    return k.psum[:, 2 * i:2 * i + 2, :].rearrange("p b n -> p (b n)")


def add_to(k, dst):
    def finish(ctx, block, done):
        added = k.sig.new()

        def take(dve):
            done(dve)
            for i in range(TILES):
                dve.tensor_tensor(dst[:, i, :], accumulated(k, i), dst[:, i, :], ALU.add).then_inc(added, 1)
        return (lambda act: None), take
    return finish


def left_in_banks(ctx, block, done):
    return (lambda act: None), (lambda dve: None)


def copy_to(k, dst):
    def finish(ctx, block, done):
        copied = k.sig.new()

        def take_dve(dve):
            done(dve)
            dve.tensor_copy(dst[:, 0, :], accumulated(k, 0)).then_inc(copied, 1)

        def take_act(act):
            done(act)
            act.activation(dst[:, 1, :], accumulated(k, 1), ACT.Copy).then_inc(copied, 1)
        return take_act, take_dve
    return finish



class Convolution:

    def __init__(self, k, padded, out, items):
        self.k, self.padded, self.out, self.items = k, padded, out, items

    def begin(self):
        self.step, self.shaped = self.k.sig.new(), self.k.sig.new()

    def load(self, sp):
        pass

    def dve(self, dve, m, result):
        item = m - 2
        if item not in self.items:
            return
        result(item)
        k, pair = self.k, self.items.index(item)
        for tap in range(4):
            for q in range(2):
                n = 2 * pair + q
                w = k.cols[:, COL_CONV + 20 * tap + n:COL_CONV + 20 * tap + n + 1]
                src, dst = self.padded[:, n, tap:tap + SEQ], self.out[:, n, :]
                if tap == 0:
                    ins = dve.tensor_scalar(dst, src, w, None, ALU.mult)
                else:
                    dve.wait_ge(self.step, 8 * pair + 2 * (tap - 1) + q + 1)
                    ins = dve.scalar_tensor_tensor(dst, src, w, dst, ALU.mult, ALU.add)
                ins.then_inc(self.step, 1)

    def act(self, act, m):
        item = m - 4
        if item not in self.items:
            return
        pair = self.items.index(item)
        part = self.out[:, 2 * pair:2 * pair + 2, :]
        act.wait_ge(self.step, 8 * (pair + 1))
        act.activation(part, part, ACT.Silu).then_inc(self.shaped, 1)


def normalise_and_gate(k, s):
    with ExitStack() as ctx, k.stage() as block:
        sq = k.sb(ctx, "qk_squares", [P, 8, SEQ])
        root = k.sb(ctx, "qk_norms", [P, 8, SEQ])
        row = k.sb(ctx, "gate_parameters", [P, 4, HEADS])
        g = k.sb(ctx, "gate_work", [P, 6, TILES, 8])
        lh = k.sb(ctx, "log_by_half", [P, 2, 16])
        squared, sums, rooted, vstep, scaled, gates_landed, expd, logs, cums, turned, copied, gstep = \
            (k.sig.new() for _ in range(12))
        qk = s.conv[:, 0:8, :]

        @block.sync
        def _(sp):
            for n, name in enumerate(("gdn_dt_bias", "gdn_a_log", "mlstm_i_bias", "mlstm_f_bias")):
                sp.dma_start(row[:, n, :], k.a[name].partition_broadcast(P).rearrange("p a h -> p (a h)")
                             ).then_inc(gates_landed, 16)
            k.stream(sp)

        @block.gpsimd
        def _(pool):
            k.sig.clear_other(pool)
            pool.tensor_tensor(sq[:, 0:4, :], s.conv[:, 0:4, :], s.conv[:, 0:4, :], ALU.mult).then_inc(squared, 1)
            pool.tensor_scalar(s.conv[:, 16:20, :], s.conv[:, 16:20, :], HD ** -0.5, None, ALU.mult).then_inc(scaled, 1)

        @block.scalar
        def _(act):
            act.activation(sq[:, 4:8, :], s.conv[:, 4:8, :], ACT.Square).then_inc(squared, 1)
            for b in range(4):
                act.wait_ge(sums, b + 1)
                act.activation(root[:, 2 * b:2 * b + 2, :], bank2(k, b), ACT.Sqrt, bias=k.eps[:, 0:1]).then_inc(rooted, 1)
            act.wait_ge(gstep, 3)
            act.activation(g[:, 2, :, :], g[:, 1, :, :], ACT.Exp, scale=-1.0).then_inc(expd, 1)
            act.activation(row[:, 1, :], row[:, 1, :], ACT.Exp).then_inc(expd, 1)
            act.wait_ge(expd, 2)
            act.activation(g[:, 3, :, :], g[:, 2, :, :], ACT.Ln, bias=1.0).then_inc(logs, 1)
            act.activation(s.beta[:, :, :], s.gates[:, :, 4:8], ACT.Sigmoid).then_inc(logs, 1)
            for n in (1, 3, 5):
                act.wait_ge(turned, n + 1)
                b = [4, 5, 6, 7, 0, 1][n]
                act.activation(s.natural[:, 4 * n:4 * n + 4, :], k.psum[:, b, :].rearrange("p (a n) -> p a n", a=4),
                               ACT.Copy).then_inc(copied, 1)

        @block.tensor
        def _(pe):
            for b in range(4):
                pe.wait_ge(squared, 2)
                pe.matmul(k.psum[:, b, :], k.ones[:, :], sq[:, 2 * b:2 * b + 2, :], start=True, stop=True).then_inc(sums, 1)
            pe.wait_ge(vstep, 8)
            pe.wait_ge(scaled, 1)
            for n in range(6):
                b = [4, 5, 6, 7, 0, 1][n]
                for q in range(4):
                    e = 4 * n + q
                    kind, head, tile = e // 8, (e % 8) // 2, e % 2
                    src = s.conv[:, (4, 8, 16)[kind] + head, tile * P:(tile + 1) * P]
                    ins = pe.transpose(k.psum[:, b, q * P:(q + 1) * P], src, k.ident[:, :])
                ins.then_inc(turned, 1)
            pe.wait_ge(k.masks_landed, 16)
            pe.wait_ge(gstep, 9)
            pe.matmul(k.psum[:, 2, 0:16], s.mask(C_TRI), s.logs[:, :, :, :].rearrange("p i t h -> p (i t h)"), start=True, stop=True)
            pe.matmul(k.psum[:, 2, 16:32], s.mask(C_SAME), s.logs[:, :, :, :].rearrange("p i t h -> p (i t h)"), start=True, stop=True)
            pe.matmul(k.psum[:, 2, 32:64], k.ones[:, :], lh[:, :, :].rearrange("p f n -> p (f n)"), start=True, stop=True).then_inc(cums, 1)

        @block.vector
        def _(dve):
            dve.wait_ge(gates_landed, 64)
            dve.tensor_tensor(g[:, 0, :, 0:4], s.gates[:, :, 0:4], over_middle(row[:, 0, :], TILES), ALU.add).then_inc(gstep, 1)
            dve.scalar_tensor_tensor(g[:, 0, :, 4:8], s.gates[:, :, 12:16], -1.0, over_middle(row[:, 3, :], TILES),
                                     ALU.mult, ALU.subtract).then_inc(gstep, 1)
            dve.wait_ge(gstep, 2)
            dve.scalar_tensor_tensor(g[:, 1, :, :], g[:, 0, :, :], -1.0, g[:, 0, :, :], ALU.mult, ALU.max).then_inc(gstep, 1)
            dve.tensor_tensor(s.log_i[:, :, :], s.gates[:, :, 8:12], over_middle(row[:, 2, :], TILES), ALU.add).then_inc(gstep, 1)
            dve.tensor_scalar(g[:, 4, :, :], g[:, 0, :, :], 0.0, None, ALU.max).then_inc(gstep, 1)
            for b in range(4):
                dve.wait_ge(rooted, b + 1)
                dve.reciprocal(root[:, 2 * b:2 * b + 2, :], root[:, 2 * b:2 * b + 2, :]).then_inc(vstep, 1)
                dve.wait_ge(vstep, 2 * b + 1)
                part = s.conv[:, 2 * b:2 * b + 2, :]
                dve.scalar_tensor_tensor(part, part, HD ** -0.5 if b < 2 else 1.0, root[:, 2 * b:2 * b + 2, :],
                                         ALU.mult, ALU.mult).then_inc(vstep, 1)
            dve.wait_ge(logs, 1)
            dve.wait_ge(gstep, 5)
            dve.tensor_tensor(g[:, 5, :, :], g[:, 4, :, :], g[:, 3, :, :], ALU.add).then_inc(gstep, 1)
            dve.wait_ge(gstep, 6)
            dve.scalar_tensor_tensor(s.logs[:, :, 0, :], g[:, 5, :, 0:4], -1.0, over_middle(row[:, 1, :], TILES),
                                     ALU.mult, ALU.mult).then_inc(gstep, 1)
            dve.tensor_scalar(s.logs[:, :, 1, :], g[:, 5, :, 4:8], -1.0, None, ALU.mult).then_inc(gstep, 1)
            dve.wait_ge(gstep, 8)
            dve.wait_ge(k.masks_landed, 16)
            dve.tensor_tensor(lh[:, :, :], over_middle(s.logs[:, :, :, :].rearrange("p i t h -> p (i t h)"), 2),
                              over_last(s.consts[:, C_MISC, 0:2], 16), ALU.mult).then_inc(gstep, 1)
            for n in (0, 2, 4):
                dve.wait_ge(turned, n + 1)
                b = [4, 5, 6, 7, 0, 1][n]
                dve.tensor_copy(s.natural[:, 4 * n:4 * n + 4, :],
                                k.psum[:, b, :].rearrange("p (a n) -> p a n", a=4)).then_inc(copied, 1)
            dve.wait_ge(cums, 1)
            for kind in range(2):
                for what in range(2):
                    src = k.psum[:, 2, 16 * what:16 * what + 16].rearrange("p (i t h) -> p t h i", i=TILES, t=2)
                    dve.tensor_copy(s.run[:, kind, what, :].rearrange("p (h i) -> p h i", h=HEADS),
                                    src[:, kind, :, :]).then_inc(copied, 1)
                for half in range(2):
                    src = k.psum[:, 2, 32 + 16 * half:48 + 16 * half].rearrange("p (i t h) -> p t h i", i=TILES, t=2)
                    dst = s.total[:, kind, :].rearrange("p (h i f) -> p h i f", h=HEADS, f=2)
                    dve.tensor_copy(dst[:, :, :, half], src[:, kind, :, :]).then_inc(copied, 1)


def gdn_prepare(k, s):
    gc = s.run[:, 0, 0, :]
    with ExitStack() as ctx, k.stage() as block:
        def mats(name):
            return k.sb(ctx, name, [P, PAIRS, P])
        diag, low, up, rowexp, A, Y, W, X = (mats(n) for n in
            ("gc_diagonal", "decay_low", "decay_up", "row_exp", "A", "AtW", "inv_T", "inv"))
        B = [mats(f"A_level_{b}") for b in range(2)]
        vb, kbg = mats("v_beta"), mats("k_beta_exp")
        col = k.sb(ctx, "gdn_columns", [P, 4, PAIRS])
        vs, ps, acts, pools, picked, multiplied, squared, Ys, updated = (k.sig.new() for _ in range(9))
        kn, vn = s.natural[:, 0:8, :], s.natural[:, 8:16, :]

        def both(n):
            return k.psum[:, 2 * n:2 * n + 2, :].rearrange("p b (a n) -> p (b a) n", n=P)

        def part(n, f):
            return k.psum[:, 2 * n + f, :].rearrange("p (a n) -> p a n", n=P)

        def half(f):
            return slice(f * PAIRS // 2, (f + 1) * PAIRS // 2)

        def square(n, e):
            return k.psum[:, 2 * n + e // 4, (e % 4) * P:(e % 4 + 1) * P]

        @block.sync
        def _(sp):
            k.stream(sp)

        @block.vector
        def _(dve):
            link = linker(dve, vs)
            link(dve.tensor_tensor(diag[:, :, :], over_middle(k.ident[:, :], PAIRS), over_last(gc, P), ALU.mult))
            link(dve.tensor_copy(col[:, 0, :].rearrange("p (h i) -> p h i", h=HEADS),
                                 s.beta[:, :, :].rearrange("p i h -> p h i")))
            link(dve.tensor_tensor(col[:, 3, :], s.run[:, 0, 1, :], gc, ALU.subtract))
            dve.wait_ge(ps, 1)
            link(dve.tensor_tensor(up[:, :, :], both(0), over_last(gc, P), ALU.subtract))
            link(dve.scalar_tensor_tensor(low[:, :, :], up[:, :, :], -1.0, over_middle(s.mask(C_NEG_LOW), PAIRS),
                                          ALU.mult, ALU.add))
            link(dve.tensor_tensor(up[:, :, :], up[:, :, :], over_middle(s.mask(C_NEG_UP), PAIRS), ALU.add))
            dve.wait_ge(acts, 1)
            link(dve.tensor_tensor(col[:, 1, :], col[:, 1, :], col[:, 0, :], ALU.mult))
            dve.wait_ge(ps, 2)
            dve.wait_ge(acts, 3)
            link(dve.tensor_tensor(A[:, :, :], both(1), low[:, :, :], ALU.mult))
            link(dve.tensor_tensor(A[:, :, :], A[:, :, :], over_last(col[:, 0, :], P), ALU.mult))
            link(dve.tensor_tensor(A[:, :, :], A[:, :, :], over_middle(s.mask(C_STRICT), PAIRS), ALU.mult))
            def pick(n):
                f = half(n % 2)
                if n >= 4:
                    dve.wait_ge(picked, n - 3)
                    dve.wait_ge(updated, 2 * (n - 3))
                dve.tensor_tensor(B[n // 2 % 2][:, f, :], A[:, f, :], over_middle(s.mask(C_LEVEL + n // 2), PAIRS // 2),
                                  ALU.mult).then_inc(picked, 1)
            pick(0)
            pick(1)
            for n in range(2 * LEVELS):
                f = half(n % 2)
                if n + 2 < 2 * LEVELS:
                    pick(n + 2)
                dve.wait_ge(squared, n + 1)
                if n < 2:
                    dve.tensor_tensor(W[:, f, :], over_middle(k.ident[:, :], PAIRS // 2), part(2, n), ALU.subtract
                                      ).then_inc(updated, 1)
                    dve.wait_ge(picked, n + 1)
                    dve.tensor_tensor(X[:, f, :], over_middle(k.ident[:, :], PAIRS // 2), B[0][:, f, :], ALU.subtract
                                      ).then_inc(updated, 1)
                else:
                    dve.wait_ge(updated, 2 * (n - 1))
                    dve.tensor_tensor(W[:, f, :], W[:, f, :], part(2, n % 2), ALU.subtract).then_inc(updated, 1)
                    if n < 2 * (LEVELS - 1):
                        dve.tensor_tensor(X[:, f, :], X[:, f, :], part(3, n % 2), ALU.subtract).then_inc(updated, 1)

        @block.scalar
        def _(act):
            act.activation(col[:, 1, :], gc, ACT.Exp).then_inc(acts, 1)
            act.wait_ge(vs, 3)
            act.activation(col[:, 2, :], col[:, 3, :], ACT.Exp).then_inc(acts, 1)
            act.wait_ge(vs, 5)
            act.activation(low[:, :, :], low[:, :, :], ACT.Exp).then_inc(acts, 1)
            act.wait_ge(vs, 6)
            act.activation(up[:, :, :], up[:, :, :], ACT.Exp).then_inc(acts, 1)
            act.activation(rowexp[:, :, :], both(0), ACT.Exp).then_inc(acts, 1)
            act.activation(s.glast[:, 0, :], s.total[:, 0, :], ACT.Exp).then_inc(acts, 1)
            for n in range(2, 2 * LEVELS):
                act.wait_ge(multiplied, n - 1)
                act.activation(Y[:, half(n % 2), :], part(1, n % 2), ACT.Copy).then_inc(Ys, 1)
            act.wait_ge(ps, 3)
            act.activation(s.u[:, :, :], both(0), ACT.Copy).then_inc(acts, 1)
            act.activation(s.wT[:, :, :], both(1), ACT.Copy).then_inc(acts, 1)

        @block.gpsimd
        def _(pool):
            k.sig.clear_other(pool)
            pool.wait_ge(vs, 2)
            pool.tensor_tensor(vb[:, :, :], vn, over_last(col[:, 0, :], P), ALU.mult).then_inc(pools, 1)
            pool.wait_ge(vs, 7)
            pool.tensor_tensor(kbg[:, :, :], kn, over_last(col[:, 1, :], P), ALU.mult).then_inc(pools, 1)
            pool.wait_ge(acts, 5)
            pool.tensor_tensor(s.kd[:, :, :], kn, over_last(col[:, 2, :], P), ALU.mult).then_inc(pools, 1)
            pool.tensor_tensor(s.qdT[:, :, :], s.conv[:, 0:4, :].rearrange("p h (i n) -> p (h i) n", n=P),
                               rowexp[:, :, :], ALU.mult).then_inc(pools, 1)
            pool.tensor_tensor(s.qkT[:, :, :], s.qk_raw[:, :, :], up[:, :, :], ALU.mult).then_inc(pools, 1)

        @block.tensor
        def _(pe):
            pe.wait_ge(vs, 1)
            for n in range(2):
                ins = pe.matmul(k.psum[:, n, :], k.ones[:, :], diag[:, 4 * n:4 * n + 4, :], start=True, stop=True)
            ins.then_inc(ps, 1)
            for e in range(PAIRS):
                kt = s.conv[:, 4 + e // 2, (e % 2) * P:(e % 2 + 1) * P]
                ins = pe.matmul(square(1, e), kt, kt, start=True, stop=True)
            ins.then_inc(ps, 1)
            def pairs(n):
                return range(n % 2 * PAIRS // 2, (n % 2 + 1) * PAIRS // 2)

            for n in range(2):
                pe.wait_ge(picked, n + 1)
                for e in pairs(n):
                    ins = pe.transpose(square(2, e), B[0][:, e, :], k.ident[:, :])
                ins.then_inc(squared, 1)
            for level in range(1, LEVELS):
                steps = (2 * level, 2 * level + 1)
                for n in steps:
                    pe.wait_ge(picked, n + 1)
                    pe.wait_ge(updated, 2 * (n - 1))
                    for e in pairs(n):
                        ins = pe.matmul(square(1, e), B[level % 2][:, e, :], W[:, e, :], start=True, stop=True)
                    ins.then_inc(multiplied, 1)
                for n in steps:
                    pe.wait_ge(Ys, n - 1)
                    for e in pairs(n):
                        ins = pe.matmul(square(2, e), X[:, e, :], Y[:, e, :], start=True, stop=True)
                        if level < LEVELS - 1:
                            ins = pe.matmul(square(3, e), Y[:, e, :], X[:, e, :], start=True, stop=True)
                    ins.then_inc(squared, 1)
            pe.wait_ge(updated, 4 * LEVELS - 2)
            pe.wait_ge(pools, 2)
            pe.wait_ge(acts, 6)
            for e in range(PAIRS):
                pe.matmul(square(0, e), W[:, e, :], vb[:, e, :], start=True, stop=True)
                ins = pe.matmul(square(1, e), kbg[:, e, :], W[:, e, :], start=True, stop=True)
            ins.then_inc(ps, 1)


def key_query_products(k, s):
    with k.stage() as block:
        ps, copied = k.sig.new(), k.sig.new()

        @block.sync
        def _(sp):
            k.stream(sp)

        @block.tensor
        def _(pe):
            for kind, (q0, k0) in enumerate(((0, 4), (12, 16))):
                for e in range(PAIRS):
                    t = slice((e % 2) * P, (e % 2 + 1) * P)
                    ins = pe.matmul(k.psum[:, 2 * kind + e // 4, (e % 4) * P:(e % 4 + 1) * P],
                                    s.conv[:, k0 + e // 2, t], s.conv[:, q0 + e // 2, t], start=True, stop=True)
                ins.then_inc(ps, 1)

        @block.vector
        def _(dve):
            dve.wait_ge(ps, 1)
            dve.tensor_copy(s.qk_raw[:, :, :], k.psum[:, 0:2, :].rearrange("p b (a n) -> p (b a) n", n=P)).then_inc(copied, 1)

        @block.scalar
        def _(act):
            act.wait_ge(ps, 2)
            act.activation(s.mqk_raw[:, :, :], k.psum[:, 2:4, :].rearrange("p b (a n) -> p (b a) n", n=P),
                           ACT.Copy).then_inc(copied, 1)

        k.idle_pool(block)


def mlstm_prepare(k, s):
    b, bl_own = s.run[:, 1, 0, :], s.run[:, 1, 1, :]
    bl_all = s.total[:, 1, :]
    with ExitStack() as ctx, k.stage() as block:
        def mats(name):
            return k.sb(ctx, name, [P, PAIRS, P])
        diag, work = mats("row_diagonal"), mats("row_work")
        c = k.sb(ctx, "mlstm_columns", [P, 16, PAIRS])
        amax = k.sb(ctx, "chunk_maxima", [P, HEADS, NCHUNK])
        m = k.sb(ctx, "running_maxima", [P, HEADS, NCHUNK + 1])
        tmp = k.sb(ctx, "decay_argument", [P, HEADS, NCHUNK])
        vs, ps, acts, pools = (k.sig.new() for _ in range(4))
        A_, MAXD, MPREV, MNEXT, INTER, MT, SCARG, WARG, R, WGT = range(10)

        def both(n):
            return k.psum[:, 2 * n:2 * n + 2, :].rearrange("p b (a n) -> p (b a) n", n=P)

        @block.sync
        def _(sp):
            k.stream(sp)

        @block.vector
        def _(dve):
            link = linker(dve, vs)
            link(dve.tensor_tensor(c[:, A_, :].rearrange("p (h i) -> p h i", h=HEADS),
                                   s.log_i[:, :, :].rearrange("p i h -> p h i"),
                                   b.rearrange("p (h i) -> p h i", h=HEADS), ALU.subtract))
            link(dve.tensor_tensor(diag[:, :, :], over_middle(k.ident[:, :], PAIRS), over_last(c[:, A_, :], P), ALU.mult))
            link(dve.memset(m[:, :, :], 0.0))
            dve.wait_ge(ps, 1)
            link(dve.tensor_reduce(amax[:, :, :].rearrange("p h n -> p (h n)"),
                                   both(0).rearrange("p e (f n) -> p (e f) n", f=2), AX_X, ALU.max))
            link(dve.tensor_tensor(work[:, :, :], both(0), over_middle(s.mask(C_NEG_LOW), PAIRS), ALU.add))
            link(dve.tensor_reduce(c[:, MAXD, :], work[:, :, :], AX_X, ALU.max))
            link(dve.tensor_tensor(c[:, MAXD, :], c[:, MAXD, :], b, ALU.add))
            total = bl_all.rearrange("p (h n) -> p h n", h=HEADS)
            for n in range(NCHUNK):
                link(dve.tensor_tensor(m[:, :, n + 1], m[:, :, n], amax[:, :, n], ALU.max))
                link(dve.tensor_tensor(m[:, :, n + 1], m[:, :, n + 1], total[:, :, n], ALU.add))
            for half in range(2):
                p = slice(half * CHUNK, (half + 1) * CHUNK)
                for what, off in ((MPREV, 0), (MNEXT, 1)):
                    src = m[p, :, off + half:off + half + 3:2]
                    link(dve.tensor_copy(c[p, what, :].rearrange("p (h i) -> p h i", h=HEADS), src))
            link(dve.tensor_tensor(c[:, INTER, :], b, c[:, MPREV, :], ALU.add))
            link(dve.tensor_tensor(c[:, MT, :], c[:, INTER, :], c[:, MAXD, :], ALU.max))
            link(dve.tensor_tensor(c[:, SCARG, :], c[:, INTER, :], c[:, MT, :], ALU.subtract))
            link(dve.tensor_tensor(c[:, WARG, :], c[:, A_, :], bl_own, ALU.add))
            link(dve.tensor_tensor(c[:, WARG, :], c[:, WARG, :], c[:, MNEXT, :], ALU.subtract))
            link(dve.tensor_tensor(tmp[:, :, :], total, m[:, :, 0:NCHUNK], ALU.add))
            link(dve.tensor_tensor(tmp[:, :, :], tmp[:, :, :], m[:, :, 1:NCHUNK + 1], ALU.subtract))
            link(dve.tensor_tensor(c[:, R, :], b, c[:, MT, :], ALU.subtract))
            link(dve.tensor_tensor(diag[:, :, :], over_middle(k.ident[:, :], PAIRS), over_last(c[:, R, :], P), ALU.mult))
            dve.wait_ge(ps, 2)
            link(dve.tensor_tensor(work[:, :, :], both(1), over_middle(s.mask(C_NEG_UP), PAIRS), ALU.add))
            link(dve.tensor_tensor(work[:, :, :], work[:, :, :], over_last(c[:, A_, :], P), ALU.add))
            dve.wait_ge(acts, 4)
            link(dve.tensor_tensor(diag[:, :, :], over_middle(k.ident[:, :], PAIRS), over_last(c[:, SCARG, :], P), ALU.mult))
            dve.wait_ge(ps, 3)
            link(dve.tensor_tensor(s.mqdT[:, :, :], s.conv[:, 12:16, :].rearrange("p h (i n) -> p (h i) n", n=P),
                                   both(2), ALU.mult))
            dve.wait_ge(acts, 5)
            link(dve.tensor_tensor(s.mqkT[:, :, :], s.mqk_raw[:, :, :], work[:, :, :], ALU.mult))

        @block.scalar
        def _(act):
            act.wait_ge(vs, 26)
            act.activation(s.emt[:, :], c[:, MT, :], ACT.Exp, scale=-1.0).then_inc(acts, 1)
            act.activation(c[:, SCARG, :], c[:, SCARG, :], ACT.Exp).then_inc(acts, 1)
            act.activation(c[:, WGT, :], c[:, WARG, :], ACT.Exp).then_inc(acts, 1)
            act.activation(s.glast[:, 1, :].rearrange("p (h n) -> p h n", h=HEADS), tmp[:, :, :], ACT.Exp).then_inc(acts, 1)
            act.wait_ge(vs, 30)
            act.activation(work[:, :, :], work[:, :, :], ACT.Exp).then_inc(acts, 1)

        @block.gpsimd
        def _(pool):
            k.sig.clear_other(pool)
            pool.memset(s.v1[:, :, :, HD:HD + 1], 1.0).then_inc(pools, 1)
            pool.tensor_copy(s.v1[:, :, :, 0:HD], s.mv[:, :, :].rearrange("p i (h d) -> p i h d", h=HEADS)).then_inc(pools, 1)
            pool.wait_ge(acts, 3)
            pool.tensor_tensor(s.kw[:, :, :], s.natural[:, 16:24, :], over_last(c[:, WGT, :], P), ALU.mult).then_inc(pools, 1)

        @block.tensor
        def _(pe):
            for n, at in enumerate((2, 28, 31)):
                pe.wait_ge(vs, at)
                for q in range(2):
                    ins = pe.matmul(k.psum[:, 2 * n + q, :], k.ones[:, :], diag[:, 4 * q:4 * q + 4, :], start=True, stop=True)
                ins.then_inc(ps, 1)


def recurrences(k, s):
    V1 = HD + 1
    with ExitStack() as ctx, k.stage() as block:
        S = k.sb(ctx, "gdn_state", [P, HEADS, HD])
        C = k.sb(ctx, "mlstm_state", [P, HEADS, V1])
        vnew = k.sb(ctx, "v_new", [P, HEADS, HD])
        den = k.sb(ctx, "denominator", [P, 2, HEADS])
        gain = k.sb(ctx, "head_gains", [P, HD + GW])
        landed, gated, gained = (k.sig.new() for _ in range(3))
        ws, outs, dstate, mouts, mdstate, vns, gds, mds, rd, mrd = (k.sig.new() for _ in range(10))
        gl = s.glast[:, 0, :].rearrange("p (h n) -> p h n", h=HEADS)
        dec = s.glast[:, 1, :].rearrange("p (h n) -> p h n", h=HEADS)

        def quad(b, p=slice(0, P)):
            return k.psum[p, b, :].rearrange("p (h d) -> p h d", h=HEADS)

        def two(b, p=slice(0, P)):
            return k.psum[p, b:b + 2, 0:2 * V1].rearrange("p b (h d) -> p b h d", h=2)

        def by_bank(ap):
            return ap.rearrange("p (b h) d -> p b h d", b=2)

        @block.sync
        def _(sp):
            sp.dma_start(gain[:, 0:HD], k.a["gdn_norm_w"].partition_broadcast(P).rearrange("p a d -> p (a d)")).then_inc(landed, 16)
            sp.dma_start(gain[:, HD:], k.a["mlstm_norm_w"].partition_broadcast(P).rearrange("p a d -> p (a d)")).then_inc(landed, 16)
            k.stream(sp)

        @block.tensor
        def _(pe):
            for n in range(NCHUNK):
                tile, half = n // 2, n % 2
                p = slice(half * CHUNK, (half + 1) * CHUNK)
                if n > 0:
                    pe.wait_ge(gds, 2 * n + 1)
                    for h in range(HEADS):
                        ins = pe.matmul(k.psum[p, 0, h * HD:(h + 1) * HD], s.wT[:, 2 * h + tile, p], S[:, h, :],
                                        start=True, stop=True)
                    ins.then_inc(ws, 1)
                    pe.wait_ge(mds, 2 * n + 1)
                    pe.wait_ge(mrd, n)
                for h in range(HEADS):
                    o = k.psum[p, 3 + h // 2, (h % 2) * V1:(h % 2 + 1) * V1]
                    if n > 0:
                        pe.matmul(o, s.mqdT[:, 2 * h + tile, p], C[:, h, :], start=True, stop=False)
                    ins = pe.matmul(o, s.mqkT[p, 2 * h + tile, p], s.v1[p, tile, h, :], start=(n == 0), stop=True)
                ins.then_inc(mouts, 1)
                for h in range(HEADS):
                    ins = pe.matmul(k.psum[:, 5 + h // 2, (h % 2) * V1:(h % 2 + 1) * V1], s.kw[p, 2 * h + tile, :],
                                    s.v1[p, tile, h, :], start=True, stop=True)
                ins.then_inc(mdstate, 1)
                pe.wait_ge(vns, n + 1)
                for h in range(HEADS):
                    ins = pe.matmul(k.psum[:, 2, h * HD:(h + 1) * HD], s.kd[p, 2 * h + tile, :], vnew[p, h, :],
                                    start=True, stop=True)
                ins.then_inc(dstate, 1)
                if n > 0:
                    pe.wait_ge(rd, n)
                for h in range(HEADS):
                    o = k.psum[p, 1, h * HD:(h + 1) * HD]
                    if n > 0:
                        pe.matmul(o, s.qdT[:, 2 * h + tile, p], S[:, h, :], start=True, stop=False)
                    ins = pe.matmul(o, s.qkT[p, 2 * h + tile, p], vnew[p, h, :], start=(n == 0), stop=True)
                ins.then_inc(outs, 1)

        @block.vector
        def _(dve):
            dve.memset(S[:, :, :], 0.0).then_inc(gds, 1)
            dve.memset(C[:, :, :], 0.0).then_inc(mds, 1)
            for n in range(NCHUNK):
                tile, half = n // 2, n % 2
                p = slice(half * CHUNK, (half + 1) * CHUNK)
                u = s.u[p, :, :].rearrange("p (h i) d -> p h i d", i=TILES)[:, :, tile, :]
                if n == 0:
                    dve.tensor_copy(vnew[p, :, :], u).then_inc(vns, 1)
                else:
                    dve.wait_ge(ws, n)
                    dve.tensor_tensor(vnew[p, :, :], u, quad(0, p), ALU.subtract).then_inc(vns, 1)
                if n == NCHUNK - 1:
                    continue
                dve.wait_ge(mds, 2 * n + 1)
                dve.wait_ge(mouts, n + 1)
                dve.tensor_tensor(C[:, :, :], C[:, :, :], over_last(dec[:, :, n], V1), ALU.mult).then_inc(mds, 1)
                dve.wait_ge(mds, 2 * n + 2)
                dve.wait_ge(mdstate, n + 1)
                dve.tensor_tensor(by_bank(C[:, :, :]), by_bank(C[:, :, :]), two(5), ALU.add).then_inc(mds, 1)
                dve.wait_ge(outs, n + 1)
                dve.wait_ge(gds, 2 * n + 1)
                dve.tensor_tensor(S[:, :, :], S[:, :, :], over_last(gl[:, :, n], HD), ALU.mult).then_inc(gds, 1)
                dve.wait_ge(gds, 2 * n + 2)
                dve.wait_ge(dstate, n + 1)
                dve.tensor_tensor(S[:, :, :], S[:, :, :], quad(2), ALU.add).then_inc(gds, 1)

        @block.scalar
        def _(act):
            act.activation(s.z[:, :, :], s.z[:, :, :], ACT.Silu).then_inc(gated, 1)
            act.activation(s.mo[:, :, :], s.mo[:, :, :], ACT.Sigmoid).then_inc(gated, 1)
            for n in range(NCHUNK):
                tile, half = n // 2, n % 2
                p = slice(half * CHUNK, (half + 1) * CHUNK)
                act.wait_ge(mouts, n + 1)
                act.activation(by_bank(s.mh[p, tile, :, :]), two(3, p), ACT.Copy).then_inc(mrd, 1)
                act.wait_ge(outs, n + 1)
                act.activation(s.go[p, tile, :, :], quad(1, p), ACT.Copy).then_inc(rd, 1)

        @block.gpsimd
        def _(pool):
            k.sig.clear_other(pool)
            pool.wait_ge(landed, 32)
            pool.wait_ge(gated, 2)
            z = s.z[:, :, :].rearrange("p i (h d) -> p (i h) d", h=HEADS)
            pool.tensor_tensor(z, z, over_middle(gain[:, 0:HD], PAIRS), ALU.mult).then_inc(gained, 1)
            pool.tensor_tensor(s.mo[:, :, :], s.mo[:, :, :], over_middle(gain[:, HD:], TILES), ALU.mult).then_inc(gained, 1)


def mixer_output(k, s, mixed, dst):
    with ExitStack() as ctx, k.stage() as block:
        sq = k.sb(ctx, "output_squares", [P, 2 * PAIRS, HD])
        c = k.sb(ctx, "output_columns", [P, 4, 2 * PAIRS])
        vs, acts, normed, banks, high, written = (k.sig.new() for _ in range(6))
        highs, lows = split_turned(k, 0, dst, banks, high, written)
        begin = Beginning(k)

        def heads(ap):
            return ap.rearrange("p i (h d) -> p i h d", h=HEADS)

        def per_head(col):
            return over_last(col, HD).rearrange("p (i h) d -> p i h d", h=HEADS)
        go, mo = mixed[:, :, 0:GW], mixed[:, :, GW:2 * GW]
        src_m = s.mh[:, :, :, 0:HD]
        sq_g, sq_m = (sq[:, 8 * n:8 * n + 8, :].rearrange("p (i h) d -> p i h d", h=HEADS) for n in range(2))

        @block.sync
        def _(sp):
            k.stream(sp)

        @block.scalar
        def _(act):
            act.activation(sq_g, s.go[:, :, :, :], ACT.Square).then_inc(acts, 1)
            begin.high(act, 0)
            act.wait_ge(vs, 4)
            act.activation(sq_m, heads(mo), ACT.Square).then_inc(acts, 1)
            act.wait_ge(vs, 6)
            act.activation(c[:, 2, :], c[:, 1, :], ACT.Sqrt, bias=k.eps[:, 0:1], scale=1.0 / HD).then_inc(acts, 1)
            begin.high(act, 1)
            highs(act)

        @block.vector
        def _(dve):
            link = linker(dve, vs)
            d = c[:, 0, 0:8].rearrange("p (i h) -> p i h", h=HEADS)
            link(dve.scalar_tensor_tensor(d, s.mh[:, :, :, HD], -1.0, s.mh[:, :, :, HD], ALU.mult, ALU.max))
            link(dve.tensor_tensor(d, d, s.emt[:, :].rearrange("p (h i) -> p i h", h=HEADS), ALU.max))
            link(dve.reciprocal(c[:, 0, 0:8], c[:, 0, 0:8]))
            link(dve.tensor_tensor(heads(mo), src_m, per_head(c[:, 0, 0:8]), ALU.mult))
            dve.wait_ge(acts, 1)
            link(dve.tensor_reduce(c[:, 1, 0:8], sq[:, 0:8, :], AX_X, ALU.add))
            begin.low(dve, 0)
            dve.wait_ge(acts, 2)
            link(dve.tensor_reduce(c[:, 1, 8:16], sq[:, 8:16, :], AX_X, ALU.add))
            dve.wait_ge(acts, 3)
            link(dve.reciprocal(c[:, 3, :], c[:, 2, :]))
            for i in range(TILES):
                for n, (src, out, gate) in enumerate(((s.go, go, s.z), (heads(mo), mo, s.mo))):
                    own = heads(out)[:, i, :, :]
                    scale = over_last(c[:, 3, 8 * n + 4 * i:8 * n + 4 * i + 4], HD)
                    link(dve.tensor_tensor(own, src[:, i, :, :], scale, ALU.mult))
                    dve.tensor_tensor(out[:, i, :], out[:, i, :], gate[:, i, :], ALU.mult).then_inc(normed, 1)
            begin.low(dve, 1)
            lows(dve)

        @block.tensor
        def _(pe):
            for i in range(TILES):
                turn_chunks(pe, k, mixed[:, i, :], i, banks, 0, normed)

        k.idle_pool(block)


class MixerState:

    def __init__(self, k, ctx):
        def sb(name, shape):
            return k.sb(ctx, name, shape)
        self.consts = sb("constants_sb", [P, NCONST, P])
        self.conv = sb("convolved_T", [P, 20, SEQ])
        self.z = sb("gdn_z", [P, TILES, GW])
        self.mv = sb("mlstm_v", [P, TILES, GW])
        self.mo = sb("mlstm_o", [P, TILES, GW])
        self.gates = sb("gates", [P, TILES, 16])
        self.beta = sb("beta", [P, TILES, HEADS])
        self.log_i = sb("log_i", [P, TILES, HEADS])
        self.logs = sb("log_alpha_f", [P, TILES, 2, HEADS])
        self.run = sb("running_logs", [P, 2, 2, PAIRS])
        self.total = sb("chunk_totals", [P, 2, HEADS * NCHUNK])
        self.glast = sb("chunk_decays", [P, 2, HEADS * NCHUNK])
        self.emt = sb("exp_minus_m", [P, PAIRS])

    def more(self, k, ctx):
        def mats(name):
            return k.sb(ctx, name, [P, PAIRS, P])
        self.natural = k.sb(ctx, "natural_k_v_mk", [P, 3 * PAIRS, P])
        self.qk_raw, self.mqk_raw = mats("key_query"), mats("mlstm_key_query")
        self.u, self.wT, self.qdT, self.kd = mats("u"), mats("w_T"), mats("q_decayed_T"), mats("k_decayed")
        self.qkT = self.qk_raw
        self.mqkT = self.mqk_raw
        self.mqdT = self.conv[:, 12:16, :].rearrange("p h (i n) -> p (h i) n", n=P)
        self.kw = self.natural[:, 16:24, :]
        self.v1 = k.sb(ctx, "mlstm_v_and_one", [P, TILES, HEADS, HD + 1])
        self.go = k.sb(ctx, "gdn_out", [P, TILES, HEADS, HD])
        self.mh = k.sb(ctx, "mlstm_out", [P, TILES, HEADS, HD + 1])

    def mask(self, n):
        return self.consts[:, n, :]



def cross_attention(k):
    a = k.a
    with ExitStack() as ctx:
        qT = k.sb(ctx, "xa_q_T", [P, DC, SEQ])
        kT = k.sb(ctx, "xa_k_T", [P, DC, SEQ])
        v = k.sb(ctx, "xa_v", [P, TILES, D])
        ctx.enter_context(k.lasting_splits())
        with ExitStack() as inner:
            mem = k.sb(inner, "memory", [P, TILES, D])
            memT = Split(k, inner, "memory_T", [P, DC, SEQ])
            norm_transpose(k, [(k.x, k.xT, COL_XA), (mem, memT, COL_MEM)],
                           [(mem[:, :, :], a["mem"][0].rearrange("(i p) d -> p i d", p=P))])
            panels(k, [("T", k.xT, qT[:, 2 * n:2 * n + 2, :], None, 1.0) for n in range(4)]
                   + [("T", memT, kT[:, 2 * n:2 * n + 2, :], None, 1.0) for n in range(4)])
            rows_product(k, memT, 4, copy_to(k, v))
        attend_memory(k, qT, kT, v)
        rows_product(k, k.xT, 4, add_to(k, k.x))


def attend_memory(k, qT, kT, v):
    DH = D // HEADS
    scale = DH ** -0.5
    with ExitStack() as ctx, k.stage() as block:
        prob = k.sb(ctx, "xa_probabilities", [P, PAIRS, SEQ])
        probT = k.sb(ctx, "xa_probabilities_T", [P, HEADS, 2, SEQ])
        c = k.sb(ctx, "xa_columns", [P, 4, PAIRS])
        scored, maxed, negated, expd, recip, scaled, turned, copied, mixed, high, written = (k.sig.new() for _ in range(11))

        highs, lows = split_banks(k, 0, k.xT, mixed, high, written)
        begin = Beginning(k)

        @block.sync
        def _(sp):
            k.stream(sp)

        @block.tensor
        def _(pe):
            for e in range(PAIRS):
                h, i = e // 2, e % 2
                for half in range(2):
                    ins = pe.matmul(k.psum[:, h, i * SEQ:(i + 1) * SEQ], qT[:, 2 * h + half, i * P:(i + 1) * P],
                                    kT[:, 2 * h + half, :], start=(half == 0), stop=(half == 1))
                if i == 1:
                    ins.then_inc(scored, 1)
            for h in range(HEADS):
                pe.wait_ge(scaled, h + 1)
                for i in range(TILES):
                    for m in range(2):
                        at = m * SEQ + i * P
                        ins = pe.transpose(k.psum[:, 4 + h, at:at + P], prob[:, 2 * h + i, m * P:(m + 1) * P], k.ident[:, :])
                ins.then_inc(turned, 1)
            for h in range(HEADS):
                pe.wait_ge(copied, h + 1)
                for half in range(2):
                    for m in range(2):
                        lo = h * DH + half * P
                        ins = pe.matmul(k.psum[:, h, half * SEQ:(half + 1) * SEQ], v[:, m, lo:lo + P],
                                        probT[:, h, m, :], start=(m == 0), stop=(m == 1))
                ins.then_inc(mixed, 1)

        @block.vector
        def _(dve):
            for h in range(HEADS):
                dve.wait_ge(scored, h + 1)
                dve.tensor_reduce(c[:, 0, 2 * h:2 * h + 2], bank2(k, h), AX_X, ALU.max).then_inc(maxed, 1)
                dve.wait_ge(maxed, h + 1)
                dve.tensor_scalar(c[:, 1, 2 * h:2 * h + 2], c[:, 0, 2 * h:2 * h + 2], -scale, None, ALU.mult).then_inc(negated, 1)
            for h in range(HEADS):
                dve.wait_ge(expd, 2 * (h + 1))
                dve.reciprocal(c[:, 3, 2 * h:2 * h + 2], c[:, 2, 2 * h:2 * h + 2]).then_inc(recip, 1)
                dve.wait_ge(recip, h + 1)
                part = prob[:, 2 * h:2 * h + 2, :]
                dve.tensor_tensor(part, part, over_last(c[:, 3, 2 * h:2 * h + 2], SEQ), ALU.mult).then_inc(scaled, 1)
            begin.lows(dve)
            lows(dve)

        @block.scalar
        def _(act):
            begin.highs(act)
            for e in range(PAIRS):
                h, i = e // 2, e % 2
                act.wait_ge(negated, h + 1)
                act.activation(prob[:, e, :], k.psum[:, h, i * SEQ:(i + 1) * SEQ], ACT.Exp, bias=c[:, 1, e:e + 1],
                               scale=scale, accum_out=c[:, 2, e:e + 1]).then_inc(expd, 1)
            for h in range(HEADS):
                act.wait_ge(turned, h + 1)
                act.activation(probT[:, h, :, :], bank2(k, 4 + h), ACT.Copy).then_inc(copied, 1)
            highs(act)

        k.idle_pool(block)



HALVES = 2 * PEER_HEADS
PICKS = PEER_HEADS * TOPK
LOW = -3.0e38


def peer(k):
    a = k.a
    picksT = k.w.ring[:, RING - 1, 0:3 * SEQ].rearrange("p (n t) -> p n t", n=3)
    iota = k.w.ring[:, RING - 1, 3 * SEQ:3 * SEQ + P]
    with k.lasting_splits():
        norm_transpose(k, [(k.x, k.xT, COL_FFN)])
        k.w.hold = k.w.taken + PEER_HEADS
        pick_experts(k, picksT, iota)
    with ExitStack() as ctx:
        loads = ExpertLoads(k)
        gates = k.sb(ctx, "gate_matrix", [P, SEQ, KEYS])
        scatter_gates(k, picksT, iota, gates, loads)
        every_expert(k, gates, loads)
    k.w.hold = 1 << 30


def pick_experts(k, picksT, iota):
    g0 = k.w.take(PEER_HEADS)
    with ExitStack() as ctx, k.stage() as block:
        split = Splitter(k, ctx, g0)
        qT = k.sb(ctx, "peer_q_T", [P, HALVES, SEQ])
        keys = k.sb(ctx, "sub_keys", [P, HALVES, KEYS])
        keysT = k.sb(ctx, "sub_keys_T", [P, HALVES, KEYS])
        numbers = k.sb(ctx, "key_numbers", [P, KEYS])
        score = [k.sb(ctx, f"key_scores_{b}", [P, 4, KEYS]) for b in range(2)]
        rest = k.sb(ctx, "scores_without_top", [P, 4, KEYS])
        top = k.sb(ctx, "top_scores", [P, PEER_HEADS, 4, TOPK])
        topi = k.sb(ctx, "top_keys_int", [P, PEER_HEADS, 4, TOPK], U32)
        topf = k.sb(ctx, "top_keys", [P, PEER_HEADS, 4, TOPK])
        cand = k.sb(ctx, "candidates", [P, TILES, TOPK, TOPK])
        crest = k.sb(ctx, "candidates_without_top", [P, TILES, TOPK * TOPK])
        best = k.sb(ctx, "best", [P, TILES, PEER_HEADS, TOPK])
        pos = k.sb(ctx, "best_position", [P, PEER_HEADS, TILES, TOPK], U32)
        ab = k.sb(ctx, "position_parts_int", [P, TILES, 2, TOPK], U32)
        abf = k.sb(ctx, "position_parts", [P, TILES, 2, TOPK])
        hit = [k.sb(ctx, f"position_hits_{b}", [P, 4, TOPK, TOPK]) for b in range(2)]
        picked = k.sb(ctx, "picked_row_and_column", [P, 4, PICKS])
        gate = k.sb(ctx, "picked_gates", [P, TILES, PICKS])
        col = k.sb(ctx, "gate_sums", [P, 2, TILES * PEER_HEADS])
        (landed, numbered, keys_turned, keys_copied, q_copied, scored, score_copied, found, hits, chosen, reduced, vs, expd,
         turned, copied) = (k.sig.new() for _ in range(15))
        STEPS = 35
        READ = 12

        @block.sync
        def _(sp):
            src = k.a["peer_sub_keys"][0].rearrange("h s n d -> (h s) n d")
            sp.dma_start(numbers[:, :], k.a["constants"][:, C_IOTA * P:(C_IOTA + 1) * P]).then_inc(numbered, 16)
            for n in range(HALVES):
                sp.dma_start(keys[:, n, :], src[n]).then_inc(landed, 16)
            k.stream(sp)

        @block.tensor
        def _(pe):
            def panel(m):
                if m >= 4:
                    pe.wait_ge(q_copied, m - 3)
                split.ready(pe, m)
                wh, wl = split.panel(m)
                for j in range(2):
                    own = slice(j * P, (j + 1) * P)
                    for c in range(DC):
                        ins = passes(pe, k.psum[:, m % 4, j * SEQ:(j + 1) * SEQ], (wh[:, c, own], wl[:, c, own]),
                                     k.xT.at(slice(0, P), c), c == 0, c == DC - 1)
                ins.then_inc(split.eaten, 1)

            def scores(h):
                pe.wait_ge(q_copied, h + 1)
                if h >= 2:
                    pe.wait_ge(score_copied, h - 1)
                for i in range(TILES):
                    for s in range(2):
                        r = 2 * i + s
                        ins = pe.matmul(k.psum[:, 4 + h % 2, r * P:(r + 1) * P], qT[:, 2 * h + s, i * P:(i + 1) * P],
                                        keysT[:, 2 * h + s, :], start=True, stop=True)
                ins.then_inc(scored, 1)

            panel(0)
            pe.wait_ge(landed, 16 * HALVES)
            for b in range(4):
                for q in range(4):
                    ins = pe.transpose(k.psum[:, 4 + b, q * P:(q + 1) * P], keys[:, 4 * b + q, :], k.ident[:, :])
                ins.then_inc(keys_turned, 1)
            panel(1)
            pe.wait_ge(keys_copied, 4)
            for h in range(PEER_HEADS):
                scores(h)
                if h + 2 < PEER_HEADS:
                    panel(h + 2)
            pe.wait_ge(reduced, PEER_HEADS)
            for i in range(TILES):
                for s in range(2):
                    at = (2 * s + i) * P
                    ins = pe.transpose(k.psum[:, 6, at:at + P], picked[:, 2 * i + s, :], k.ident[:, :])
            ins.then_inc(turned, 1)
            pe.wait_ge(vs, 5)
            for i in range(TILES):
                ins = pe.transpose(k.psum[:, 7, i * P:(i + 1) * P], gate[:, i, :], k.ident[:, :])
            ins.then_inc(turned, 1)

        @block.scalar
        def _(act):
            def queries(m):
                split.finished(act, m)
                act.activation(qT[:, 2 * m:2 * m + 2, :], bank2(k, m % 4), ACT.Copy).then_inc(q_copied, 1)

            def scores(h):
                act.wait_ge(scored, h + 1)
                if h >= 2:
                    act.wait_ge(found, STEPS * (h - 2) + READ)
                act.activation(score[h % 2][:, :, :], k.psum[:, 4 + h % 2, :].rearrange("p (a n) -> p a n", a=4),
                               ACT.Copy).then_inc(score_copied, 1)

            for m in range(3):
                split.high(act, m)
            queries(0)
            for b in range(4):
                act.wait_ge(keys_turned, b + 1)
                act.activation(keysT[:, 4 * b:4 * b + 4, :], k.psum[:, 4 + b, :].rearrange("p (a n) -> p a n", a=4),
                               ACT.Copy).then_inc(keys_copied, 1)
            for h in range(PEER_HEADS):
                if h + 3 < PEER_HEADS:
                    split.high(act, h + 3)
                if h + 1 < PEER_HEADS:
                    queries(h + 1)
                scores(h)
            act.wait_ge(vs, 2)
            act.activation(gate[:, :, :].rearrange("p i n -> p (i n)"), best[:, :, :, :].rearrange("p i h n -> p (i h n)"),
                           ACT.Exp).then_inc(expd, 1)
            act.wait_ge(turned, 1)
            act.activation(picksT[:, 0:2, :], bank2(k, 6), ACT.Copy).then_inc(copied, 1)

        @block.gpsimd
        def _(pool):
            k.sig.clear_other(pool)
            for h in range(PEER_HEADS):
                if h + 3 < PEER_HEADS:
                    split.low(pool, h + 3)
                pool.wait_ge(hits, h + 1)
                part = hit[h % 2][:, :, :, :]
                pool.tensor_tensor(part, part, topf[:, h, :, :].unsqueeze(2).broadcast_to([P, 4, TOPK, TOPK]),
                                   ALU.mult).then_inc(chosen, 1)

        @block.vector
        def _(dve):
            done = [0]

            def step(ins):
                ins.then_inc(found, 1)
                done[0] += 1

            def top16(n, values, without, v16, i16):
                sweeps = (lambda m: dve.max(v16(m, 0), values(m)),
                          lambda m: dve.max_index(i16(m, 0), v16(m, 0), values(m)),
                          lambda m: dve.match_replace(without(m), v16(m, 0), values(m), LOW),
                          lambda m: dve.max(v16(m, 1), without(m)),
                          lambda m: dve.max_index(i16(m, 1), v16(m, 1), without(m)))
                for number, sweep in enumerate(sweeps):
                    for m in range(n):
                        if number:
                            dve.wait_ge(found, done[0] - n + 1)
                        step(sweep(m))

            def reduce(h):
                dve.wait_ge(chosen, h + 1)
                dve.tensor_reduce(picked[:, :, TOPK * h:TOPK * (h + 1)], hit[h % 2][:, :, :, :], AX_X, ALU.add
                                  ).then_inc(reduced, 1)

            def head(h):
                dve.wait_ge(score_copied, h + 1)
                top16(4, lambda m: score[h % 2][:, m, :], lambda m: rest[:, m, :],
                      lambda m, r: top[:, h, m, 8 * r:8 * r + 8], lambda m, r: topi[:, h, m, 8 * r:8 * r + 8])
                pairs = top[:, h, :, :].rearrange("p (i s) n -> p s i n", s=2)
                size = [P, TILES, TOPK, TOPK]
                step(dve.tensor_tensor(cand[:, :, :, :], pairs[:, 0, :, :].unsqueeze(3).broadcast_to(size),
                                       pairs[:, 1, :, :].unsqueeze(2).broadcast_to(size), ALU.add))
                if h >= 1:
                    reduce(h - 1)
                dve.wait_ge(found, done[0])
                top16(TILES, lambda m: cand[:, m, :, :].rearrange("p a b -> p (a b)"), lambda m: crest[:, m, :],
                      lambda m, r: best[:, m, h, 8 * r:8 * r + 8], lambda m, r: pos[:, h, m, 8 * r:8 * r + 8])
                step(dve.tensor_copy(topf[:, h, :, :], topi[:, h, :, :]))
                dve.wait_ge(found, done[0] - 1)
                step(dve.tensor_scalar(ab[:, :, 0, :], pos[:, h, :, :], 4, None, ALU.logical_shift_right))
                step(dve.tensor_scalar(ab[:, :, 1, :], pos[:, h, :, :], 15, None, ALU.bitwise_and))
                dve.wait_ge(found, done[0])
                flat = lambda ap: ap[:, :, :, :].rearrange("p i s n -> p (i s n)")
                step(dve.tensor_copy(flat(abf), flat(ab)))
                dve.wait_ge(found, done[0])
                if h == 0:
                    dve.wait_ge(numbered, 16)
                dve.tensor_tensor(hit[h % 2][:, :, :, :].rearrange("p r n a -> p (r n) a"), over_last(flat(abf), TOPK),
                                  over_middle(numbers[:, 0:TOPK], 4 * TOPK), ALU.is_equal).then_inc(hits, 1)
                assert done[0] == STEPS * (h + 1)

            for m in range(3):
                split.low(dve, m)
            for h in range(PEER_HEADS):
                head(h)
            link = linker(dve, vs)
            rows = best[:, :, :, :].rearrange("p i h n -> p (i h) n")
            g = gate[:, :, :].rearrange("p i (h n) -> p (i h) n", h=PEER_HEADS)
            link(dve.tensor_copy(col[:, 0, :], rows[:, :, 0]))
            link(dve.tensor_tensor(rows, rows, over_last(col[:, 0, :], TOPK), ALU.subtract))
            reduce(PEER_HEADS - 1)
            dve.wait_ge(expd, 1)
            link(dve.tensor_reduce(col[:, 0, :], g, AX_X, ALU.add))
            link(dve.reciprocal(col[:, 1, :], col[:, 0, :]))
            link(dve.tensor_tensor(g, g, over_last(col[:, 1, :], TOPK), ALU.mult))
            split.finished(dve, PEER_HEADS - 1)
            dve.tensor_copy(iota, numbers[:, :]).then_inc(copied, 1)
            dve.wait_ge(turned, 2)
            dve.tensor_copy(picksT[:, 2, :], k.psum[:, 7, 0:SEQ]).then_inc(copied, 1)


def scatter_gates(k, picksT, iota, gates, loads):
    GROUP = 4
    BANKS = 4
    TURN = BANKS * GROUP
    with ExitStack() as ctx, k.stage() as block:
        rows = [k.sb(ctx, f"row_onehot_{b}", [P, GROUP, P]) for b in range(BANKS)]
        cols = [k.sb(ctx, f"column_onehot_{b}", [P, GROUP, P]) for b in range(BANKS)]
        rows_hit, rows_ready, cols_ready, made, emptied = (k.sig.new() for _ in range(5))
        turns = SEQ // TURN

        @block.sync
        def _(sp):
            for m in range(2):
                loads.step(sp, m, 0)

        def hits(dve, t, b):
            for which, dst, count in ((0, rows[b], rows_hit), (1, cols[b], cols_ready)):
                dve.tensor_tensor(dst[:, :, :], over_middle(iota, GROUP),
                                  over_last(picksT[:, which, bass.ds(t, GROUP)], P), ALU.is_equal).then_inc(count, 1)

        @block.gpsimd
        def _(pool):
            k.sig.clear_other(pool)
            with pool.Fori(0, turns) as i:
                for b in range(BANKS):
                    pool.wait_ge(rows_hit, BANKS * i + b + 1)
                    pool.tensor_tensor(rows[b][:, :, :], rows[b][:, :, :],
                                       over_last(picksT[:, 2, bass.ds(TURN * i + GROUP * b, GROUP)], P),
                                       ALU.mult).then_inc(rows_ready, 1)

        @block.vector
        def _(dve):
            for b in range(BANKS):
                hits(dve, GROUP * b, b)
            with dve.Fori(1, turns) as i:
                for b in range(BANKS):
                    dve.wait_ge(made, BANKS * i + (b + 1 - BANKS))
                    hits(dve, TURN * i + GROUP * b, b)

        def products(pe, b, count, empty=None):
            pe.wait_ge(rows_ready, count)
            pe.wait_ge(cols_ready, count)
            if empty is not None:
                pe.wait_ge(emptied, empty)
            for q in range(GROUP):
                ins = pe.matmul(k.psum[:, b, q * P:(q + 1) * P], rows[b][:, q, :], cols[b][:, q, :], start=True, stop=True)
            ins.then_inc(made, 1)

        @block.tensor
        def _(pe):
            for b in range(BANKS):
                products(pe, b, b + 1)
            with pe.Fori(1, turns) as i:
                for b in range(BANKS):
                    products(pe, b, BANKS * i + b + 1, BANKS * i + (b + 1 - BANKS))

        @block.scalar
        def _(act):
            with act.Fori(0, turns) as i:
                for b in range(BANKS):
                    act.wait_ge(made, BANKS * i + b + 1)
                    act.activation(gates[:, bass.ds(TURN * i + GROUP * b, GROUP), :],
                                   k.psum[:, b, :].rearrange("p (a n) -> p a n", a=GROUP), ACT.Copy).then_inc(emptied, 1)


class ExpertLoads:

    def __init__(self, k):
        self.k = k
        self.tables = [k.a[n][0].rearrange("(i j) d -> i j d", j=KEYS) for n in ("peer_u", "peer_v")]
        self.sixths = k.w.ring[:, :, :].rearrange("p r (f n) -> p (r f) n", f=2)
        self.u_turned = self.v_split = None

    def part(self, m, what):
        return self.sixths[:, 2 * (m % 3) + what, :]

    def step(self, sp, m, i):
        for what in range(2):
            if m >= 3:
                if what == 0:
                    sp.wait_ge(self.u_turned, 2 * (m - 2) + 12 * i)
                else:
                    sp.wait_ge(self.v_split, m - 2 + 6 * i)
            src = self.tables[what][:, bass.ds(m + 6 * i, 1), :].rearrange("p o d -> p (o d)")
            sp.dma_start(self.part(m, what), src).then_inc(self.k.expert_landed[2 * (m % 3) + what], 16)

    def landed(self, engine, m, what, i):
        engine.wait_ge(self.k.expert_landed[2 * (m % 3) + what], 16 * (m // 3 + 1 + 2 * i))


def every_expert(k, gates, loads):
    TURN = 6
    turns = (KEYS - 2) // TURN
    assert KEYS == 2 + TURN * turns
    with ExitStack() as ctx, k.stage() as block:
        uT = Split(k, ctx, "u_T", [P, DC, P])
        v_split = k.sb(ctx, "v_split", [P, 2, 2, D], F32R)
        w_split = k.sb(ctx, "weighted_split", [P, 2, 2, SEQ], F32R)
        gelu = k.sb(ctx, "gelu", [P, SEQ])
        turned, u_high, u_low, v_high, v_low, products, gelus, weights, w_high, w_low, outs, added = \
            (k.sig.new() for _ in range(12))
        loads.v_split = v_low
        loads.u_turned = turned

        @block.sync
        def _(sp):
            for m in range(2, 1 + TURN):
                loads.step(sp, m, 0)
            with sp.Fori(0, turns - 1) as i:
                for m in range(1 + TURN, 1 + 2 * TURN):
                    loads.step(sp, m, i)
            loads.step(sp, KEYS - 1, 0)

        def turn_u(pe, m, i):
            loads.landed(pe, m, 0, i)
            for half in range(2):
                n = 2 * m + half
                if n >= 3:
                    pe.wait_ge(u_low, n - 2 + 2 * TURN * i)
                for q in range(4):
                    c = 4 * half + q
                    ins = pe.transpose(k.psum[:, 4 + n % 3, q * P:(q + 1) * P], loads.part(m, 0)[:, c * P:(c + 1) * P],
                                       k.ident[:, :])
                ins.then_inc(turned, 1)

        def u_products(pe, m, i):
            if m >= 1:
                pe.wait_ge(gelus, m + TURN * i)
            for c in range(DC):
                if c % 4 == 0:
                    pe.wait_ge(u_low, 2 * m + c // 4 + 1 + 2 * TURN * i)
                ins = passes(pe, k.psum[:, 7, 0:SEQ], uT.at(slice(0, P), c), k.xT.at(slice(0, P), c), c == 0, c == DC - 1)
            ins.then_inc(products, 1)

        def v_products(pe, m, i, stop=False):
            pe.wait_ge(v_low, m + 1 + TURN * i)
            pe.wait_ge(w_low, m + 1 + TURN * i)
            b = m % 2
            down(pe, k, (w_split[:, b, 0, :], w_split[:, b, 1, :]), (v_split[:, b, 0, :], v_split[:, b, 1, :]),
                 m == 0, stop).then_inc(outs, 1)

        def run(engine, step):
            for m in range(1, 1 + TURN):
                step(m, 0)
            with engine.Fori(0, turns - 1) as i:
                for m in range(1 + TURN, 1 + 2 * TURN):
                    step(m, i)

        @block.tensor
        def _(pe):
            def step(m, i):
                turn_u(pe, m + 1, i)
                u_products(pe, m, i)
                v_products(pe, m - 1, i)
            turn_u(pe, 0, 0)
            turn_u(pe, 1, 0)
            u_products(pe, 0, 0)
            run(pe, step)
            u_products(pe, KEYS - 1, 0)
            v_products(pe, KEYS - 2, 0)
            v_products(pe, KEYS - 1, 0, True)

        def u_half(m, half):
            n = 2 * m + half
            return k.psum[:, 4 + n % 3, :].rearrange("p (a n) -> p a n", a=4), slice(4 * half, 4 * half + 4)

        @block.scalar
        def _(act):
            def u(m, i):
                if m >= 1:
                    act.wait_ge(products, m + TURN * i)
                for half in range(2):
                    src, c = u_half(m, half)
                    act.wait_ge(turned, 2 * m + half + 1 + 2 * TURN * i)
                    split_high(act, uT.hi[:, c, :], src).then_inc(u_high, 1)

            def v(m, i):
                loads.landed(act, m, 1, i)
                if m >= 2:
                    act.wait_ge(outs, m - 1 + TURN * i)
                split_high(act, v_split[:, m % 2, 0, :], loads.part(m, 1)).then_inc(v_high, 1)

            def activate(m, i):
                act.wait_ge(products, m + 1 + TURN * i)
                if m >= 1:
                    act.wait_ge(w_low, m + TURN * i)
                act.activation(gelu[:, :], k.psum[:, 7, 0:SEQ], ACT.Gelu).then_inc(gelus, 1)

            def weighted(m, i):
                act.wait_ge(weights, m + 1 + TURN * i)
                if m >= 2:
                    act.wait_ge(outs, m - 1 + TURN * i)
                split_high(act, w_split[:, m % 2, 0, :], gelu[:, :]).then_inc(w_high, 1)

            def step(m, i):
                v(m, i)
                activate(m, i)
                u(m + 1, i)
                weighted(m, i)
            u(0, 0)
            v(0, 0)
            activate(0, 0)
            u(1, 0)
            weighted(0, 0)
            run(act, step)
            v(KEYS - 1, 0)
            activate(KEYS - 1, 0)
            weighted(KEYS - 1, 0)

        @block.vector
        def _(dve):
            def u(m, i):
                for half in range(2):
                    src, c = u_half(m, half)
                    dve.wait_ge(u_high, 2 * m + half + 1 + 2 * TURN * i)
                    split_low(dve, uT.lo[:, c, :], src, uT.hi[:, c, :]).then_inc(u_low, 1)

            def v(m, i):
                dve.wait_ge(v_high, m + 1 + TURN * i)
                b = m % 2
                split_low(dve, v_split[:, b, 1, :], loads.part(m, 1), v_split[:, b, 0, :]).then_inc(v_low, 1)

            def weigh(m, i):
                dve.wait_ge(gelus, m + 1 + TURN * i)
                dve.tensor_tensor(gelu[:, :], gelu[:, :], gates[:, :, bass.ds(m + TURN * i, 1)].rearrange("p t o -> p (t o)"),
                                  ALU.mult).then_inc(weights, 1)

            def weighted(m, i):
                dve.wait_ge(w_high, m + 1 + TURN * i)
                split_low(dve, w_split[:, m % 2, 1, :], gelu[:, :], w_split[:, m % 2, 0, :]).then_inc(w_low, 1)

            def step(m, i):
                v(m, i)
                weigh(m, i)
                u(m + 1, i)
                weighted(m, i)
            u(0, 0)
            v(0, 0)
            weigh(0, 0)
            u(1, 0)
            weighted(0, 0)
            run(dve, step)
            v(KEYS - 1, 0)
            weigh(KEYS - 1, 0)
            weighted(KEYS - 1, 0)
            dve.wait_ge(outs, KEYS)
            for t in range(TILES):
                dve.tensor_tensor(k.x[:, t, :], accumulated(k, t), k.x[:, t, :], ALU.add).then_inc(added, 1)

        k.idle_pool(block)


def final_norm(k, rows):
    with ExitStack() as ctx, k.stage() as block:
        gain = k.sb(ctx, "final_gain", [P, D])
        sq = k.sb(ctx, "final_squares", [P, TILES, D])
        stat = k.sb(ctx, "final_stats", [P, 3, TILES])
        table = k.sb(ctx, "relative_table", [33, NH])
        onehot = k.sb(ctx, "bucket_onehot", [33, DISTS])
        banks, high, written, normed = (k.sig.new() for _ in range(4))
        highs, lows = split_turned(k, 4, k.xT, banks, high, written)
        begin = Beginning(k)
        landed, squares, rooted, vs, table_landed, future, made, copied = (k.sig.new() for _ in range(8))

        @block.sync
        def _(sp):
            sp.dma_start(gain[:, :], k.a["norm_final_w"].partition_broadcast(P)).then_inc(landed, 16)
            sp.dma_start(table[0:32, :], k.a["rel_table_2"]).then_inc(table_landed, 16)
            sp.dma_start(onehot[:, :], k.a["bucket_onehot"]).then_inc(table_landed, 16)
            k.stream(sp)

        @block.tensor
        def _(pe):
            pe.wait_ge(table_landed, 32)
            pe.wait_ge(future, 1)
            pe.matmul(k.psum[0:NH, 0, :], table[:, :], onehot[:, :], start=True, stop=True).then_inc(made, 1)
            for i in range(TILES):
                turn_chunks(pe, k, k.x[:, i, :], i, banks, 4, normed)

        @block.scalar
        def _(act):
            for i in range(TILES):
                act.activation(sq[:, i, :], k.x[:, i, :], ACT.Square, accum_out=stat[:, 0, i:i + 1]).then_inc(squares, 1)
            act.wait_ge(squares, TILES)
            act.activation(stat[:, 1, :], stat[:, 0, :], ACT.Sqrt, bias=k.eps[:, 0:1], scale=1.0 / D).then_inc(rooted, 1)
            act.wait_ge(made, 1)
            act.activation(rows[:, :], k.psum[0:NH, 0, :], ACT.Copy).then_inc(copied, 1)
            begin.highs(act)
            highs(act)

        @block.vector
        def _(dve):
            link = linker(dve, vs)
            dve.memset(table[32:33, :], NEG).then_inc(future, 1)
            dve.wait_ge(rooted, 1)
            link(dve.reciprocal(stat[:, 2, :], stat[:, 1, :]))
            dve.wait_ge(landed, 16)
            for i in range(TILES):
                for n in range(2):
                    part = k.x[:, i, n * D // 2:(n + 1) * D // 2]
                    dve.scalar_tensor_tensor(part, part, stat[:, 2, i:i + 1], gain[:, n * D // 2:(n + 1) * D // 2],
                                             ALU.mult, ALU.mult).then_inc(normed, 1)
            begin.lows(dve)
            lows(dve)

        k.idle_pool(block)



def load_gains(k, sp, gains, landed, which):
    layer, n = divmod(which, 3)
    sp.dma_start(gains[:, 0, :], k.a["ln_g_2"][layer, n].partition_broadcast(P)).then_inc(landed, 16)
    sp.dma_start(gains[:, 1, :], k.a["ln_b_2"][layer, n].partition_broadcast(P)).then_inc(landed, 16)


def post_norm(k, gains, last=False):
    with ExitStack() as ctx, k.stage() as block:
        sq = k.sb(ctx, "centred_squares", [P, TILES, D])
        stat = k.sb(ctx, "norm_stats", [P, 7, TILES])
        summed, negated, squared, rooted, recip, shift, scaled, gained, normed, banks, high, written = \
            (k.sig.new() for _ in range(12))
        highs, lows = split_turned(k, 4, k.xT, banks, high, written)
        begin = None if last else Beginning(k)
        halves = [slice(n * D // 2, (n + 1) * D // 2) for n in range(2)]

        @block.sync
        def _(sp):
            k.stream(sp)
            if last:
                for i in range(TILES):
                    sp.wait_ge(normed, 2 * i + 2)
                    sp.dma_start(k.a["out"][0][i * P:(i + 1) * P, :], k.x[:, i, :]).then_inc(k.stored, 16)
                sp.wait_ge(k.stored, 16 * TILES)

        @block.vector
        def _(dve):
            def mean(i):
                dve.scalar_tensor_tensor(k.x[:, i, :], k.x[:, i, :], DN_ALPHA, accumulated(k, i), ALU.mult, ALU.add,
                                         accum_out=stat[:, 0, i:i + 1]).then_inc(summed, 1)
                dve.wait_ge(summed, i + 1)
                dve.tensor_scalar(stat[:, 1, i:i + 1], stat[:, 0, i:i + 1], -1.0 / D, None, ALU.mult).then_inc(negated, 1)

            def scale(i):
                dve.wait_ge(rooted, i + 1)
                dve.reciprocal(stat[:, 4, i:i + 1], stat[:, 3, i:i + 1]).then_inc(recip, 1)
                dve.wait_ge(recip, i + 1)
                dve.tensor_tensor(stat[:, 5, i:i + 1], stat[:, 1, i:i + 1], stat[:, 4, i:i + 1], ALU.mult).then_inc(shift, 1)

            def gain(i):
                dve.wait_ge(scaled, i + 1)
                dve.tensor_tensor(k.x[:, i, :], sq[:, i, :], gains[:, 0, :], ALU.mult).then_inc(gained, 1)

            def bias(i):
                dve.wait_ge(gained, i + 1)
                for cols in halves:
                    dve.tensor_tensor(k.x[:, i, cols], k.x[:, i, cols], gains[:, 1, cols], ALU.add).then_inc(normed, 1)

            mean(0)
            mean(1)
            scale(0)
            if begin:
                begin.low(dve, 0)
            gain(0)
            scale(1)
            bias(0)
            gain(1)
            bias(1)
            if begin:
                begin.low(dve, 1)
                lows(dve)

        @block.scalar
        def _(act):
            def squares(i):
                act.wait_ge(negated, i + 1)
                act.activation(sq[:, i, :], k.x[:, i, :], ACT.Square, bias=stat[:, 1, i:i + 1],
                               accum_out=stat[:, 2, i:i + 1]).then_inc(squared, 1)
                act.wait_ge(squared, i + 1)
                act.activation(stat[:, 3, i:i + 1], stat[:, 2, i:i + 1], ACT.Sqrt, bias=k.eps[:, 1:2],
                               scale=1.0 / D).then_inc(rooted, 1)

            def scaling(i):
                act.wait_ge(shift, i + 1)
                act.activation(sq[:, i, :], k.x[:, i, :], ACT.Identity, bias=stat[:, 5, i:i + 1],
                               scale=stat[:, 4, i:i + 1]).then_inc(scaled, 1)

            act.activation(stat[:, 6, 0:1], k.eps[:, 1:2], ACT.Sqrt)
            if begin:
                begin.high(act, 0)
            squares(0)
            scaling(0)
            squares(1)
            scaling(1)
            if begin:
                begin.high(act, 1)
                highs(act)

        @block.tensor
        def _(pe):
            if not last:
                for i in range(TILES):
                    turn_chunks(pe, k, k.x[:, i, :], i, banks, 4, normed)

        k.idle_pool(block)


def swiglu(k, gains, which, rows=None, final=False):
    UNITS = FFN_DIM // COLS
    TURN = 2
    PER = 3 * TURN
    turns = (UNITS - 1) // TURN
    assert UNITS == 1 + TURN * turns and PER % RING == 0 and PER % BUFFERS == 0
    g0 = k.w.take(3 * UNITS)
    with ExitStack() as ctx, k.stage() as block:
        split = Splitter(k, ctx, g0)
        act_out = k.sb(ctx, "silu", [P, 2, 2, SEQ])
        hidden = Split(k, ctx, "hidden", [P, 2, 2, SEQ])
        gains_landed, silus, gated, highs, lows = (k.sig.new() for _ in range(5))

        def first(u, n):
            return n if u == 0 else 3 * u - 1 + n

        def last(u):
            return 3 * u + 4 if u < UNITS - 1 else 3 * UNITS - 1

        @block.sync
        def _(sp):
            load_gains(k, sp, gains, gains_landed, which)
            k.stream(sp)
            sp.wait_ge(gains_landed, 32)

        def up(pe, u, i):
            for n in range(2):
                if u >= 2:
                    pe.wait_ge((silus, gated)[n], u - 1 + TURN * i)
                split.ready(pe, first(u, n), i, PER)
                wh, wl = split.panel(first(u, n))
                for j in range(2):
                    own = slice(j * P, (j + 1) * P)
                    for c in range(DC):
                        ins = passes(pe, k.psum[:, 4 + 2 * (u % 2) + n, j * SEQ:(j + 1) * SEQ],
                                     (wh[:, c, own], wl[:, c, own]), k.xT.at(slice(0, P), c), c == 0, c == DC - 1)
                ins.then_inc(split.eaten, 1)

        def down_unit(pe, u, i):
            split.ready(pe, last(u), i, PER)
            wh, wl = split.rows(last(u))
            pe.wait_ge(lows, u + 1 + TURN * i)
            for r in range(2):
                ins = down(pe, k, hidden.at(slice(0, P), u % 2, r), (wh[:, r, :], wl[:, r, :]), u == 0 and r == 0,
                           u == UNITS - 1 and r == 1)
            ins.then_inc(split.eaten, 1)

        def run(engine, unit):
            for u in range(1, 1 + TURN):
                unit(u, 0)
            with engine.Fori(0, turns - 1) as i:
                for u in range(1 + TURN, 1 + 2 * TURN):
                    unit(u, i)

        @block.tensor
        def _(pe):
            def unit(u, i):
                up(pe, u, i)
                down_unit(pe, u - 1, i)
            up(pe, 0, 0)
            run(pe, unit)
            down_unit(pe, UNITS - 1, 0)

        @block.scalar
        def _(act):
            def silu(u, i):
                split.finished(act, first(u, 0), i, PER)
                if u >= 2:
                    act.wait_ge(gated, u - 1 + TURN * i)
                act.activation(act_out[:, u % 2, :, :], bank2(k, 4 + 2 * (u % 2)), ACT.Silu).then_inc(silus, 1)

            def high(u, i):
                act.wait_ge(gated, u + 1 + TURN * i)
                if u >= 2:
                    split.finished(act, last(u - 2), i, PER)
                split_high(act, hidden.hi[:, u % 2, :, :], act_out[:, u % 2, :, :]).then_inc(highs, 1)

            def unit(u, i):
                split.high(act, first(u, 0) + 1, i, PER)
                split.high(act, first(u, 0) + 2, i, PER)
                silu(u, i)
                split.high(act, first(u, 0) + 3, i, PER)
                high(u, i)
            split.high(act, 0)
            split.high(act, 1)
            split.high(act, 2)
            silu(0, 0)
            high(0, 0)
            run(act, unit)

        @block.vector
        def _(dve):
            def gate(u, i):
                split.finished(dve, first(u, 1), i, PER)
                dve.wait_ge(silus, u + 1 + TURN * i)
                if u >= 2:
                    dve.wait_ge(lows, u - 1 + TURN * i)
                out = act_out[:, u % 2, :, :]
                dve.scalar_tensor_tensor(out, out, 0.5, bank2(k, 5 + 2 * (u % 2)), ALU.mult, ALU.mult).then_inc(gated, 1)

            def low(u, i):
                dve.wait_ge(highs, u + 1 + TURN * i)
                split_low(dve, hidden.lo[:, u % 2, :, :], act_out[:, u % 2, :, :], hidden.hi[:, u % 2, :, :]).then_inc(lows, 1)

            def unit(u, i):
                split.low(dve, first(u, 0) + 1, i, PER)
                split.low(dve, first(u, 0) + 2, i, PER)
                split.low(dve, first(u, 0) + 3, i, PER)
                gate(u, i)
                low(u, i)
            split.low(dve, 0)
            split.low(dve, 1)
            split.low(dve, 2)
            gate(0, 0)
            low(0, 0)
            run(dve, unit)

        @block.gpsimd
        def _(pool):
            k.sig.clear_other(pool)
            if rows is not None:
                pool.dma_start(k.a["bias_rows"].rearrange("p h x -> h p x"),
                               rows[:, :].unsqueeze(1).broadcast_to([NH, P, DISTS])).then_inc(k.bias_stored, 16)
    post_norm(k, gains, final)


def spatial_gating(k, gains):
    with ExitStack() as ctx:
        mixedT = Split(k, ctx, "sgu_mixed_T", [P, 16, SEQ])
        with ExitStack() as inner:
            gatedT = k.sb(inner, "sgu_u_T", [P, 16, SEQ])
            v = k.sb(inner, "sgu_v", [P, TILES, SGU_HALF])
            gb = k.sb(inner, "sgu_gain_bias", [P, 2, SGU_HALF])
            panels(k, [("N", k.xT, v[:, :, n * COLS:(n + 1) * COLS], ACT.Gelu, 1.0) for n in range(8)]
                   + [("T", k.xT, gatedT[:, 2 * n:2 * n + 2, :], ACT.Gelu, 1.0) for n in range(8)],
                   along=GateNorm(k, inner, v, gb, mixedT))
            mix_tokens(k, v, gatedT, mixedT, gb)
        rows_product(k, mixedT, 8, left_in_banks, (gains, 1))
    post_norm(k, gains)


class GateNorm:

    def __init__(self, k, ctx, v, gb, unused):
        self.k, self.v, self.gb = k, v, gb
        self.sq = unused.hi[:, 0:SGU_HALF // SEQ, :].rearrange("p c t -> p (c t)")
        self.stat = k.sb(ctx, "sgu_stats", [P, 6, TILES])
        self.first = SGU_HALF // COLS + 1

    def begin(self):
        (self.landed, self.summed, self.negated, self.squared, self.rooted, self.recip, self.shift, self.scaled,
         self.gained, self.normed) = (self.k.sig.new() for _ in range(10))

    def load(self, sp):
        for n, name in enumerate(("sgu_ln_g_2", "sgu_ln_b_2")):
            sp.dma_start(self.gb[:, n, :], self.k.a[name][0].partition_broadcast(P)).then_inc(self.landed, 16)

    def dve(self, dve, m, result):
        v, stat, gb, step = self.v, self.stat, self.gb, m - self.first
        if step in (0, 1):
            i = step
            if i == 0:
                result(SGU_HALF // COLS - 1)
            dve.tensor_reduce(stat[:, 0, i:i + 1], v[:, i, :], AX_X, ALU.add).then_inc(self.summed, 1)
            dve.wait_ge(self.summed, i + 1)
            dve.tensor_scalar(stat[:, 1, i:i + 1], stat[:, 0, i:i + 1], -1.0 / SGU_HALF, None, ALU.mult
                              ).then_inc(self.negated, 1)
        if step == 3:
            dve.wait_ge(self.rooted, 1)
            dve.reciprocal(stat[:, 4, :], stat[:, 3, :]).then_inc(self.recip, 1)
            dve.wait_ge(self.recip, 1)
            dve.tensor_tensor(stat[:, 5, :], stat[:, 1, :], stat[:, 4, :], ALU.mult).then_inc(self.shift, 1)
        if step in (5, 6):
            i = step - 5
            dve.wait_ge(self.landed, 32)
            dve.wait_ge(self.scaled, i + 1)
            dve.tensor_tensor(v[:, i, :], v[:, i, :], gb[:, 0, :], ALU.mult).then_inc(self.gained, 1)
            dve.wait_ge(self.gained, i + 1)
            dve.tensor_tensor(v[:, i, :], v[:, i, :], gb[:, 1, :], ALU.add).then_inc(self.normed, 1)

    def act(self, act, m):
        v, stat, step = self.v, self.stat, m - self.first
        if step in (0, 1):
            i = step
            act.wait_ge(self.negated, i + 1)
            if i == 1:
                act.wait_ge(self.squared, 1)
            act.activation(self.sq[:, :], v[:, i, :], ACT.Square, bias=stat[:, 1, i:i + 1],
                           accum_out=stat[:, 2, i:i + 1]).then_inc(self.squared, 1)
        if step == 2:
            act.wait_ge(self.squared, 2)
            act.activation(stat[:, 3, :], stat[:, 2, :], ACT.Sqrt, bias=self.k.eps[:, 1:2],
                           scale=1.0 / SGU_HALF).then_inc(self.rooted, 1)
        if step in (4, 5):
            i = step - 4
            act.wait_ge(self.shift, 1)
            act.activation(v[:, i, :], v[:, i, :], ACT.Identity, bias=stat[:, 5, i:i + 1],
                           scale=stat[:, 4, i:i + 1]).then_inc(self.scaled, 1)


def mix_tokens(k, v, gatedT, mixedT, scratch):
    with ExitStack() as ctx, k.stage() as block:
        ws = k.sb(ctx, "sgu_ws", [P, SGU_GROUPS, P])
        wsT = k.sb(ctx, "sgu_ws_T", [P, SGU_GROUPS, P])
        bs = k.sb(ctx, "sgu_bias", [P, SGU_GROUPS, P])
        causal = k.sb(ctx, "sgu_causal", [P, P])
        ws_landed, turned, masked, mixed, biased, gated, high, low = (k.sig.new() for _ in range(8))
        begin = Beginning(k)
        a = k.a

        @block.sync
        def _(sp):
            sp.dma_start(ws[:, :, :], a["sgu_w_s_2"][0].rearrange("g t s -> t g s")).then_inc(ws_landed, 16)
            sp.dma_start(causal[:, :], a["constants"][:, C_CAUSAL_T * P:(C_CAUSAL_T + 1) * P]).then_inc(ws_landed, 16)
            sp.dma_start(bs[:, :, :].rearrange("p g t -> p (g t)"),
                         a["sgu_b_s_2"][0].rearrange("g t -> (g t)").partition_broadcast(P)).then_inc(ws_landed, 16)
            k.stream(sp)

        @block.tensor
        def _(pe):
            pe.wait_ge(ws_landed, 48)
            for b in range(2):
                for q in range(4):
                    ins = pe.transpose(k.psum[:, b, q * P:(q + 1) * P], ws[:, 4 * b + q, :], k.ident[:, :])
                ins.then_inc(turned, 1)
            pe.wait_ge(masked, 2)
            for g in range(SGU_GROUPS):
                for half in range(2):
                    for i in range(TILES):
                        lo = g * COLS + half * P
                        at = half * SEQ + i * P
                        ins = pe.matmul(k.psum[:, g, at:at + P], v[:, i, lo:lo + P], wsT[:, g, :], start=True, stop=True)
                ins.then_inc(mixed, 1)

        @block.scalar
        def _(act):
            begin.highs(act)
            for g in range(SGU_GROUPS):
                act.wait_ge(gated, g + 1)
                split_high(act, mixedT.hi[:, 2 * g:2 * g + 2, :], gatedT[:, 2 * g:2 * g + 2, :]).then_inc(high, 1)

        @block.vector
        def _(dve):
            begin.lows(dve)
            dve.wait_ge(ws_landed, 48)
            for b in range(2):
                dve.wait_ge(turned, b + 1)
                dve.tensor_tensor(wsT[:, 4 * b:4 * b + 4, :], k.psum[:, b, :].rearrange("p (a n) -> p a n", a=4),
                                  over_middle(causal[:, :], 4), ALU.mult).then_inc(masked, 1)
            def low_of(g):
                dve.wait_ge(high, g + 1)
                own = slice(2 * g, 2 * g + 2)
                split_low(dve, mixedT.lo[:, own, :], gatedT[:, own, :], mixedT.hi[:, own, :]).then_inc(low, 1)

            work = scratch[:, :, :].rearrange("p i (c n) -> p (i c) n", n=P)
            for g in range(SGU_GROUPS):
                dve.wait_ge(mixed, g + 1)
                part = work[:, 4 * g:4 * g + 4, :]
                dve.tensor_tensor(part, k.psum[:, g, :].rearrange("p (a n) -> p a n", a=4), over_middle(bs[:, g, :], 4),
                                  ALU.add).then_inc(biased, 1)
                dve.wait_ge(biased, g + 1)
                dst = gatedT[:, 2 * g:2 * g + 2, :]
                dve.tensor_tensor(dst, dst, part.rearrange("p (a b) n -> p a (b n)", a=2), ALU.mult).then_inc(gated, 1)
                if g >= 1:
                    low_of(g - 1)
            low_of(SGU_GROUPS - 1)

        k.idle_pool(block)


class SharedKV:

    def __init__(self, k, ctx):
        self.k_sel = k.sb(ctx, "k_sel_T", [P, KVG, SEQ])
        self.k_win = k.sb(ctx, "k_win_T", [P, KVG, SEQ])
        self.v_sel = k.sb(ctx, "v_sel", [P, TILES, KVG * HDIM])
        self.v_win = k.sb(ctx, "v_win", [P, TILES, KVG * HDIM])
        self.k_cmp = k.sb(ctx, "k_cmp_T", [P, KVG, 16])
        self.v_cmp = k.sb(ctx, "v_cmp", [16, KVG, HDIM])
        self.bias = k.sb(ctx, "position_bias", [P, NH, BIAS_W])


def shared_kv(k, s):
    with ExitStack() as ctx:
        raw = [k.sb(ctx, f"kv_T_{n}", [P, 2, SEQ]) for n in range(4)]
        panels(k, [("T", k.xT, raw[0][:, :, :], None, 1.0), ("T", k.xT, raw[1][:, :, :], None, 1.0),
                   ("T", k.xT, raw[2][:, :, :], None, 1.0), ("N", k.xT, s.v_sel[:, :, :], None, 1.0),
                   ("T", k.xT, raw[3][:, :, :], None, 1.0), ("N", k.xT, s.v_win[:, :, :], None, 1.0)])
        compress(k, s, raw)


def compress(k, s, raw):
    J = CMP_LEN // 2
    g0 = k.w.take(4)
    GN = KVG * NCMP
    with ExitStack() as ctx, k.stage() as block:
        two = [k.sb(ctx, f"token_pairs_{n}", [P, KVG, SEQ]) for n in range(2)]
        blocks = [k.sb(ctx, f"cmp_blocks_{n}", [P, J, KVG, NCMP]) for n in range(2)]
        sums = k.sb(ctx, "cmp_hidden_sums", [GN, 2, COLS])
        hid = k.sb(ctx, "cmp_hidden", [P, 2, 2, GN])
        pe_rows = k.sb(ctx, "cmp_pe_rows", [2 * J, P])
        pe_cols = k.sb(ctx, "cmp_pe_columns", [P, 2 * J])
        w2 = k.sb(ctx, "cmp_w2", [P, 2, 2, HDIM])
        landed, vs, paired, pe_turned, blocked, summed, turned, gelud, outs, copied = (k.sig.new() for _ in range(10))
        half = [slice(0, HDIM), slice(HDIM, P)]

        @block.sync
        def _(sp):
            sp.dma_start(pe_rows[:, :], k.a["cmp_pe_2"].rearrange("s (j l) d -> (s j) (l d)", l=2)).then_inc(landed, 16)
            sp.dma_start(w2[:, :, :, :], k.a["cmp_w2_2"].rearrange("s (c p) d -> p s c d", p=P)).then_inc(landed, 16)
            k.stream(sp)
            sp.wait_ge(k.bias_stored, 16)
            view = bass.AP(k.a["bias_rows"].tensor, SEQ // 2 - 1, [[NH * DISTS - 1, P], [DISTS, NH], [1, BIAS_W]])
            sp.dma_start(s.bias[:, :, :], view).then_inc(k.bias_spread, 16)

        @block.vector
        def _(dve):
            dve.wait_ge(pe_turned, 1)
            dve.tensor_copy(pe_cols[:, :], k.psum[:, 7, 0:2 * J]).then_inc(vs, 1)
            for n in range(2):
                for g in range(KVG):
                    src = raw[n][half[g % 2], g // 2, :]
                    dve.tensor_copy(two[n][half[0], g, :], src).then_inc(paired, 1)
                    dve.tensor_copy(two[n][half[1], g, 0:SEQ - 1], src[:, 1:SEQ]).then_inc(paired, 1)
            dve.wait_ge(paired, 4 * KVG)
            dve.wait_ge(vs, 1)
            for n in range(2):
                for j in range(J):
                    src = two[n][:, :, 2 * j:2 * j + CMP_STRIDE * (NCMP - 1) + 1:CMP_STRIDE]
                    ins = dve.tensor_scalar(blocks[n][:, j, :, :], src, pe_cols[:, J * n + j:J * n + j + 1], None, ALU.add)
                ins.then_inc(blocked, 1)
            for which, dst in ((2, s.k_sel), (3, s.k_win)):
                for g in range(KVG):
                    for h in range(2):
                        dve.tensor_copy(dst[half[h], g, :], raw[which][half[g % 2], g // 2, :]).then_inc(copied, 1)
            dve.wait_ge(outs, 1)
            for h in range(2):
                dve.tensor_copy(s.k_cmp[half[h], :, 0:NCMP], k.psum[half[h], 4, 0:GN].rearrange("p (g n) -> p g n", g=KVG)
                                ).then_inc(copied, 1)
            dve.wait_ge(outs, 2)
            dve.tensor_copy(s.v_cmp[0:NCMP, :, :], k.psum[0:NCMP, 5, 0:KVG * HDIM].rearrange("p (g d) -> p g d", g=KVG)
                            ).then_inc(copied, 1)

        @block.tensor
        def _(pe):
            pe.wait_ge(landed, 32)
            pe.transpose(k.psum[:, 7, 0:2 * J], pe_rows[:, :], k.ident[0:2 * J, 0:2 * J]).then_inc(pe_turned, 1)
            for n in range(2):
                pe.wait_ge(blocked, n + 1)
                for q in range(2):
                    use_slot(pe, k, g0 + 2 * n + q)
                for j in range(J):
                    w = k.w.panel(g0 + 2 * n + j // DC)
                    ins = pe.matmul(k.psum[0:GN, n, 0:COLS], blocks[n][:, j, :, :].rearrange("p g n -> p (g n)"),
                                    w[:, j % DC, :], start=(j == 0), stop=(j == J - 1))
                    if j % DC == DC - 1:
                        ins.then_inc(k.w.used[(g0 + 2 * n + j // DC) % RING], 1)
            for n in range(2):
                pe.wait_ge(summed, n + 1)
                for c in range(2):
                    ins = pe.transpose(k.psum[:, 2 + n, c * GN:(c + 1) * GN], sums[:, n, c * P:(c + 1) * P],
                                       k.ident[0:GN, 0:GN])
                ins.then_inc(turned, 1)
            pe.wait_ge(gelud, 2)
            for h in range(2):
                for c in range(2):
                    ins = pe.matmul(k.psum[half[h], 4, 0:GN], w2[:, 0, c, :], hid[:, 0, c, :], start=(c == 0), stop=(c == 1))
            ins.then_inc(outs, 1)
            pe.wait_ge(gelud, 4)
            for g in range(KVG):
                for c in range(2):
                    ins = pe.matmul(k.psum[0:NCMP, 5, g * HDIM:(g + 1) * HDIM], hid[:, 1, c, g * NCMP:(g + 1) * NCMP],
                                    w2[:, 1, c, :], start=(c == 0), stop=(c == 1))
            ins.then_inc(outs, 1)

        @block.scalar
        def _(act):
            for n in range(2):
                used_slot(act, k, g0 + 2 * n + 1)
                act.activation(sums[:, n, :], k.psum[0:GN, n, 0:COLS], ACT.Copy).then_inc(summed, 1)
            for n in range(2):
                act.wait_ge(turned, n + 1)
                for c in range(2):
                    act.activation(hid[:, n, c, :], k.psum[:, 2 + n, c * GN:(c + 1) * GN], ACT.Gelu,
                                   bias=k.cols[:, COL_B1 + 2 * n + c:COL_B1 + 2 * n + c + 1]).then_inc(gelud, 1)

        k.idle_pool(block)


def sparse_attention(k, s, gains):
    with ExitStack() as ctx:
        qT = k.sb(ctx, "nsa_q_T", [P, DC, SEQ])
        gates = k.sb(ctx, "nsa_gates", [P, TILES, 3 * NH])
        view = k.a["nsa_w_qg_2"][0][:, NH * HDIM:NH * HDIM + 3 * NH].rearrange("(c p) n -> p c n", p=P)
        panels(k, [("T", k.xT, qT[:, 2 * n:2 * n + 2, :], None, HDIM ** -0.5) for n in range(4)],
               (view, k.xT, gates[:, :, :], ACT.Sigmoid, 3 * NH))
        attend(k, s, qT, gates)
    rows_product(k, k.xT, 4, left_in_banks, (gains, 4))
    post_norm(k, gains)


def attend(k, s, qT, gates):
    A, B = SEQ // 2, SEQ
    with ExitStack() as ctx, k.stage() as block:
        masks = k.sb(ctx, "cmp_masks", [P, 2, 16])
        first = [k.sb(ctx, f"scores_first_{b}", [P, 2, A]) for b in range(3)]
        second = [k.sb(ctx, f"scores_second_{b}", [P, 2, B]) for b in range(3)]
        cs = [k.sb(ctx, f"cmp_scores_{b}", [P, TILES, 16]) for b in range(3)]
        pT = k.sb(ctx, "probabilities_T", [P, 2, 2, A])
        pT_last = k.sb(ctx, "probabilities_last_T", [P, 2, A])
        cT = k.sb(ctx, "cmp_probabilities_T", [16, SEQ])
        c = [k.sb(ctx, f"softmax_columns_{b}", [P, 3, TILES, 3]) for b in range(3)]
        landed, scored, biased, negmax, expd, vs, weighed, turned, copied, outs, high, written = \
            (k.sig.new() for _ in range(12))

        begin = Beginning(k)

        def parts(h):
            return h // 4, slice((h % 2) * HDIM, (h % 2 + 1) * HDIM)

        @block.sync
        def _(sp):
            lo = C_MISC * P + 16
            sp.dma_start(masks[:, :, :], k.a["constants"][:, lo:lo + 32].rearrange("p (i n) -> p i n", i=2)).then_inc(landed, 16)
            k.stream(sp)

        def scores(pe, h):
            g, p = parts(h)
            bank = 2 * (h % 2)
            if h >= 2:
                pe.wait_ge(biased, 3 * (h - 1))
            for i, at, n in ((1, bank, B), (0, bank + 1, A)):
                q = qT[p, h // 2, i * P:(i + 1) * P]
                for branch, keys in enumerate((s.k_sel, s.k_win)):
                    pe.matmul(k.psum[:, at, branch * n:(branch + 1) * n], q, keys[p, g, 0:n], start=True, stop=True)
                ins = pe.matmul(k.psum[:, bank + 1, B + 16 * i:B + 16 * i + NCMP], q, s.k_cmp[p, g, 0:NCMP],
                                start=True, stop=True)
            ins.then_inc(scored, 1)

        def turn(pe, h):
            b = h % 3
            pe.wait_ge(weighed, h + 1)
            if h >= 1:
                pe.wait_ge(copied, 3 * h)
            for branch in range(2):
                pe.transpose(k.psum[:, 4, branch * B:branch * B + A], first[b][:, branch, :], k.ident[:, :])
                pe.transpose(k.psum[:, 4, branch * B + A:(branch + 1) * B], second[b][:, branch, 0:A], k.ident[:, :])
                pe.transpose(k.psum[:, 5, branch * A:(branch + 1) * A], second[b][:, branch, A:B], k.ident[:, :])
            for i in range(TILES):
                ins = pe.transpose(k.psum[0:NCMP, 5, B + i * A:B + (i + 1) * A], cs[b][:, i, 0:NCMP], k.ident[:, :])
            ins.then_inc(turned, 1)

        def mix(pe, h):
            g, p = parts(h)
            pe.wait_ge(copied, 3 * h + 3)
            j = h // 2
            if j >= 2 and h % 2 == 0:
                pe.wait_ge(written, j - 1)
            o = k.psum[p, 6 + j % 2, :]
            d = slice(g * HDIM, (g + 1) * HDIM)
            pe.matmul(o[:, 0:SEQ], s.v_cmp[0:NCMP, g, :], cT[0:NCMP, :], start=True, stop=False)
            for branch, v in enumerate((s.v_sel, s.v_win)):
                pe.matmul(o[:, 0:SEQ], v[:, 0, d], pT[:, branch, :, :].rearrange("p i t -> p (i t)"), start=False, stop=False)
                ins = pe.matmul(o[:, A:B], v[:, 1, d], pT_last[:, branch, :], start=False, stop=(branch == 1))
            ins.then_inc(outs, 1)

        @block.tensor
        def _(pe):
            for n in range(NH + 3):
                if n < NH:
                    scores(pe, n)
                if 2 <= n < NH + 2:
                    turn(pe, n - 2)
                if n >= 3:
                    mix(pe, n - 3)

        def mask(dve, h):
            b = h % 3
            dve.wait_ge(expd, h + 1)
            dve.tensor_tensor(cs[b][:, :, 0:NCMP], cs[b][:, :, 0:NCMP], masks[:, :, 0:NCMP], ALU.mult).then_inc(vs, 1)

        def total(dve, h):
            b = h % 3
            dve.wait_ge(vs, 5 * h + 1)
            dve.tensor_reduce(c[b][:, 1, :, 0], cs[b][:, :, 0:NCMP], AX_X, ALU.add).then_inc(vs, 1)

        def guard(dve, h):
            dve.wait_ge(vs, 5 * h + 2)
            dve.tensor_scalar(flat(h, 1), flat(h, 1), 1e-30, None, ALU.max).then_inc(vs, 1)

        def inverse(dve, h):
            dve.wait_ge(vs, 5 * h + 3)
            dve.reciprocal(flat(h, 2), flat(h, 1)).then_inc(vs, 1)

        def gate(dve, h):
            dve.wait_ge(vs, 5 * h + 4)
            weight = c[h % 3][:, 2, :, :]
            dve.tensor_tensor(weight, weight, gates[:, :, 3 * h:3 * h + 3], ALU.mult).then_inc(vs, 1)

        def weigh(dve, h):
            b = h % 3
            dve.wait_ge(vs, 5 * h + 5)
            dve.tensor_tensor(cs[b][:, :, 0:NCMP], cs[b][:, :, 0:NCMP], over_last(c[b][:, 2, :, 0], NCMP), ALU.mult)
            dve.tensor_tensor(first[b][:, :, :], first[b][:, :, :], over_last(c[b][:, 2, 0, 1:3], A), ALU.mult)
            dve.tensor_tensor(second[b][:, :, :], second[b][:, :, :], over_last(c[b][:, 2, 1, 1:3], B), ALU.mult).then_inc(weighed, 1)

        def flat(h, kind):
            return c[h % 3][:, kind, :, :].rearrange("p i n -> p (i n)")

        def head(dve, h, last):
            steps = [mask, total, guard, inverse, gate, weigh] if last is not None else []
            between = lambda: steps and steps.pop(0)(dve, last)
            b = h % 3
            bank = 2 * (h % 2)
            dve.wait_ge(scored, h + 1)
            if h >= 3:
                dve.wait_ge(turned, h - 2)
            both = lambda ap, n: ap[:, 0:2 * n].rearrange("p (a n) -> p a n", a=2)
            dve.tensor_tensor(second[b][:, :, :], both(k.psum[:, bank, :], B), over_middle(s.bias[:, h, 0:B], 2),
                              ALU.add).then_inc(biased, 1)
            dve.tensor_tensor(first[b][:, :, :], both(k.psum[:, bank + 1, :], A), over_middle(s.bias[:, h, P:P + A], 2),
                              ALU.add).then_inc(biased, 1)
            between()
            for i in range(TILES):
                x = P * (TILES - 1 - i) + CMP_LEN - 1
                ins = dve.tensor_tensor(cs[b][:, i, 0:NCMP], k.psum[:, bank + 1, B + 16 * i:B + 16 * i + NCMP],
                                        s.bias[:, h, x:x + CMP_STRIDE * (NCMP - 1) + 1:CMP_STRIDE], ALU.add)
            ins.then_inc(biased, 1)
            between()
            dve.wait_ge(biased, 3 * h + 1)
            dve.tensor_reduce(c[b][:, 0, 1, 1:3], second[b][:, :, :], AX_X, ALU.max, negate=True).then_inc(negmax, 1)
            between()
            dve.wait_ge(biased, 3 * h + 2)
            dve.tensor_reduce(c[b][:, 0, 0, 1:3], first[b][:, :, :], AX_X, ALU.max, negate=True).then_inc(negmax, 1)
            between()
            dve.wait_ge(biased, 3 * h + 3)
            dve.tensor_reduce(c[b][:, 0, :, 0], cs[b][:, :, 0:NCMP], AX_X, ALU.max, negate=True).then_inc(negmax, 1)
            between()
            between()

        @block.vector
        def _(dve):
            def output(j):
                dve.wait_ge(high, j + 1)
                split_low(dve, k.xT.lo[:, j, :], k.psum[:, 6 + j % 2, 0:SEQ], k.xT.hi[:, j, :]).then_inc(written, 1)

            begin.lows(dve)
            dve.wait_ge(landed, 16)
            dve.wait_ge(k.bias_spread, 16)
            for n in range(NH + 1):
                if n < NH:
                    head(dve, n, n - 1 if n >= 1 else None)
                else:
                    for step in (mask, total, guard, inverse, gate, weigh):
                        step(dve, n - 1)
                if n >= 6 and n % 2 == 0:
                    output((n - 6) // 2)
            for j in range(NH // 2 - 2, NH // 2):
                output(j)

        @block.scalar
        def _(act):
            def exps(h):
                b = h % 3
                for i, scored_of, done in ((1, second, 1), (0, first, 2)):
                    act.wait_ge(negmax, 3 * h + done)
                    for branch in range(2):
                        act.activation(scored_of[b][:, branch, :], scored_of[b][:, branch, :], ACT.Exp,
                                       bias=c[b][:, 0, i, branch + 1:branch + 2], accum_out=c[b][:, 1, i, branch + 1:branch + 2])
                act.wait_ge(negmax, 3 * h + 3)
                for i in range(TILES):
                    ins = act.activation(cs[b][:, i, 0:NCMP], cs[b][:, i, 0:NCMP], ACT.Exp, bias=c[b][:, 0, i, 0:1])
                ins.then_inc(expd, 1)

            def copy(h):
                act.wait_ge(turned, h + 1)
                if h >= 1:
                    act.wait_ge(outs, h)
                flat = lambda ap: ap.rearrange("p a n -> p (a n)")
                act.activation(pT[:, :, :, :].rearrange("p a i n -> p (a i n)"), k.psum[:, 4, :], ACT.Copy).then_inc(copied, 1)
                act.activation(flat(pT_last[:, :, :]), k.psum[:, 5, 0:B], ACT.Copy).then_inc(copied, 1)
                act.activation(cT[0:NCMP, :], k.psum[0:NCMP, 5, B:2 * B], ACT.Copy).then_inc(copied, 1)

            def output(j):
                act.wait_ge(outs, 2 * (j + 1))
                split_high(act, k.xT.hi[:, j, :], k.psum[:, 6 + j % 2, 0:SEQ]).then_inc(high, 1)

            begin.highs(act)
            for n in range(NH + 2):
                if n >= 2:
                    copy(n - 2)
                if n < NH:
                    exps(n)
                if n >= 5 and n % 2 == 1:
                    output((n - 5) // 2)
            output(NH // 2 - 1)

        k.idle_pool(block)


def second_block(k):
    with ExitStack() as ctx:
        gains = k.sb(ctx, "norm_gain_bias", [P, 2, D])
        ctx.enter_context(k.lasting_splits())
        rows = k.sb(ctx, "bias_by_distance", [NH, DISTS])
        final_norm(k, rows)
        swiglu(k, gains, 0, rows)
        spatial_gating(k, gains)
        swiglu(k, gains, 2)
        s = SharedKV(k, ctx)
        shared_kv(k, s)
        swiglu(k, gains, 3)
        sparse_attention(k, s, gains)
        swiglu(k, gains, 5, final=True)


def column_panels(w, first=0):
    v = w.rearrange("(c p) n -> p c n", p=P)
    return lambda u: v[:, :, bass.ds(first + COLS * u, COLS)]


def row_slots(w, first=0):
    v = w.rearrange("(u r p) n -> u p r n", r=2, p=P)
    return lambda u: v[u, :, :, first:first + D]


def plan_weights(k):
    a, w = k.a, k.w
    w_in = a["w_in"][0]
    for first, n in ((0, 6), (1536, 2), (2056, 4), (3080, 2), (3592, 2)):
        w.add(n, column_panels(w_in, first))
    w.add(4, row_slots(a["w_out"][0]))
    w.add(4, column_panels(a["xa_wq"][0]))
    w.add(4, column_panels(a["xa_wkv"][0]))
    w.add(4, row_slots(a["xa_wkv"][0], D))
    w.add(4, row_slots(a["xa_wo"][0]))
    w.add(8, column_panels(a["peer_wq"][0]))
    def ffn(layer, which):
        w2 = a["ffn_w2_2"][layer, which].rearrange("(u r p) n -> u p r n", r=2, p=P)
        w1, w3 = (column_panels(a[n][layer, which]) for n in ("ffn_w1_2", "ffn_w3_2"))
        w.add(1, w1)
        w.add(1, w3)
        w.add(FFN_DIM // COLS - 1, lambda u: w1(u + 1), lambda u: w3(u + 1), lambda u: w2[u])
        w.add(1, lambda u: w2[u + FFN_DIM // COLS - 1])
    ffn(0, 0)
    w.add(8, column_panels(a["sgu_w_in_2"][0], SGU_HALF))
    w.add(8, column_panels(a["sgu_w_in_2"][0]))
    w.add(8, row_slots(a["sgu_w_out_2"][0]))
    ffn(0, 1)
    w.add(SLOTS_KV, column_panels(a["kv_w_2"]))
    for n in range(2):
        v = a["cmp_w1_2"][n].rearrange("(u j p) n -> u p j n", j=DC, p=P)
        w.add(2, lambda u, v=v: v[u])
    ffn(1, 0)
    w.add(4, column_panels(a["nsa_w_qg_2"][0]))
    w.add(4, row_slots(a["nsa_w_o_2"][0]))
    ffn(1, 1)



def mixer(k):
    a = k.a
    with ExitStack() as ctx:
        s = MixerState(k, ctx)
        with ExitStack() as inner:
            padded = k.sb(inner, "conv_input_T", [P, 20, 3 + SEQ])
            mixer_load(k, s, padded)
            inner.enter_context(k.lasting_splits())
            norm_transpose(k, [(k.x, k.xT, COL_MIX)])
            gates = [a["w_in"][0][:, lo:lo + 8].rearrange("(c p) n -> p c n", p=P) for lo in (2048, 4104)]
            items = []
            for n in range(6):
                items.append(("T", k.xT, padded[:, 2 * n:2 * n + 2, 3:], None, 1.0))
            for n in range(2):
                items.append(("N", k.xT, s.z[:, :, n * COLS:(n + 1) * COLS], None, 1.0))
            for n in range(4):
                items.append(("T", k.xT, padded[:, 12 + 2 * n:14 + 2 * n, 3:], None, 1.0))
            for buf in (s.mv, s.mo):
                for n in range(2):
                    items.append(("N", k.xT, buf[:, :, n * COLS:(n + 1) * COLS], None, 1.0))
            panels(k, items, (gates, k.xT, s.gates[:, :, :], None, 16),
                   Convolution(k, padded, s.conv, [0, 1, 2, 3, 4, 5, 8, 9, 10, 11]))
        s.more(k, ctx)
        normalise_and_gate(k, s)
        key_query_products(k, s)
        gdn_prepare(k, s)
        mlstm_prepare(k, s)
        recurrences(k, s)
        with ExitStack() as inner:
            inner.enter_context(k.lasting_splits())
            mixed = k.sb(inner, "mixed", [P, TILES, D])
            mixer_output(k, s, mixed, k.xT)
            rows_product(k, k.xT, 4, add_to(k, k.x))


def mixer_load(k, s, padded):
    with k.stage() as block:
        zeroed = k.sig.new()

        @block.sync
        def _(sp):
            sp.dma_start(s.consts[:, :, :], k.a["constants"].rearrange("p (c n) -> p c n", n=P)
                         ).then_inc(k.masks_landed, 16)
            k.stream(sp)

        @block.vector
        def _(dve):
            dve.memset(padded[:, :, 0:3], 0.0).then_inc(zeroed, 1)

        k.idle_pool(block)


def build(nc, a):
    with ExitStack() as ctx:
        k = Program(nc, ctx, a)
        plan_weights(k)
        load_parameters(k)
        mixer(k)
        cross_attention(k)
        peer(k)
        second_block(k)


_NAMES = ["x", "mem", "norm_mix_w", "w_in", "gdn_conv_w", "gdn_a_log", "gdn_dt_bias", "gdn_norm_w", "mlstm_conv_w",
          "mlstm_i_bias", "mlstm_f_bias", "mlstm_norm_w", "w_out", "norm_xa_w", "norm_mem_w", "xa_wq", "xa_wkv",
          "xa_wo", "norm_ffn_w", "peer_wq", "peer_sub_keys", "peer_u", "peer_v", "norm_final_w", "rel_table_2",
          "ln_g_2", "ln_b_2", "ffn_w1_2", "ffn_w3_2", "ffn_w2_2", "sgu_w_in_2", "sgu_ln_g_2", "sgu_ln_b_2",
          "sgu_w_s_2", "sgu_b_s_2", "sgu_w_out_2", "kv_w_2", "cmp_pe_2", "cmp_w1_2", "cmp_b1_2", "cmp_w2_2",
          "nsa_w_qg_2", "nsa_w_o_2"]


def kernel(**inputs):
    import concourse.bacc as bacc
    from concourse.bass_utils import run_bass_kernel_spmd

    nc = bacc.Bacc("TRN2", target_bir_lowering=False, num_devices=1)
    masks, buckets = constants()
    arrays = {f"in_{n}": np.ascontiguousarray(inputs[n]) for n in _NAMES}
    arrays["in_constants"] = masks
    arrays["in_bucket_onehot"] = buckets
    a = {n[3:]: nc.dram_tensor(n, v.shape, F32, kind="ExternalInput").ap() for n, v in arrays.items()}
    a["out"] = nc.dram_tensor("out_x", (1, SEQ, D), F32, kind="ExternalOutput").ap()
    a["bias_rows"] = nc.dram_tensor("bias_rows", (P, NH, DISTS), F32, kind="Internal").ap()
    build(nc, a)
    r = run_bass_kernel_spmd(nc, [arrays], core_ids=[0])
    return r.results[0]["out_x"]
```
